# Optimizing a Trainium2 kernel written in Bass

```python
import math
import jax, jax.numpy as jnp
from jax import lax
import numpy as np

D_MODEL = 1024
BATCH = 1
SEQ = 1024
DEPTH = 2
DEC_BATCH = 1
DEC_SEQ = 64
PAST_LEN = 128

CHUNK = 64
PLE_DIM = 256
ALPHA = (2 * DEPTH) ** 0.25
BETA = (8 * DEPTH) ** -0.25
NORM_EPS = 1e-5
A_WIDTH = D_MODEL // 2
A_BLOCKS = 8
A_BLOCK_DIM = A_WIDTH // A_BLOCKS
A_CONV = 4
A_C = 8.0
B_HEADS = 4
B_HEAD_DIM = 128
B_WIDTH = B_HEADS * B_HEAD_DIM
B_CONV = 4
C_HEAD_DIM = 64
C_WIDTH = D_MODEL // 2
C_HEADS = C_WIDTH // C_HEAD_DIM
C_DECAY_LORA = 64
C_AAA_LORA = 64
C_GATE_LORA = 128
C_LNX_EPS = 64e-5
C_PROJ = 3 * C_WIDTH + C_DECAY_LORA + C_AAA_LORA + C_GATE_LORA
D_HEADS = 4
D_Q_LORA = 384
D_KV_LORA = 256
D_NOPE = 128
D_ROPE = 64
D_V = 128
D_WIDTH = D_HEADS * D_V
D_PROJ = D_Q_LORA + D_KV_LORA + D_ROPE
MLA_SCALE = (D_NOPE + D_ROPE) ** -0.5
ROPE_THETA = 10000.0
Q_BLOCK = 128
D_FF = 2816
FFN_CONV = 3
IN0 = 2 * A_WIDTH + 4 * B_WIDTH + 2 * B_HEADS
IN1 = C_PROJ + D_PROJ

kernel_name = 'hybrid_streaming_encoder_step'

def split_cols(x, sizes):
    offs = np.cumsum(sizes)[:-1].tolist()
    return jnp.split(x, offs, axis=-1)

def layer_norm(x, g, b):
    xf = x.astype(jnp.float32)
    mu = jnp.mean(xf, -1, keepdims=True)
    var = jnp.mean(jnp.square(xf - mu), -1, keepdims=True)
    return ((xf - mu) * lax.rsqrt(var + NORM_EPS) * g + b).astype(x.dtype)

def rms_norm(x, g, eps=1e-6):
    xf = x.astype(jnp.float32)
    return (xf * lax.rsqrt(jnp.mean(xf * xf, -1, keepdims=True) + eps) * g).astype(x.dtype)

def l2norm(x, eps=1e-6):
    xf = x.astype(jnp.float32)
    return xf * lax.rsqrt(jnp.sum(xf * xf, -1, keepdims=True) + eps)

def causal_dwconv(x, buf, w, b=None):
    width = w.shape[0]
    length = x.shape[1]
    xp = jnp.concatenate([buf.astype(x.dtype), x], axis=1)
    y = xp[:, 0:length] * w[0]
    for j in range(1, width):
        y = y + xp[:, j:j + length] * w[j]
    if b is not None:
        y = y + b
    return y, xp[:, length:]

def linear_scan(a, b, h0):
    b = b.at[:, 0].add(a[:, 0] * h0)

    def combine(left, right):
        a_l, b_l = left
        a_r, b_r = right
        return a_l * a_r, a_r * b_l + b_r

    _, h = lax.associative_scan(combine, (a, b), axis=1)
    return h

def rope(x, pos):
    half = x.shape[-1] // 2
    inv = ROPE_THETA ** (-jnp.arange(half, dtype=jnp.float32) / half)
    ang = pos.astype(jnp.float32)[:, None] * inv[None, :]
    cos = jnp.cos(ang)[None, :, None, :].astype(x.dtype)
    sin = jnp.sin(ang)[None, :, None, :].astype(x.dtype)
    x1, x2 = x[..., :half], x[..., half:]
    return jnp.concatenate([x1 * cos - x2 * sin, x2 * cos + x1 * sin], axis=-1)

def rglru_mixer(gate_in, x_in, conv_buf, h0, conv_w, conv_b, w_r, b_r, w_i, b_i, lam):
    bsz, length, _ = x_in.shape
    xc, new_buf = causal_dwconv(x_in, conv_buf, conv_w, conv_b)
    xb = xc.reshape(bsz, length, A_BLOCKS, A_BLOCK_DIM)
    r = jax.nn.sigmoid(jnp.einsum('blhi,hij->blhj', xb, w_r).reshape(bsz, length, A_WIDTH) + b_r)
    i = jax.nn.sigmoid(jnp.einsum('blhi,hij->blhj', xb, w_i).reshape(bsz, length, A_WIDTH) + b_i)
    log_a = -A_C * r.astype(jnp.float32) * jax.nn.softplus(-lam.astype(jnp.float32))
    a = jnp.exp(log_a)
    u = jnp.sqrt(-jnp.expm1(2.0 * log_a)) * (i * xc).astype(jnp.float32)
    h = linear_scan(a, u, h0.astype(jnp.float32))
    out = h.astype(x_in.dtype) * jax.nn.gelu(gate_in)
    return out, new_buf, h[:, -1].astype(h0.dtype)

def gated_delta_rule(q, k, v, g, beta, s0, chunk):
    bsz, length, heads, dk = q.shape
    n = length // chunk

    def blocks(t):
        t = t.astype(jnp.float32).reshape((bsz, n, chunk, heads) + t.shape[3:])
        return jnp.moveaxis(t, 3, 1)

    q = blocks(q) * dk ** -0.5
    k, v, g, beta = blocks(k), blocks(v), blocks(g), blocks(beta)
    gc = jnp.cumsum(g, axis=-1)
    idx = jnp.arange(chunk)
    decay = jnp.exp(jnp.where(idx[:, None] >= idx[None, :], gc[..., :, None] - gc[..., None, :], -jnp.inf))
    kb = k * beta[..., None]
    lmat = jnp.where(idx[:, None] > idx[None, :], jnp.einsum('bhncd,bhnsd->bhncs', kb, k) * decay, 0.0)
    eye = jnp.eye(chunk, dtype=jnp.float32)
    tmat = lax.linalg.triangular_solve(lmat + eye, jnp.broadcast_to(eye, lmat.shape),
                                       left_side=True, lower=True, unit_diagonal=True)
    u = jnp.einsum('bhncs,bhnsd->bhncd', tmat, v * beta[..., None])
    w = jnp.einsum('bhncs,bhnsd->bhncd', tmat, kb * jnp.exp(gc)[..., None])
    qk = jnp.einsum('bhncd,bhnsd->bhncs', q, k) * decay
    q_in = q * jnp.exp(gc)[..., None]
    g_last = gc[..., -1]
    k_out = k * jnp.exp(g_last[..., None] - gc)[..., None]

    def step(s, xs):
        u_c, w_c, qk_c, q_c, k_c, gl_c = xs
        v_new = u_c - jnp.einsum('bhcd,bhde->bhce', w_c, s)
        o = jnp.einsum('bhcd,bhde->bhce', q_c, s) + jnp.einsum('bhcs,bhse->bhce', qk_c, v_new)
        s = s * jnp.exp(gl_c)[..., None, None] + jnp.einsum('bhcd,bhce->bhde', k_c, v_new)
        return s, o

    xs = tuple(jnp.moveaxis(t, 2, 0) for t in (u, w, qk, q_in, k_out, g_last))
    s, o = lax.scan(step, s0.astype(jnp.float32), xs)
    o = jnp.moveaxis(jnp.moveaxis(o, 0, 2), 1, 3).reshape(bsz, length, heads, v.shape[-1])
    return o, s

def gdn_mixer(qkv, z, beta_in, alpha_in, conv_buf, s0, chunk, conv_w, a_log, dt_bias, norm_g):
    bsz, length, _ = qkv.shape
    qkv, new_buf = causal_dwconv(qkv, conv_buf, conv_w)
    qkv = jax.nn.silu(qkv).reshape(bsz, length, 3, B_HEADS, B_HEAD_DIM)
    q, k, v = l2norm(qkv[:, :, 0]), l2norm(qkv[:, :, 1]), qkv[:, :, 2]
    beta = jax.nn.sigmoid(beta_in.astype(jnp.float32))
    g = -jnp.exp(a_log.astype(jnp.float32)) * jax.nn.softplus((alpha_in + dt_bias).astype(jnp.float32))
    o, s = gated_delta_rule(q, k, v, g, beta, s0, chunk)
    o = rms_norm(o, norm_g).astype(z.dtype) * jax.nn.silu(z.reshape(bsz, length, B_HEADS, B_HEAD_DIM))
    return o.reshape(bsz, length, B_WIDTH), new_buf, s.astype(s0.dtype)

def rwkv7_scan(r, w, k, v, a, b, s0):
    def step(s, xs):
        r_t, w_t, k_t, v_t, a_t, b_t = xs
        sa = jnp.einsum('bhvk,bhk->bhv', s, a_t)
        s = s * w_t[:, :, None, :] + sa[..., None] * b_t[:, :, None, :] + v_t[..., None] * k_t[:, :, None, :]
        return s, jnp.einsum('bhvk,bhk->bhv', s, r_t)

    xs = tuple(jnp.moveaxis(t, 1, 0) for t in (r, w, k, v, a, b))
    s, o = lax.scan(step, s0, xs)
    return jnp.moveaxis(o, 0, 1), s

def rwkv7_mixer(proj, shift_buf, s0, mu, w0, w2, a0, a2, g2, k_k, k_a, r_k, lnx_g, lnx_b):
    bsz, length, _ = proj.shape
    xp = jnp.concatenate([shift_buf.astype(proj.dtype), proj], axis=1)
    xs = proj + (xp[:, :length] - proj) * mu
    r, k, v, xw, xa, xg = split_cols(xs, (C_WIDTH, C_WIDTH, C_WIDTH, C_DECAY_LORA, C_AAA_LORA, C_GATE_LORA))
    w = -jax.nn.softplus(-(w0 + jnp.tanh(xw) @ w2)) - 0.5
    a = jax.nn.sigmoid(a0 + xa @ a2)
    g = jax.nn.sigmoid(xg) @ g2

    def heads(t):
        return t.astype(jnp.float32).reshape(bsz, length, C_HEADS, C_HEAD_DIM)

    kk = l2norm(heads(k * k_k))
    k = k * (1.0 + (a - 1.0) * k_a)
    rh, kh, vh, ah = heads(r), heads(k), heads(v), heads(a)
    decay = jnp.exp(-jnp.exp(heads(w)))
    o, s = rwkv7_scan(rh, decay, kh, vh, -kk, kk * ah, s0.astype(jnp.float32))
    mu_o = jnp.mean(o, -1, keepdims=True)
    var_o = jnp.mean(jnp.square(o - mu_o), -1, keepdims=True)
    o = ((o - mu_o) * lax.rsqrt(var_o + C_LNX_EPS)).reshape(bsz, length, C_WIDTH) * lnx_g + lnx_b
    o = o + (jnp.sum(rh * kh * r_k, -1, keepdims=True) * vh).reshape(bsz, length, C_WIDTH)
    return o.astype(proj.dtype) * g, xp[:, length:], s.astype(s0.dtype)

def mla_mixer(proj, ckv_cache, krope_cache, pos, qa_g, w_qb, kva_g, w_kvb):
    bsz, length, _ = proj.shape
    q_a, c_raw, kr_raw = split_cols(proj, (D_Q_LORA, D_KV_LORA, D_ROPE))
    q = (rms_norm(q_a, qa_g) @ w_qb).reshape(bsz, length, D_HEADS, D_NOPE + D_ROPE)
    q_nope = q[..., :D_NOPE]
    q_rope = rope(q[..., D_NOPE:], pos)
    c_new = rms_norm(c_raw, kva_g)
    kr_new = rope(kr_raw[:, :, None, :], pos)[:, :, 0]
    c_all = jnp.concatenate([ckv_cache.astype(c_new.dtype), c_new], axis=1)
    kr_all = jnp.concatenate([krope_cache.astype(kr_new.dtype), kr_new], axis=1)
    kv = (c_all @ w_kvb).reshape(bsz, c_all.shape[1], D_HEADS, D_NOPE + D_V)
    k_nope, v = kv[..., :D_NOPE], kv[..., D_NOPE:]
    k_chunk = jnp.arange(c_all.shape[1]) // CHUNK
    qb = min(Q_BLOCK, length)
    nb = length // qb

    def to_blocks(t):
        return jnp.moveaxis(t.reshape((bsz, nb, qb) + t.shape[2:]), 1, 0)

    def attend(blk):
        qn, qr, qp = blk
        s = (jnp.einsum('bqhd,bkhd->bhqk', qn, k_nope)
             + jnp.einsum('bqhr,bkr->bhqk', qr, kr_all)).astype(jnp.float32) * MLA_SCALE
        visible = k_chunk[None, :] <= (qp // CHUNK)[:, None]
        p = jax.nn.softmax(jnp.where(visible, s, -jnp.inf), axis=-1)
        return jnp.einsum('bhqk,bkhd->bqhd', p.astype(v.dtype), v)

    o = lax.map(attend, (to_blocks(q_nope), to_blocks(q_rope), pos.reshape(nb, qb)))
    o = jnp.moveaxis(o, 0, 1).reshape(bsz, length, D_WIDTH)
    return o, c_new, kr_new

def conv_ffn(x, buf, w_up, conv_w, conv_b, w_down):
    h, new_buf = causal_dwconv(x @ w_up, buf, conv_w, conv_b)
    gate, val = jnp.split(h, 2, axis=-1)
    return (jax.nn.silu(gate) * val) @ w_down, new_buf

def trunk(x, pe, pos, gdn_chunk, a_conv, a_h, b_conv, b_s, c_shift, c_s, d_ckv, d_krope, f_conv, params):
    (w_in0, a_conv_w, a_conv_b, a_w_r, a_b_r, a_w_i, a_b_i, a_lambda, b_conv_w, b_a_log, b_dt_bias,
     b_norm_g, w_out0, w_in1, c_mu, c_w0, c_w2, c_a0, c_a2, c_g2, c_k_k, c_k_a, c_r_k, c_lnx_g, c_lnx_b,
     d_qa_g, d_w_qb, d_kva_g, d_w_kvb, w_out1, ln_mix_g, ln_mix_b, ffn_w_up, ffn_conv_w, ffn_conv_b,
     ffn_w_down, ln_ffn_g, ln_ffn_b, ple_w_gate, ple_b_gate, ple_w_proj) = params
    f_new = []
    for i in range(DEPTH):
        if i % 2 == 0:
            a_gate, a_x, b_qkv, b_z, b_beta, b_alpha = split_cols(
                x @ w_in0, (A_WIDTH, A_WIDTH, 3 * B_WIDTH, B_WIDTH, B_HEADS, B_HEADS))
            a_out, a_conv, a_h = rglru_mixer(a_gate, a_x, a_conv, a_h, a_conv_w, a_conv_b,
                                             a_w_r, a_b_r, a_w_i, a_b_i, a_lambda)
            b_out, b_conv, b_s = gdn_mixer(b_qkv, b_z, b_beta, b_alpha, b_conv, b_s, gdn_chunk,
                                           b_conv_w, b_a_log, b_dt_bias, b_norm_g)
            mix = jnp.concatenate([a_out, b_out], axis=-1) @ w_out0
        else:
            c_in, d_in = split_cols(x @ w_in1, (C_PROJ, D_PROJ))
            c_out, c_shift, c_s = rwkv7_mixer(c_in, c_shift, c_s, c_mu, c_w0, c_w2, c_a0, c_a2, c_g2,
                                              c_k_k, c_k_a, c_r_k, c_lnx_g, c_lnx_b)
            d_out, d_ckv, d_krope = mla_mixer(d_in, d_ckv, d_krope, pos, d_qa_g, d_w_qb, d_kva_g, d_w_kvb)
            mix = jnp.concatenate([c_out, d_out], axis=-1) @ w_out1
        x = layer_norm(ALPHA * x + mix, ln_mix_g[i], ln_mix_b[i])
        f_out, f_buf = conv_ffn(x, f_conv[i], ffn_w_up[i], ffn_conv_w[i], ffn_conv_b[i], ffn_w_down[i])
        f_new.append(f_buf)
        x = layer_norm(ALPHA * x + f_out, ln_ffn_g[i], ln_ffn_b[i])
        x = x + jax.nn.sigmoid(x @ ple_w_gate[i] + ple_b_gate[i]) * (pe[i] @ ple_w_proj[i])
    return x, a_conv, a_h, b_conv, b_s, c_shift, c_s, d_ckv, d_krope, jnp.stack(f_new)

def setup_inputs(seed: int = 0) -> dict:
    key = jax.random.key(seed)
    keys = iter(jax.random.split(key, 96))

    def nrm(shape, scale):
        return scale * jax.random.normal(next(keys), shape, jnp.float32)

    def uni(shape, lo, hi):
        return jax.random.uniform(next(keys), shape, jnp.float32, lo, hi)

    def gain(shape):
        return 1.0 + nrm(shape, 0.02)

    a_base = uni((A_WIDTH,), 0.9, 0.999) ** (1.0 / A_C)
    a_lambda = jnp.log(a_base) - jnp.log1p(-a_base)
    dt0 = jnp.exp(uni((B_HEADS,), math.log(1e-3), math.log(1e-1)))
    b_dt_bias = dt0 + jnp.log(-jnp.expm1(-dt0))
    d = D_MODEL
    return {
        'x_prompt': nrm((BATCH, SEQ, d), 1.0),
        'x_sample': nrm((DEC_BATCH, DEC_SEQ, d), 1.0),
        'state_a_conv': nrm((DEC_BATCH, A_CONV - 1, A_WIDTH), 1.0),
        'state_a_h': nrm((DEC_BATCH, A_WIDTH), 0.5),
        'state_b_conv': nrm((DEC_BATCH, B_CONV - 1, 3 * B_WIDTH), 1.0),
        'state_b_s': nrm((DEC_BATCH, B_HEADS, B_HEAD_DIM, B_HEAD_DIM), 0.1),
        'state_c_shift': nrm((DEC_BATCH, 1, C_PROJ), 1.0),
        'state_c_s': nrm((DEC_BATCH, C_HEADS, C_HEAD_DIM, C_HEAD_DIM), 0.5),
        'cache_d_ckv': nrm((DEC_BATCH, PAST_LEN, D_KV_LORA), 1.0),
        'cache_d_krope': nrm((DEC_BATCH, PAST_LEN, D_ROPE), 1.0),
        'state_ffn_conv': nrm((DEPTH, DEC_BATCH, FFN_CONV - 1, 2 * D_FF), 1.0),
        'p_prompt': nrm((DEPTH, BATCH, SEQ, PLE_DIM), 1.0),
        'p_sample': nrm((DEPTH, DEC_BATCH, DEC_SEQ, PLE_DIM), 1.0),
        'w_in0': nrm((d, IN0), d ** -0.5),
        'a_conv_w': nrm((A_CONV, A_WIDTH), A_CONV ** -0.5),
        'a_conv_b': nrm((A_WIDTH,), 0.02),
        'a_w_r': nrm((A_BLOCKS, A_BLOCK_DIM, A_BLOCK_DIM), A_BLOCK_DIM ** -0.5),
        'a_b_r': nrm((A_WIDTH,), 0.02),
        'a_w_i': nrm((A_BLOCKS, A_BLOCK_DIM, A_BLOCK_DIM), A_BLOCK_DIM ** -0.5),
        'a_b_i': nrm((A_WIDTH,), 0.02),
        'a_lambda': a_lambda,
        'b_conv_w': nrm((B_CONV, 3 * B_WIDTH), B_CONV ** -0.5),
        'b_a_log': jnp.log(uni((B_HEADS,), 1.0, 16.0)),
        'b_dt_bias': b_dt_bias,
        'b_norm_g': gain((B_HEAD_DIM,)),
        'w_out0': nrm((A_WIDTH + B_WIDTH, d), BETA * (A_WIDTH + B_WIDTH) ** -0.5),
        'w_in1': nrm((d, IN1), d ** -0.5),
        'c_mu': uni((C_PROJ,), 0.0, 1.0),
        'c_w0': uni((C_WIDTH,), -6.0, -1.0),
        'c_w2': nrm((C_DECAY_LORA, C_WIDTH), 0.1),
        'c_a0': nrm((C_WIDTH,), 0.1),
        'c_a2': nrm((C_AAA_LORA, C_WIDTH), 0.1),
        'c_g2': nrm((C_GATE_LORA, C_WIDTH), C_GATE_LORA ** -0.5),
        'c_k_k': 0.85 + nrm((C_WIDTH,), 0.02),
        'c_k_a': gain((C_WIDTH,)),
        'c_r_k': nrm((C_HEADS, C_HEAD_DIM), 0.1),
        'c_lnx_g': gain((C_WIDTH,)),
        'c_lnx_b': nrm((C_WIDTH,), 0.02),
        'd_qa_g': gain((D_Q_LORA,)),
        'd_w_qb': nrm((D_Q_LORA, D_HEADS * (D_NOPE + D_ROPE)), D_Q_LORA ** -0.5),
        'd_kva_g': gain((D_KV_LORA,)),
        'd_w_kvb': nrm((D_KV_LORA, D_HEADS * (D_NOPE + D_V)), D_KV_LORA ** -0.5),
        'w_out1': nrm((C_WIDTH + D_WIDTH, d), BETA * (C_WIDTH + D_WIDTH) ** -0.5),
        'ln_mix_g': gain((DEPTH, d)),
        'ln_mix_b': nrm((DEPTH, d), 0.02),
        'ffn_w_up': nrm((DEPTH, d, 2 * D_FF), d ** -0.5),
        'ffn_conv_w': nrm((DEPTH, FFN_CONV, 2 * D_FF), FFN_CONV ** -0.5),
        'ffn_conv_b': nrm((DEPTH, 2 * D_FF), 0.02),
        'ffn_w_down': nrm((DEPTH, D_FF, d), BETA * D_FF ** -0.5),
        'ln_ffn_g': gain((DEPTH, d)),
        'ln_ffn_b': nrm((DEPTH, d), 0.02),
        'ple_w_gate': nrm((DEPTH, d, d), d ** -0.5),
        'ple_b_gate': nrm((DEPTH, d), 0.02),
        'ple_w_proj': nrm((DEPTH, PLE_DIM, d), PLE_DIM ** -0.5),
    }

def reference(x_prompt, x_sample, state_a_conv, state_a_h, state_b_conv, state_b_s, state_c_shift,
              state_c_s, cache_d_ckv, cache_d_krope, state_ffn_conv, p_prompt, p_sample,
              w_in0, a_conv_w, a_conv_b, a_w_r, a_b_r, a_w_i, a_b_i, a_lambda, b_conv_w, b_a_log,
              b_dt_bias, b_norm_g, w_out0, w_in1, c_mu, c_w0, c_w2, c_a0, c_a2, c_g2, c_k_k, c_k_a,
              c_r_k, c_lnx_g, c_lnx_b, d_qa_g, d_w_qb, d_kva_g, d_w_kvb, w_out1, ln_mix_g, ln_mix_b,
              ffn_w_up, ffn_conv_w, ffn_conv_b, ffn_w_down, ln_ffn_g, ln_ffn_b, ple_w_gate,
              ple_b_gate, ple_w_proj):
    params = (w_in0, a_conv_w, a_conv_b, a_w_r, a_b_r, a_w_i, a_b_i, a_lambda, b_conv_w, b_a_log,
              b_dt_bias, b_norm_g, w_out0, w_in1, c_mu, c_w0, c_w2, c_a0, c_a2, c_g2, c_k_k, c_k_a,
              c_r_k, c_lnx_g, c_lnx_b, d_qa_g, d_w_qb, d_kva_g, d_w_kvb, w_out1, ln_mix_g, ln_mix_b,
              ffn_w_up, ffn_conv_w, ffn_conv_b, ffn_w_down, ln_ffn_g, ln_ffn_b, ple_w_gate,
              ple_b_gate, ple_w_proj)
    dt = x_prompt.dtype
    bp, lp = x_prompt.shape[0], x_prompt.shape[1]
    (y_prompt, a_conv_p, a_h_p, b_conv_p, b_s_p, c_shift_p, c_s_p, ckv_p, krope_p, ffn_conv_p) = trunk(
        x_prompt, p_prompt, jnp.arange(lp), CHUNK,
        jnp.zeros((bp, A_CONV - 1, A_WIDTH), dt), jnp.zeros((bp, A_WIDTH), dt),
        jnp.zeros((bp, B_CONV - 1, 3 * B_WIDTH), dt), jnp.zeros((bp, B_HEADS, B_HEAD_DIM, B_HEAD_DIM), dt),
        jnp.zeros((bp, 1, C_PROJ), dt), jnp.zeros((bp, C_HEADS, C_HEAD_DIM, C_HEAD_DIM), dt),
        jnp.zeros((bp, 0, D_KV_LORA), dt), jnp.zeros((bp, 0, D_ROPE), dt),
        jnp.zeros((DEPTH, bp, FFN_CONV - 1, 2 * D_FF), dt), params)
    ls = x_sample.shape[1]
    past = cache_d_ckv.shape[1]
    (y_sample, a_conv_s, a_h_s, b_conv_s, b_s_s, c_shift_s, c_s_s, ckv_s, krope_s, ffn_conv_s) = trunk(
        x_sample, p_sample, past + jnp.arange(ls), ls,
        state_a_conv, state_a_h, state_b_conv, state_b_s, state_c_shift, state_c_s,
        cache_d_ckv, cache_d_krope, state_ffn_conv, params)
    return (y_prompt, y_sample, a_conv_p, a_conv_s, a_h_p, a_h_s, b_conv_p, b_conv_s, b_s_p, b_s_s,
            c_shift_p, c_shift_s, c_s_p, c_s_s, ckv_p, ckv_s, krope_p, krope_s, ffn_conv_p, ffn_conv_s)


_drawn_inputs = setup_inputs


def setup_inputs(seed=0):
    import zlib

    import numpy as np

    out = dict(_drawn_inputs(seed))
    spreads = {}
    factors = {'cache_d_ckv': 2.981,
     'cache_d_krope': 5.78,
     'a_b_r': 8.0,
     'a_b_i': 8.0,
     'b_norm_g': 8.0,
     'c_lnx_g': 8.0,
     'c_lnx_b': 8.0,
     'd_qa_g': 8.0,
     'ffn_conv_b': 6.739,
     'ple_b_gate': 8.0}
    for name, (base, spread) in spreads.items():
        noise = np.random.default_rng([zlib.crc32(name.encode()), seed]).standard_normal(out[name].shape)
        drawn = base * np.exp(spread * noise) if base else spread * noise
        out[name] = __import__('jax').numpy.asarray(drawn.astype(out[name].dtype))
    for name, factor in factors.items():
        out[name] = (out[name] * factor).astype(out[name].dtype)
    return out
```

```python
def _np():
    import numpy as np
    return np


def column_plan():
    names = [("a_conv_w0", 4), ("a_conv_w1", 4), ("a_conv_w2", 4), ("a_conv_w3", 4)]
    plan, at = {}, 0
    for name, n in [("conv0_w0", 16), ("conv0_w1", 16), ("conv0_w2", 16), ("conv0_w3", 16), ("conv0_b", 16),
                    ("a_b_r", 4), ("a_b_i", 4), ("a_lambda", 4), ("b_norm_g", 1), ("c_mu", 14), ("c_w0", 4), ("c_a0", 4),
                    ("c_k_k", 4), ("c_k_a", 4), ("c_r_k", 4), ("c_lnx_g", 4), ("c_lnx_b", 4), ("d_qa_g", 3), ("d_kva_g", 2)]:
        plan[name] = at
        at += n
    for layer in range(2):
        for name, n in [("ffn_w0", 44), ("ffn_w1", 44), ("ffn_w2", 44), ("ffn_b", 44), ("ln_mix_g", 8), ("ln_mix_b", 8),
                        ("ln_ffn_g", 8), ("ln_ffn_b", 8), ("ple_b", 8)]:
            plan[name + str(layer)] = at
            at += n
    return plan, at


def small_plan():
    plan, at = {}, 0
    for name, n in [("identity", 128), ("ones", 128), ("pair_ones", 128), ("upper", 128), ("level", 7 * 128), ("half_swap", 128),
                    ("pair_upper", 64), ("pair_strict", 64), ("pair_identity", 64),
                    ("w_beta_alpha", 64), ("dt_bias", 36), ("a_log", 36),
                    ("hist_conv0", 48), ("h0", 4), ("hist_shift", 14), ("hist_ffn", 2 * 88)]:
        plan[name] = at
        at += n
    return plan, at


def out_plan():
    plan, at = {}, 0
    for name, n in [("conv0", 16 * 6), ("h", 8), ("shift", 28), ("ffn", 2 * 44 * 4)]:
        plan[name] = at
        at += n
    return plan, at


S0, P0, NT = 4, 72, 1096


def lay_out(inp):
    np = _np()
    f32 = np.float32
    a = {k: np.asarray(v) for k, v in inp.items()}

    def tokens(sample, prompt):
        n = sample.shape[1]
        t = np.zeros((n, NT), f32)
        t[:, S0:S0 + 64] = sample.T
        t[:, P0:] = prompt.T
        return np.ascontiguousarray(t.reshape(n // 128, 128, NT).transpose(1, 0, 2))

    def unit(w):
        k, m = w.shape
        u = w.reshape(k // 128, 128, m // 128, 128).transpose(1, 2, 0, 3).reshape(128, -1)
        out = np.zeros((128, 1024), f32)
        out[:, :u.shape[1]] = u
        return out

    units = []

    def full(w):
        for m in range(w.shape[1] // 128):
            units.append(unit(w[:, m * 128:(m + 1) * 128]))

    def ffn(layer):
        up, down = a["ffn_w_up"][layer], a["ffn_w_down"][layer]

        def ups(g):
            for f in (2 * g, 2 * g + 1, 22 + 2 * g, 23 + 2 * g):
                units.append(unit(up[:, f * 128:(f + 1) * 128]))

        def downs(g):
            for d in range(2):
                units.append(unit(down[g * 256:(g + 1) * 256, d * 512:(d + 1) * 512]))
        ups(0)
        for g in range(1, 11):
            ups(g)
            downs(g - 1)
        downs(10)

    def ple(layer):
        for d in range(2):
            units.append(unit(a["ple_w_proj"][layer][:, d * 512:(d + 1) * 512]))
        full(a["ple_w_gate"][layer])

    full(a["w_in0"][:, :3072])
    full(a["w_out0"])
    ffn(0)
    ple(0)
    w1 = a["w_in1"]
    full(w1[:, :1792])
    full(w1[:, 1792:2432])
    full(np.concatenate([w1[:, 2432:2496], w1[:, 2432:2496]], 1))
    qb = a["d_w_qb"]
    cols = [qb[:, h * 192:h * 192 + 128] for h in range(4)]
    cols += [np.concatenate([qb[:, h * 192 + 128:(h + 1) * 192] for h in (2 * r, 2 * r + 1)], 1) for r in range(2)]
    for m in range(0, 6, 2):
        units.append(unit(np.concatenate(cols[m:m + 2], 1)))
    kvb = a["d_w_kvb"]
    for m in range(0, 4, 2):
        units.append(unit(np.concatenate([kvb[:, h * 256:h * 256 + 128] for h in (m, m + 1)], 1)))
    v = np.concatenate([kvb[:, h * 256 + 128:(h + 1) * 256] for h in range(4)], 1)
    units.append(np.ascontiguousarray(v.reshape(2, 128, 512).transpose(1, 0, 2).reshape(128, 1024)))
    full(a["w_out1"])
    ffn(1)
    ple(1)

    def col(v):
        return np.asarray(v).reshape(-1, 128).T

    cp, ncol = column_plan()
    columns = np.zeros((128, ncol), f32)

    def put(name, v):
        c = col(v)
        columns[:, cp[name]:cp[name] + c.shape[1]] = c
    for j in range(4):
        put("conv0_w%d" % j, np.concatenate([a["a_conv_w"][j], a["b_conv_w"][j]]))
    put("conv0_b", a["a_conv_b"])
    for n in ("a_b_r", "a_b_i", "a_lambda", "b_norm_g", "c_mu", "c_w0", "c_a0", "c_k_k", "c_k_a", "c_r_k", "c_lnx_g",
              "c_lnx_b", "d_qa_g", "d_kva_g"):
        put(n, a[n])
    for i in range(2):
        for j in range(3):
            put("ffn_w%d%d" % (j, i), a["ffn_conv_w"][i][j])
        put("ffn_b%d" % i, a["ffn_conv_b"][i])
        put("ln_mix_g%d" % i, a["ln_mix_g"][i])
        put("ln_mix_b%d" % i, a["ln_mix_b"][i])
        put("ln_ffn_g%d" % i, a["ln_ffn_g"][i])
        put("ln_ffn_b%d" % i, a["ln_ffn_b"][i])
        put("ple_b%d" % i, a["ple_b_gate"][i])

    sp, nsmall = small_plan()
    small = np.zeros((128, nsmall), f32)

    def sput(name, v):
        v = np.asarray(v).reshape(128, -1)
        small[:, sp[name]:sp[name] + v.shape[1]] = v
    t = np.arange(128)
    same_half = (t[:, None] // 64) == (t[None, :] // 64)
    sput("identity", np.eye(128, dtype=f32))
    sput("ones", np.ones((128, 128), f32))
    sput("pair_ones", same_half.astype(f32))
    sput("upper", (t[:, None] <= t[None, :]).astype(f32))
    sput("level", np.stack([((t[:, None] // m) % 2 == 1) & (t[None, :] // m == t[:, None] // m - 1)
                            for m in (1, 2, 4, 8, 16, 32, 64)], 1).astype(f32))
    swap = np.zeros((128, 128), f32)
    swap[(t // 64) * 64 + (t % 64 + 32) % 64, t] = 1
    sput("half_swap", swap)
    sput("pair_upper", (t[:, None] % 64 <= np.arange(64)[None, :]).astype(f32))
    sput("pair_strict", (t[:, None] % 64 < np.arange(64)[None, :]).astype(f32))
    sput("pair_identity", (t[:, None] % 64 == np.arange(64)[None, :]).astype(f32))
    sput("w_beta_alpha", a["w_in0"][:, 3072:3080].reshape(8, 128, 8).transpose(1, 0, 2))
    w_gates = np.zeros((128, 2, 4, 128), f32)
    for g, key in enumerate(("a_w_r", "a_w_i")):
        for b in range(8):
            h = (b % 2) * 64
            w_gates[h:h + 64, g, b // 2, h:h + 64] = a[key][b]
    sput("dt_bias", np.broadcast_to(a["b_dt_bias"], (128, 9, 4)))
    sput("a_log", np.broadcast_to(a["b_a_log"], (128, 9, 4)))
    hist = np.concatenate([a["state_a_conv"][0], a["state_b_conv"][0]], 1)
    sput("hist_conv0", hist.reshape(3, 16, 128).transpose(2, 1, 0))
    sput("h0", a["state_a_h"].reshape(4, 128).T)
    sput("hist_shift", a["state_c_shift"].reshape(14, 128).T)
    sput("hist_ffn", a["state_ffn_conv"][:, 0].reshape(2, 2, 44, 128).transpose(3, 0, 2, 1))

    inv = (f32(10000.0) ** (-np.arange(32, dtype=f32) / f32(32))).astype(f32)
    pos = np.zeros(NT, f32)
    pos[S0:S0 + 64] = 128 + np.arange(64)
    pos[P0:] = np.arange(1024)
    ang = (pos[:, None] * inv[None, :]).astype(f32)
    cos, sin = np.cos(ang).T.astype(f32), np.sin(ang).T.astype(f32)
    rope = np.stack([np.concatenate([cos] * 4, 0), np.concatenate([-sin, sin] * 2, 0)], 1)
    ckv = a["cache_d_ckv"][0].T.reshape(2, 128, 128).transpose(1, 0, 2)
    kr = np.concatenate([a["cache_d_krope"][0].T] * 2, 0)
    return {
        "x": tokens(a["x_sample"][0], a["x_prompt"][0]),
        "p": np.stack([tokens(a["p_sample"][i, 0], a["p_prompt"][i, 0]) for i in range(2)]),
        "units": np.stack(units), "columns": columns, "small": small,
        "w_gates": w_gates, "w_lora": np.stack([np.concatenate([a["c_w2"], a["c_a2"]], 0), a["c_g2"]], 1),
        "s_b": np.ascontiguousarray(a["state_b_s"][0].transpose(1, 0, 2)),
        "s_c": np.ascontiguousarray(a["state_c_s"][0].reshape(4, 2, 64, 64).transpose(1, 3, 0, 2).reshape(128, 4, 64)),
        "rope": np.ascontiguousarray(rope), "cache_ckv": np.ascontiguousarray(ckv), "cache_krope": kr,
    }


def outputs():
    _, n = out_plan()
    return {"y": (128, 8, NT), "kept": (128, n), "s_b_p": (128, 4, 128), "s_b_s": (128, 4, 128),
            "s_c_p": (128, 4, 64), "s_c_s": (128, 4, 64), "ckv": (128, 2, NT), "krope": (64, NT)}


def gather(r):
    np = _np()
    op, _ = out_plan()

    def rows(v, at, n):
        return np.ascontiguousarray(v[:, :, at:at + n].transpose(2, 1, 0).reshape(1, n, -1))

    def kept(name, tiles, each):
        return r["kept"][:, op[name]:op[name] + tiles * each].reshape(128, tiles, each)
    y, ckv = r["y"], r["ckv"]
    conv, h, shift = kept("conv0", 16, 6), kept("h", 4, 2), kept("shift", 14, 2)
    f = kept("ffn", 88, 4)
    out = [rows(y, P0, 1024), rows(y, S0, 64)]
    for at in (3, 0):
        out.append(rows(conv[:, 0:4], at, 3))
    for at in (1, 0):
        out.append(rows(h, at, 1)[0])
    for at in (3, 0):
        out.append(rows(conv[:, 4:16], at, 3))
    for n in ("s_b_p", "s_b_s"):
        out.append(np.ascontiguousarray(r[n].transpose(1, 0, 2))[None])
    for at in (1, 0):
        out.append(rows(shift, at, 1))
    for n in ("s_c_p", "s_c_s"):
        out.append(np.ascontiguousarray(r[n].reshape(2, 64, 4, 64).transpose(2, 0, 3, 1).reshape(1, 8, 64, 64)))
    out += [rows(ckv, P0, 1024), rows(ckv, S0, 64)]
    kr = r["krope"][:, None, :]
    out += [rows(kr, P0, 1024), rows(kr, S0, 64)]
    for at in (2, 0):
        out.append(np.stack([rows(f[:, i * 44:(i + 1) * 44], at, 2) for i in range(2)]))
    return tuple(out)


def build(nc, io, NU):
    import concourse.bass as bass
    from concourse import mybir
    from contextlib import ExitStack

    F32, F32R = mybir.dt.float32, mybir.dt.float32r
    ACT, ALU, AX = mybir.ActivationFunctionType, mybir.AluOpType, mybir.AxisListType
    ds = bass.ds
    NB, BW = 4, NT // 4
    TILE = NT * 4
    cp, NCOL = column_plan()
    sp_, NSMALL = small_plan()
    op, NKEPT = out_plan()
    PROMPT_TILES = 8
    SAMPLE = PROMPT_TILES
    ALPHA = 4.0 ** 0.25

    ctx = ExitStack()
    with ctx:
        def sb(name, shape, dt=F32):
            return ctx.enter_context(nc.sbuf_tensor(name, shape, dt))

        def sem(name):
            return ctx.enter_context(nc.semaphore(name))

        RAW = sb("RAW", [128, 2, 1024])
        WHI = sb("WHI", [128, 2, 1024], F32R)
        WLO = sb("WLO", [128, 2, 1024], F32R)
        COL = sb("COL", [128, NCOL])
        SMALL = sb("SMALL", [128, NSMALL])
        KEPT = sb("KEPT", [128, NKEPT])
        EPS = sb("EPS", [128, 4])
        WBAH, WBAL = sb("WBAH", [128, 64], F32R), sb("WBAL", [128, 64], F32R)
        BETA36, GTMP, GB = sb("BETA36", [128, 36]), sb("GTMP", [128, 3, 36]), sb("GB", [128, 36])
        GC, EGC, NBEG = sb("GC", [128, 36]), sb("EGC", [128, 36]), sb("NBEG", [128, 36])
        LAM = sb("LAM", [128, 16])
        KOC = [sb("KOC%d" % p, [128, 4]) for p in range(2)]
        base = -(-nc.sbuf_base // 32) * 32
        SLAB = (nc.sbuf_usable_end - base) // 32 * 32
        PS = ctx.enter_context(nc.psum_tensor("PS", [128, 8, 512], F32))

        def at(name, shape, offset, dt=F32):
            assert offset % 32 == 0
            n = 4
            for x in shape[1:]:
                n *= x
            assert offset + n <= SLAB, (name, offset + n, SLAB)
            return nc.alloc_sbuf_tensor_at(name, shape, dt, offset=base + offset)

        XH = at("XH", [128, 8, NT], 0, F32R)
        XL = at("XL", [128, 8, NT], 8 * TILE, F32R)
        AR = 16 * TILE
        X32 = at("X32", [128, 8, NT], AR)
        XCQ = at("XCQ", [128, 16, NT], AR)
        U0 = at("U0", [128, 2, NT], AR + 16 * TILE)
        RGW = at("RGW", [128, 2, 4, 128], AR + 16 * TILE)
        MIX = [at("MIX%d" % n, [128, NT], AR + (18 + n) * TILE) for n in range(5)]
        OT = at("OT", [128, 4, NT], AR)

        SET = 4 * 128 * 4
        SETS = [[AR + 16 * TILE + n * SET for n in range(14)],
                [4 * TILE + n * SET for n in range(8)] + [12 * TILE + n * SET for n in range(6)]]

        def pair(name, n):
            return [at("%s%d" % (name, p), [128, 4, 128], SETS[p][n]) for p in range(2)]

        KT, QT, VT, DA, DB, EG, LM = [pair(x, n) for n, x in enumerate(("KT", "QT", "VT", "DA", "DB", "EG", "LM"))]
        TA, TT, WW, VB, KO, RR, VN = [pair(x, 7 + n) for n, x in enumerate(("TA", "TT", "WW", "VB", "KO", "RR", "VN"))]
        SP, SS = at("SP", [128, 4, 128], AR + 16 * TILE + 14 * SET), at("SS", [128, 4, 128], AR + 16 * TILE + 15 * SET)
        RN = [at("RN%d" % n, [128, NT], AR + (18 + n) * TILE) for n in range(4)]

        ZT = at("ZT", [128, 4, NT], AR + 4 * TILE)
        Y = at("Y", [128, 8, NT], AR)
        XR = at("XR", [128, 8, NT], AR + 8 * TILE)
        CB = at("CB", [128, 4, NT], AR + 8 * TILE)
        UF = at("UF", [128, 2, NT], AR + 12 * TILE)
        HH, HL = at("HH", [128, 2, NT], AR + 14 * TILE, F32R), at("HL", [128, 2, NT], AR + 16 * TILE, F32R)
        PP = at("PP", [128, 8, NT], AR + 8 * TILE)
        P32 = at("P32", [128, 2, NT], AR + 16 * TILE)
        PH, PL = at("PH", [128, 2, NT], AR + 18 * TILE, F32R), at("PL", [128, 2, NT], AR + 20 * TILE, F32R)
        SQ = [at("SQ%d" % n, [128, NT], AR + (16 + n) * TILE) for n in range(2)]
        SG = [at("SG%d" % n, [128, NT], AR + (16 + n) * TILE) for n in range(2)]
        RS = at("RS", [128, NT], AR + 22 * TILE)

        NK = NT + 128
        KW = NK // 4
        QA, CR = at("QA", [128, 3, NT], AR), at("CR", [128, 2, NT], AR + 3 * TILE)
        KRW = at("KRW", [128, NT], AR + 5 * TILE)
        U1 = at("U1", [128, 2, NT], AR + 6 * TILE)
        DX = at("DX", [128, 2, NT], AR + 8 * TILE)
        SQD = [at("SQD%d" % n, [128, NT], AR + (6 + n) * TILE) for n in range(2)]
        RSD = [at("RSD%d" % n, [128, NT], AR + (8 + n) * TILE) for n in range(2)]
        ROPE = at("ROPE", [128, 2, NT], AR + 10 * TILE)
        QAH, QAL = at("QAH", [128, 3, NT], AR + 12 * TILE, F32R), at("QAL", [128, 3, NT], AR + 15 * TILE, F32R)
        CH, CL = at("CH", [128, 2, NK], AR + 18 * TILE, F32R), at("CL", [128, 2, NK], AR + 18 * TILE + 8 * NK, F32R)
        CCK = at("CCK", [128, 2, 128], AR + 18 * TILE + 16 * NK)
        KRR = at("KRR", [128, NK], 0)
        QR = at("QR", [128, 2, NT], 4 * NK)
        QN = at("QN", [128, 4, NT], 8 * TILE)
        TK = at("TK", [128, NT], 8 * TILE)
        TQ = [at("TQ%d" % n, [128, NT], AR + (12 + n) * TILE) for n in range(2)]
        KN = at("KN", [128, 4, NK], AR)
        VTOK = at("VTOK", [128, 10, 512], AR + 16 * NK)
        QS, QRS = at("QS", [128, 2, NT], AR + 12 * TILE), at("QRS", [128, NT], AR + 14 * TILE)
        PB = at("PB", [128, 2, 1024], AR + 15 * TILE)
        PTB = at("PTB", [128, 1024], AR + 15 * TILE + 8192)
        OB = at("OB", [128, 2, 128], AR + 15 * TILE + 12288)
        AST = [at("AST%d" % n, [128, 4], AR + 15 * TILE + 13312 + 32 * n) for n in range(2)]

        place = [AR]

        def room(name, shape, dt=F32):
            t, n = at(name, shape, place[0], dt), 4
            for x in shape[1:]:
                n *= x
            place[0] += -(-n // 32) * 32
            return t

        def take(name):
            return room(name, [128, 4, 128])

        CIN = room("CIN", [128, 14, 128])
        LORA = room("LORA", [128, 2, 512])
        CUM, SA, CG, KKN, K2, BK, BONUS, CT, CO = [take(x) for x in (
            "CUM", "SA", "CG", "KKN", "K2", "BK", "BONUS", "CT", "CO")]
        TW, SX = room("TW", [128, 128]), room("SX", [128, 128])
        RUN = room("RUN", [128, 512])
        MS = [room("MS%d" % n, [128, 4, 64]) for n in range(2)]
        MB = take("MB")

        def both(name, width):
            return [room("%s%d" % (name, p), [128, 4, width]) for p in range(2)]

        A_B, B_B, K_B, V_B, LM_B, W_B, TA_B, AK_B, BT_B, KT_B, VT_B = [both(x, 128) for x in (
            "A_B", "B_B", "K_B", "V_B", "LM_B", "W_B", "TA_B", "AK_B", "BT_B", "KT_B", "VT_B")]
        A_S, B_S, R_S, PI_S, TT_S, W_S, RB_S, RK_S, V_S = [both(x, 64) for x in (
            "A_S", "B_S", "R_S", "PI_S", "TT_S", "W_S", "RB_S", "RK_S", "V_S")]
        PX = both("PX", 65)
        TT_B, U_B, X_S, U_S = V_B, K_B, W_S, B_S
        ZEROED = [x[p] for x in (A_B, B_B, K_B, V_B, LM_B, W_B, AK_B, BT_B, KT_B, VT_B) for p in range(2)] + [MB]

        def small(name, n, first=0):
            return SMALL[:, sp_[name] + first:sp_[name] + first + n]

        IDENT, ONES, UPPER = small("identity", 128), small("ones", 128), small("upper", 128)

        def col(name, j=0):
            return COL[:, cp[name] + j:cp[name] + j + 1]

        def col_at(name, j):
            return COL[:, ds(cp[name] + j, 1)]

        BETA = BETA36[:, :].rearrange("p (c h) -> p c h", h=4)
        PSBA = PS[:, 7, 0:72].rearrange("p (c j) -> p c j", j=8)

        def col4(name):
            return COL[:, cp[name]:cp[name] + 4]

        GATE = nc.dram_tensor("gate_rows", [4, 128, NT], F32).ap()
        XROW = nc.dram_tensor("x_rows", [128, 8, NT], F32).ap()
        CROW = nc.dram_tensor("c_rows", [14, 128, NT], F32).ap()
        ZROW = nc.dram_tensor("z_rows", [4, 128, NT], F32).ap()

        params_in, x_in = sem("params_in"), sem("x_in")
        raw_in = [sem("raw_in0"), sem("raw_in1")]
        hi_split, unit_split = sem("hi_split"), sem("unit_split")
        unit_done, part_done = sem("unit_done"), sem("part_done")
        slot_act, slot_dve = sem("slot_act"), sem("slot_dve")
        xh_ready, xl_ready = sem("xh_ready"), sem("xl_ready")
        row_out = [sem("row_out0"), sem("row_out1")]
        conv_done = sem("conv_done")
        dve_step, act_step = sem("dve_step"), sem("act_step")
        ba_done, ba_copied = sem("ba_done"), sem("ba_copied")
        eps_set = sem("eps_set")
        ba_split, g_ready, ba_act, ba_vec = sem("ba_split"), sem("g_ready"), sem("ba_act"), sem("ba_vec")
        rg_done, rg_read, rg_vec, rg_act = sem("rg_done"), sem("rg_read"), sem("rg_vec"), sem("rg_act")
        silu_done, lam_vec, lam_act, gate_in = sem("silu_done"), sem("lam_vec"), sem("lam_act"), sem("gate_in")
        gates_in, kept_ready = sem("gates_in"), sem("kept_ready")
        outs_done = sem("outs_done")

        sq_ready, norm_sum, norm_root, norm_done = sem("sq_ready"), sem("norm_sum"), sem("norm_root"), sem("norm_done")
        gdn_staged, pad_zeroed, state_in = sem("gdn_staged"), sem("pad_zeroed"), sem("state_in")
        gdn_pe = [sem("gdn_pe%d" % p) for p in range(2)]
        gdn_dve = [sem("gdn_dve%d" % p) for p in range(2)]
        gdn_act = [sem("gdn_act%d" % p) for p in range(2)]
        state_out = sem("state_out")
        o_zeroed, z_in, o_square, o_sum, o_root, o_gated = [sem(x) for x in ("o_zeroed", "z_in", "o_square", "o_sum", "o_root", "o_gated")]
        mix_ready = [sem("mix_ready%d" % l) for l in range(2)]

        x_back, out_read, up_read, down_read = sem("x_back"), sem("out_read"), sem("up_read"), sem("down_read")
        ffn_conv, ffn_silu, ffn_mul, h_hi, h_done = [sem(x) for x in ("ffn_conv", "ffn_silu", "ffn_mul", "h_hi", "h_done")]
        p_in, p_hi, p_split, wp_read = sem("p_in"), sem("p_hi"), sem("p_split"), sem("wp_read")
        gate_read, gate_added, gaps_zeroed = sem("gate_read"), sem("gate_added"), sem("gaps_zeroed")
        ln_mean, ln_sub, ln_sq, ln_var = sem("ln_mean"), sem("ln_sub"), sem("ln_sq"), sem("ln_var")
        ln_root, ln_scaled, ln_hi, ln_lo = sem("ln_root"), sem("ln_scaled"), sem("ln_hi"), sem("ln_lo")
        LN_LO = (0, 16, 24, 40, 48)
        in_ready = sem("in_ready")
        in1_read, shifted, row1_out = sem("in1_read"), sem("shifted"), [sem("row1_out0"), sem("row1_out1")]
        mla_in, cache_in, kr_cache_in = sem("mla_in"), sem("cache_in"), sem("kr_cache_in")
        m_square, m_sum, m_root, m_inv = sem("m_square"), sem("m_sum"), sem("m_root"), sem("m_inv")
        m_scaled, m_hi, m_lo, c_out = sem("m_scaled"), sem("m_hi"), sem("m_lo"), sem("c_out")
        swapped, kr_done, kr_out, qkv_read = sem("swapped"), sem("kr_done"), sem("kr_out"), sem("qkv_read")
        q_rotated, v_done, v_read = sem("q_rotated"), sem("v_done"), sem("v_read")
        a_scores, a_max, a_probs, a_turned, a_keys, a_keys2 = [sem("a_" + x) for x in (
            "scores", "max", "probs", "turned", "keys", "keys2")]
        a_out, a_inv, a_scaled, a_back, a_hi, q_staged = [sem("a_" + x) for x in (
            "out", "inv", "scaled", "back", "hi", "staged")]
        c_ready, c_in, lora_in, c_state_in, c_state_out = [sem(x) for x in (
            "c_ready", "c_in", "lora_in", "c_state_in", "c_state_out")]
        c_pe, c_act, c_dve, c_pool = sem("c_pe"), sem("c_act"), sem("c_dve"), sem("c_pool")
        x_hi, x_lo, x_out, y_out = sem("x_hi"), sem("x_lo"), sem("x_out"), sem("y_out")

        OUT_UNIT, OUT_PART = (24, 108 + 26), (0, 72 + 5)

        def up_unit(l, g):
            return OUT_UNIT[l] + 8 + 6 * g - 2

        def down_unit(l, g):
            return OUT_UNIT[l] + 8 + 6 * g + 8

        class Stages:

            def __init__(self, *names):
                self.index = {n: k + 1 for k, n in enumerate(names)}
                self.count = len(names)

            def at(self, i, name):
                return i * self.count + self.index[name] + 1

            def before(self, i):
                return i * self.count + 1

        LEVELS = 7
        G_PE = Stages("rows", "gram", "qk", "k_turned", "v_turned", "m_turned",
                      *[x + str(l) for l in range(1, 7) for x in ("w", "tt", "ta")][:-1], "ks", "v_new", "o", "s")
        G_DVE = Stages("decayed", "diff", "lower", "qk", "q_in", "m0", "t0", "m1",
                       *[x for l in range(1, 6) for x in ("tt%d" % l, "ta%d" % l, "m%d" % (l + 1))], "tt6", "r", "s")

        def level_mask(l):
            return small("level", 128, 128 * l)
        G_ACT = Stages("staged", "exps", "ko", "vb", *["w%d" % l for l in range(1, 7)], "v_new", "out")

        def heads_of(x):
            if x.shape[1] == 4:
                return x.unsqueeze(2).to_broadcast([128, 4, 128])
            return x.unsqueeze(1).to_broadcast([128, 4, 128])

        def per_head(bank):
            return PS[:, bank, :].rearrange("p (h n) -> p h n", h=4)

        class Steps:

            def __init__(self, eng, s):
                self.eng, self.sem, self.n, self.i, self.per = eng, s, 0, None, 0

            def value(self):
                return self.n if self.i is None else self.i * self.per + self.n

            def __call__(self, instruction):
                instruction.then_inc(self.sem, 1)
                self.n += 1
                self.eng.wait_ge(self.sem, self.value())

            def enter(self, i, per):
                self.i, self.per, self.start = i, per, self.n

            def leave(self, count):
                assert self.n - self.start == self.per, (self.n - self.start, self.per)
                self.n, self.i = self.start + self.per * count, None

        def banks(slot, width=BW):
            return PS[:, 4 * slot:4 * slot + 4, 0:width]

        def rows(x, width=BW):
            return x.rearrange("p (b n) -> p b n", n=width)

        class ChunkStages:

            def __init__(self, names):
                self.index = {n: k + 1 for k, n in enumerate(names(2))}
                self.last = {n: k + 1 for k, n in enumerate(names(1))}
                self.count = len(self.index)

            def at(self, i, name, p=""):
                return 8 * self.count + self.last[name + str(p)] if i is LAST else i * self.count + self.index[name + str(p)]

        LAST = "the sample"
        C_LEVELS = range(1, 6)

        def over(n, *names):
            return [x + str(p) for p in range(n) for x in names]

        def by_level(n, names):
            return [x + str(l) + str(p) for l in C_LEVELS for p in range(n) for x in names(l)]

        C_PE = ChunkStages(lambda n: ["w", "a", "g", "norm", "bonus"] + over(n, "l", "rb", "kt", "mt", "vt")
                           + by_level(n, lambda l: ("lw", "tt", "ta")[:3 - (l == 5)]) + over(n, "x", "u", "m", "o")
                           + ["mean", "var"])
        C_ACT = ChunkStages(lambda n: ["tanh", "sx", "c", "a", "g", "square", "ln", "inv"]
                            + over(n, "px", "pi", "bt", "kt", "vs", "vt")
                            + by_level(n, lambda l: ("ws", "wb")[:2 - (l == 5)]) + over(n, "x", "u", "o", "mb")
                            + ["square2", "ln2", "inv2", "affine", "hi"])
        C_DVE = ChunkStages(lambda n: ["scan", "kk0", "k2a", "k2b", "k2", "kk", "b", "rk", "rkk", "bonus"]
                            + over(n, "as", "bs", "kb", "rs", "lm0", "ta0", "tt0", "lm1", "ak", "rb", "rk")
                            + [x + str(p) for l in C_LEVELS for p in range(n)
                               for x in ["tt%d" % l] + (["ta%d" % l, "lm%d" % (l + 1)] if l < 5 else [])]
                            + over(n, "u", "m0", "m")
                            + ["centred", "scaled", "plus", "gated", "lo"])
        C_POOL = ChunkStages(lambda n: over(n, "v", "a", "b"))
        DECAY = 0.6065306597126334

        def stacked(p, n, half):
            return PS[:, 4 * p + n, 256 * half:256 * half + 256].rearrange("p (m n) -> p m n", m=4)

        def cols_of(name):
            return COL[:, cp[name]:cp[name] + 4].unsqueeze(2).to_broadcast([128, 4, 128])

        def pairs_of(x, n=64):
            return x.unsqueeze(1).to_broadcast([x.shape[0], 4, n])

        def half(h):
            return slice(64 * h, 64 * h + 64)

        PAIR_ID = small("pair_identity", 64)

        IN1 = 108
        D_SCALE = 192.0 ** -0.5
        STEPS = 9

        def queries(n):
            return (P0 + 128 * n if n < 8 else S0), 128

        def key_runs(n):
            if n == 8:
                return [(NT, 128, 0), (S0, 128, 128)]
            keys = 128 * (n + 1)
            return [(P0 + k, min(512, keys - k), k) for k in range(0, keys, 512)]

        def key_blocks(n):
            return [(8, 128), (9, 128)] if n == 8 else [(j, 128) for j in range(n + 1)]

        block = ctx.enter_context(nc.Block())
        def matmul_unit(slot, ring, first, nk, hi, lo, width=BW):
            for b in range(NB):
                n, last = 0, None
                for k in range(nk):
                    w = slice(first + k * 128, first + (k + 1) * 128)
                    for wt, r in ((WHI, hi), (WHI, lo), (WLO, hi)):
                        last = nc.tensor.matmul(PS[:, 4 * slot + b, 0:width], wt[:, ring, w],
                                                r[:, k, b * width:(b + 1) * width],
                                                start=n == 0, stop=n == 3 * nk - 1)
                        n += 1
            return last

        @block.sync
        def _(sp):
            sp.dma_start(COL[:, :], io["columns"]).then_inc(params_in, 16)
            sp.dma_start(SMALL[:, :], io["small"]).then_inc(params_in, 16)
            for k in range(8):
                sp.dma_start(X32[:, k, :], io["x"][:, k, :]).then_inc(x_in, 16)
            for s in range(2):
                sp.dma_start(RAW[:, s, :], io["units"][s]).then_inc(raw_in[s], 16)
            def load_units(first, last):
                with sp.Fori(first, last) as i:
                    for s in range(2):
                        sp.wait_ge(unit_split, 2 * i + s - 1)
                        sp.dma_start(RAW[:, s, :], io["units"][ds(2 * i + s, 1), :, :].rearrange("a p n -> p (a n)"))\
                          .then_inc(raw_in[s], 16)

            load_units(1, OUT_UNIT[1] // 2 + 2)
            sp.wait_ge(a_hi, 73)
            sp.dma_start(LORA[:, :, :], io["w_lora"]).then_inc(lora_in, 16)
            sp.dma_start(MS[1][:, :, :], io["s_c"]).then_inc(c_state_in, 16)
            sp.dma_start(CIN[:, :, :], CROW[:, :, P0:P0 + 128].rearrange("a p n -> p a n")).then_inc(c_in, 16)
            with sp.Fori(0, 7) as i:
                sp.wait_ge(c_pool, C_POOL.at(i, "v", 1))
                sp.wait_ge(c_dve, C_DVE.at(i, "rs", 1))
                sp.wait_ge(c_in, 16 * i + 16)
                sp.dma_start(CIN[:, :, :], CROW[:, :, ds(128 * i + (P0 + 128), 128)].rearrange("a p n -> p a n"))\
                  .then_inc(c_in, 16)
            sp.wait_ge(c_pool, C_POOL.at(7, "v", 1))
            sp.wait_ge(c_dve, C_DVE.at(7, "rs", 1))
            sp.wait_ge(c_in, 16 * 8)
            sp.dma_start(CIN[:, :, :], CROW[:, :, S0:S0 + 128].rearrange("a p n -> p a n")).then_inc(c_in, 16)
            load_units(OUT_UNIT[1] // 2 + 2, NU // 2)
            sp.wait_ge(kept_ready, 1)
            sp.dma_start(io["kept"], KEPT[:, :]).then_inc(outs_done, 16)
            sp.wait_ge(outs_done, 16)

        @block.gpsimd
        def _(pool):
            ZERO = EPS[:, 3:4]

            def zeros(h):
                return EPS[half(h), 3:4].unsqueeze(2).to_broadcast([64, 4, 64])

            pool.wait_ge(eps_set, 4)
            def split_units(first, last):
                with pool.Fori(first, last) as i:
                    for s in range(2):
                        pool.wait_ge(raw_in[s], 16 * i + 16)
                        pool.wait_ge(unit_done, 2 * i + s + 1)
                        nc.gpsimd.tensor_tensor(WHI[:, s, :], RAW[:, s, :], ZERO.to_broadcast([128, 1024]), ALU.add)\
                            .then_inc(hi_split, 1)
                        pool.wait_ge(hi_split, 2 * i + s + 1)
                        nc.gpsimd.tensor_tensor(WLO[:, s, :], RAW[:, s, :], WHI[:, s, :], ALU.subtract)\
                          .then_inc(unit_split, 1)

            split_units(0, OUT_UNIT[1] // 2 + 1)

            def chunk_blocks(i, p):
                t = half(p)
                pool.wait_ge(c_in, 144 if i is LAST else 16 * i + 16)
                pool.wait_ge(c_act, C_ACT.at(i, "px", p))
                for h in range(2):
                    last = nc.gpsimd.tensor_tensor(V_B[p][half(h), :, half(h)], CIN[half(h), 8:12, t], zeros(h), ALU.add)
                last.then_inc(c_pool, 1)
                for name, block, x in (("as", A_B, A_S), ("bs", B_B, B_S)):
                    pool.wait_ge(c_dve, C_DVE.at(i, name, p))
                    for h in range(2):
                        last = nc.gpsimd.tensor_tensor(block[p][half(h), :, half(h)], x[p][half(h), :, :], zeros(h),
                                                       ALU.add)
                    last.then_inc(c_pool, 1)

            pool.wait_ge(c_ready, 1)
            with pool.Fori(0, 8) as i:
                for p in range(2):
                    chunk_blocks(i, p)
            chunk_blocks(LAST, 0)
            split_units(OUT_UNIT[1] // 2 + 1, NU // 2)

        @block.tensor
        def _(pe):
            pe.sem_inc(unit_done, 2)
            pe.wait_ge(xl_ready, 8)
            with pe.Fori(0, 12) as i:
                for s in range(2):
                    pe.wait_ge(unit_split, 2 * i + s + 1)
                    pe.wait_ge(slot_act, 2 * i + s + 1)
                    matmul_unit(s, s, 0, 8, XH, XL).then_inc(unit_done, 1)
            pe.wait_ge(slot_act, 26)
            pe.wait_ge(ba_split, 1)
            for c in range(9):
                t0 = P0 + 128 * c if c < 8 else S0
                n = 0
                for k in range(8):
                    for x, w in ((XH, WBAH), (XL, WBAH), (XH, WBAL)):
                        last = nc.tensor.matmul(PS[:, 7, 8 * c:8 * c + 8], x[:, k, t0:t0 + 128],
                                                w[:, 8 * k:8 * k + 8], start=n == 0, stop=n == 23)
                        n += 1
            last.then_inc(ba_done, 1)
            pe.wait_ge(g_ready, 1)
            nc.tensor.matmul(PS[:, 7, 128:164], UPPER, GB[:, :], start=True, stop=True).then_inc(ba_done, 1)
            pe.wait_ge(gates_in, 16)
            for m in range(4):
                if m:
                    pe.wait_ge(rg_read, 2 * m)
                for g in range(2):
                    if g:
                        pe.wait_ge(ba_copied, 2)
                    for b in range(NB):
                        last = nc.tensor.matmul(PS[:, 4 * g + b, 0:BW], RGW[:, g, m, :],
                                                XCQ[:, m, b * BW:(b + 1) * BW], start=True, stop=True)
                    last.then_inc(rg_done, 1)
            for j in range(8):
                pe.wait_ge(sq_ready, j + 1)
                if j >= 2:
                    pe.wait_ge(norm_root, j - 1)
                for b in range(NB):
                    last = nc.tensor.matmul(PS[:, 4 * (j % 2) + b, 0:BW], ONES, RN[j % 2][:, b * BW:(b + 1) * BW],
                                            start=True, stop=True)
                last.then_inc(norm_sum, 1)
            pe.wait_ge(norm_root, 8)
            for p in range(2):
                pe.sem_inc(gdn_pe[p], 1)

            def by_head(bank, lhs, rhs, start=True, stop=True):
                for h in range(4):
                    last = nc.tensor.matmul(PS[:, bank, 128 * h:128 * h + 128], lhs[:, h, :], rhs[:, h, :],
                                            start=start, stop=stop)
                return last

            def turned(bank, x):
                for h in range(4):
                    last = nc.tensor.transpose(PS[:, bank, 128 * h:128 * h + 128], x[:, h, :], IDENT)
                return last

            def prepare(i, p):
                s, b = gdn_pe[p], 4 * p
                pe.wait_ge(gdn_dve[p], G_DVE.at(i, "decayed"))
                nc.tensor.matmul(PS[:, b, :], ONES, LM[p][:, :, :].rearrange("p h n -> p (h n)"), start=True, stop=True)\
                  .then_inc(s, 1)
                pe.wait_ge(gdn_act[p], G_ACT.at(i, "staged"))
                by_head(b + 1, KT[p], KT[p]).then_inc(s, 1)
                by_head(b + 2, KT[p], QT[p]).then_inc(s, 1)
                turned(b + 3, KT[p]).then_inc(s, 1)
                pe.wait_ge(gdn_act[p], G_ACT.at(i, "exps"))
                turned(b, VT[p]).then_inc(s, 1)
                pe.wait_ge(gdn_dve[p], G_DVE.at(i, "m0"))
                turned(b + 1, LM[p]).then_inc(s, 1)

            def level(l, i, p):
                s, b = gdn_pe[p], 4 * p
                pe.wait_ge(gdn_dve[p], G_DVE.at(i, "m%d" % l))
                by_head(b + 1, LM[p], TT[p]).then_inc(s, 1)
                pe.wait_ge(gdn_act[p], G_ACT.at(i, "w%d" % l))
                by_head(b + 2, TA[p], WW[p]).then_inc(s, 1)
                if l < 6:
                    by_head(b + 3, WW[p], TA[p]).then_inc(s, 1)

            def carry(i, p, before, state):
                s, b = gdn_pe[p], 4 * p
                if before:
                    pe.wait_ge(*before)
                by_head(b, KT[p], state).then_inc(s, 1)
                pe.wait_ge(gdn_dve[p], G_DVE.at(i, "r"))
                by_head(b + 1, TT[p], RR[p]).then_inc(s, 1)
                pe.wait_ge(gdn_act[p], G_ACT.at(i, "v_new"))
                for h in range(4):
                    o = PS[:, b + 2, 128 * h:128 * h + 128]
                    nc.tensor.matmul(o, state[:, h, :], QT[p][:, h, :], start=True, stop=False)
                    last = nc.tensor.matmul(o, VN[p][:, h, :], DA[p][:, h, :], start=False, stop=True)
                last.then_inc(s, 1)
                by_head(b + 3, KO[p], VN[p]).then_inc(s, 1)

            with pe.Fori(0, 4) as i:
                for p in range(2):
                    prepare(i, p)
                for l in range(1, 7):
                    for p in range(2):
                        level(l, i, p)
                carry(i, 0, (gdn_dve[1], G_DVE.before(i)), SP)
                carry(i, 1, (gdn_dve[0], G_DVE.at(i, "s")), SP)
            pe.wait_ge(pad_zeroed, 1)
            prepare(4, 0)
            for l in range(1, 7):
                level(l, 4, 0)
            carry(4, 0, (state_in, 16), SS)
            for h in range(4):
                pe.wait_ge(o_square, h + 1)
                if h >= 2:
                    pe.wait_ge(o_root, h - 1)
                for b in range(NB):
                    last = nc.tensor.matmul(PS[:, 4 * (h % 2) + b, 0:BW], ONES, RN[h % 2][:, b * BW:(b + 1) * BW],
                                            start=True, stop=True)
                last.then_inc(o_sum, 1)

            def norm_sums(n):
                for b in range(NB):
                    for k in range(8):
                        last = nc.tensor.matmul(PS[:, b, 0:BW], ONES, Y[:, k, b * BW:(b + 1) * BW],
                                                start=k == 0, stop=k == 7)
                last.then_inc(ln_mean, 1)
                for k in range(8):
                    pe.wait_ge(ln_sq, k + 1 + 8 * n)
                    for b in range(NB):
                        last = nc.tensor.matmul(PS[:, 4 + b, 0:BW], ONES, SQ[k % 2][:, b * BW:(b + 1) * BW],
                                                start=k == 0, stop=k == 7)
                    last.then_inc(ln_var, 1)

            def up(l, g, unit):
                for t in range(4):
                    pe.wait_ge(unit_split, unit + t + 1)
                    matmul_unit(t % 2, t % 2, 0, 8, XH, XL).then_inc(unit_done, 1)

            def down(l, g, unit, slots=True):
                pe.wait_ge(h_done, g + 2 + 12 * l)
                for m in range(8):
                    if m % 4 == 0:
                        pe.wait_ge(unit_split, unit + m // 4 + 1)
                    if m < 2:
                        pe.wait_ge(up_read, slots + m + 45 * l)
                    else:
                        pe.wait_ge(down_read, 8 * g + m + 1 + 90 * l)
                    last = matmul_unit(m % 2, m // 4, 256 * (m % 4), 2, HH, HL)
                    last.then_inc(part_done if m % 4 < 3 else unit_done, 1)

            def layer_end(l):
                first = OUT_UNIT[l]
                pe.wait_ge(mix_ready[l], 4)
                with pe.Fori(0, 4) as i:
                    for s in range(2):
                        pe.wait_ge(unit_split, first + 2 * i + s + 1)
                        pe.wait_ge(out_read, 2 * i + s + 1 + 10 * l)
                        matmul_unit(s, s, 0, 8, XH, XL).then_inc(unit_done, 1)
                pe.wait_ge(out_read, 10 + 10 * l)
                norm_sums(2 * l)
                pe.wait_ge(gaps_zeroed, 1 + 2 * l)
                for t in range(4):
                    pe.wait_ge(unit_split, first + 8 + t + 1)
                    if t >= 2:
                        pe.wait_ge(up_read, t + 45 * l)
                    matmul_unit(t % 2, t % 2, 0, 8, XH, XL).then_inc(unit_done, 1)
                with pe.Fori(1, 11) as g:
                    for t in range(4):
                        pe.wait_ge(unit_split, 6 * g + first + 6 + t + 1)
                        pe.wait_ge(up_read, 4 * g + t + 45 * l)
                        pe.wait_ge(down_read, 8 * g - 7 + min(t, 1) + 90 * l)
                        matmul_unit(t % 2, t % 2, 0, 8, XH, XL).then_inc(unit_done, 1)
                    down(l, g - 1, 6 * g + first + 10, 4 * g + 4)
                down(l, 10, first + 72, 44)
                pe.wait_ge(down_read, 90 + 90 * l)
                norm_sums(2 * l + 1)
                pe.wait_ge(p_split, 2 + 2 * l)
                pe.wait_ge(ln_root, 1 + (2 * l + 1))
                for m in range(8):
                    if m % 4 == 0:
                        pe.wait_ge(unit_split, first + 74 + m // 4 + 1)
                    if m >= 2:
                        pe.wait_ge(wp_read, m - 1 + 8 * l)
                    last = matmul_unit(m % 2, m // 4, 256 * (m % 4), 2, PH, PL)
                    last.then_inc(part_done if m % 4 < 3 else unit_done, 1)
                pe.wait_ge(wp_read, 8 + 8 * l)
                pe.wait_ge(gaps_zeroed, 1 + (2 * l + 1))
                with pe.Fori(0, 4) as i:
                    for s in range(2):
                        pe.wait_ge(unit_split, 2 * i + s + first + 77)
                        pe.wait_ge(gate_read, 2 * i + s + 1 + 10 * l)
                        matmul_unit(s, s, 0, 8, XH, XL).then_inc(unit_done, 1)

            layer_end(0)
            pe.wait_ge(in_ready, 1)
            pe.wait_ge(gate_read, 10)
            with pe.Fori(0, 10) as i:
                for s in range(2):
                    pe.wait_ge(unit_split, 2 * i + s + IN1 + 1)
                    pe.wait_ge(in1_read, 2 * i + s + 1)
                    matmul_unit(s, s, 0, 8, XH, XL).then_inc(unit_done, 1)
            pe.wait_ge(in1_read, 22)
            for j in range(5):
                slot, k, nk = (0, j, 3) if j < 3 else (1, j - 3, 2)
                pe.wait_ge(m_square, j + 1)
                for b in range(NB):
                    last = nc.tensor.matmul(PS[:, 4 * slot + b, 0:BW], ONES, SQD[j % 2][:, b * BW:(b + 1) * BW],
                                            start=k == 0, stop=k == nk - 1)
                last.then_inc(m_sum, 1)

            def swap_halves(slot, x):
                for b in range(NB):
                    last = nc.tensor.matmul(PS[:, 4 * slot + b, 0:BW], small("half_swap", 128), x[:, b * BW:(b + 1) * BW],
                                            start=True, stop=True)
                last.then_inc(swapped, 1)

            pe.wait_ge(m_root, 1)
            swap_halves(0, KRW)
            pe.wait_ge(m_lo, 5)
            pe.wait_ge(kr_done, 1)
            for m in range(6):
                if m % 2 == 0:
                    pe.wait_ge(unit_split, IN1 + 20 + m // 2 + 1)
                if m >= 2:
                    pe.wait_ge(qkv_read, m - 1)
                last = matmul_unit(m % 2, (m // 2) % 2, 384 * (m % 2), 3, QAH, QAL)
                last.then_inc(unit_done if m % 2 else part_done, 1)
            for m in range(4):
                if m % 2 == 0:
                    pe.wait_ge(unit_split, IN1 + 23 + m // 2 + 1)
                pe.wait_ge(qkv_read, 6 + m - 1)
                last = matmul_unit(m % 2, (m // 2 + 1) % 2, 256 * (m % 2), 2, CH, CL, KW)
                last.then_inc(unit_done if m % 2 else part_done, 1)
            for r in range(2):
                pe.wait_ge(qkv_read, 9 + r)
                swap_halves(r, QR[:, r, :])
            pe.wait_ge(unit_split, IN1 + 26)
            pe.wait_ge(q_rotated, 2)
            for j in range(10):
                t0 = P0 + 128 * j if j < 8 else (NT if j == 8 else S0)
                if j >= 8:
                    pe.wait_ge(v_read, j - 7)
                n = 0
                for k in range(2):
                    for c, w in ((CH, WHI), (CL, WHI), (CH, WLO)):
                        last = nc.tensor.matmul(PS[:, j % 8, :], c[:, k, t0:t0 + 128], w[:, 1, 512 * k:512 * k + 512],
                                                start=n == 0, stop=n == 5)
                        n += 1
                last.then_inc(v_done if j < 9 else unit_done, 1)

            def scores(i, hh, n):
                t0, nq = queries(n)
                s = 18 * i + 9 * hh + n
                if n == 0 or n == 1:
                    pe.wait_ge(q_staged, 2 * i + hh + 1)
                pe.wait_ge(a_probs, s + 1)
                g = (9 * hh + n) % 2
                for c, nk, at_ in key_runs(n):
                    out = PS[0:nq, 2 * g + at_ // 512, at_ % 512:at_ % 512 + nk]
                    nc.tensor.matmul(out, QS[:, hh, t0:t0 + nq], KN[:, ds(2 * i + hh, 1), c:c + nk].rearrange("p a n -> p (a n)"),
                                     start=True, stop=False)
                    r = slice(64 * hh, 64 * hh + 64)
                    last = nc.tensor.matmul(out, QRS[r, t0:t0 + nq], KRR[r, c:c + nk], start=False, stop=True)
                last.then_inc(a_scores, 1)

            def weigh(i, hh, n):
                t0, nq = queries(n)
                s, g = 18 * i + 9 * hh + n, (9 * hh + n) % 2
                pe.wait_ge(a_probs, s + 3)
                for j, (_, nk) in enumerate(key_blocks(n)):
                    last = nc.tensor.transpose(PS[0:nk, 4 + j // 4, 128 * (j % 4):128 * (j % 4) + nq],
                                               PB[0:nq, g, 128 * j:128 * j + nk], IDENT[0:nq, 0:nq])
                last.then_inc(a_turned, 1)
                pe.wait_ge(a_keys, s + 1)
                if 4 <= n < 8:
                    pe.wait_ge(a_keys2, 8 * i + 4 * hh + n - 3)
                pe.wait_ge(a_scaled, s + 1)
                blocks = key_blocks(n)
                for j, (v, nk) in enumerate(blocks):
                    last = nc.tensor.matmul(PS[0:nq, 6, 0:128], PTB[0:nk, 128 * j:128 * j + nq],
                                            VTOK[0:nk, v, ds(256 * i + 128 * hh, 128)], start=j == 0, stop=j == len(blocks) - 1)
                last.then_inc(a_out, 1)

            def back(i, hh, n):
                t0, nq = queries(n)
                s, g = 18 * i + 9 * hh + n, (9 * hh + n) % 2
                pe.wait_ge(a_scaled, s + 2)
                pe.wait_ge(a_hi, 2 * s + 1)
                nc.tensor.transpose(PS[:, 7, 0:nq], OB[0:nq, g, :], IDENT[0:nq, 0:nq]).then_inc(a_back, 1)

            pe.wait_ge(v_read, 10)
            order = [(hh, n) for hh in range(2) for n in range(STEPS)]
            pe.sem_inc(a_scores, 1)
            pe.sem_inc(a_turned, 1)
            pe.sem_inc(a_out, 1)
            with pe.Fori(0, 2) as i:
                scores(i, 0, 0)
                for x, (hh, n) in enumerate(order):
                    if x + 1 < len(order):
                        scores(i, *order[x + 1])
                    weigh(i, hh, n)
                    back(i, hh, n)
            def c_blocks(out, lhs, rhs, more=()):
                terms = [(lhs, rhs)] + list(more)
                for m in range(4):
                    for n, (l, r) in enumerate(terms):
                        last = nc.tensor.matmul(out[:, m, :], l[:, m, :], r if len(r.shape) == 2 else r[:, m, :],
                                                start=n == 0, stop=n == len(terms) - 1)
                return last

            def c_rows(i):
                pe.wait_ge(c_act, C_ACT.at(i, "tanh"))
                for m in range(4):
                    last = nc.tensor.matmul(per_head(4)[:, m, :], LORA[0:64, 0, 128 * m:128 * m + 128], TW[0:64, :],
                                            start=True, stop=True)
                last.then_inc(c_pe, 1)
                for m in range(4):
                    last = nc.tensor.matmul(per_head(5)[:, m, :], LORA[64:128, 0, 128 * m:128 * m + 128], CIN[64:128, 12, :],
                                            start=True, stop=True)
                last.then_inc(c_pe, 1)
                pe.wait_ge(c_act, C_ACT.at(i, "sx"))
                for m in range(4):
                    last = nc.tensor.matmul(per_head(6)[:, m, :], LORA[:, 1, 128 * m:128 * m + 128], SX[:, :],
                                            start=True, stop=True)
                last.then_inc(c_pe, 1)
                pe.wait_ge(c_act, C_ACT.at(i, "square"))
                nc.tensor.matmul(PS[:, 7, :], small("pair_ones", 128), CT[:, :, :].rearrange("p m n -> p (m n)"),
                                 start=True, stop=True).then_inc(c_pe, 1)
                pe.wait_ge(c_dve, C_DVE.at(i, "rkk"))
                nc.tensor.matmul(PS[:, 4, :], small("pair_ones", 128), CT[:, :, :].rearrange("p m n -> p (m n)"),
                                 start=True, stop=True).then_inc(c_pe, 1)

            def c_prepare(i, p):
                pe.wait_ge(c_pool, C_POOL.at(i, "a", p))
                pe.wait_ge(c_dve, C_DVE.at(i, "bs", p))
                pe.wait_ge(c_dve, C_DVE.at(i, "bonus"))
                c_blocks(stacked(p, 0, 0), A_B[p], B_S[p]).then_inc(c_pe, 1)
                pe.wait_ge(c_dve, C_DVE.at(i, "kb", p))
                c_blocks(stacked(p, 1, 0), K_B[p], A_S[p])
                pe.wait_ge(c_pool, C_POOL.at(i, "b", p))
                pe.wait_ge(c_dve, C_DVE.at(i, "rs", p))
                c_blocks(stacked(p, 1, 1), B_B[p], R_S[p]).then_inc(c_pe, 1)
                c_blocks(stacked(p, 3, 0), B_B[p], PAIR_ID)
                c_blocks(stacked(p, 3, 1), K_B[p], PAIR_ID).then_inc(c_pe, 1)
                c_blocks(stacked(p, 2, 0), K_B[p], R_S[p])
                pe.wait_ge(c_dve, C_DVE.at(i, "lm0", p))
                c_blocks(stacked(p, 2, 1), LM_B[p], PAIR_ID).then_inc(c_pe, 1)
                pe.wait_ge(c_act, C_ACT.at(i, "kt", p))
                c_blocks(stacked(p, 3, 0), V_B[p], PAIR_ID).then_inc(c_pe, 1)

            def c_level(l, i, p):
                pe.wait_ge(c_dve, C_DVE.at(i, "lm%d" % l, p))
                if l == 1:
                    pe.wait_ge(c_dve, C_DVE.at(i, "rk", p))
                    pe.wait_ge(c_act, C_ACT.at(i, "vt", p))
                c_blocks(stacked(p, 1, 0), LM_B[p], TT_S[p]).then_inc(c_pe, 1)
                pe.wait_ge(c_act, C_ACT.at(i, "ws%d" % l, p))
                c_blocks(stacked(p, 2, 0), TA_B[p], W_S[p]).then_inc(c_pe, 1)
                if l < 5:
                    pe.wait_ge(c_act, C_ACT.at(i, "wb%d" % l, p))
                    by_head(4 * p + 3, W_B[p], TA_B[p]).then_inc(c_pe, 1)

            def c_carry(i, p, state):
                if i is LAST:
                    pe.wait_ge(c_state_in, 16)
                elif p == 1:
                    pe.wait_ge(c_dve, C_DVE.at(i, "m", 0))
                pe.wait_ge(c_dve, C_DVE.at(i, "rk", p))
                pe.wait_ge(c_act, C_ACT.at(i, "vt", p))
                c_blocks(stacked(p, 1, 0), A_B[p], state, [(AK_B[p], V_S[p])]).then_inc(c_pe, 1)
                pe.wait_ge(c_act, C_ACT.at(i, "x", p))
                pe.wait_ge(c_dve, C_DVE.at(i, "tt5", p))
                c_blocks(stacked(p, 2, 0), TT_B[p], X_S[p]).then_inc(c_pe, 1)
                pe.wait_ge(c_act, C_ACT.at(i, "u", p))
                c_blocks(stacked(p, 3, 0), BT_B[p], U_S[p], [(KT_B[p], V_S[p])]).then_inc(c_pe, 1)
                if i is LAST:
                    pe.wait_ge(c_act, C_ACT.at(7, "hi"))
                pe.wait_ge(c_dve, C_DVE.at(i, "u", p))
                if p == 1:
                    pe.wait_ge(c_act, C_ACT.at(i, "mb", 0))
                c_blocks(stacked(p, 1, 0), MB, R_S[p], [(U_B[p], RB_S[p]), (VT_B[p], RK_S[p])]).then_inc(c_pe, 1)

            def c_end(i, n):
                pe.wait_ge(c_act, C_ACT.at(i, "o", n // 64 - 1))
                nc.tensor.matmul(PS[:, 0, 0:4 * n], small("pair_ones", 128), CO[:, :, 0:n], start=True, stop=True)\
                  .then_inc(c_pe, 1)
                pe.wait_ge(c_act, C_ACT.at(i, "square2"))
                nc.tensor.matmul(PS[:, 0, 0:4 * n], small("pair_ones", 128), SA[:, :, 0:n], start=True, stop=True)\
                  .then_inc(c_pe, 1)

            pe.wait_ge(lora_in, 16)
            pe.wait_ge(a_hi, 73)
            with pe.Fori(0, 8) as i:
                c_rows(i)
                for p in range(2):
                    c_prepare(i, p)
                for l in C_LEVELS:
                    for p in range(2):
                        c_level(l, i, p)
                for p in range(2):
                    c_carry(i, p, MS[0])
                c_end(i, 128)
            c_rows(LAST)
            c_prepare(LAST, 0)
            for l in C_LEVELS:
                c_level(l, LAST, 0)
            c_carry(LAST, 0, MS[1])
            c_end(LAST, 64)
            layer_end(1)

        @block.scalar
        def _(act):
            step = Steps(act, act_step)

            def root(j):
                act.wait_ge(norm_sum, j + 1)
                if j >= 2:
                    act.wait_ge(norm_done, j - 1)
                nc.scalar.activation(rows(RN[2 + j % 2][:, :]), banks(j % 2), ACT.Sqrt, bias=EPS[:, 1:2])\
                  .then_inc(norm_root, 1)

            act.wait_ge(eps_set, 4)
            act.sem_inc(slot_act, 2)
            for s in range(2):
                act.sem_inc(row_out[s], 16)
            for k in range(8):
                act.wait_ge(x_in, 128)
                nc.scalar.activation(XH[:, k, :], X32[:, k, :], ACT.Copy).then_inc(xh_ready, 1)
            with act.Fori(0, 2) as i:
                for s in range(2):
                    act.wait_ge(unit_done, 2 * i + s + 3)
                    act.wait_ge(row_out[s], 16 * i + 16)
                    nc.scalar.activation(rows(U0[:, s, :]), banks(s), ACT.Gelu_apprx_tanh).then_inc(slot_act, 1)
                    act.wait_ge(slot_act, 2 * i + s + 3)
                    act.dma_start(GATE[ds(2 * i + s, 1), :, :].rearrange("a p n -> p (a n)"), U0[:, s, :])\
                       .then_inc(row_out[s], 16)
            act.wait_ge(params_in, 32)
            for s in range(2):
                act.wait_ge(row_out[s], 48)
            with act.Fori(0, 8) as i:
                for s in range(2):
                    act.wait_ge(unit_done, 2 * i + s + 7)
                    act.wait_ge(conv_done, 2 * i + s + 1)
                    nc.scalar.activation(rows(U0[:, s, :]), banks(s), ACT.Copy)
                    nc.scalar.activation(rows(XCQ[:, ds(2 * i + s, 1), :].rearrange("p a n -> p (a n)")), banks(s),
                                         ACT.Identity, scale=col_at("conv0_w3", 2 * i + s),
                                         bias=col_at("conv0_b", 2 * i + s)).then_inc(slot_act, 1)
            with act.Fori(0, 2) as i:
                for s in range(2):
                    act.wait_ge(unit_done, 2 * i + s + 23)
                    act.wait_ge(conv_done, 18)
                    act.wait_ge(row_out[s], 16 * i + 48)
                    nc.scalar.activation(rows(U0[:, s, :]), banks(s), ACT.Silu).then_inc(slot_act, 1)
                    act.wait_ge(slot_act, 2 * i + s + 23)
                    act.dma_start(ZROW[ds(2 * i + s, 1), :, :].rearrange("a p n -> p (a n)"), U0[:, s, :])\
                       .then_inc(row_out[s], 16)
            for m in range(4, 16):
                nc.scalar.activation(XCQ[:, m, 4:NT], XCQ[:, m, 4:NT], ACT.Silu).then_inc(silu_done, 1)
            for s in range(2):
                act.wait_ge(row_out[s], 80)
            act.dma_start(RGW[:, :, :, :], io["w_gates"]).then_inc(gates_in, 16)
            act.wait_ge(ba_done, 1)
            nc.scalar.activation(BETA, PSBA[:, :, 0:4], ACT.Sigmoid).then_inc(ba_act, 1)
            act.wait_ge(ba_vec, 1)
            nc.scalar.activation(GTMP[:, 1, :], GTMP[:, 1, :], ACT.Exp, scale=-1.0).then_inc(ba_act, 1)
            nc.scalar.activation(GTMP[:, 2, :], small("a_log", 36), ACT.Exp).then_inc(ba_act, 1)
            act.wait_ge(ba_act, 2)
            nc.scalar.activation(GTMP[:, 1, :], GTMP[:, 1, :], ACT.Ln, bias=1.0).then_inc(ba_act, 1)
            act.wait_ge(ba_done, 2)
            nc.scalar.activation(GC[:, :], PS[:, 7, 128:164], ACT.Copy).then_inc(ba_copied, 1)
            act.wait_ge(ba_copied, 1)
            nc.scalar.activation(EGC[:, :], GC[:, :], ACT.Exp).then_inc(ba_copied, 1)
            act.wait_ge(lam_vec, 1)
            nc.scalar.activation(LAM[:, 4:8], LAM[:, 4:8], ACT.Exp, scale=-1.0).then_inc(lam_act, 1)
            act.wait_ge(lam_act, 1)
            nc.scalar.activation(LAM[:, 4:8], LAM[:, 4:8], ACT.Ln, bias=1.0).then_inc(lam_act, 1)
            act.wait_ge(lam_vec, 2)
            for m in range(4):
                act.wait_ge(rg_done, 2 * m + 1)
                if m:
                    act.wait_ge(rg_vec, 4 * m)
                    act.wait_ge(gate_in, 16 * m)
                act.dma_start(MIX[4][:, :], GATE[m]).then_inc(gate_in, 16)
                nc.scalar.activation(rows(MIX[0][:, :]), banks(0), ACT.Sigmoid, bias=col("a_b_r", m)).then_inc(rg_read, 1)
                act.wait_ge(rg_done, 2 * m + 2)
                nc.scalar.activation(rows(MIX[1][:, :]), banks(1), ACT.Sigmoid, bias=col("a_b_i", m)).then_inc(rg_read, 1)
                act.wait_ge(rg_read, 2 * m + 1)
                nc.scalar.activation(MIX[2][:, :], MIX[0][:, :], ACT.Exp, scale=LAM[:, 8 + m:9 + m]).then_inc(rg_act, 1)
                nc.scalar.activation(MIX[3][:, :], MIX[0][:, :], ACT.Tanh, scale=LAM[:, 12 + m:13 + m]).then_inc(rg_act, 1)
                act.wait_ge(rg_vec, 4 * m + 2)
                nc.scalar.activation(MIX[3][:, :], MIX[3][:, :], ACT.Sqrt, scale=2.0).then_inc(rg_act, 1)
                act.wait_ge(rg_vec, 4 * m + 3)
                nc.scalar.activation(XH[:, m, 4:NT], MIX[0][:, 4:NT], ACT.Copy).then_inc(xh_ready, 1)
            act.wait_ge(rg_vec, 16)
            for j in range(8):
                act.wait_ge(silu_done, j + 1)
                if j >= 2:
                    act.wait_ge(norm_sum, j - 1)
                nc.scalar.activation(RN[j % 2][:, :], XCQ[:, 4 + j, :], ACT.Square).then_inc(sq_ready, 1)
                if j:
                    root(j - 1)
            root(7)
            for p in range(2):
                act.sem_inc(gdn_act[p], 1)
            act.dma_start(SS[:, :, :], io["s_b"]).then_inc(state_in, 16)
            act.wait_ge(norm_done, 8)

            def prepare(i, p, n=128):
                s, b = gdn_act[p], 4 * p
                t0 = 256 * i + 128 * p + P0 if n == 128 else S0
                act.wait_ge(gdn_pe[p], G_PE.before(i))
                for first, x in ((8, KT), (4, QT), (12, VT)):
                    last = nc.scalar.activation(x[p][:, :, 0:n], XCQ[:, first:first + 4, ds(t0, n)], ACT.Copy)
                last.then_inc(s, 1)
                act.wait_ge(gdn_dve[p], G_DVE.at(i, "diff"))
                nc.scalar.activation(EG[p][:, :, :], per_head(b), ACT.Exp)
                nc.scalar.activation(DA[p][:, :, :], DA[p][:, :, :], ACT.Exp)
                nc.scalar.activation(DB[p][:, :, :], DB[p][:, :, :], ACT.Exp, scale=-1.0)
                nc.scalar.activation(KOC[p][:, :], KOC[p][:, :], ACT.Exp).then_inc(s, 1)
                act.wait_ge(s, G_ACT.at(i, "exps"))
                act.wait_ge(gdn_pe[p], G_PE.at(i, "k_turned"))
                for h in range(4):
                    last = nc.scalar.activation(KO[p][:, h, :], PS[:, b + 3, 128 * h:128 * h + 128], ACT.Copy,
                                                scale=KOC[p][:, h:h + 1])
                last.then_inc(s, 1)
                act.wait_ge(gdn_pe[p], G_PE.at(i, "v_turned"))
                for h in range(4):
                    beta = BETA36[:, ds(8 * i + 4 * p + h, 1)]
                    last = nc.scalar.activation(VB[p][:, h, :], PS[:, b, 128 * h:128 * h + 128], ACT.Copy, scale=beta)
                last.then_inc(s, 1)

            def level(l, i, p):
                act.wait_ge(gdn_pe[p], G_PE.at(i, "w%d" % l))
                nc.scalar.activation(WW[p][:, :, :], per_head(4 * p + 1), ACT.Copy).then_inc(gdn_act[p], 1)

            def carry(i, p, n=128):
                s, b = gdn_act[p], 4 * p
                t0 = 256 * i + 128 * p + P0 if n == 128 else S0
                act.wait_ge(gdn_pe[p], G_PE.at(i, "v_new"))
                nc.scalar.activation(VN[p][:, :, :], per_head(b + 1), ACT.Copy).then_inc(s, 1)
                act.wait_ge(gdn_pe[p], G_PE.at(i, "o"))
                nc.scalar.activation(OT[:, :, ds(t0, n)], per_head(b + 2)[:, :, 0:n], ACT.Copy).then_inc(s, 1)

            with act.Fori(0, 4) as i:
                for p in range(2):
                    prepare(i, p)
                for l in range(1, 7):
                    for p in range(2):
                        level(l, i, p)
                for p in range(2):
                    carry(i, p)
            prepare(4, 0, 64)
            for l in range(1, 7):
                level(l, 4, 0)
            carry(4, 0, 64)
            act.wait_ge(gdn_dve[1], G_DVE.before(4))
            act.dma_start(io["s_b_p"], SP[:, :, :]).then_inc(state_out, 16)
            act.wait_ge(gdn_dve[0], G_DVE.before(5))
            act.dma_start(io["s_b_s"], SS[:, :, :]).then_inc(state_out, 16)
            act.wait_ge(state_out, 32)
            act.wait_ge(o_zeroed, 1)
            act.dma_start(ZT[:, :, :], ZROW.rearrange("t p n -> p t n")).then_inc(z_in, 16)
            act.dma_start(XR[:, :, :], io["x"]).then_inc(x_back, 16)

            def o_norm_root(h):
                act.wait_ge(o_sum, h + 1)
                if h >= 2:
                    act.wait_ge(o_gated, h - 1)
                nc.scalar.activation(rows(RN[2 + h % 2][:, :]), banks(h % 2), ACT.Sqrt, bias=EPS[:, 1:2], scale=1 / 128)\
                  .then_inc(o_root, 1)

            def o_hi(h):
                act.wait_ge(o_gated, h + 1)
                nc.scalar.activation(XH[:, 4 + h, :], OT[:, h, :], ACT.Copy).then_inc(xh_ready, 1)

            for h in range(4):
                if h >= 2:
                    act.wait_ge(o_sum, h - 1)
                nc.scalar.activation(RN[h % 2][:, :], OT[:, h, :], ACT.Square).then_inc(o_square, 1)
                if h:
                    o_norm_root(h - 1)
                if h >= 2:
                    o_hi(h - 2)
            o_norm_root(3)
            o_hi(2)
            o_hi(3)

            def norm(n, gain, bias):
                for k in range(8):
                    act.wait_ge(ln_sub, k + 1 + 8 * n)
                    if k >= 2:
                        act.wait_ge(ln_var, k - 1 + 8 * n)
                    nc.scalar.activation(SQ[k % 2][:, :], Y[:, k, :], ACT.Square).then_inc(ln_sq, 1)
                act.wait_ge(ln_var, 8 + 8 * n)
                nc.scalar.activation(rows(RS[:, :]), banks(1), ACT.Sqrt, bias=EPS[:, 0:1], scale=1 / 1024)\
                  .then_inc(ln_root, 1)
                for k in range(8):
                    act.wait_ge(ln_scaled, k + 1 + 8 * n)
                    nc.scalar.activation(Y[:, k, :], Y[:, k, :], ACT.Identity, scale=col(gain, k), bias=col(bias, k))\
                      .then_inc(ln_hi, 1)
                    act.wait_ge(ln_hi, 2 * k + 1 + 16 * n)
                    nc.scalar.activation(XH[:, k, :], Y[:, k, :], ACT.Copy).then_inc(ln_hi, 1)

            def chunk(l, g, unit, first=False):
                for t in range(4):
                    act.wait_ge(unit_done, unit + t + 3)
                    act.wait_ge(ffn_conv, 4 * g + t + 1 + 46 * l)
                    nc.scalar.activation(rows(UF[:, t % 2, :]), banks(t % 2), ACT.Copy)
                    if t == 0:
                        act.wait_ge(h_done, g + 1 + 12 * l)
                    f = 2 * g + (t if t < 2 else 20 + t)
                    nc.scalar.activation(rows(CB[:, t, :]), banks(t % 2), ACT.Identity, scale=col_at("ffn_w2%d" % l, f),
                                         bias=col_at("ffn_b%d" % l, f)).then_inc(up_read, 1)
                    if t >= 2:
                        act.wait_ge(ffn_conv, 4 * g + t + 1 + 46 * l)
                        nc.scalar.activation(CB[:, t - 2, :], CB[:, t - 2, :], ACT.Silu).then_inc(ffn_silu, 1)
                if not first:
                    act.wait_ge(unit_done, unit + 8)
                for j in range(2):
                    act.wait_ge(ffn_mul, 2 * g + j + 1 + 22 * l)
                    nc.scalar.activation(HH[:, j, :], CB[:, 2 + j, :], ACT.Copy).then_inc(h_hi, 1)

            def layer_end(l):
                first, part = OUT_UNIT[l], OUT_PART[l]
                act.sem_inc(up_read, 1)
                act.sem_inc(gate_read, 2)
                norm(2 * l, "ln_mix_g%d" % l, "ln_mix_b%d" % l)
                chunk(l, 0, first + 8, True)
                with act.Fori(1, 11) as g:
                    chunk(l, g, 6 * g + first + 6)
                act.wait_ge(unit_done, first + 76)
                act.dma_start(P32[:, :, :], io["p"][l]).then_inc(p_in, 16)
                act.wait_ge(p_in, 16 + 16 * l)
                nc.scalar.activation(PH[:, :, :], P32[:, :, :], ACT.Copy).then_inc(p_hi, 1)
                act.wait_ge(p_split, 2 + 2 * l)
                norm(2 * l + 1, "ln_ffn_g%d" % l, "ln_ffn_b%d" % l)
                for m in range(8):
                    if m % 4 < 3:
                        act.wait_ge(part_done, part + 66 + 3 * (m // 4) + m % 4 + 1)
                    else:
                        act.wait_ge(unit_done, first + 74 + m // 4 + 3)
                    nc.scalar.activation(rows(PP[:, m, :]), banks(m % 2), ACT.Copy).then_inc(wp_read, 1)
                act.wait_ge(wp_read, 8 + 8 * l)
                with act.Fori(0, 4) as i:
                    for s in range(2):
                        act.wait_ge(unit_done, 2 * i + s + first + 79)
                        act.wait_ge(gate_added, 2 * i + s + 1 + 10 * l)
                        nc.scalar.activation(rows(SG[s][:, :]), banks(s), ACT.Sigmoid, bias=col_at("ple_b%d" % l, 2 * i + s))\
                          .then_inc(gate_read, 1)

            layer_end(0)
            act.wait_ge(unit_done, 110)
            act.wait_ge(gate_added, 10)
            act.dma_start(XROW, Y[:, :, :]).then_inc(x_out, 16)
            for k in range(8):
                nc.scalar.activation(XH[:, k, :], Y[:, k, :], ACT.Copy).then_inc(x_hi, 1)
            act.sem_inc(in1_read, 2)
            act.sem_inc(a_probs, 2)
            act.sem_inc(a_scaled, 1)
            act.sem_inc(a_hi, 1)
            for s in range(2):
                act.sem_inc(row1_out[s], 16)
            act.wait_ge(x_out, 16)
            act.wait_ge(in_ready, 1)
            with act.Fori(0, 7) as i:
                for s in range(2):
                    act.wait_ge(unit_done, 2 * i + s + IN1 + 3)
                    act.wait_ge(row1_out[s], 16 * i + 16)
                    nc.scalar.activation(rows(U1[:, s, :]), banks(s), ACT.Copy).then_inc(in1_read, 1)
                for s in range(2):
                    act.wait_ge(shifted, 2 * i + s + 1)
                    act.dma_start(CROW[ds(2 * i + s, 1), :, :].rearrange("a p n -> p (a n)"), DX[:, s, :])\
                       .then_inc(row1_out[s], 16)
            for m, x in enumerate((QA[:, 0, :], QA[:, 1, :], QA[:, 2, :], CR[:, 0, :], CR[:, 1, :], KRW[:, :])):
                act.wait_ge(unit_done, IN1 + 14 + m + 3)
                nc.scalar.activation(rows(x), banks(m % 2), ACT.Copy).then_inc(in1_read, 1)
            for s in range(2):
                act.wait_ge(row1_out[s], 16 * 8)
            act.dma_start(ROPE[:, :, :], io["rope"]).then_inc(mla_in, 16)
            act.dma_start(CCK[:, :, :], io["cache_ckv"]).then_inc(cache_in, 16)
            act.dma_start(KRR[:, NT:NK], io["cache_krope"]).then_inc(kr_cache_in, 16)
            act.wait_ge(in1_read, 22)
            for j in range(5):
                if j >= 2:
                    act.wait_ge(m_sum, j - 1)
                x = QA[:, j, :] if j < 3 else CR[:, j - 3, :]
                nc.scalar.activation(SQD[j % 2][:, :], x, ACT.Square).then_inc(m_square, 1)
            for slot in range(2):
                act.wait_ge(m_sum, 3 + 2 * slot)
                nc.scalar.activation(rows(RSD[slot][:, :]), banks(slot), ACT.Sqrt, bias=EPS[:, 1:2],
                                     scale=1 / 384 if slot == 0 else 1 / 256).then_inc(m_root, 1)
            act.wait_ge(cache_in, 16)
            nc.scalar.activation(CH[:, :, NT:NK], CCK[:, :, :], ACT.Copy).then_inc(m_hi, 1)
            for j in range(5):
                act.wait_ge(m_scaled, j + 1)
                h, x = (QAH[:, j, :], QA[:, j, :]) if j < 3 else (CH[:, j - 3, 0:NT], CR[:, j - 3, :])
                nc.scalar.activation(h, x, ACT.Copy).then_inc(m_hi, 1)
            act.dma_start(io["ckv"], CR[:, :, :]).then_inc(c_out, 16)
            act.wait_ge(kr_done, 1)
            act.dma_start(io["krope"], KRR[0:64, 0:NT]).then_inc(kr_out, 16)
            for m in range(6):
                if m % 2:
                    act.wait_ge(unit_done, IN1 + 20 + m // 2 + 3)
                else:
                    act.wait_ge(part_done, 72 + m // 2 + 1)
                nc.scalar.activation(rows(QN[:, m, :] if m < 4 else QR[:, m - 4, :]), banks(m % 2), ACT.Copy)\
                  .then_inc(qkv_read, 1)
            act.wait_ge(c_out, 16)
            act.wait_ge(m_lo, 6)
            for m in range(4):
                if m % 2:
                    act.wait_ge(unit_done, IN1 + 23 + m // 2 + 3)
                else:
                    act.wait_ge(part_done, 75 + m // 2 + 1)
                nc.scalar.activation(rows(KN[:, m, :], KW), banks(m % 2, KW), ACT.Copy).then_inc(qkv_read, 1)
            act.wait_ge(q_rotated, 2)
            for j in range(10):
                if j < 9:
                    act.wait_ge(v_done, j + 1)
                else:
                    act.wait_ge(unit_done, IN1 + 26 + 2)
                nc.scalar.activation(VTOK[:, j, :], PS[:, j % 8, :], ACT.Copy).then_inc(v_read, 1)

            def probs(i, hh, n):
                t0, nq = queries(n)
                s, g = 18 * i + 9 * hh + n, (9 * hh + n) % 2
                nk = 256 if n == 8 else 128 * (n + 1)
                act.wait_ge(a_max, s + 1)
                act.wait_ge(a_turned, s)
                nc.scalar.activation(PB[0:nq, g, 0:nk], PS[0:nq, 2 * g:2 * g + 2, :].rearrange("p b n -> p (b n)")[:, 0:nk],
                                     ACT.Exp, scale=D_SCALE, bias=AST[g][0:nq, 0:1], accum_out=AST[g][0:nq, 1:2])\
                  .then_inc(a_probs, 1)

            def keys(i, hh, n):
                s = 18 * i + 9 * hh + n
                act.wait_ge(a_turned, s + 2)
                act.wait_ge(a_out, s + 1)
                nk = 256 if n == 8 else 128 * min(4, n + 1)
                nc.scalar.activation(PTB[:, 0:nk], PS[:, 4, 0:nk], ACT.Copy).then_inc(a_keys, 1)

            def scaled(i, hh, n):
                t0, nq = queries(n)
                s, g = 18 * i + 9 * hh + n, (9 * hh + n) % 2
                act.wait_ge(a_out, s + 2)
                act.wait_ge(a_inv, s + 1)
                own = 64 if n == 8 else 128
                nc.scalar.activation(OB[0:nq, g, :], PS[0:nq, 6, 0:128], ACT.Copy, scale=AST[g][0:nq, 2:3]).then_inc(a_scaled, 1)
                act.wait_ge(a_back, s + 1)
                nc.scalar.activation(XH[:, ds(2 * i + hh + 4, 1), t0:t0 + own].rearrange("p a n -> p (a n)"), PS[:, 7, 0:own],
                                     ACT.Copy).then_inc(a_hi, 1)

            order = [(hh, n) for hh in range(2) for n in range(STEPS)]
            with act.Fori(0, 2) as i:
                act.wait_ge(a_scores, 18 * i + 1)
                nc.scalar.activation(QRS[:, :], QR[:, ds(i, 1), :].rearrange("p a n -> p (a n)"), ACT.Copy)
                for hh in range(2):
                    nc.scalar.activation(QS[:, hh, :], QN[:, ds(2 * i + hh, 1), :].rearrange("p a n -> p (a n)"), ACT.Copy)\
                      .then_inc(q_staged, 1)
                probs(i, 0, 0)
                for x, (hh, n) in enumerate(order):
                    if x + 1 < len(order):
                        probs(i, *order[x + 1])
                    keys(i, hh, n)
                    scaled(i, hh, n)
            def c_rows(i):
                act.wait_ge(c_in, 144 if i is LAST else 16 * i + 16)
                nc.scalar.activation(TW[0:64, :], CIN[0:64, 12, :], ACT.Tanh).then_inc(c_act, 1)
                nc.scalar.activation(SX[:, :], CIN[:, 13, :], ACT.Sigmoid).then_inc(c_act, 1)
                for name, out, bias in (("w", CUM, "c_w0"), ("a", SA, "c_a0")):
                    act.wait_ge(c_pe, C_PE.at(i, name))
                    bank = 4 if name == "w" else 5
                    for m in range(4):
                        last = nc.scalar.activation(out[:, m, :], per_head(bank)[:, m, :], ACT.Sigmoid, bias=col(bias, m))
                    last.then_inc(c_act, 1)
                act.wait_ge(c_pe, C_PE.at(i, "g"))
                nc.scalar.activation(CG[:, :, :], per_head(6), ACT.Copy).then_inc(c_act, 1)
                act.wait_ge(c_dve, C_DVE.at(i, "kk0"))
                nc.scalar.activation(CT[:, :, :], KKN[:, :, :], ACT.Square).then_inc(c_act, 1)
                act.wait_ge(c_pe, C_PE.at(i, "norm"))
                nc.scalar.activation(CT[:, :, :], per_head(7), ACT.Ln, bias=EPS[:, 1:2]).then_inc(c_act, 1)
                act.wait_ge(c_act, C_ACT.at(i, "ln"))
                nc.scalar.activation(CT[:, :, :], CT[:, :, :], ACT.Exp, scale=-0.5).then_inc(c_act, 1)

            def c_prepare(i, p):
                act.wait_ge(c_dve, C_DVE.at(i, "scan"))
                nc.scalar.activation(PX[p][:, :, 1:65], CUM[:, :, half(p)], ACT.Exp, scale=-DECAY).then_inc(c_act, 1)
                nc.scalar.activation(PI_S[p][:, :, :], CUM[:, :, half(p)], ACT.Exp, scale=DECAY).then_inc(c_act, 1)
                act.wait_ge(c_pe, C_PE.at(i, "kt", p))
                for name, block, bank, side in (("bt", BT_B, 3, 0), ("kt", KT_B, 3, 1)):
                    for h in range(2):
                        last = nc.scalar.activation(block[p][half(h), :, half(h)], stacked(p, bank, side)[half(h), :, :],
                                                    ACT.Copy, scale=-1.0 if name == "bt" else 1.0)
                    last.then_inc(c_act, 1)
                act.wait_ge(c_pe, C_PE.at(i, "vt", p))
                nc.scalar.activation(V_S[p][:, :, :], stacked(p, 3, 0), ACT.Copy).then_inc(c_act, 1)
                for h in range(2):
                    last = nc.scalar.activation(VT_B[p][half(h), :, half(h)], stacked(p, 3, 0)[half(h), :, :], ACT.Copy)
                last.then_inc(c_act, 1)

            def c_level(l, i, p):
                act.wait_ge(c_pe, C_PE.at(i, "lw%d" % l, p))
                nc.scalar.activation(W_S[p][:, :, :], stacked(p, 1, 0), ACT.Copy).then_inc(c_act, 1)
                if l == 5:
                    return
                for h in range(2):
                    last = nc.scalar.activation(W_B[p][half(h), :, half(h)], stacked(p, 1, 0)[half(h), :, :], ACT.Copy)
                last.then_inc(c_act, 1)

            def c_carry(i, p, state):
                act.wait_ge(c_pe, C_PE.at(i, "x", p))
                nc.scalar.activation(X_S[p][:, :, :], stacked(p, 1, 0), ACT.Copy).then_inc(c_act, 1)
                act.wait_ge(c_pe, C_PE.at(i, "u", p))
                nc.scalar.activation(U_S[p][:, :, :], stacked(p, 2, 0), ACT.Copy).then_inc(c_act, 1)
                act.wait_ge(c_pe, C_PE.at(i, "o", p))
                nc.scalar.activation(CO[:, :, half(p)], stacked(p, 1, 0), ACT.Copy).then_inc(c_act, 1)
                act.wait_ge(c_dve, C_DVE.at(i, "m", p))
                for h in range(2):
                    last = nc.scalar.activation(MB[half(h), :, half(h)], state[half(h), :, :], ACT.Copy)
                last.then_inc(c_act, 1)

            def c_end(i, n):
                t0 = S0 if i is LAST else ds(128 * i + P0, 128)
                act.wait_ge(c_dve, C_DVE.at(i, "centred"))
                nc.scalar.activation(SA[:, :, 0:n], CO[:, :, 0:n], ACT.Square).then_inc(c_act, 1)
                act.wait_ge(c_pe, C_PE.at(i, "var"))
                nc.scalar.activation(SA[:, :, 0:n], PS[:, 0, 0:4 * n].rearrange("p (m n) -> p m n", m=4), ACT.Ln,
                                     bias=EPS[:, 2:3], scale=1 / 64).then_inc(c_act, 1)
                act.wait_ge(c_act, C_ACT.at(i, "ln2"))
                nc.scalar.activation(SA[:, :, 0:n], SA[:, :, 0:n], ACT.Exp, scale=-0.5).then_inc(c_act, 1)
                act.wait_ge(c_dve, C_DVE.at(i, "scaled"))
                for m in range(4):
                    last = nc.scalar.activation(CO[:, m, 0:n], CO[:, m, 0:n], ACT.Identity, scale=col("c_lnx_g", m),
                                                bias=col("c_lnx_b", m))
                last.then_inc(c_act, 1)
                act.wait_ge(c_dve, C_DVE.at(i, "gated"))
                where = slice(S0, S0 + n) if i is LAST else ds(128 * i + P0, n)
                nc.scalar.activation(XH[:, 0:4, where], CO[:, :, 0:n], ACT.Copy).then_inc(c_act, 1)

            act.wait_ge(a_hi, 73)
            act.wait_ge(c_ready, 1)
            with act.Fori(0, 8) as i:
                c_rows(i)
                for p in range(2):
                    c_prepare(i, p)
                for l in C_LEVELS:
                    for p in range(2):
                        c_level(l, i, p)
                for p in range(2):
                    c_carry(i, p, MS[0])
                c_end(i, 128)
            act.dma_start(io["s_c_p"], MS[0][:, :, :]).then_inc(c_state_out, 16)
            act.wait_ge(c_state_in, 16)
            for h in range(2):
                last = nc.scalar.activation(MB[half(h), :, half(h)], MS[1][half(h), :, :], ACT.Copy)
            c_rows(LAST)
            c_prepare(LAST, 0)
            for l in C_LEVELS:
                c_level(l, LAST, 0)
            c_carry(LAST, 0, MS[1])
            c_end(LAST, 64)
            act.dma_start(io["s_c_s"], MS[1][:, :, :]).then_inc(c_state_out, 16)
            act.wait_ge(c_state_out, 32)
            act.wait_ge(c_dve, C_DVE.at(LAST, "lo"))
            act.dma_start(XR[:, :, :], XROW).then_inc(x_back, 16)
            layer_end(1)
            act.wait_ge(gate_added, 20)
            act.dma_start(io["y"], Y[:, :, :]).then_inc(y_out, 16)
            act.wait_ge(y_out, 16)
            act.wait_ge(kr_out, 16)

        @block.vector
        def _(dve):
            step = Steps(dve, dve_step)
            dve.sem_inc(conv_done, 2)
            for n, e in enumerate((1e-5, 1e-6, 64e-5, 0.0)):
                nc.vector.memset(EPS[:, n:n + 1], e).then_inc(eps_set, 1)
            for k in range(8):
                dve.wait_ge(xh_ready, k + 1)
                nc.vector.tensor_tensor(XL[:, k, :], X32[:, k, :], XH[:, k, :], ALU.subtract).then_inc(xl_ready, 1)
            dve.wait_ge(params_in, 32)
            step(nc.vector.tensor_copy(WBAH[:, :], small("w_beta_alpha", 64)))
            nc.vector.tensor_tensor(WBAL[:, :], small("w_beta_alpha", 64), WBAH[:, :], ALU.subtract).then_inc(ba_split, 1)
            with dve.Fori(0, 8) as i:
                step.enter(i, 10)
                for s in range(2):
                    dve.wait_ge(slot_act, 2 * i + s + 7)
                    step(nc.vector.tensor_copy(U0[:, s, S0 - 3:S0],
                                               SMALL[:, ds(sp_["hist_conv0"] + 6 * i + 3 * s, 3)]))
                    kept = op["conv0"] + 12 * i + 6 * s
                    step(nc.vector.tensor_copy(KEPT[:, ds(kept, 3)], U0[:, s, S0 + 61:S0 + 64]))
                    step(nc.vector.tensor_copy(KEPT[:, ds(kept + 3, 3)], U0[:, s, NT - 3:NT]))
                    y = XCQ[:, ds(2 * i + s, 1), 4:NT].rearrange("p a n -> p (a n)")
                    for j in (1, 2):
                        step(nc.vector.scalar_tensor_tensor(y, U0[:, s, 4 - j:NT - j], col_at("conv0_w%d" % (3 - j), 2 * i + s),
                                                            y, ALU.mult, ALU.add))
                    nc.vector.scalar_tensor_tensor(y, U0[:, s, 1:NT - 3], col_at("conv0_w0", 2 * i + s), y,
                                                   ALU.mult, ALU.add).then_inc(conv_done, 1)
            step.leave(8)
            dve.wait_ge(ba_done, 1)
            dve.wait_ge(ba_act, 1)
            step(nc.vector.tensor_tensor(GTMP[:, 0, :].rearrange("p (c h) -> p c h", h=4), PSBA[:, :, 4:8],
                                         small("dt_bias", 36).rearrange("p (c h) -> p c h", h=4), ALU.add))
            nc.vector.scalar_tensor_tensor(GTMP[:, 1, :], GTMP[:, 0, :], -1.0, GTMP[:, 0, :], ALU.mult, ALU.max).then_inc(ba_vec, 1)
            dve.wait_ge(ba_act, 4)
            step(nc.vector.scalar_tensor_tensor(GTMP[:, 0, :], GTMP[:, 0, :], 0.0, GTMP[:, 1, :], ALU.max, ALU.add))
            step(nc.vector.scalar_tensor_tensor(GB[:, :], GTMP[:, 0, :], -1.0, GTMP[:, 2, :], ALU.mult, ALU.mult))
            nc.vector.memset(GB[64:128, 32:36], 0.0).then_inc(g_ready, 1)
            dve.wait_ge(ba_copied, 2)
            step(nc.vector.scalar_tensor_tensor(NBEG[:, :], EGC[:, :], -1.0, BETA36[:, :], ALU.mult, ALU.mult))
            lam = col4("a_lambda")
            nc.vector.scalar_tensor_tensor(LAM[:, 4:8], lam, -1.0, lam, ALU.mult, ALU.max).then_inc(lam_vec, 1)
            step(nc.vector.tensor_scalar(LAM[:, 0:4], lam, -1.0, 0.0, ALU.mult, ALU.max))
            dve.wait_ge(lam_act, 2)
            step(nc.vector.tensor_tensor(LAM[:, 0:4], LAM[:, 0:4], LAM[:, 4:8], ALU.add))
            step(nc.vector.tensor_scalar(LAM[:, 12:16], LAM[:, 0:4], 8.0, None, ALU.mult))
            nc.vector.tensor_scalar(LAM[:, 8:12], LAM[:, 0:4], -8.0, None, ALU.mult).then_inc(lam_vec, 1)
            for m in range(4):
                dve.wait_ge(rg_read, 2 * m + 2)
                step(nc.vector.tensor_tensor(MIX[1][:, 4:NT], MIX[1][:, 4:NT], XCQ[:, m, 4:NT], ALU.mult))
                dve.wait_ge(rg_act, 3 * m + 2)
                step(nc.vector.tensor_scalar(MIX[0][:, :], MIX[3][:, :], 1.0, None, ALU.add))
                nc.vector.reciprocal(MIX[0][:, :], MIX[0][:, :]).then_inc(rg_vec, 1)
                dve.wait_ge(rg_vec, 4 * m + 1)
                step(nc.vector.tensor_tensor(MIX[3][:, :], MIX[3][:, :], MIX[0][:, :], ALU.mult))
                nc.vector.tensor_scalar(MIX[3][:, :], MIX[3][:, :], 1e-34, None, ALU.max).then_inc(rg_vec, 1)
                dve.wait_ge(rg_act, 3 * m + 3)
                step(nc.vector.tensor_tensor(MIX[1][:, 4:NT], MIX[1][:, 4:NT], MIX[3][:, 4:NT], ALU.mult))
                step(nc.vector.tensor_tensor_scan(MIX[0][:, S0:S0 + 64], MIX[2][:, S0:S0 + 64], MIX[1][:, S0:S0 + 64],
                                                  small("h0", 1, m), ALU.mult, ALU.add))
                step(nc.vector.tensor_tensor_scan(MIX[0][:, P0:NT], MIX[2][:, P0:NT], MIX[1][:, P0:NT], 0.0,
                                                  ALU.mult, ALU.add))
                for n, c in enumerate((S0 + 63, NT - 1)):
                    step(nc.vector.tensor_copy(KEPT[:, op["h"] + 2 * m + n:op["h"] + 2 * m + n + 1], MIX[0][:, c:c + 1]))
                step(nc.vector.memset(MIX[0][:, S0 + 64:P0], 0.0))
                dve.wait_ge(gate_in, 16 * m + 16)
                nc.vector.tensor_tensor(MIX[0][:, 4:NT], MIX[0][:, 4:NT], MIX[4][:, 4:NT], ALU.mult).then_inc(rg_vec, 1)
                dve.wait_ge(xh_ready, 8 + m + 1)
                nc.vector.tensor_tensor(XL[:, m, 4:NT], MIX[0][:, 4:NT], XH[:, m, 4:NT], ALU.subtract).then_inc(rg_vec, 1)
            for j in range(8):
                dve.wait_ge(norm_root, j + 1)
                step(nc.vector.reciprocal(RN[2 + j % 2][:, :], RN[2 + j % 2][:, :]))
                x = XCQ[:, 4 + j, 4:NT]
                nc.vector.scalar_tensor_tensor(x, x, 128.0 ** -0.5 if j < 4 else 1.0, RN[2 + j % 2][:, 4:NT],
                                               ALU.mult, ALU.mult).then_inc(norm_done, 1)
            step(nc.vector.memset(SP[:, :, :], 0.0))
            for p in range(2):
                nc.vector.engine_nop().then_inc(gdn_dve[p], 1)

            def prepare(i, p):
                s, b = gdn_dve[p], 4 * p
                g0 = 8 * i + 4 * p
                dve.wait_ge(gdn_pe[p], G_PE.before(i))
                nc.vector.tensor_tensor(LM[p][:, :, :], heads_of(UPPER), heads_of(GB[:, ds(g0, 4)]), ALU.mult).then_inc(s, 1)
                dve.wait_ge(gdn_pe[p], G_PE.at(i, "rows"))
                step(nc.vector.tensor_tensor(DA[p][:, :, :], per_head(b), heads_of(GC[:, ds(g0, 4)]), ALU.subtract))
                nc.vector.tensor_tensor(KOC[p][:, :], per_head(b)[:, :, 127], GC[:, ds(g0, 4)], ALU.subtract)
                step(nc.vector.tensor_scalar(DB[p][:, :, :], DA[p][:, :, :], 0.0, None, ALU.max))
                nc.vector.tensor_scalar(DA[p][:, :, :], DA[p][:, :, :], 0.0, None, ALU.min).then_inc(s, 1)
                dve.wait_ge(gdn_act[p], G_ACT.at(i, "exps"))
                step(nc.vector.tensor_tensor(DB[p][:, :, :], DB[p][:, :, :], heads_of(BETA36[:, ds(g0, 4)]), ALU.mult))
                dve.wait_ge(gdn_pe[p], G_PE.at(i, "gram"))
                nc.vector.tensor_tensor(DB[p][:, :, :], per_head(b + 1), DB[p][:, :, :], ALU.mult).then_inc(s, 1)
                step(nc.vector.tensor_tensor(DA[p][:, :, :], DA[p][:, :, :], heads_of(UPPER), ALU.mult))
                dve.wait_ge(gdn_pe[p], G_PE.at(i, "qk"))
                nc.vector.tensor_tensor(DA[p][:, :, :], per_head(b + 2), DA[p][:, :, :], ALU.mult).then_inc(s, 1)
                nc.vector.tensor_tensor(QT[p][:, :, :], QT[p][:, :, :], EG[p][:, :, :], ALU.mult).then_inc(s, 1)
                dve.wait_ge(s, G_DVE.at(i, "lower"))
                nc.vector.tensor_tensor(LM[p][:, :, :], DB[p][:, :, :], heads_of(level_mask(0)), ALU.mult).then_inc(s, 1)
                dve.wait_ge(s, G_DVE.at(i, "m0"))
                nc.vector.tensor_tensor(TA[p][:, :, :], heads_of(IDENT), LM[p][:, :, :], ALU.subtract)
                dve.wait_ge(gdn_pe[p], G_PE.at(i, "m_turned"))
                nc.vector.tensor_tensor(TT[p][:, :, :], heads_of(IDENT), per_head(b + 1), ALU.subtract).then_inc(s, 1)
                dve.wait_ge(s, G_DVE.at(i, "t0"))
                nc.vector.tensor_tensor(LM[p][:, :, :], DB[p][:, :, :], heads_of(level_mask(1)), ALU.mult).then_inc(s, 1)

            def level(l, i, p):
                s, b = gdn_dve[p], 4 * p
                dve.wait_ge(gdn_pe[p], G_PE.at(i, "tt%d" % l))
                nc.vector.tensor_tensor(TT[p][:, :, :], TT[p][:, :, :], per_head(b + 2), ALU.subtract).then_inc(s, 1)
                if l < 6:
                    dve.wait_ge(gdn_pe[p], G_PE.at(i, "ta%d" % l))
                    nc.vector.tensor_tensor(TA[p][:, :, :], TA[p][:, :, :], per_head(b + 3), ALU.subtract).then_inc(s, 1)
                    nc.vector.tensor_tensor(LM[p][:, :, :], DB[p][:, :, :], heads_of(level_mask(l + 1)), ALU.mult)\
                      .then_inc(s, 1)

            def carry(i, p, state):
                s, b = gdn_dve[p], 4 * p
                g0 = 8 * i + 4 * p
                dve.wait_ge(gdn_pe[p], G_PE.at(i, "ks"))
                step(nc.vector.tensor_tensor(RR[p][:, :, :], per_head(b), heads_of(NBEG[:, ds(g0, 4)]), ALU.mult))
                dve.wait_ge(gdn_act[p], G_ACT.at(i, "vb"))
                nc.vector.tensor_tensor(RR[p][:, :, :], RR[p][:, :, :], VB[p][:, :, :], ALU.add).then_inc(s, 1)
                dve.wait_ge(gdn_pe[p], G_PE.at(i, "o"))
                step(nc.vector.tensor_tensor(state[:, :, :], state[:, :, :],
                                             EG[p][:, :, 127:128].to_broadcast([128, 4, 128]), ALU.mult))
                dve.wait_ge(gdn_pe[p], G_PE.at(i, "s"))
                nc.vector.tensor_tensor(state[:, :, :], state[:, :, :], per_head(b + 3), ALU.add).then_inc(s, 1)

            with dve.Fori(0, 4) as i:
                step.enter(i, 2 * 6)
                for p in range(2):
                    prepare(i, p)
                for l in range(1, 7):
                    for p in range(2):
                        level(l, i, p)
                for p in range(2):
                    carry(i, p, SP)
            step.leave(4)
            dve.wait_ge(gdn_pe[0], G_PE.before(4))
            for x in (KT, QT, VT):
                last = nc.vector.memset(x[0][:, :, 64:128], 0.0)
            last.then_inc(pad_zeroed, 1)
            prepare(4, 0)
            for l in range(1, 7):
                level(l, 4, 0)
            dve.wait_ge(state_in, 16)
            carry(4, 0, SS)
            dve.wait_ge(gdn_act[1], G_ACT.before(4))
            dve.wait_ge(gdn_act[0], G_ACT.before(5))
            nc.vector.memset(OT[:, :, 0:S0], 0.0)
            nc.vector.memset(OT[:, :, S0 + 64:P0], 0.0).then_inc(o_zeroed, 1)

            def o_lo(h):
                dve.wait_ge(xh_ready, 12 + h + 1)
                nc.vector.tensor_tensor(XL[:, 4 + h, :], OT[:, h, :], XH[:, 4 + h, :], ALU.subtract).then_inc(mix_ready[0], 1)

            dve.wait_ge(z_in, 16)
            for h in range(4):
                dve.wait_ge(o_root, h + 1)
                step(nc.vector.reciprocal(RN[2 + h % 2][:, :], RN[2 + h % 2][:, :]))
                step(nc.vector.scalar_tensor_tensor(OT[:, h, :], OT[:, h, :], col("b_norm_g"), RN[2 + h % 2][:, :],
                                                    ALU.mult, ALU.mult))
                nc.vector.tensor_tensor(OT[:, h, :], OT[:, h, :], ZT[:, h, :], ALU.mult).then_inc(o_gated, 1)
                if h >= 1:
                    o_lo(h - 1)
            o_lo(3)

            def norm(n):
                dve.wait_ge(ln_mean, 1 + n)
                for k in range(8):
                    nc.vector.scalar_tensor_tensor(rows(Y[:, k, :]), banks(0), -1 / 1024, rows(Y[:, k, :]),
                                                   ALU.mult, ALU.add).then_inc(ln_sub, 1)
                dve.wait_ge(ln_root, 1 + n)
                step(nc.vector.reciprocal(RS[:, :], RS[:, :]))
                dve.wait_ge(ln_sub, 8 + 8 * n)
                dve.wait_ge(ln_sq, 8 + 8 * n)

                def lo(k):
                    dve.wait_ge(ln_hi, 2 * k + 2 + 16 * n)
                    nc.vector.tensor_tensor(XL[:, k, :], Y[:, k, :], XH[:, k, :], ALU.subtract).then_inc(ln_lo, 1)
                    if n % 2 == 0:
                        dve.wait_ge(ln_lo, 2 * k + 1 + LN_LO[n])
                        nc.vector.tensor_scalar(Y[:, k, :], Y[:, k, :], ALPHA, None, ALU.mult).then_inc(ln_lo, 1)
                for k in range(8):
                    nc.vector.tensor_tensor(Y[:, k, :], Y[:, k, :], RS[:, :], ALU.mult).then_inc(ln_scaled, 1)
                    if k >= 2:
                        lo(k - 2)
                lo(6)
                lo(7)
                gaps(ln_lo, LN_LO[n + 1], gaps_zeroed)

            def gaps(s, value, done):
                dve.wait_ge(s, value)
                for x in (XH, XL):
                    nc.vector.memset(x[:, :, 0:S0].bitcast(F32), 0.0)
                    last = nc.vector.memset(x[:, :, S0 + 64:P0].bitcast(F32), 0.0)
                last.then_inc(done, 1)

            def convolve(l, g, t):
                dve.wait_ge(up_read, 4 * g + t + 2 + 45 * l)
                f = 2 * g + (t if t < 2 else 20 + t)
                u, y = UF[:, t % 2, :], CB[:, t, 4:NT]
                hist, kept = sp_["hist_ffn"] + 88 * l + 2 * f, op["ffn"] + 176 * l + 4 * f
                step(nc.vector.tensor_copy(u[:, S0 - 2:S0], SMALL[:, ds(hist, 2)]))
                nc.vector.tensor_copy(KEPT[:, ds(kept, 2)], u[:, S0 + 62:S0 + 64])
                nc.vector.tensor_copy(KEPT[:, ds(kept + 2, 2)], u[:, NT - 2:NT])
                step(nc.vector.scalar_tensor_tensor(y, u[:, 3:NT - 1], col_at("ffn_w1%d" % l, f), y, ALU.mult, ALU.add))
                nc.vector.scalar_tensor_tensor(y, u[:, 2:NT - 2], col_at("ffn_w0%d" % l, f), y, ALU.mult, ALU.add)\
                  .then_inc(ffn_conv, 1)

            def multiply(l, g):
                for j in range(2):
                    dve.wait_ge(ffn_silu, 2 * g + j + 1 + 22 * l)
                    dve.wait_ge(ffn_conv, 4 * g + 2 + j + 3 + 46 * l)
                    nc.vector.tensor_tensor(CB[:, 2 + j, :], CB[:, 2 + j, :], CB[:, j, :], ALU.mult).then_inc(ffn_mul, 1)

            def low(l, g):
                for j in range(2):
                    dve.wait_ge(h_hi, 2 * g + j + 1 + 22 * l)
                    last = nc.vector.tensor_tensor(HL[:, j, :], CB[:, 2 + j, :], HH[:, j, :], ALU.subtract)
                last.then_inc(h_done, 1)

            def add_down(l, g, unit):
                for m in range(8):
                    if m % 4 < 3:
                        dve.wait_ge(part_done, 6 * g + OUT_PART[l] + 3 * (m // 4) + m % 4 + 1)
                    else:
                        dve.wait_ge(unit_done, unit + m // 4 + 3)
                    nc.vector.tensor_tensor(rows(Y[:, m, :]), rows(Y[:, m, :]), banks(m % 2), ALU.add)\
                      .then_inc(down_read, 1)

            def layer_end(l):
                first = OUT_UNIT[l]
                dve.sem_inc(out_read, 2)
                dve.sem_inc(down_read, 2)
                dve.sem_inc(ffn_conv, 2)
                dve.sem_inc(h_done, 1)
                dve.sem_inc(gate_added, 2)
                dve.wait_ge(x_back, 16 + 16 * l)
                with dve.Fori(0, 4) as i:
                    for s in range(2):
                        dve.wait_ge(unit_done, 2 * i + s + first + 3)
                        nc.vector.scalar_tensor_tensor(
                            rows(Y[:, ds(2 * i + s, 1), :].rearrange("p a n -> p (a n)")),
                            rows(XR[:, ds(2 * i + s, 1), :].rearrange("p a n -> p (a n)")), ALPHA, banks(s),
                            ALU.mult, ALU.add).then_inc(out_read, 1)
                dve.wait_ge(out_read, 10 + 10 * l)
                norm(2 * l)
                for t in range(4):
                    convolve(l, 0, t)
                multiply(l, 0)
                low(l, 0)
                with dve.Fori(1, 11) as g:
                    step.enter(g - 1, 8)
                    for t in range(4):
                        convolve(l, g, t)
                    multiply(l, g)
                    dve.wait_ge(down_read, 8 * g - 6 + 90 * l)
                    add_down(l, g - 1, 6 * g + first + 10)
                    low(l, g)
                step.leave(10)
                dve.wait_ge(down_read, 82 + 90 * l)
                add_down(l, 10, first + 72)
                dve.wait_ge(down_read, 90 + 90 * l)
                dve.wait_ge(p_hi, 1 + l)
                for j in range(2):
                    nc.vector.tensor_tensor(PL[:, j, :], P32[:, j, :], PH[:, j, :], ALU.subtract).then_inc(p_split, 1)
                norm(2 * l + 1)
                with dve.Fori(0, 4) as i:
                    step.enter(i, 2)
                    for s in range(2):
                        m = ds(2 * i + s, 1)
                        dve.wait_ge(gate_read, 2 * i + s + 3 + 10 * l)
                        dve.wait_ge(wp_read, 8 + 8 * l)
                        step(nc.vector.tensor_tensor(SG[s][:, :], SG[s][:, :],
                                                     PP[:, m, :].rearrange("p a n -> p (a n)"), ALU.mult))
                        y = Y[:, m, :].rearrange("p a n -> p (a n)")
                        nc.vector.tensor_tensor(y, y, SG[s][:, :], ALU.add).then_inc(gate_added, 1)
                step.leave(4)

            layer_end(0)
            for k in range(8):
                dve.wait_ge(x_hi, k + 1)
                nc.vector.tensor_tensor(XL[:, k, :], Y[:, k, :], XH[:, k, :], ALU.subtract).then_inc(x_lo, 1)
            gaps(x_lo, 8, in_ready)
            dve.wait_ge(x_out, 16)
            with dve.Fori(0, 7) as i:
                step.enter(i, 10)
                for s in range(2):
                    dve.wait_ge(in1_read, 2 * i + s + 3)
                    step(nc.vector.tensor_copy(U1[:, s, S0 - 1:S0], SMALL[:, ds(sp_["hist_shift"] + 2 * i + s, 1)]))
                    kept = op["shift"] + 4 * i + 2 * s
                    step(nc.vector.tensor_copy(KEPT[:, ds(kept, 1)], U1[:, s, S0 + 63:S0 + 64]))
                    step(nc.vector.tensor_copy(KEPT[:, ds(kept + 1, 1)], U1[:, s, NT - 1:NT]))
                    step(nc.vector.memset(DX[:, s, 0:4], 0.0))
                    step(nc.vector.tensor_tensor(DX[:, s, 4:NT], U1[:, s, 3:NT - 1], U1[:, s, 4:NT], ALU.subtract))
                    nc.vector.scalar_tensor_tensor(DX[:, s, 4:NT], DX[:, s, 4:NT], col_at("c_mu", 2 * i + s), U1[:, s, 4:NT],
                                                   ALU.mult, ALU.add).then_inc(shifted, 1)
            step.leave(7)
            for slot in range(2):
                dve.wait_ge(m_root, slot + 1)
                nc.vector.reciprocal(RSD[slot][:, :], RSD[slot][:, :]).then_inc(m_inv, 1)
            for j in range(5):
                x, g = (QA[:, j, :], col("d_qa_g", j)) if j < 3 else (CR[:, j - 3, :], col("d_kva_g", j - 3))
                dve.wait_ge(m_inv, 1 + j // 3)
                nc.vector.scalar_tensor_tensor(x, x, g, RSD[j // 3][:, :], ALU.mult, ALU.mult).then_inc(m_scaled, 1)
            dve.wait_ge(m_hi, 1)
            nc.vector.tensor_tensor(CL[:, :, NT:NK], CCK[:, :, :], CH[:, :, NT:NK], ALU.subtract).then_inc(m_lo, 1)
            for j in range(5):
                dve.wait_ge(m_hi, j + 2)
                l, x, h = (QAL[:, j, :], QA[:, j, :], QAH[:, j, :]) if j < 3 else (
                    CL[:, j - 3, 0:NT], CR[:, j - 3, :], CH[:, j - 3, 0:NT])
                nc.vector.tensor_tensor(l, x, h, ALU.subtract).then_inc(m_lo, 1)

            def rotate(out, x, slot, tmp, done):
                step(nc.vector.tensor_tensor(rows(tmp), banks(slot), rows(ROPE[:, 1, :]), ALU.mult))
                step(nc.vector.tensor_tensor(out, x, ROPE[:, 0, :], ALU.mult))
                nc.vector.tensor_tensor(out, out, tmp, ALU.add).then_inc(done, 1)

            dve.wait_ge(mla_in, 16)
            dve.wait_ge(swapped, 1)
            rotate(KRR[:, 0:NT], KRW[:, :], 0, TK[:, :], kr_done)
            dve.wait_ge(kr_out, 16)
            for r in range(2):
                dve.wait_ge(swapped, 2 + r)
                dve.wait_ge(qkv_read, 10)
                rotate(QR[:, r, :], QR[:, r, :], r, TQ[r][:, :], q_rotated)

            def top(i, hh, n):
                t0, nq = queries(n)
                s, g = 18 * i + 9 * hh + n, (9 * hh + n) % 2
                nk = 256 if n == 8 else 128 * (n + 1)
                dve.wait_ge(a_scores, s + 2)
                dve.wait_ge(a_scaled, s)
                sc = PS[0:nq, 2 * g:2 * g + 2, :].rearrange("p b n -> p (b n)")
                if n < 8:
                    step(nc.vector.memset(sc[0:64, nk - 64:nk], -1e30))
                else:
                    step(nc.vector.memset(sc[:, nk - 64:nk], -1e30))
                step(nc.vector.tensor_reduce(AST[g][0:nq, 3:4], sc[:, 0:nk], AX.X, ALU.max))
                nc.vector.tensor_scalar(AST[g][0:nq, 0:1], AST[g][0:nq, 3:4], -D_SCALE, None, ALU.mult).then_inc(a_max, 1)

            def keys2(i, hh, n):
                t0, nq = queries(n)
                s, g = 18 * i + 9 * hh + n, (9 * hh + n) % 2
                dve.wait_ge(a_probs, s + 3)
                nc.vector.reciprocal(AST[g][0:nq, 2:3], AST[g][0:nq, 1:2]).then_inc(a_inv, 1)
                if 4 <= n < 8:
                    dve.wait_ge(a_turned, s + 2)
                    dve.wait_ge(a_out, s + 1)
                    nk = 128 * (n - 3)
                    nc.vector.tensor_copy(PTB[:, 512:512 + nk], PS[:, 5, 0:nk]).then_inc(a_keys2, 1)

            def low_out(i, hh, n):
                t0, nq = queries(n)
                s = 18 * i + 9 * hh + n
                dve.wait_ge(a_hi, 2 * s + 2)
                m, own = ds(2 * i + hh + 4, 1), 64 if n == 8 else 128
                nc.vector.tensor_tensor(XL[:, m, t0:t0 + own].rearrange("p a n -> p (a n)"), PS[:, 7, 0:own],
                                        XH[:, m, t0:t0 + own].rearrange("p a n -> p (a n)"), ALU.subtract).then_inc(a_hi, 1)

            order = [(hh, n) for hh in range(2) for n in range(STEPS)]
            with dve.Fori(0, 2) as i:
                step.enter(i, 2 * 9 * 2)
                top(i, 0, 0)
                for x, (hh, n) in enumerate(order):
                    if x + 1 < len(order):
                        top(i, *order[x + 1])
                    keys2(i, hh, n)
                    low_out(i, hh, n)
            step.leave(2)
            def c_rows(i):
                dve.wait_ge(c_in, 144 if i is LAST else 16 * i + 16)
                dve.wait_ge(c_act, C_ACT.at(i, "c"))
                flat = CUM[:, :, :].rearrange("p m n -> p (m n)")
                nc.vector.tensor_tensor_scan(flat, RUN[:, :], flat, 0.0, ALU.mult, ALU.add).then_inc(c_dve, 1)
                nc.vector.tensor_tensor(KKN[:, :, :], CIN[:, 4:8, :], cols_of("c_k_k"), ALU.mult).then_inc(c_dve, 1)
                dve.wait_ge(c_act, C_ACT.at(i, "a"))
                nc.vector.scalar_tensor_tensor(K2[:, :, :], SA[:, :, :], -1.0, CIN[:, 4:8, :], ALU.add, ALU.mult)\
                  .then_inc(c_dve, 1)
                dve.wait_ge(c_dve, C_DVE.at(i, "k2a"))
                nc.vector.tensor_tensor(K2[:, :, :], K2[:, :, :], cols_of("c_k_a"), ALU.mult).then_inc(c_dve, 1)
                dve.wait_ge(c_dve, C_DVE.at(i, "k2b"))
                nc.vector.tensor_tensor(K2[:, :, :], K2[:, :, :], CIN[:, 4:8, :], ALU.add).then_inc(c_dve, 1)
                dve.wait_ge(c_act, C_ACT.at(i, "inv"))
                nc.vector.tensor_tensor(KKN[:, :, :], KKN[:, :, :], CT[:, :, :], ALU.mult).then_inc(c_dve, 1)
                dve.wait_ge(c_dve, C_DVE.at(i, "kk"))
                nc.vector.tensor_tensor(BK[:, :, :], KKN[:, :, :], SA[:, :, :], ALU.mult).then_inc(c_dve, 1)
                nc.vector.tensor_tensor(CT[:, :, :], CIN[:, 0:4, :], K2[:, :, :], ALU.mult).then_inc(c_dve, 1)
                dve.wait_ge(c_dve, C_DVE.at(i, "rk"))
                nc.vector.tensor_tensor(CT[:, :, :], CT[:, :, :], cols_of("c_r_k"), ALU.mult).then_inc(c_dve, 1)
                dve.wait_ge(c_pe, C_PE.at(i, "bonus"))
                nc.vector.tensor_tensor(BONUS[:, :, :], per_head(4), CIN[:, 8:12, :], ALU.mult).then_inc(c_dve, 1)

            def level_blocks(l, p):
                for h in range(2):
                    mask = SMALL[half(h), sp_["level"] + 128 * l + 64 * h:sp_["level"] + 128 * l + 64 * h + 64]
                    last = nc.vector.tensor_tensor(LM_B[p][half(h), :, half(h)], stacked(p, 0, 0)[half(h), :, :],
                                                   pairs_of(mask), ALU.mult)
                return last

            def c_prepare(i, p):
                t = half(p)
                dve.wait_ge(c_act, C_ACT.at(i, "pi", p))
                nc.vector.tensor_tensor(A_S[p][:, :, :], KKN[:, :, t], PX[p][:, :, 0:64], ALU.mult).then_inc(c_dve, 1)
                nc.vector.tensor_tensor(B_S[p][:, :, :], BK[:, :, t], PI_S[p][:, :, :], ALU.mult).then_inc(c_dve, 1)
                for h in range(2):
                    last = nc.vector.tensor_tensor(K_B[p][half(h), :, half(h)], K2[half(h), :, t], PI_S[p][half(h), :, :],
                                                   ALU.mult)
                last.then_inc(c_dve, 1)
                nc.vector.tensor_tensor(R_S[p][:, :, :], CIN[:, 0:4, t], PX[p][:, :, 1:65], ALU.mult).then_inc(c_dve, 1)
                dve.wait_ge(c_pe, C_PE.at(i, "l", p))
                level_blocks(0, p).then_inc(c_dve, 1)
                dve.wait_ge(c_dve, C_DVE.at(i, "lm0", p))
                nc.vector.tensor_tensor(TA_B[p][:, :, :], heads_of(IDENT), LM_B[p][:, :, :], ALU.subtract).then_inc(c_dve, 1)
                dve.wait_ge(c_pe, C_PE.at(i, "mt", p))
                nc.vector.tensor_tensor(TT_S[p][:, :, :], pairs_of(PAIR_ID), stacked(p, 2, 1), ALU.subtract).then_inc(c_dve, 1)
                dve.wait_ge(c_dve, C_DVE.at(i, "ta0", p))
                level_blocks(1, p).then_inc(c_dve, 1)
                for h in range(2):
                    strict = small("pair_strict", 64)[half(h), :]
                    last = nc.vector.tensor_tensor(AK_B[p][half(h), :, half(h)], stacked(p, 1, 0)[half(h), :, :],
                                                   pairs_of(strict), ALU.mult)
                last.then_inc(c_dve, 1)
                upper = pairs_of(small("pair_upper", 64))
                nc.vector.scalar_tensor_tensor(RB_S[p][:, :, :], stacked(p, 1, 1), -1.0, upper, ALU.mult, ALU.mult)\
                  .then_inc(c_dve, 1)
                nc.vector.tensor_tensor(RK_S[p][:, :, :], stacked(p, 2, 0), upper, ALU.mult).then_inc(c_dve, 1)

            def c_level(l, i, p):
                dve.wait_ge(c_pe, C_PE.at(i, "tt%d" % l, p))
                if l == 5:
                    for h in range(2):
                        last = nc.vector.tensor_tensor(TT_B[p][half(h), :, half(h)], TT_S[p][half(h), :, :],
                                                       stacked(p, 2, 0)[half(h), :, :], ALU.subtract)
                    last.then_inc(c_dve, 1)
                    return
                nc.vector.tensor_tensor(TT_S[p][:, :, :], TT_S[p][:, :, :], stacked(p, 2, 0), ALU.subtract).then_inc(c_dve, 1)
                dve.wait_ge(c_pe, C_PE.at(i, "ta%d" % l, p))
                nc.vector.tensor_tensor(TA_B[p][:, :, :], TA_B[p][:, :, :], per_head(4 * p + 3), ALU.subtract)\
                  .then_inc(c_dve, 1)
                level_blocks(l + 1, p).then_inc(c_dve, 1)

            def c_carry(i, p, state):
                dve.wait_ge(c_act, C_ACT.at(i, "u", p))
                for h in range(2):
                    last = nc.vector.tensor_copy(U_B[p][half(h), :, half(h)], U_S[p][half(h), :, :])
                last.then_inc(c_dve, 1)
                dve.wait_ge(c_pe, C_PE.at(i, "m", p))
                nc.vector.tensor_tensor(state[:, :, :], state[:, :, :], stacked(p, 3, 0), ALU.add).then_inc(c_dve, 1)
                dve.wait_ge(c_dve, C_DVE.at(i, "m0", p))
                nc.vector.tensor_tensor(state[:, :, :], state[:, :, :], PX[p][:, :, 64:65].to_broadcast([128, 4, 64]),
                                        ALU.mult).then_inc(c_dve, 1)

            def c_end(i, n):
                dve.wait_ge(c_pe, C_PE.at(i, "mean"))
                o = CO[:, :, 0:n]
                nc.vector.scalar_tensor_tensor(o, PS[:, 0, 0:4 * n].rearrange("p (m n) -> p m n", m=4), -1 / 64, o,
                                               ALU.mult, ALU.add).then_inc(c_dve, 1)
                dve.wait_ge(c_act, C_ACT.at(i, "inv2"))
                nc.vector.tensor_tensor(o, o, SA[:, :, 0:n], ALU.mult).then_inc(c_dve, 1)
                dve.wait_ge(c_act, C_ACT.at(i, "affine"))
                nc.vector.tensor_tensor(o, o, BONUS[:, :, 0:n], ALU.add).then_inc(c_dve, 1)
                dve.wait_ge(c_dve, C_DVE.at(i, "plus"))
                nc.vector.tensor_tensor(o, o, CG[:, :, 0:n], ALU.mult).then_inc(c_dve, 1)
                where = slice(S0, S0 + n) if i is LAST else ds(128 * i + P0, n)
                dve.wait_ge(c_act, C_ACT.at(i, "hi"))
                nc.vector.tensor_tensor(XL[:, 0:4, where], o, XH[:, 0:4, where], ALU.subtract).then_inc(c_dve, 1)

            dve.wait_ge(a_hi, 73)
            for x in ZEROED:
                nc.vector.memset(x[:, :, :], 0.0)
            step(nc.vector.memset(MS[0][:, :, :], 0.0))
            step(nc.vector.memset(RUN[:, :], 1.0))
            nc.vector.memset(RUN[:, :].rearrange("p (c t) -> p c t", t=64)[:, :, 0:1], 0.0)
            for p in range(2):
                nc.vector.memset(PX[p][:, :, 0:1], 1.0)
            for x in (XH, XL):
                nc.vector.memset(x[:, 0:4, 0:S0].bitcast(F32), 0.0)
                nc.vector.memset(x[:, 0:4, S0 + 64:P0].bitcast(F32), 0.0)
            nc.vector.engine_nop().then_inc(c_ready, 1)
            dve.wait_ge(c_ready, 1)
            with dve.Fori(0, 8) as i:
                c_rows(i)
                for p in range(2):
                    c_prepare(i, p)
                for l in C_LEVELS:
                    for p in range(2):
                        c_level(l, i, p)
                for p in range(2):
                    c_carry(i, p, MS[0])
                c_end(i, 128)
            dve.wait_ge(c_state_in, 16)
            c_rows(LAST)
            c_prepare(LAST, 0)
            for l in C_LEVELS:
                c_level(l, LAST, 0)
            c_carry(LAST, 0, MS[1])
            c_end(LAST, 64)
            dve.wait_ge(c_dve, C_DVE.at(LAST, "lo"))
            dve.sem_inc(mix_ready[1], 4)
            layer_end(1)
            nc.vector.engine_nop().then_inc(kept_ready, 1)


def kernel(**inputs):
    import numpy as np
    import concourse.bacc as bacc
    from concourse import mybir
    from concourse.bass_utils import run_bass_kernel_spmd

    nc = bacc.Bacc("TRN2", target_bir_lowering=False, num_devices=1)
    arrays, io = {}, {}
    for name, v in lay_out(inputs).items():
        arrays["in_" + name] = v
        io[name] = nc.dram_tensor("in_" + name, v.shape, mybir.dt.float32, kind="ExternalInput").ap()
    for name, shape in outputs().items():
        io[name] = nc.dram_tensor("out_" + name, shape, mybir.dt.float32, kind="ExternalOutput").ap()
    build(nc, io, arrays["in_units"].shape[0])
    r = run_bass_kernel_spmd(nc, [arrays], core_ids=[0])
    return gather({name: r.results[0]["out_" + name] for name in outputs()})
```

```python
def _np():
    import numpy as np
    return np


def column_plan():
    names = [("a_conv_w0", 4), ("a_conv_w1", 4), ("a_conv_w2", 4), ("a_conv_w3", 4)]
    plan, at = {}, 0
    for name, n in [("conv0_w0", 16), ("conv0_w1", 16), ("conv0_w2", 16), ("conv0_w3", 16), ("conv0_b", 16),
                    ("a_b_r", 4), ("a_b_i", 4), ("a_lambda", 4), ("b_norm_g", 1), ("c_mu", 14), ("c_w0", 4), ("c_a0", 4),
                    ("c_k_k", 4), ("c_k_a", 4), ("c_r_k", 4), ("c_lnx_g", 4), ("c_lnx_b", 4), ("d_qa_g", 3), ("d_kva_g", 2)]:
        plan[name] = at
        at += n
    for layer in range(2):
        for name, n in [("ffn_w0", 44), ("ffn_w1", 44), ("ffn_w2", 44), ("ffn_b", 44), ("ln_mix_g", 8), ("ln_mix_b", 8),
                        ("ln_ffn_g", 8), ("ln_ffn_b", 8), ("ple_b", 8)]:
            plan[name + str(layer)] = at
            at += n
    return plan, at


def small_plan():
    plan, at = {}, 0
    for name, n in [("identity", 128), ("ones", 128), ("pair_ones", 128), ("upper", 128), ("level", 7 * 128), ("half_swap", 128),
                    ("pair_upper", 64), ("pair_strict", 64), ("pair_identity", 64),
                    ("w_beta_alpha", 64), ("dt_bias", 36), ("a_log", 36),
                    ("hist_conv0", 48), ("h0", 4), ("hist_shift", 14), ("hist_ffn", 2 * 88)]:
        plan[name] = at
        at += n
    return plan, at


def out_plan():
    plan, at = {}, 0
    for name, n in [("conv0", 16 * 6), ("h", 8), ("shift", 28), ("ffn", 2 * 44 * 4)]:
        plan[name] = at
        at += n
    return plan, at


S0, P0, NT = 4, 72, 1096


def lay_out(inp):
    np = _np()
    f32 = np.float32
    a = {k: np.asarray(v) for k, v in inp.items()}

    def tokens(sample, prompt):
        n = sample.shape[1]
        t = np.zeros((n, NT), f32)
        t[:, S0:S0 + 64] = sample.T
        t[:, P0:] = prompt.T
        return np.ascontiguousarray(t.reshape(n // 128, 128, NT).transpose(1, 0, 2))

    def unit(w):
        k, m = w.shape
        u = w.reshape(k // 128, 128, m // 128, 128).transpose(1, 2, 0, 3).reshape(128, -1)
        out = np.zeros((128, 1024), f32)
        out[:, :u.shape[1]] = u
        return out

    units = []

    def full(w):
        for m in range(w.shape[1] // 128):
            units.append(unit(w[:, m * 128:(m + 1) * 128]))

    def ffn(layer):
        up, down = a["ffn_w_up"][layer], a["ffn_w_down"][layer]

        def ups(g):
            for f in (2 * g, 2 * g + 1, 22 + 2 * g, 23 + 2 * g):
                units.append(unit(up[:, f * 128:(f + 1) * 128]))

        def downs(g):
            for d in range(2):
                units.append(unit(down[g * 256:(g + 1) * 256, d * 512:(d + 1) * 512]))
        ups(0)
        for g in range(1, 11):
            ups(g)
            downs(g - 1)
        downs(10)

    def ple(layer):
        for d in range(2):
            units.append(unit(a["ple_w_proj"][layer][:, d * 512:(d + 1) * 512]))
        full(a["ple_w_gate"][layer])

    full(a["w_in0"][:, :3072])
    full(a["w_out0"])
    ffn(0)
    ple(0)
    w1 = a["w_in1"]
    full(w1[:, :1792])
    full(w1[:, 1792:2432])
    full(np.concatenate([w1[:, 2432:2496], w1[:, 2432:2496]], 1))
    qb = a["d_w_qb"]
    cols = [qb[:, h * 192:h * 192 + 128] for h in range(4)]
    cols += [np.concatenate([qb[:, h * 192 + 128:(h + 1) * 192] for h in (2 * r, 2 * r + 1)], 1) for r in range(2)]
    for m in range(0, 6, 2):
        units.append(unit(np.concatenate(cols[m:m + 2], 1)))
    kvb = a["d_w_kvb"]
    for m in range(0, 4, 2):
        units.append(unit(np.concatenate([kvb[:, h * 256:h * 256 + 128] for h in (m, m + 1)], 1)))
    v = np.concatenate([kvb[:, h * 256 + 128:(h + 1) * 256] for h in range(4)], 1)
    units.append(np.ascontiguousarray(v.reshape(2, 128, 512).transpose(1, 0, 2).reshape(128, 1024)))
    full(a["w_out1"])
    ffn(1)
    ple(1)

    def col(v):
        return np.asarray(v).reshape(-1, 128).T

    cp, ncol = column_plan()
    columns = np.zeros((128, ncol), f32)

    def put(name, v):
        c = col(v)
        columns[:, cp[name]:cp[name] + c.shape[1]] = c
    for j in range(4):
        put("conv0_w%d" % j, np.concatenate([a["a_conv_w"][j], a["b_conv_w"][j]]))
    put("conv0_b", a["a_conv_b"])
    for n in ("a_b_r", "a_b_i", "a_lambda", "b_norm_g", "c_mu", "c_w0", "c_a0", "c_k_k", "c_k_a", "c_r_k", "c_lnx_g",
              "c_lnx_b", "d_qa_g", "d_kva_g"):
        put(n, a[n])
    for i in range(2):
        for j in range(3):
            put("ffn_w%d%d" % (j, i), a["ffn_conv_w"][i][j])
        put("ffn_b%d" % i, a["ffn_conv_b"][i])
        put("ln_mix_g%d" % i, a["ln_mix_g"][i])
        put("ln_mix_b%d" % i, a["ln_mix_b"][i])
        put("ln_ffn_g%d" % i, a["ln_ffn_g"][i])
        put("ln_ffn_b%d" % i, a["ln_ffn_b"][i])
        put("ple_b%d" % i, a["ple_b_gate"][i])

    sp, nsmall = small_plan()
    small = np.zeros((128, nsmall), f32)

    def sput(name, v):
        v = np.asarray(v).reshape(128, -1)
        small[:, sp[name]:sp[name] + v.shape[1]] = v
    t = np.arange(128)
    same_half = (t[:, None] // 64) == (t[None, :] // 64)
    sput("identity", np.eye(128, dtype=f32))
    sput("ones", np.ones((128, 128), f32))
    sput("pair_ones", same_half.astype(f32))
    sput("upper", (t[:, None] <= t[None, :]).astype(f32))
    sput("level", np.stack([((t[:, None] // m) % 2 == 1) & (t[None, :] // m == t[:, None] // m - 1)
                            for m in (1, 2, 4, 8, 16, 32, 64)], 1).astype(f32))
    swap = np.zeros((128, 128), f32)
    swap[(t // 64) * 64 + (t % 64 + 32) % 64, t] = 1
    sput("half_swap", swap)
    sput("pair_upper", (t[:, None] % 64 <= np.arange(64)[None, :]).astype(f32))
    sput("pair_strict", (t[:, None] % 64 < np.arange(64)[None, :]).astype(f32))
    sput("pair_identity", (t[:, None] % 64 == np.arange(64)[None, :]).astype(f32))
    sput("w_beta_alpha", a["w_in0"][:, 3072:3080].reshape(8, 128, 8).transpose(1, 0, 2))
    w_gates = np.zeros((128, 2, 4, 128), f32)
    for g, key in enumerate(("a_w_r", "a_w_i")):
        for b in range(8):
            h = (b % 2) * 64
            w_gates[h:h + 64, g, b // 2, h:h + 64] = a[key][b]
    sput("dt_bias", np.broadcast_to(a["b_dt_bias"], (128, 9, 4)))
    sput("a_log", np.broadcast_to(a["b_a_log"], (128, 9, 4)))
    hist = np.concatenate([a["state_a_conv"][0], a["state_b_conv"][0]], 1)
    sput("hist_conv0", hist.reshape(3, 16, 128).transpose(2, 1, 0))
    sput("h0", a["state_a_h"].reshape(4, 128).T)
    sput("hist_shift", a["state_c_shift"].reshape(14, 128).T)
    sput("hist_ffn", a["state_ffn_conv"][:, 0].reshape(2, 2, 44, 128).transpose(3, 0, 2, 1))

    inv = (f32(10000.0) ** (-np.arange(32, dtype=f32) / f32(32))).astype(f32)
    pos = np.zeros(NT, f32)
    pos[S0:S0 + 64] = 128 + np.arange(64)
    pos[P0:] = np.arange(1024)
    ang = (pos[:, None] * inv[None, :]).astype(f32)
    cos, sin = np.cos(ang).T.astype(f32), np.sin(ang).T.astype(f32)
    rope = np.stack([np.concatenate([cos] * 4, 0), np.concatenate([-sin, sin] * 2, 0)], 1)
    ckv = a["cache_d_ckv"][0].T.reshape(2, 128, 128).transpose(1, 0, 2)
    kr = np.concatenate([a["cache_d_krope"][0].T] * 2, 0)
    return {
        "x": tokens(a["x_sample"][0], a["x_prompt"][0]),
        "p": np.stack([tokens(a["p_sample"][i, 0], a["p_prompt"][i, 0]) for i in range(2)]),
        "units": np.stack(units), "columns": columns, "small": small,
        "w_gates": w_gates, "w_lora": np.stack([np.concatenate([a["c_w2"], a["c_a2"]], 0), a["c_g2"]], 1),
        "s_b": np.ascontiguousarray(a["state_b_s"][0].transpose(1, 0, 2)),
        "s_c": np.ascontiguousarray(a["state_c_s"][0].reshape(4, 2, 64, 64).transpose(1, 3, 0, 2).reshape(128, 4, 64)),
        "rope": np.ascontiguousarray(rope), "cache_ckv": np.ascontiguousarray(ckv), "cache_krope": kr,
    }


def outputs():
    _, n = out_plan()
    return {"y": (128, 8, NT), "kept": (128, n), "s_b_p": (128, 4, 128), "s_b_s": (128, 4, 128),
            "s_c_p": (128, 4, 64), "s_c_s": (128, 4, 64), "ckv": (128, 2, NT), "krope": (64, NT)}


def gather(r):
    np = _np()
    op, _ = out_plan()

    def rows(v, at, n):
        return np.ascontiguousarray(v[:, :, at:at + n].transpose(2, 1, 0).reshape(1, n, -1))

    def kept(name, tiles, each):
        return r["kept"][:, op[name]:op[name] + tiles * each].reshape(128, tiles, each)
    y, ckv = r["y"], r["ckv"]
    conv, h, shift = kept("conv0", 16, 6), kept("h", 4, 2), kept("shift", 14, 2)
    f = kept("ffn", 88, 4)
    out = [rows(y, P0, 1024), rows(y, S0, 64)]
    for at in (3, 0):
        out.append(rows(conv[:, 0:4], at, 3))
    for at in (1, 0):
        out.append(rows(h, at, 1)[0])
    for at in (3, 0):
        out.append(rows(conv[:, 4:16], at, 3))
    for n in ("s_b_p", "s_b_s"):
        out.append(np.ascontiguousarray(r[n].transpose(1, 0, 2))[None])
    for at in (1, 0):
        out.append(rows(shift, at, 1))
    for n in ("s_c_p", "s_c_s"):
        out.append(np.ascontiguousarray(r[n].reshape(2, 64, 4, 64).transpose(2, 0, 3, 1).reshape(1, 8, 64, 64)))
    out += [rows(ckv, P0, 1024), rows(ckv, S0, 64)]
    kr = r["krope"][:, None, :]
    out += [rows(kr, P0, 1024), rows(kr, S0, 64)]
    for at in (2, 0):
        out.append(np.stack([rows(f[:, i * 44:(i + 1) * 44], at, 2) for i in range(2)]))
    return tuple(out)


def build(nc, io, NU):
    import concourse.bass as bass
    from concourse import mybir
    from contextlib import ExitStack

    F32, F32R = mybir.dt.float32, mybir.dt.float32r
    ACT, ALU, AX = mybir.ActivationFunctionType, mybir.AluOpType, mybir.AxisListType
    ds = bass.ds
    NB, BW = 4, NT // 4
    TILE = NT * 4
    cp, NCOL = column_plan()
    sp_, NSMALL = small_plan()
    op, NKEPT = out_plan()
    PROMPT_TILES = 8
    SAMPLE = PROMPT_TILES
    ALPHA = 4.0 ** 0.25

    ctx = ExitStack()
    with ctx:
        def sb(name, shape, dt=F32):
            return ctx.enter_context(nc.sbuf_tensor(name, shape, dt))

        def sem(name):
            return ctx.enter_context(nc.semaphore(name))

        RAW = sb("RAW", [128, 2, 1024])
        WHI = sb("WHI", [128, 2, 1024], F32R)
        WLO = sb("WLO", [128, 2, 1024], F32R)
        COL = sb("COL", [128, NCOL])
        SMALL = sb("SMALL", [128, NSMALL])
        KEPT = sb("KEPT", [128, NKEPT])
        EPS = sb("EPS", [128, 4])
        WBAH, WBAL = sb("WBAH", [128, 64], F32R), sb("WBAL", [128, 64], F32R)
        BETA36, GTMP, GB = sb("BETA36", [128, 36]), sb("GTMP", [128, 3, 36]), sb("GB", [128, 36])
        GC, EGC, NBEG = sb("GC", [128, 36]), sb("EGC", [128, 36]), sb("NBEG", [128, 36])
        LAM = sb("LAM", [128, 16])
        KOC = [sb("KOC%d" % p, [128, 4]) for p in range(2)]
        base = -(-nc.sbuf_base // 32) * 32
        SLAB = (nc.sbuf_usable_end - base) // 32 * 32
        PS = ctx.enter_context(nc.psum_tensor("PS", [128, 8, 512], F32))

        def at(name, shape, offset, dt=F32):
            assert offset % 32 == 0
            n = 4
            for x in shape[1:]:
                n *= x
            assert offset + n <= SLAB, (name, offset + n, SLAB)
            return nc.alloc_sbuf_tensor_at(name, shape, dt, offset=base + offset)

        XH = at("XH", [128, 8, NT], 0, F32R)
        XL = at("XL", [128, 8, NT], 8 * TILE, F32R)
        AR = 16 * TILE
        X32 = at("X32", [128, 8, NT], AR)
        XCQ = at("XCQ", [128, 16, NT], AR)
        U0 = at("U0", [128, 2, NT], AR + 16 * TILE)
        RGW = at("RGW", [128, 2, 4, 128], AR + 16 * TILE)
        MIX = [at("MIX%d" % n, [128, NT], AR + (18 + n) * TILE) for n in range(5)]
        OT = at("OT", [128, 4, NT], AR)

        SET = 4 * 128 * 4
        SETS = [[AR + 16 * TILE + n * SET for n in range(14)],
                [4 * TILE + n * SET for n in range(8)] + [12 * TILE + n * SET for n in range(6)]]

        def pair(name, n):
            return [at("%s%d" % (name, p), [128, 4, 128], SETS[p][n]) for p in range(2)]

        KT, QT, VT, DA, DB, EG, LM = [pair(x, n) for n, x in enumerate(("KT", "QT", "VT", "DA", "DB", "EG", "LM"))]
        TA, TT, WW, VB, KO, RR, VN = [pair(x, 7 + n) for n, x in enumerate(("TA", "TT", "WW", "VB", "KO", "RR", "VN"))]
        SP, SS = at("SP", [128, 4, 128], AR + 16 * TILE + 14 * SET), at("SS", [128, 4, 128], AR + 16 * TILE + 15 * SET)
        RN = [at("RN%d" % n, [128, NT], AR + (18 + n) * TILE) for n in range(4)]

        ZT = at("ZT", [128, 4, NT], AR + 4 * TILE)
        Y = at("Y", [128, 8, NT], AR)
        XR = at("XR", [128, 8, NT], AR + 8 * TILE)
        CB = at("CB", [128, 4, NT], AR + 8 * TILE)
        UF = at("UF", [128, 2, NT], AR + 12 * TILE)
        HH, HL = at("HH", [128, 2, NT], AR + 14 * TILE, F32R), at("HL", [128, 2, NT], AR + 16 * TILE, F32R)
        PP = at("PP", [128, 8, NT], AR + 8 * TILE)
        P32 = at("P32", [128, 2, NT], AR + 16 * TILE)
        PH, PL = at("PH", [128, 2, NT], AR + 18 * TILE, F32R), at("PL", [128, 2, NT], AR + 20 * TILE, F32R)
        SQ = [at("SQ%d" % n, [128, NT], AR + (16 + n) * TILE) for n in range(2)]
        SG = [at("SG%d" % n, [128, NT], AR + (16 + n) * TILE) for n in range(2)]
        RS = at("RS", [128, NT], AR + 22 * TILE)

        NK = NT + 128
        KW = NK // 4
        QA, CR = at("QA", [128, 3, NT], AR), at("CR", [128, 2, NT], AR + 3 * TILE)
        KRW = at("KRW", [128, NT], AR + 5 * TILE)
        U1 = at("U1", [128, 2, NT], AR + 6 * TILE)
        DX = at("DX", [128, 2, NT], AR + 8 * TILE)
        SQD = [at("SQD%d" % n, [128, NT], AR + (6 + n) * TILE) for n in range(2)]
        RSD = [at("RSD%d" % n, [128, NT], AR + (8 + n) * TILE) for n in range(2)]
        ROPE = at("ROPE", [128, 2, NT], AR + 10 * TILE)
        QAH, QAL = at("QAH", [128, 3, NT], AR + 12 * TILE, F32R), at("QAL", [128, 3, NT], AR + 15 * TILE, F32R)
        CH, CL = at("CH", [128, 2, NK], AR + 18 * TILE, F32R), at("CL", [128, 2, NK], AR + 18 * TILE + 8 * NK, F32R)
        CCK = at("CCK", [128, 2, 128], AR + 18 * TILE + 16 * NK)
        KRR = at("KRR", [128, NK], 0)
        QR = at("QR", [128, 2, NT], 4 * NK)
        QN = at("QN", [128, 4, NT], 8 * TILE)
        TK = at("TK", [128, NT], 8 * TILE)
        TQ = [at("TQ%d" % n, [128, NT], AR + (12 + n) * TILE) for n in range(2)]
        KN = at("KN", [128, 4, NK], AR)
        VTOK = at("VTOK", [128, 10, 512], AR + 16 * NK)
        QS, QRS = at("QS", [128, 2, NT], AR + 12 * TILE), at("QRS", [128, NT], AR + 14 * TILE)
        PB = at("PB", [128, 2, 1024], AR + 15 * TILE)
        PTB = at("PTB", [128, 1024], AR + 15 * TILE + 8192)
        OB = at("OB", [128, 2, 128], AR + 15 * TILE + 12288)
        AST = [at("AST%d" % n, [128, 4], AR + 15 * TILE + 13312 + 32 * n) for n in range(2)]

        place = [AR]

        def room(name, shape, dt=F32):
            t, n = at(name, shape, place[0], dt), 4
            for x in shape[1:]:
                n *= x
            place[0] += -(-n // 32) * 32
            return t

        def both(name, *shape):
            return [room("%s%d" % (name, p), [128, *shape]) for p in range(2)]

        LORA = room("LORA", [128, 2, 512])
        WG = room("WG", [128, 2, NT])
        RKV, PREP, BG, NORM = both("RKV", 3, NT), both("PREP", 4, NT), both("BG", 2, NT), both("NORM", NT)
        K2R, SIGR, KKR, KKAR, BONUSR, GR = 0, 1, 2, 3, 0, 1
        place[0] = AR
        RUN = room("RUN", [128, 256])
        MB = [room("MB%d" % n, [128, 4, 128]) for n in range(2)]
        behind_states = place[0]
        CIN = both("CIN", 24, 64)
        A_B, B_B, K_B, V_B, LM_B, W_B, TA_B, TT_B, AK_B, BT_B, KT_B, VT_B = [both(x, 4, 128) for x in (
            "A_B", "B_B", "K_B", "V_B", "LM_B", "W_B", "TA_B", "TT_B", "AK_B", "BT_B", "KT_B", "VT_B")]
        ARI = both("ARI", 4, 192)
        B_S, PI_S, RB_S, RK_S = [both(x, 4, 64) for x in ("B_S", "PI_S", "RB_S", "RK_S")]
        PX = both("PX", 4, 65)
        U_B, X_B = K_B, W_B
        ZEROED = [x[p] for x in (A_B, B_B, K_B, V_B, AK_B, BT_B, KT_B) for p in range(2)] + MB
        TAIL = SLAB // 32 * 32
        CO = at("CO", [128, 4, NT], TAIL - 4 * TILE)
        assert place[0] <= TAIL - 4 * TILE, (place[0], TAIL - 4 * TILE)
        place[0] = behind_states
        BGL, SQC, INC = both("BGL", 2, NT), both("SQC", NT), both("INC", NT)

        def small(name, n, first=0):
            return SMALL[:, sp_[name] + first:sp_[name] + first + n]

        IDENT, ONES, UPPER = small("identity", 128), small("ones", 128), small("upper", 128)

        def col(name, j=0):
            return COL[:, cp[name] + j:cp[name] + j + 1]

        def col_at(name, j):
            return COL[:, ds(cp[name] + j, 1)]

        BETA = BETA36[:, :].rearrange("p (c h) -> p c h", h=4)
        PSBA = PS[:, 7, 0:72].rearrange("p (c j) -> p c j", j=8)

        def col4(name):
            return COL[:, cp[name]:cp[name] + 4]

        GATE = nc.dram_tensor("gate_rows", [4, 128, NT], F32).ap()
        XROW = nc.dram_tensor("x_rows", [128, 8, NT], F32).ap()
        CROW = nc.dram_tensor("c_rows", [14, 128, NT], F32).ap()
        PROW = nc.dram_tensor("prepared_rows", [16, 128, NT], F32).ap()
        BROW = nc.dram_tensor("bonus_gate_rows", [8, 128, NT], F32).ap()
        ZROW = nc.dram_tensor("z_rows", [4, 128, NT], F32).ap()

        params_in, x_in = sem("params_in"), sem("x_in")
        raw_in = [sem("raw_in0"), sem("raw_in1")]
        hi_split, unit_split = sem("hi_split"), sem("unit_split")
        unit_done, part_done = sem("unit_done"), sem("part_done")
        slot_act, slot_dve = sem("slot_act"), sem("slot_dve")
        xh_ready, xl_ready = sem("xh_ready"), sem("xl_ready")
        row_out = [sem("row_out0"), sem("row_out1")]
        conv_done = sem("conv_done")
        dve_step, act_step = sem("dve_step"), sem("act_step")
        ba_done, ba_copied = sem("ba_done"), sem("ba_copied")
        eps_set = sem("eps_set")
        ba_split, g_ready, ba_act, ba_vec = sem("ba_split"), sem("g_ready"), sem("ba_act"), sem("ba_vec")
        rg_done, rg_read, rg_vec, rg_act = sem("rg_done"), sem("rg_read"), sem("rg_vec"), sem("rg_act")
        silu_done, lam_vec, lam_act, gate_in = sem("silu_done"), sem("lam_vec"), sem("lam_act"), sem("gate_in")
        gates_in, kept_ready = sem("gates_in"), sem("kept_ready")
        outs_done = sem("outs_done")

        sq_ready, norm_sum, norm_root, norm_done = sem("sq_ready"), sem("norm_sum"), sem("norm_root"), sem("norm_done")
        gdn_staged, pad_zeroed, state_in = sem("gdn_staged"), sem("pad_zeroed"), sem("state_in")
        gdn_pe = [sem("gdn_pe%d" % p) for p in range(2)]
        gdn_dve = [sem("gdn_dve%d" % p) for p in range(2)]
        gdn_act = [sem("gdn_act%d" % p) for p in range(2)]
        gdn_pool = [sem("gdn_pool%d" % p) for p in range(2)]
        state_out = sem("state_out")
        o_zeroed, z_in, o_square, o_sum, o_root, o_gated = [sem(x) for x in ("o_zeroed", "z_in", "o_square", "o_sum", "o_root", "o_gated")]
        mix_ready = [sem("mix_ready%d" % l) for l in range(2)]

        x_back, out_read, up_read, down_read = sem("x_back"), sem("out_read"), sem("up_read"), sem("down_read")
        ffn_conv, ffn_silu, ffn_mul, h_hi, h_done = [sem(x) for x in ("ffn_conv", "ffn_silu", "ffn_mul", "h_hi", "h_done")]
        p_in, p_hi, p_split, wp_read = sem("p_in"), sem("p_hi"), sem("p_split"), sem("wp_read")
        gate_read, gate_added, gaps_zeroed = sem("gate_read"), sem("gate_added"), sem("gaps_zeroed")
        ln_mean, ln_sub, ln_sq, ln_var = sem("ln_mean"), sem("ln_sub"), sem("ln_sq"), sem("ln_var")
        ln_root, ln_scaled, ln_hi, ln_lo = sem("ln_root"), sem("ln_scaled"), sem("ln_hi"), sem("ln_lo")
        in_ready = sem("in_ready")
        in1_read, shifted, row1_out = sem("in1_read"), sem("shifted"), [sem("row1_out0"), sem("row1_out1")]
        mla_in, cache_in, kr_cache_in = sem("mla_in"), sem("cache_in"), sem("kr_cache_in")
        m_square, m_sum, m_root = sem("m_square"), sem("m_sum"), sem("m_root")
        m_scaled, m_hi, m_lo, c_out = sem("m_scaled"), sem("m_hi"), sem("m_lo"), sem("c_out")
        swapped, kr_done, kr_out, qkv_read = sem("swapped"), sem("kr_done"), sem("kr_out"), sem("qkv_read")
        q_rotated, v_done, v_read = sem("q_rotated"), sem("v_done"), sem("v_read")
        a_scores, a_max, a_probs, a_turned, a_keys, a_keys2 = [sem("a_" + x) for x in (
            "scores", "max", "probs", "turned", "keys", "keys2")]
        a_out, a_inv, a_scaled, a_back, a_hi, q_staged = [sem("a_" + x) for x in (
            "out", "inv", "scaled", "back", "hi", "staged")]
        e_wg, wg_ready, e_in, e_out = sem("e_wg"), sem("wg_ready"), [sem("e_in0"), sem("e_in1")], [sem("e_out0"), sem("e_out1")]
        e_pe, e_act, e_dve, f_mean, f_var, f_act, f_dve = [sem(x) for x in (
            "e_pe", "e_act", "e_dve", "f_mean", "f_var", "f_act", "f_dve")]
        f_in = [sem("f_in0"), sem("f_in1")]
        c_ready, lora_in, c_state_in, c_state_set, c_state_out = [sem(x) for x in (
            "c_ready", "lora_in", "c_state_in", "c_state_set", "c_state_out")]
        c_in, c_pe, c_act, c_dve, c_pool = [[sem("%s%d" % (x, p)) for p in range(2)] for x in (
            "c_in", "c_pe", "c_act", "c_dve", "c_pool")]
        x_hi, x_lo, x_out, y_out = sem("x_hi"), sem("x_lo"), sem("x_out"), sem("y_out")

        OUT_UNIT, OUT_PART = (24, 108 + 26), (0, 72 + 5)

        def up_unit(l, g):
            return OUT_UNIT[l] + 8 + 6 * g - 2

        def down_unit(l, g):
            return OUT_UNIT[l] + 8 + 6 * g + 8

        class Stages:

            def __init__(self, *names):
                self.index = {n: k + 1 for k, n in enumerate(names)}
                self.count = len(names)

            def at(self, i, name):
                return i * self.count + self.index[name] + 1

            def before(self, i):
                return i * self.count + 1

        def level_mask(l):
            return small("level", 128, 128 * l)

        def heads_of(x):
            if x.shape[1] == 4:
                return x.unsqueeze(2).to_broadcast([128, 4, 128])
            return x.unsqueeze(1).to_broadcast([128, 4, 128])

        def per_head(bank):
            return PS[:, bank, :].rearrange("p (h n) -> p h n", h=4)

        class Steps:

            def __init__(self, eng, s):
                self.eng, self.sem, self.n, self.i, self.per = eng, s, 0, None, 0

            def value(self):
                return self.n if self.i is None else self.i * self.per + self.n

            def __call__(self, instruction):
                instruction.then_inc(self.sem, 1)
                self.n += 1
                self.eng.wait_ge(self.sem, self.value())

            def enter(self, i, per, first=0):
                self.n -= first * per
                self.i, self.per, self.start = i, per, self.n

            def leave(self, count):
                assert self.n - self.start == self.per, (self.n - self.start, self.per)
                self.n, self.i = self.start + self.per * count, None

        def banks(slot, width=BW):
            return PS[:, 4 * slot:4 * slot + 4, 0:width]

        def rows(x, width=BW):
            return x.rearrange("p (b n) -> p b n", n=width)

        G_FIRST = ["decays", "diffs", "grams", "blocks", "w1", "t1", "w2", "t2", "w3"]
        G_SECOND = ["t3", "w4", "t4", "w5", "t5", "w6", "t6", "carry1", "carry2"]
        C_LEVELS = range(1, 6)
        FIRST = ["prep0", "prep1", "prep2", "prep3", "w1", "t1", "w2", "t2"]
        SECOND = ["w3", "t3", "w4", "t4", "w5", "t5", "carry1", "carry2", "carry3"]

        class ChunkStages:

            def __init__(self, *names):
                self.index = {n: k + 1 for k, n in enumerate(names)}
                self.count = len(names)

            def at(self, j, name):
                return j[0] * self.count + (self.index[name] + self.count * j[1])

            def before(self, j):
                return j[0] * self.count + self.count * j[1]

        G_PE = ChunkStages("rows", "gram", "qk", "k_turned", "v_turned", "m_turned",
                           *[x + str(l) for l in range(1, 7) for x in ("w", "tt", "ta")][:-1], "ks", "v_new", "o", "s")
        G_DVE = ChunkStages("decayed", "diff", "lower", "m0", "ta0", "t0", "qk",
                            *[x + str(l) for l in range(1, 7) for x in ("tt", "ta")][:-1], "r", "s")
        G_ACT = ChunkStages("staged", "exps", "ko", "vb", *["w%d" % l for l in range(1, 7)], "v_new", "out")
        G_POOL = ChunkStages("upper", "m1", "q_in", *["m%d" % l for l in range(2, 7)])
        C_PE = ChunkStages("l", "kg", "bg", "mt", "vt",
                           *[x + str(l) for l in C_LEVELS for x in (("lw", "tt", "ta") if l < 5 else ("lw", "tt"))],
                           "x", "u", "o", "m")
        C_ACT = ChunkStages("px", "pi", "bt", "kt", "vt", *["w%d" % l for l in C_LEVELS], "x", "u", "o")
        C_DVE = ChunkStages("scan", "as", "bs", "kb", "rs", "lm0", "ta0", "rb", "ak", "rk", "tt0", "lm1",
                            *[x for l in C_LEVELS for x in (["lm%d" % (l + 1), "tt%d" % l, "ta%d" % l] if l < 5 else ["tt5"])],
                            "m0", "m")
        E_PE = Stages("w", "a", "g", "norm", "bonus")
        E_ACT = Stages("w", "a", "g", "square", "ln", "inv")
        E_DVE = Stages("kk0", "k2a", "k2", "kk", "b", "rkk", "bonus")
        F_ACT = Stages("square", "ln", "inv", "affine", "hi")
        F_DVE = Stages("centred", "scaled", "plus", "gated", "lo")
        C_POOL = ChunkStages("a", "b", "v")
        G_SAMPLE, C_SAMPLE = (0, 4), (0, 8)

        def is_sample(j, sample=C_SAMPLE):
            return isinstance(j[0], int) and j == sample

        def starts_set(j):
            return isinstance(j[0], int) and j == (0, 0)

        def is_first(j, p):
            return isinstance(j[0], int) and j == (0, 0) and p == 0

        def other(j, p):
            return (j[0], j[1] - 1) if p == 0 else j

        def chunk_columns(j, p):
            if is_sample(j):
                return slice(S0, S0 + 64)
            first = P0 + 64 * p + 128 * j[1]
            return slice(first, first + 64) if isinstance(j[0], int) else ds(128 * j[0] + first, 64)

        def tile_columns(j, p):
            return S0 if is_sample(j, G_SAMPLE) else 256 * j[0] + (256 * j[1] + 128 * p + P0)

        def tile_place(j, p):
            return ds(8 * j[0] + (8 * j[1] + 4 * p), 4)

        def run_chunks(eng, do, first_half=FIRST, second_half=SECOND, sample=C_SAMPLE, loop_start=None, loop_end=None):
            def together(j0, p0, j1, p1):
                for n in range(max(len(first_half), len(second_half))):
                    if n < len(second_half):
                        do(second_half[n], j1, p1)
                    if n < len(first_half):
                        do(first_half[n], j0, p0)
            count = sample[1]
            for x in first_half:
                do(x, (0, 0), 0)
            together((0, 0), 1, (0, 0), 0)
            with eng.Fori(1, count) as i:
                if loop_start:
                    loop_start(i)
                together((i, 0), 0, (i, -1), 1)
                together((i, 0), 1, (i, 0), 0)
            if loop_end:
                loop_end()
            together(sample, 0, (0, count - 1), 1)
            for x in second_half:
                do(x, sample, 0)

        DECAY = 0.6065306597126334

        def stacked(p, n, half):
            return PS[:, 4 * p + n, 256 * half:256 * half + 256].rearrange("p (m n) -> p m n", m=4)

        def pairs_of(x, n=64):
            return x.unsqueeze(1).to_broadcast([x.shape[0], 4, n])

        def half(h):
            return slice(64 * h, 64 * h + 64)

        PAIR_ID, PAIR_ONES = small("pair_identity", 64), small("pair_ones", 128)

        def flat(x):
            return x[:, :, :].rearrange("p m n -> p (m n)")

        def k_group(p):
            return PS[:, 4 * p + 1:4 * p + 3, 0:384]

        IN1 = 108
        D_SCALE = 192.0 ** -0.5
        STEPS = 9

        def queries(n):
            return (P0 + 128 * n if n < 8 else S0), 128

        def key_runs(n):
            if n == 8:
                return [(NT, 128, 0), (S0, 128, 128)]
            keys = 128 * (n + 1)
            return [(P0 + k, min(512, keys - k), k) for k in range(0, keys, 512)]

        def key_blocks(n):
            return [(8, 128), (9, 128)] if n == 8 else [(j, 128) for j in range(n + 1)]

        block = ctx.enter_context(nc.Block())
        def matmul_unit(slot, ring, first, nk, hi, lo, width=BW):
            for b in range(NB):
                n, last = 0, None
                for k in range(nk):
                    w = slice(first + k * 128, first + (k + 1) * 128)
                    for wt, r in ((WHI, hi), (WHI, lo), (WLO, hi)):
                        last = nc.tensor.matmul(PS[:, 4 * slot + b, 0:width], wt[:, ring, w],
                                                r[:, k, b * width:(b + 1) * width],
                                                start=n == 0, stop=n == 3 * nk - 1)
                        n += 1
            return last

        @block.sync
        def _(sp):
            sp.dma_start(COL[:, :], io["columns"]).then_inc(params_in, 16)
            sp.dma_start(SMALL[:, :], io["small"]).then_inc(params_in, 16)
            for k in range(8):
                sp.dma_start(X32[:, k, :], io["x"][:, k, :]).then_inc(x_in, 16)
            for s in range(2):
                sp.dma_start(RAW[:, s, :], io["units"][s]).then_inc(raw_in[s], 16)
            def load_units(first, last):
                with sp.Fori(first, last) as i:
                    for s in range(2):
                        sp.wait_ge(unit_split, 2 * i + s - 1)
                        sp.dma_start(RAW[:, s, :], io["units"][ds(2 * i + s, 1), :, :].rearrange("a p n -> p (a n)"))\
                          .then_inc(raw_in[s], 16)

            load_units(1, OUT_UNIT[1] // 2 + 2)
            sp.wait_ge(a_hi, 73)
            sp.dma_start(WG[:, :, :], CROW[12:14, :, :].rearrange("k p n -> p k n")).then_inc(e_wg, 16)
            sp.dma_start(LORA[:, :, :], io["w_lora"]).then_inc(lora_in, 16)

            def load_rows(m):
                sp.dma_start(RKV[m % 2][:, :, :], CROW[0:12, :, :].rearrange("(k m) p n -> m p k n", m=4)[m])\
                  .then_inc(e_in[m % 2], 16)

            load_rows(0)
            load_rows(1)
            for m in range(4):
                sp.wait_ge(e_dve, E_DVE.at(m, "bonus") - 1)
                sp.wait_ge(e_act, E_ACT.at(m, "g") - 1)
                sp.dma_start(PROW.rearrange("(k m) p n -> m p k n", m=4)[m], PREP[m % 2][:, :, :]).then_inc(e_out[m % 2], 16)
                sp.dma_start(BROW.rearrange("(k m) p n -> m p k n", m=4)[m], BG[m % 2][:, :, :]).then_inc(e_out[m % 2], 16)
                if m < 2:
                    load_rows(m + 2)
            for p in range(2):
                sp.wait_ge(e_out[p], 64)

            def load_tokens(p, columns):
                for first, rows_of in ((0, CROW[0:4]), (4, CROW[8:12]), (8, PROW)):
                    n = rows_of.shape[0]
                    sp.dma_start(CIN[p][:, first:first + n, :], rows_of[:, :, columns].rearrange("a p n -> p a n"))\
                      .then_inc(c_in[p], 16)

            sp.wait_ge(c_ready, 1)
            for h in range(2):
                sp.dma_start(MB[1][half(h), :, half(h)], io["s_c"][half(h)]).then_inc(c_state_in, 16)
            for p in range(2):
                load_tokens(p, chunk_columns((0, 0), p))
            with sp.Fori(0, 7) as i:
                for p in range(2):
                    sp.wait_ge(c_pool[p], C_POOL.at((i, 0), "v"))
                    sp.wait_ge(c_dve[p], C_DVE.at((i, 0), "rs"))
                    load_tokens(p, chunk_columns((i, 1), p))
            sp.wait_ge(c_pool[0], C_POOL.at((0, 7), "v"))
            sp.wait_ge(c_dve[0], C_DVE.at((0, 7), "rs"))
            load_tokens(0, chunk_columns(C_SAMPLE, 0))
            sp.wait_ge(c_act[0], C_ACT.at(C_SAMPLE, "o"))
            for m in range(4):
                if m >= 2:
                    sp.wait_ge(f_dve, F_DVE.at(m - 2, "gated") - 1)
                sp.dma_start(BGL[m % 2][:, :, :], BROW.rearrange("(k m) p n -> m p k n", m=4)[m]).then_inc(f_in[m % 2], 16)
            load_units(OUT_UNIT[1] // 2 + 2, NU // 2)
            sp.wait_ge(kept_ready, 1)
            sp.dma_start(io["kept"], KEPT[:, :]).then_inc(outs_done, 16)
            sp.wait_ge(outs_done, 16)

        @block.gpsimd
        def _(pool):
            ZERO = EPS[:, 3:4]

            def zeros(h):
                return EPS[half(h), 3:4].unsqueeze(2).to_broadcast([64, 4, 64])

            pool.wait_ge(eps_set, 4)
            def split_units(first, last):
                with pool.Fori(first, last) as i:
                    for s in range(2):
                        pool.wait_ge(raw_in[s], 16 * i + 16)
                        pool.wait_ge(unit_done, 2 * i + s + 1)
                        nc.gpsimd.tensor_tensor(WHI[:, s, :], RAW[:, s, :], ZERO.to_broadcast([128, 1024]), ALU.add)\
                            .then_inc(hi_split, 1)
                        pool.wait_ge(hi_split, 2 * i + s + 1)
                        nc.gpsimd.tensor_tensor(WLO[:, s, :], RAW[:, s, :], WHI[:, s, :], ALU.subtract)\
                          .then_inc(unit_split, 1)

            def norm_low(n):
                for k in range(8):
                    pool.wait_ge(ln_hi, 2 * k + 2 + 16 * n)
                    nc.gpsimd.tensor_tensor(XL[:, k, :], Y[:, k, :], XH[:, k, :], ALU.subtract).then_inc(ln_lo, 1)

            def layer_end(l, last):
                first = OUT_UNIT[l]
                norm_low(2 * l)
                split_units((first + 10) // 2, (first + 76) // 2)
                norm_low(2 * l + 1)
                split_units((first + 76) // 2, last)

            split_units(0, OUT_UNIT[0] // 2 + 1)

            def g_step(name, j, p):
                s = gdn_pool[p]

                def masked(l):
                    nc.gpsimd.tensor_tensor(LM[p][:, :, :], DB[p][:, :, :], heads_of(level_mask(l)), ALU.mult).then_inc(s, 1)

                if name == "diffs":
                    pool.wait_ge(gdn_act[p], G_ACT.at(j, "exps"))
                    nc.gpsimd.tensor_tensor(DA[p][:, :, :], DA[p][:, :, :], heads_of(UPPER), ALU.mult).then_inc(s, 1)
                elif name == "blocks":
                    pool.wait_ge(gdn_pe[p], G_PE.at(j, "m_turned"))
                    pool.wait_ge(gdn_dve[p], G_DVE.at(j, "ta0"))
                    masked(1)
                    nc.gpsimd.tensor_tensor(QT[p][:, :, :], QT[p][:, :, :], EG[p][:, :, :], ALU.mult).then_inc(s, 1)
                elif name[0] == "w" and name != "w6":
                    pool.wait_ge(gdn_pe[p], G_PE.at(j, name))
                    masked(int(name[1]) + 1)

            run_chunks(pool, g_step, G_FIRST, G_SECOND, G_SAMPLE)
            split_units(OUT_UNIT[0] // 2 + 1, (OUT_UNIT[0] + 10) // 2)
            layer_end(0, OUT_UNIT[1] // 2 + 1)

            def c_step(name, j, p):
                if name != "prep1":
                    return
                pool.wait_ge(c_dve[p], C_DVE.at(j, "as"))
                for h in range(2):
                    last = nc.gpsimd.tensor_tensor(A_B[p][half(h), :, half(h)], ARI[p][half(h), :, 0:64], zeros(h), ALU.add)
                last.then_inc(c_pool[p], 1)
                pool.wait_ge(c_dve[p], C_DVE.at(j, "bs"))
                for h in range(2):
                    last = nc.gpsimd.tensor_tensor(B_B[p][half(h), :, half(h)], B_S[p][half(h), :, :], zeros(h), ALU.add)
                last.then_inc(c_pool[p], 1)
                for h in range(2):
                    last = nc.gpsimd.tensor_tensor(V_B[p][half(h), :, half(h)], CIN[p][half(h), 4:8, :], zeros(h), ALU.add)
                last.then_inc(c_pool[p], 1)

            pool.wait_ge(c_ready, 1)
            run_chunks(pool, c_step)
            split_units(OUT_UNIT[1] // 2 + 1, (OUT_UNIT[1] + 10) // 2)
            layer_end(1, NU // 2)

        @block.tensor
        def _(pe):
            pe.sem_inc(unit_done, 2)
            pe.wait_ge(xl_ready, 8)
            with pe.Fori(0, 12) as i:
                for s in range(2):
                    pe.wait_ge(unit_split, 2 * i + s + 1)
                    pe.wait_ge(slot_act, 2 * i + s + 1)
                    matmul_unit(s, s, 0, 8, XH, XL).then_inc(unit_done, 1)
            pe.wait_ge(slot_act, 26)
            pe.wait_ge(ba_split, 1)
            for c in range(9):
                t0 = P0 + 128 * c if c < 8 else S0
                n = 0
                for k in range(8):
                    for x, w in ((XH, WBAH), (XL, WBAH), (XH, WBAL)):
                        last = nc.tensor.matmul(PS[:, 7, 8 * c:8 * c + 8], x[:, k, t0:t0 + 128],
                                                w[:, 8 * k:8 * k + 8], start=n == 0, stop=n == 23)
                        n += 1
            last.then_inc(ba_done, 1)
            pe.wait_ge(g_ready, 1)
            nc.tensor.matmul(PS[:, 7, 128:164], UPPER, GB[:, :], start=True, stop=True).then_inc(ba_done, 1)
            pe.wait_ge(gates_in, 16)
            for m in range(4):
                if m:
                    pe.wait_ge(rg_read, 2 * m)
                for g in range(2):
                    if g:
                        pe.wait_ge(ba_copied, 2)
                    for b in range(NB):
                        last = nc.tensor.matmul(PS[:, 4 * g + b, 0:BW], RGW[:, g, m, :],
                                                XCQ[:, m, b * BW:(b + 1) * BW], start=True, stop=True)
                    last.then_inc(rg_done, 1)
            for j in range(8):
                pe.wait_ge(sq_ready, j + 1)
                if j >= 2:
                    pe.wait_ge(norm_root, j - 1)
                for b in range(NB):
                    last = nc.tensor.matmul(PS[:, 4 * (j % 2) + b, 0:BW], ONES, RN[j % 2][:, b * BW:(b + 1) * BW],
                                            start=True, stop=True)
                last.then_inc(norm_sum, 1)
            pe.wait_ge(norm_root, 8)

            def by_head(bank, lhs, rhs, start=True, stop=True):
                for h in range(4):
                    last = nc.tensor.matmul(PS[:, bank, 128 * h:128 * h + 128], lhs[:, h, :], rhs[:, h, :],
                                            start=start, stop=stop)
                return last

            def turned(bank, x):
                for h in range(4):
                    last = nc.tensor.transpose(PS[:, bank, 128 * h:128 * h + 128], x[:, h, :], IDENT)
                return last

            def g_step(name, j, p):
                s, b = gdn_pe[p], 4 * p
                state = SS if is_sample(j, G_SAMPLE) else SP
                if name == "decays":
                    pe.wait_ge(gdn_dve[p], G_DVE.at(j, "decayed"))
                    nc.tensor.matmul(PS[:, b, :], ONES, LM[p][:, :, :].rearrange("p h n -> p (h n)"), start=True, stop=True)\
                      .then_inc(s, 1)
                elif name == "diffs":
                    if is_sample(j, G_SAMPLE):
                        pe.wait_ge(pad_zeroed, 1)
                    pe.wait_ge(gdn_act[p], G_ACT.at(j, "staged"))
                    by_head(b + 1, KT[p], KT[p]).then_inc(s, 1)
                    by_head(b + 2, KT[p], QT[p]).then_inc(s, 1)
                    turned(b + 3, KT[p]).then_inc(s, 1)
                elif name == "grams":
                    pe.wait_ge(gdn_act[p], G_ACT.at(j, "exps"))
                    turned(b, VT[p]).then_inc(s, 1)
                elif name == "blocks":
                    pe.wait_ge(gdn_dve[p], G_DVE.at(j, "m0"))
                    turned(b + 1, LM[p]).then_inc(s, 1)
                elif name[0] == "w":
                    l = int(name[1])
                    pe.wait_ge(gdn_dve[p], G_DVE.at(j, "tt%d" % (l - 1) if l > 1 else "t0"))
                    pe.wait_ge(gdn_pool[p], G_POOL.at(j, "m%d" % l))
                    by_head(b + 1, LM[p], TT[p]).then_inc(s, 1)
                elif name[0] == "t":
                    l = int(name[1])
                    pe.wait_ge(gdn_dve[p], G_DVE.at(j, "ta%d" % (l - 1) if l > 1 else "qk"))
                    pe.wait_ge(gdn_act[p], G_ACT.at(j, "w%d" % l))
                    by_head(b + 2, TA[p], WW[p]).then_inc(s, 1)
                    if l < 6:
                        by_head(b + 3, WW[p], TA[p]).then_inc(s, 1)
                    else:
                        if is_sample(j, G_SAMPLE):
                            pe.wait_ge(state_in, 16)
                        elif not is_first(j, p):
                            pe.wait_ge(gdn_dve[1 - p], G_DVE.at(other(j, p), "s"))
                        by_head(b, KT[p], state).then_inc(s, 1)
                elif name == "carry1":
                    pe.wait_ge(gdn_dve[p], G_DVE.at(j, "r"))
                    by_head(b + 1, TT[p], RR[p]).then_inc(s, 1)
                else:
                    pe.wait_ge(gdn_act[p], G_ACT.at(j, "v_new"))
                    for h in range(4):
                        o = PS[:, b + 2, 128 * h:128 * h + 128]
                        nc.tensor.matmul(o, state[:, h, :], QT[p][:, h, :], start=True, stop=False)
                        last = nc.tensor.matmul(o, VN[p][:, h, :], DA[p][:, h, :], start=False, stop=True)
                    last.then_inc(s, 1)
                    by_head(b + 3, KO[p], VN[p]).then_inc(s, 1)

            run_chunks(pe, g_step, G_FIRST, G_SECOND, G_SAMPLE)
            for h in range(4):
                pe.wait_ge(o_square, h + 1)
                if h >= 2:
                    pe.wait_ge(o_root, h - 1)
                for b in range(NB):
                    last = nc.tensor.matmul(PS[:, 4 * (h % 2) + b, 0:BW], ONES, RN[h % 2][:, b * BW:(b + 1) * BW],
                                            start=True, stop=True)
                last.then_inc(o_sum, 1)

            def norm_sums(n):
                for b in range(NB):
                    for k in range(8):
                        last = nc.tensor.matmul(PS[:, b, 0:BW], ONES, Y[:, k, b * BW:(b + 1) * BW],
                                                start=k == 0, stop=k == 7)
                last.then_inc(ln_mean, 1)
                for k in range(8):
                    pe.wait_ge(ln_sq, k + 1 + 8 * n)
                    for b in range(NB):
                        last = nc.tensor.matmul(PS[:, 4 + b, 0:BW], ONES, SQ[k % 2][:, b * BW:(b + 1) * BW],
                                                start=k == 0, stop=k == 7)
                    last.then_inc(ln_var, 1)

            def up(l, g, unit):
                for t in range(4):
                    pe.wait_ge(unit_split, unit + t + 1)
                    matmul_unit(t % 2, t % 2, 0, 8, XH, XL).then_inc(unit_done, 1)

            def down(l, g, unit, slots=True):
                pe.wait_ge(h_done, g + 2 + 12 * l)
                for m in range(8):
                    if m % 4 == 0:
                        pe.wait_ge(unit_split, unit + m // 4 + 1)
                    if m < 2:
                        pe.wait_ge(up_read, slots + m + 45 * l)
                    else:
                        pe.wait_ge(down_read, 8 * g + m + 1 + 90 * l)
                    last = matmul_unit(m % 2, m // 4, 256 * (m % 4), 2, HH, HL)
                    last.then_inc(part_done if m % 4 < 3 else unit_done, 1)

            def layer_end(l):
                first = OUT_UNIT[l]
                pe.wait_ge(mix_ready[l], 4)
                with pe.Fori(0, 4) as i:
                    for s in range(2):
                        pe.wait_ge(unit_split, first + 2 * i + s + 1)
                        pe.wait_ge(out_read, 2 * i + s + 1 + 10 * l)
                        matmul_unit(s, s, 0, 8, XH, XL).then_inc(unit_done, 1)
                pe.wait_ge(out_read, 10 + 10 * l)
                norm_sums(2 * l)
                pe.wait_ge(gaps_zeroed, 1 + 2 * l)
                for t in range(4):
                    pe.wait_ge(unit_split, first + 8 + t + 1)
                    if t >= 2:
                        pe.wait_ge(up_read, t + 45 * l)
                    matmul_unit(t % 2, t % 2, 0, 8, XH, XL).then_inc(unit_done, 1)
                with pe.Fori(1, 11) as g:
                    for t in range(4):
                        pe.wait_ge(unit_split, 6 * g + first + 6 + t + 1)
                        pe.wait_ge(up_read, 4 * g + t + 45 * l)
                        pe.wait_ge(down_read, 8 * g - 7 + min(t, 1) + 90 * l)
                        matmul_unit(t % 2, t % 2, 0, 8, XH, XL).then_inc(unit_done, 1)
                    down(l, g - 1, 6 * g + first + 10, 4 * g + 4)
                down(l, 10, first + 72, 44)
                pe.wait_ge(down_read, 90 + 90 * l)
                norm_sums(2 * l + 1)
                pe.wait_ge(p_split, 2 + 2 * l)
                pe.wait_ge(ln_root, 1 + (2 * l + 1))
                for m in range(8):
                    if m % 4 == 0:
                        pe.wait_ge(unit_split, first + 74 + m // 4 + 1)
                    if m >= 2:
                        pe.wait_ge(wp_read, m - 1 + 8 * l)
                    last = matmul_unit(m % 2, m // 4, 256 * (m % 4), 2, PH, PL)
                    last.then_inc(part_done if m % 4 < 3 else unit_done, 1)
                pe.wait_ge(wp_read, 8 + 8 * l)
                pe.wait_ge(gaps_zeroed, 1 + (2 * l + 1))
                with pe.Fori(0, 4) as i:
                    for s in range(2):
                        pe.wait_ge(unit_split, 2 * i + s + first + 77)
                        pe.wait_ge(gate_read, 2 * i + s + 1 + 10 * l)
                        matmul_unit(s, s, 0, 8, XH, XL).then_inc(unit_done, 1)

            layer_end(0)
            pe.wait_ge(in_ready, 1)
            pe.wait_ge(gate_read, 10)
            with pe.Fori(0, 10) as i:
                for s in range(2):
                    pe.wait_ge(unit_split, 2 * i + s + IN1 + 1)
                    pe.wait_ge(in1_read, 2 * i + s + 1)
                    matmul_unit(s, s, 0, 8, XH, XL).then_inc(unit_done, 1)
            pe.wait_ge(in1_read, 22)
            for j in range(5):
                slot, k, nk = (0, j, 3) if j < 3 else (1, j - 3, 2)
                pe.wait_ge(m_square, j + 1)
                for b in range(NB):
                    last = nc.tensor.matmul(PS[:, 4 * slot + b, 0:BW], ONES, SQD[j % 2][:, b * BW:(b + 1) * BW],
                                            start=k == 0, stop=k == nk - 1)
                last.then_inc(m_sum, 1)

            def swap_halves(slot, x):
                for b in range(NB):
                    last = nc.tensor.matmul(PS[:, 4 * slot + b, 0:BW], small("half_swap", 128), x[:, b * BW:(b + 1) * BW],
                                            start=True, stop=True)
                last.then_inc(swapped, 1)

            pe.wait_ge(m_root, 1)
            swap_halves(0, KRW)
            pe.wait_ge(m_lo, 5)
            pe.wait_ge(kr_done, 1)
            for m in range(6):
                if m % 2 == 0:
                    pe.wait_ge(unit_split, IN1 + 20 + m // 2 + 1)
                if m >= 2:
                    pe.wait_ge(qkv_read, m - 1)
                last = matmul_unit(m % 2, (m // 2) % 2, 384 * (m % 2), 3, QAH, QAL)
                last.then_inc(unit_done if m % 2 else part_done, 1)
            for m in range(4):
                if m % 2 == 0:
                    pe.wait_ge(unit_split, IN1 + 23 + m // 2 + 1)
                pe.wait_ge(qkv_read, 6 + m - 1)
                last = matmul_unit(m % 2, (m // 2 + 1) % 2, 256 * (m % 2), 2, CH, CL, KW)
                last.then_inc(unit_done if m % 2 else part_done, 1)
            for r in range(2):
                pe.wait_ge(qkv_read, 9 + r)
                swap_halves(r, QR[:, r, :])
            pe.wait_ge(unit_split, IN1 + 26)
            pe.wait_ge(q_rotated, 2)
            for j in range(10):
                t0 = P0 + 128 * j if j < 8 else (NT if j == 8 else S0)
                if j >= 8:
                    pe.wait_ge(v_read, j - 7)
                n = 0
                for k in range(2):
                    for c, w in ((CH, WHI), (CL, WHI), (CH, WLO)):
                        last = nc.tensor.matmul(PS[:, j % 8, :], c[:, k, t0:t0 + 128], w[:, 1, 512 * k:512 * k + 512],
                                                start=n == 0, stop=n == 5)
                        n += 1
                last.then_inc(v_done if j < 9 else unit_done, 1)

            def scores(i, hh, n):
                t0, nq = queries(n)
                s = 18 * i + 9 * hh + n
                if n == 0 or n == 1:
                    pe.wait_ge(q_staged, 2 * i + hh + 1)
                pe.wait_ge(a_probs, s + 1)
                g = (9 * hh + n) % 2
                for c, nk, at_ in key_runs(n):
                    out = PS[0:nq, 2 * g + at_ // 512, at_ % 512:at_ % 512 + nk]
                    nc.tensor.matmul(out, QS[:, hh, t0:t0 + nq], KN[:, ds(2 * i + hh, 1), c:c + nk].rearrange("p a n -> p (a n)"),
                                     start=True, stop=False)
                    r = slice(64 * hh, 64 * hh + 64)
                    last = nc.tensor.matmul(out, QRS[r, t0:t0 + nq], KRR[r, c:c + nk], start=False, stop=True)
                last.then_inc(a_scores, 1)

            def weigh(i, hh, n):
                t0, nq = queries(n)
                s, g = 18 * i + 9 * hh + n, (9 * hh + n) % 2
                pe.wait_ge(a_probs, s + 3)
                for j, (_, nk) in enumerate(key_blocks(n)):
                    last = nc.tensor.transpose(PS[0:nk, 4 + j // 4, 128 * (j % 4):128 * (j % 4) + nq],
                                               PB[0:nq, g, 128 * j:128 * j + nk], IDENT[0:nq, 0:nq])
                last.then_inc(a_turned, 1)
                pe.wait_ge(a_keys, s + 1)
                if 4 <= n < 8:
                    pe.wait_ge(a_keys2, 8 * i + 4 * hh + n - 3)
                pe.wait_ge(a_scaled, s + 1)
                blocks = key_blocks(n)
                for j, (v, nk) in enumerate(blocks):
                    last = nc.tensor.matmul(PS[0:nq, 6, 0:128], PTB[0:nk, 128 * j:128 * j + nq],
                                            VTOK[0:nk, v, ds(256 * i + 128 * hh, 128)], start=j == 0, stop=j == len(blocks) - 1)
                last.then_inc(a_out, 1)

            def back(i, hh, n):
                t0, nq = queries(n)
                s, g = 18 * i + 9 * hh + n, (9 * hh + n) % 2
                pe.wait_ge(a_scaled, s + 2)
                pe.wait_ge(a_hi, 2 * s + 1)
                nc.tensor.transpose(PS[:, 7, 0:nq], OB[0:nq, g, :], IDENT[0:nq, 0:nq]).then_inc(a_back, 1)

            pe.wait_ge(v_read, 10)
            order = [(hh, n) for hh in range(2) for n in range(STEPS)]
            pe.sem_inc(a_scores, 1)
            pe.sem_inc(a_turned, 1)
            pe.sem_inc(a_out, 1)
            with pe.Fori(0, 2) as i:
                scores(i, 0, 0)
                for x, (hh, n) in enumerate(order):
                    if x + 1 < len(order):
                        scores(i, *order[x + 1])
                    weigh(i, hh, n)
                    back(i, hh, n)
            def c_blocks(out, lhs, rhs, more=()):
                terms = [(lhs, rhs)] + list(more)
                for m in range(4):
                    for n, (l, r) in enumerate(terms):
                        last = nc.tensor.matmul(out[:, m, :], l[:, m, :], r if len(r.shape) == 2 else r[:, m, :],
                                                start=n == 0, stop=n == len(terms) - 1)
                return last

            def c_step(name, j, p):
                b, s = 4 * p, c_pe[p]
                level = int(name[1:]) if name[0] in "wt" else 0
                if name == "prep2":
                    pe.wait_ge(c_pool[p], C_POOL.at(j, "b"))
                    c_blocks(per_head(b), A_B[p], B_B[p]).then_inc(s, 1)
                    pe.wait_ge(c_dve[p], C_DVE.at(j, "rs"))
                    for m in range(4):
                        last = nc.tensor.matmul(k_group(p)[:, m // 2, 192 * (m % 2):192 * (m % 2) + 192], K_B[p][:, m, :],
                                                ARI[p][:, m, :], start=True, stop=True)
                    last.then_inc(s, 1)
                    for m in range(4):
                        last = nc.tensor.matmul(per_head(b + 3)[:, m, :], B_B[p][:, m, :], ARI[p][:, m, 64:192],
                                                start=True, stop=True)
                    last.then_inc(s, 1)
                elif name == "prep3":
                    pe.wait_ge(c_act[p], C_ACT.at(j, "kt"))
                    pe.wait_ge(c_dve[p], C_DVE.at(j, "rk"))
                    c_blocks(per_head(b + 1), LM_B[p], IDENT).then_inc(s, 1)
                    pe.wait_ge(c_pool[p], C_POOL.at(j, "v"))
                    c_blocks(per_head(b + 2), V_B[p], IDENT).then_inc(s, 1)
                elif name[0] == "w":
                    pe.wait_ge(c_dve[p], C_DVE.at(j, "tt%d" % (level - 1) if level > 1 else "lm1"))
                    c_blocks(per_head(b + 1), LM_B[p], TT_B[p]).then_inc(s, 1)
                elif name[0] == "t":
                    if level == 1:
                        pe.wait_ge(c_act[p], C_ACT.at(j, "vt"))
                    pe.wait_ge(c_dve[p], C_DVE.at(j, "ta%d" % (level - 1)))
                    pe.wait_ge(c_act[p], C_ACT.at(j, "w%d" % level))
                    c_blocks(per_head(b + 2), TA_B[p], W_B[p]).then_inc(s, 1)
                    if level < 5:
                        c_blocks(per_head(b + 3), W_B[p], TA_B[p]).then_inc(s, 1)
                elif name == "carry1":
                    if is_sample(j):
                        pe.wait_ge(c_state_in, 32)
                    elif not is_first(j, p):
                        pe.wait_ge(c_dve[1 - p], C_DVE.at(other(j, p), "m"))
                    c_blocks(per_head(b + 1), A_B[p], MB[is_sample(j)], [(AK_B[p], VT_B[p])]).then_inc(s, 1)
                elif name == "carry2":
                    pe.wait_ge(c_act[p], C_ACT.at(j, "x"))
                    pe.wait_ge(c_dve[p], C_DVE.at(j, "tt5"))
                    c_blocks(per_head(b + 2), TT_B[p], X_B[p]).then_inc(s, 1)
                elif name == "carry3":
                    pe.wait_ge(c_act[p], C_ACT.at(j, "u"))
                    c_blocks(stacked(p, 1, 0), MB[is_sample(j)], ARI[p][:, :, 64:128], [(U_B[p], RB_S[p]), (VT_B[p], RK_S[p])])\
                        .then_inc(s, 1)
                    c_blocks(per_head(b + 3), BT_B[p], U_B[p], [(KT_B[p], VT_B[p])]).then_inc(s, 1)

            def e_product(m, use, lhs, rhs, partitions):
                for n in range(NB):
                    last = nc.tensor.matmul(PS[:, 4 * ((5 * m + use) % 2) + n, 0:BW], lhs, rhs[partitions, n * BW:(n + 1) * BW],
                                            start=True, stop=True)
                return last

            whole = slice(0, 128)
            pe.wait_ge(a_hi, 73)
            pe.wait_ge(lora_in, 16)
            pe.wait_ge(wg_ready, 2)
            for m in range(4):
                if m:
                    pe.wait_ge(e_act, E_ACT.at(m - 1, "ln") - 1)
                e_product(m, 0, LORA[0:64, 0, 128 * m:128 * m + 128], WG[:, 0, :], half(0)).then_inc(e_pe, 1)
                if m:
                    pe.wait_ge(e_dve, E_DVE.at(m - 1, "bonus") - 1)
                e_product(m, 1, LORA[64:128, 0, 128 * m:128 * m + 128], WG[:, 0, :], half(1)).then_inc(e_pe, 1)
                pe.wait_ge(e_act, E_ACT.at(m, "w") - 1)
                e_product(m, 2, LORA[:, 1, 128 * m:128 * m + 128], WG[:, 1, :], whole).then_inc(e_pe, 1)
                pe.wait_ge(e_act, E_ACT.at(m, "square") - 1)
                e_product(m, 3, PAIR_ONES, NORM[m % 2], whole).then_inc(e_pe, 1)
                pe.wait_ge(e_dve, E_DVE.at(m, "rkk") - 1)
                e_product(m, 4, PAIR_ONES, NORM[m % 2], whole).then_inc(e_pe, 1)
            pe.wait_ge(e_dve, E_DVE.at(3, "bonus") - 1)
            run_chunks(pe, c_step)
            pe.wait_ge(c_act[0], C_ACT.at(C_SAMPLE, "o"))
            pe.wait_ge(c_dve[0], C_DVE.at(C_SAMPLE, "m"))
            for m in range(5):
                if m < 4:
                    if m:
                        pe.wait_ge(f_dve, F_DVE.at(m - 1, "centred") - 1)
                    for n in range(NB):
                        last = nc.tensor.matmul(PS[:, n, 0:BW], PAIR_ONES, CO[:, m, n * BW:(n + 1) * BW], start=True, stop=True)
                    last.then_inc(f_mean, 1)
                if m:
                    pe.wait_ge(f_act, F_ACT.at(m - 1, "square") - 1)
                    if m > 1:
                        pe.wait_ge(f_act, F_ACT.at(m - 2, "ln") - 1)
                    for n in range(NB):
                        last = nc.tensor.matmul(PS[:, 4 + n, 0:BW], PAIR_ONES, SQC[(m - 1) % 2][:, n * BW:(n + 1) * BW],
                                                start=True, stop=True)
                    last.then_inc(f_var, 1)
            layer_end(1)

        @block.scalar
        def _(act):
            step = Steps(act, act_step)

            def root(j):
                act.wait_ge(norm_sum, j + 1)
                if j >= 2:
                    act.wait_ge(norm_done, j - 1)
                step(nc.scalar.activation(rows(RN[2 + j % 2][:, :]), banks(j % 2), ACT.Ln, bias=EPS[:, 1:2]))
                nc.scalar.activation(RN[2 + j % 2][:, :], RN[2 + j % 2][:, :], ACT.Exp, scale=-0.5).then_inc(norm_root, 1)

            act.wait_ge(eps_set, 4)
            act.sem_inc(slot_act, 2)
            for s in range(2):
                act.sem_inc(row_out[s], 16)
            for k in range(8):
                act.wait_ge(x_in, 128)
                nc.scalar.activation(XH[:, k, :], X32[:, k, :], ACT.Copy).then_inc(xh_ready, 1)
            with act.Fori(0, 2) as i:
                for s in range(2):
                    act.wait_ge(unit_done, 2 * i + s + 3)
                    act.wait_ge(row_out[s], 16 * i + 16)
                    nc.scalar.activation(rows(U0[:, s, :]), banks(s), ACT.Gelu_apprx_tanh).then_inc(slot_act, 1)
                    act.wait_ge(slot_act, 2 * i + s + 3)
                    act.dma_start(GATE[ds(2 * i + s, 1), :, :].rearrange("a p n -> p (a n)"), U0[:, s, :])\
                       .then_inc(row_out[s], 16)
            act.wait_ge(params_in, 32)
            for s in range(2):
                act.wait_ge(row_out[s], 48)
            with act.Fori(0, 8) as i:
                for s in range(2):
                    act.wait_ge(unit_done, 2 * i + s + 7)
                    act.wait_ge(conv_done, 2 * i + s + 1)
                    nc.scalar.activation(rows(U0[:, s, :]), banks(s), ACT.Copy)
                    nc.scalar.activation(rows(XCQ[:, ds(2 * i + s, 1), :].rearrange("p a n -> p (a n)")), banks(s),
                                         ACT.Identity, scale=col_at("conv0_w3", 2 * i + s),
                                         bias=col_at("conv0_b", 2 * i + s)).then_inc(slot_act, 1)
            with act.Fori(0, 2) as i:
                for s in range(2):
                    act.wait_ge(unit_done, 2 * i + s + 23)
                    act.wait_ge(conv_done, 18)
                    act.wait_ge(row_out[s], 16 * i + 48)
                    nc.scalar.activation(rows(U0[:, s, :]), banks(s), ACT.Silu).then_inc(slot_act, 1)
                    act.wait_ge(slot_act, 2 * i + s + 23)
                    act.dma_start(ZROW[ds(2 * i + s, 1), :, :].rearrange("a p n -> p (a n)"), U0[:, s, :])\
                       .then_inc(row_out[s], 16)
            for m in range(4, 16):
                nc.scalar.activation(XCQ[:, m, 4:NT], XCQ[:, m, 4:NT], ACT.Silu).then_inc(silu_done, 1)
            for s in range(2):
                act.wait_ge(row_out[s], 80)
            act.dma_start(RGW[:, :, :, :], io["w_gates"]).then_inc(gates_in, 16)
            act.wait_ge(ba_done, 1)
            nc.scalar.activation(BETA, PSBA[:, :, 0:4], ACT.Sigmoid).then_inc(ba_act, 1)
            act.wait_ge(ba_vec, 1)
            nc.scalar.activation(GTMP[:, 1, :], GTMP[:, 1, :], ACT.Exp, scale=-1.0).then_inc(ba_act, 1)
            nc.scalar.activation(GTMP[:, 2, :], small("a_log", 36), ACT.Exp).then_inc(ba_act, 1)
            act.wait_ge(ba_act, 2)
            nc.scalar.activation(GTMP[:, 1, :], GTMP[:, 1, :], ACT.Ln, bias=1.0).then_inc(ba_act, 1)
            act.wait_ge(ba_done, 2)
            nc.scalar.activation(GC[:, :], PS[:, 7, 128:164], ACT.Copy).then_inc(ba_copied, 1)
            act.wait_ge(ba_copied, 1)
            nc.scalar.activation(EGC[:, :], GC[:, :], ACT.Exp).then_inc(ba_copied, 1)
            act.wait_ge(lam_vec, 1)
            nc.scalar.activation(LAM[:, 4:8], LAM[:, 4:8], ACT.Exp, scale=-1.0).then_inc(lam_act, 1)
            act.wait_ge(lam_act, 1)
            nc.scalar.activation(LAM[:, 4:8], LAM[:, 4:8], ACT.Ln, bias=1.0).then_inc(lam_act, 1)
            act.wait_ge(lam_vec, 2)
            for m in range(4):
                act.wait_ge(rg_done, 2 * m + 1)
                if m:
                    act.wait_ge(rg_vec, 4 * m)
                    act.wait_ge(gate_in, 16 * m)
                act.dma_start(MIX[4][:, :], GATE[m]).then_inc(gate_in, 16)
                nc.scalar.activation(rows(MIX[0][:, :]), banks(0), ACT.Sigmoid, bias=col("a_b_r", m)).then_inc(rg_read, 1)
                act.wait_ge(rg_done, 2 * m + 2)
                nc.scalar.activation(rows(MIX[1][:, :]), banks(1), ACT.Sigmoid, bias=col("a_b_i", m)).then_inc(rg_read, 1)
                act.wait_ge(rg_read, 2 * m + 1)
                nc.scalar.activation(MIX[2][:, :], MIX[0][:, :], ACT.Exp, scale=LAM[:, 8 + m:9 + m]).then_inc(rg_act, 1)
                nc.scalar.activation(MIX[3][:, :], MIX[0][:, :], ACT.Tanh, scale=LAM[:, 12 + m:13 + m]).then_inc(rg_act, 1)
                act.wait_ge(rg_vec, 4 * m + 2)
                nc.scalar.activation(MIX[3][:, :], MIX[3][:, :], ACT.Sqrt, scale=2.0).then_inc(rg_act, 1)
                act.wait_ge(rg_vec, 4 * m + 3)
                nc.scalar.activation(XH[:, m, 4:NT], MIX[0][:, 4:NT], ACT.Copy).then_inc(xh_ready, 1)
            act.wait_ge(rg_vec, 16)
            for j in range(8):
                act.wait_ge(silu_done, j + 1)
                if j >= 2:
                    act.wait_ge(norm_sum, j - 1)
                nc.scalar.activation(RN[j % 2][:, :], XCQ[:, 4 + j, :], ACT.Square).then_inc(sq_ready, 1)
                if j:
                    root(j - 1)
            root(7)
            act.dma_start(SS[:, :, :], io["s_b"]).then_inc(state_in, 16)
            act.wait_ge(norm_done, 8)

            def g_step(name, j, p):
                s, b = gdn_act[p], 4 * p
                n = 64 if is_sample(j, G_SAMPLE) else 128
                t0 = tile_columns(j, p)
                if name == "decays":
                    if not starts_set(j):
                        act.wait_ge(gdn_pe[p], G_PE.before(j))
                    for first, x in ((8, KT), (4, QT), (12, VT)):
                        last = nc.scalar.activation(x[p][:, :, 0:n], XCQ[:, first:first + 4, ds(t0, n)], ACT.Copy)
                    last.then_inc(s, 1)
                elif name == "diffs":
                    act.wait_ge(gdn_dve[p], G_DVE.at(j, "diff"))
                    nc.scalar.activation(DA[p][:, :, :], DA[p][:, :, :], ACT.Exp)
                    nc.scalar.activation(DB[p][:, :, :], DB[p][:, :, :], ACT.Exp, scale=-1.0)
                    nc.scalar.activation(KOC[p][:, :], KOC[p][:, :], ACT.Exp)
                    nc.scalar.activation(EG[p][:, :, :], per_head(b), ACT.Exp).then_inc(s, 1)
                elif name == "grams":
                    act.wait_ge(s, G_ACT.at(j, "exps"))
                    act.wait_ge(gdn_pe[p], G_PE.at(j, "k_turned"))
                    for h in range(4):
                        last = nc.scalar.activation(KO[p][:, h, :], PS[:, b + 3, 128 * h:128 * h + 128], ACT.Copy,
                                                    scale=KOC[p][:, h:h + 1])
                    last.then_inc(s, 1)
                elif name == "blocks":
                    act.wait_ge(gdn_pe[p], G_PE.at(j, "v_turned"))
                    for h in range(4):
                        beta = BETA36[:, ds(8 * j[0] + (8 * j[1] + 4 * p + h), 1)]
                        last = nc.scalar.activation(VB[p][:, h, :], PS[:, b, 128 * h:128 * h + 128], ACT.Copy, scale=beta)
                    last.then_inc(s, 1)
                elif name[0] == "w":
                    act.wait_ge(gdn_pe[p], G_PE.at(j, name))
                    nc.scalar.activation(WW[p][:, :, :], per_head(b + 1), ACT.Copy).then_inc(s, 1)
                elif name == "carry1":
                    act.wait_ge(gdn_pe[p], G_PE.at(j, "v_new"))
                    nc.scalar.activation(VN[p][:, :, :], per_head(b + 1), ACT.Copy).then_inc(s, 1)
                elif name == "carry2":
                    act.wait_ge(gdn_pe[p], G_PE.at(j, "o"))
                    nc.scalar.activation(OT[:, :, ds(t0, n)], per_head(b + 2)[:, :, 0:n], ACT.Copy).then_inc(s, 1)

            run_chunks(act, g_step, G_FIRST, G_SECOND, G_SAMPLE)
            act.wait_ge(gdn_dve[1], G_DVE.at((0, 3), "s"))
            act.dma_start(io["s_b_p"], SP[:, :, :]).then_inc(state_out, 16)
            act.wait_ge(gdn_dve[0], G_DVE.at(G_SAMPLE, "s"))
            act.dma_start(io["s_b_s"], SS[:, :, :]).then_inc(state_out, 16)
            act.wait_ge(state_out, 32)
            act.wait_ge(o_zeroed, 1)
            act.dma_start(ZT[:, :, :], ZROW.rearrange("t p n -> p t n")).then_inc(z_in, 16)
            act.dma_start(XR[:, :, :], io["x"]).then_inc(x_back, 16)

            def o_norm_root(h):
                act.wait_ge(o_sum, h + 1)
                if h >= 2:
                    act.wait_ge(o_gated, h - 1)
                step(nc.scalar.activation(rows(RN[2 + h % 2][:, :]), banks(h % 2), ACT.Ln, bias=EPS[:, 1:2], scale=1 / 128))
                nc.scalar.activation(RN[2 + h % 2][:, :], RN[2 + h % 2][:, :], ACT.Exp, scale=-0.5).then_inc(o_root, 1)

            def o_hi(h):
                act.wait_ge(o_gated, h + 1)
                nc.scalar.activation(XH[:, 4 + h, :], OT[:, h, :], ACT.Copy).then_inc(xh_ready, 1)

            for h in range(4):
                if h >= 2:
                    act.wait_ge(o_sum, h - 1)
                nc.scalar.activation(RN[h % 2][:, :], OT[:, h, :], ACT.Square).then_inc(o_square, 1)
                if h:
                    o_norm_root(h - 1)
                if h >= 2:
                    o_hi(h - 2)
            o_norm_root(3)
            o_hi(2)
            o_hi(3)

            def norm(n, gain, bias):
                for k in range(8):
                    act.wait_ge(ln_sub, k + 1 + 8 * n)
                    if k >= 2:
                        act.wait_ge(ln_var, k - 1 + 8 * n)
                    nc.scalar.activation(SQ[k % 2][:, :], Y[:, k, :], ACT.Square).then_inc(ln_sq, 1)
                act.wait_ge(ln_var, 8 + 8 * n)
                step(nc.scalar.activation(rows(RS[:, :]), banks(1), ACT.Ln, bias=EPS[:, 0:1], scale=1 / 1024))
                nc.scalar.activation(RS[:, :], RS[:, :], ACT.Exp, scale=-0.5).then_inc(ln_root, 1)
                for k in range(8):
                    act.wait_ge(ln_scaled, k + 1 + 8 * n)
                    nc.scalar.activation(Y[:, k, :], Y[:, k, :], ACT.Identity, scale=col(gain, k), bias=col(bias, k))\
                      .then_inc(ln_hi, 1)
                    act.wait_ge(ln_hi, 2 * k + 1 + 16 * n)
                    nc.scalar.activation(XH[:, k, :], Y[:, k, :], ACT.Copy).then_inc(ln_hi, 1)

            def chunk(l, g, unit, first=False):
                for t in range(4):
                    act.wait_ge(unit_done, unit + t + 3)
                    act.wait_ge(ffn_conv, 4 * g + t + 1 + 46 * l)
                    nc.scalar.activation(rows(UF[:, t % 2, :]), banks(t % 2), ACT.Copy)
                    if t == 0:
                        act.wait_ge(h_done, g + 1 + 12 * l)
                    f = 2 * g + (t if t < 2 else 20 + t)
                    nc.scalar.activation(rows(CB[:, t, :]), banks(t % 2), ACT.Identity, scale=col_at("ffn_w2%d" % l, f),
                                         bias=col_at("ffn_b%d" % l, f)).then_inc(up_read, 1)
                    if t >= 2:
                        act.wait_ge(ffn_conv, 4 * g + t + 1 + 46 * l)
                        nc.scalar.activation(CB[:, t - 2, :], CB[:, t - 2, :], ACT.Silu).then_inc(ffn_silu, 1)
                if not first:
                    act.wait_ge(unit_done, unit + 8)
                for j in range(2):
                    act.wait_ge(ffn_mul, 2 * g + j + 1 + 22 * l)
                    nc.scalar.activation(HH[:, j, :], CB[:, 2 + j, :], ACT.Copy).then_inc(h_hi, 1)

            def layer_end(l):
                first, part = OUT_UNIT[l], OUT_PART[l]
                act.sem_inc(up_read, 1)
                act.sem_inc(gate_read, 2)
                norm(2 * l, "ln_mix_g%d" % l, "ln_mix_b%d" % l)
                chunk(l, 0, first + 8, True)
                with act.Fori(1, 11) as g:
                    chunk(l, g, 6 * g + first + 6)
                act.wait_ge(unit_done, first + 76)
                act.dma_start(P32[:, :, :], io["p"][l]).then_inc(p_in, 16)
                act.wait_ge(p_in, 16 + 16 * l)
                nc.scalar.activation(PH[:, :, :], P32[:, :, :], ACT.Copy).then_inc(p_hi, 1)
                act.wait_ge(p_split, 2 + 2 * l)
                norm(2 * l + 1, "ln_ffn_g%d" % l, "ln_ffn_b%d" % l)
                for m in range(8):
                    if m % 4 < 3:
                        act.wait_ge(part_done, part + 66 + 3 * (m // 4) + m % 4 + 1)
                    else:
                        act.wait_ge(unit_done, first + 74 + m // 4 + 3)
                    nc.scalar.activation(rows(PP[:, m, :]), banks(m % 2), ACT.Copy).then_inc(wp_read, 1)
                act.wait_ge(wp_read, 8 + 8 * l)
                with act.Fori(0, 4) as i:
                    for s in range(2):
                        act.wait_ge(unit_done, 2 * i + s + first + 79)
                        act.wait_ge(gate_added, 2 * i + s + 1 + 10 * l)
                        nc.scalar.activation(rows(SG[s][:, :]), banks(s), ACT.Sigmoid, bias=col_at("ple_b%d" % l, 2 * i + s))\
                          .then_inc(gate_read, 1)

            layer_end(0)
            act.wait_ge(unit_done, 110)
            act.wait_ge(gate_added, 10)
            act.dma_start(XROW, Y[:, :, :]).then_inc(x_out, 16)
            for k in range(8):
                nc.scalar.activation(XH[:, k, :], Y[:, k, :], ACT.Copy).then_inc(x_hi, 1)
            act.sem_inc(in1_read, 2)
            act.sem_inc(a_probs, 2)
            act.sem_inc(a_scaled, 1)
            act.sem_inc(a_hi, 1)
            for s in range(2):
                act.sem_inc(row1_out[s], 16)
            act.wait_ge(x_out, 16)
            act.wait_ge(in_ready, 1)
            with act.Fori(0, 7) as i:
                for s in range(2):
                    act.wait_ge(unit_done, 2 * i + s + IN1 + 3)
                    act.wait_ge(row1_out[s], 16 * i + 16)
                    nc.scalar.activation(rows(U1[:, s, :]), banks(s), ACT.Copy).then_inc(in1_read, 1)
                for s in range(2):
                    act.wait_ge(shifted, 2 * i + s + 1)
                    act.dma_start(CROW[ds(2 * i + s, 1), :, :].rearrange("a p n -> p (a n)"), DX[:, s, :])\
                       .then_inc(row1_out[s], 16)
            for m, x in enumerate((QA[:, 0, :], QA[:, 1, :], QA[:, 2, :], CR[:, 0, :], CR[:, 1, :], KRW[:, :])):
                act.wait_ge(unit_done, IN1 + 14 + m + 3)
                nc.scalar.activation(rows(x), banks(m % 2), ACT.Copy).then_inc(in1_read, 1)
            for s in range(2):
                act.wait_ge(row1_out[s], 16 * 8)
            act.dma_start(ROPE[:, :, :], io["rope"]).then_inc(mla_in, 16)
            act.dma_start(CCK[:, :, :], io["cache_ckv"]).then_inc(cache_in, 16)
            act.dma_start(KRR[:, NT:NK], io["cache_krope"]).then_inc(kr_cache_in, 16)
            act.wait_ge(in1_read, 22)
            for j in range(5):
                if j >= 2:
                    act.wait_ge(m_sum, j - 1)
                x = QA[:, j, :] if j < 3 else CR[:, j - 3, :]
                nc.scalar.activation(SQD[j % 2][:, :], x, ACT.Square).then_inc(m_square, 1)
            for slot in range(2):
                act.wait_ge(m_sum, 3 + 2 * slot)
                step(nc.scalar.activation(rows(RSD[slot][:, :]), banks(slot), ACT.Ln, bias=EPS[:, 1:2],
                                          scale=1 / 384 if slot == 0 else 1 / 256))
                nc.scalar.activation(RSD[slot][:, :], RSD[slot][:, :], ACT.Exp, scale=-0.5).then_inc(m_root, 1)
            act.wait_ge(cache_in, 16)
            nc.scalar.activation(CH[:, :, NT:NK], CCK[:, :, :], ACT.Copy).then_inc(m_hi, 1)
            for j in range(5):
                act.wait_ge(m_scaled, j + 1)
                h, x = (QAH[:, j, :], QA[:, j, :]) if j < 3 else (CH[:, j - 3, 0:NT], CR[:, j - 3, :])
                nc.scalar.activation(h, x, ACT.Copy).then_inc(m_hi, 1)
            act.dma_start(io["ckv"], CR[:, :, :]).then_inc(c_out, 16)
            act.wait_ge(kr_done, 1)
            act.dma_start(io["krope"], KRR[0:64, 0:NT]).then_inc(kr_out, 16)
            for m in range(6):
                if m % 2:
                    act.wait_ge(unit_done, IN1 + 20 + m // 2 + 3)
                else:
                    act.wait_ge(part_done, 72 + m // 2 + 1)
                nc.scalar.activation(rows(QN[:, m, :] if m < 4 else QR[:, m - 4, :]), banks(m % 2), ACT.Copy)\
                  .then_inc(qkv_read, 1)
            act.wait_ge(c_out, 16)
            act.wait_ge(m_lo, 6)
            for m in range(4):
                if m % 2:
                    act.wait_ge(unit_done, IN1 + 23 + m // 2 + 3)
                else:
                    act.wait_ge(part_done, 75 + m // 2 + 1)
                nc.scalar.activation(rows(KN[:, m, :], KW), banks(m % 2, KW), ACT.Copy).then_inc(qkv_read, 1)
            act.wait_ge(q_rotated, 2)
            for j in range(10):
                if j < 9:
                    act.wait_ge(v_done, j + 1)
                else:
                    act.wait_ge(unit_done, IN1 + 26 + 2)
                nc.scalar.activation(VTOK[:, j, :], PS[:, j % 8, :], ACT.Copy).then_inc(v_read, 1)

            def probs(i, hh, n):
                t0, nq = queries(n)
                s, g = 18 * i + 9 * hh + n, (9 * hh + n) % 2
                nk = 256 if n == 8 else 128 * (n + 1)
                act.wait_ge(a_max, s + 1)
                act.wait_ge(a_turned, s)
                nc.scalar.activation(PB[0:nq, g, 0:nk], PS[0:nq, 2 * g:2 * g + 2, :].rearrange("p b n -> p (b n)")[:, 0:nk],
                                     ACT.Exp, scale=D_SCALE, bias=AST[g][0:nq, 0:1], accum_out=AST[g][0:nq, 1:2])\
                  .then_inc(a_probs, 1)

            def keys(i, hh, n):
                s = 18 * i + 9 * hh + n
                act.wait_ge(a_turned, s + 2)
                act.wait_ge(a_out, s + 1)
                nk = 256 if n == 8 else 128 * min(4, n + 1)
                nc.scalar.activation(PTB[:, 0:nk], PS[:, 4, 0:nk], ACT.Copy).then_inc(a_keys, 1)

            def scaled(i, hh, n):
                t0, nq = queries(n)
                s, g = 18 * i + 9 * hh + n, (9 * hh + n) % 2
                act.wait_ge(a_out, s + 2)
                act.wait_ge(a_inv, s + 1)
                own = 64 if n == 8 else 128
                nc.scalar.activation(OB[0:nq, g, :], PS[0:nq, 6, 0:128], ACT.Copy, scale=AST[g][0:nq, 2:3]).then_inc(a_scaled, 1)
                act.wait_ge(a_back, s + 1)
                nc.scalar.activation(XH[:, ds(2 * i + hh + 4, 1), t0:t0 + own].rearrange("p a n -> p (a n)"), PS[:, 7, 0:own],
                                     ACT.Copy).then_inc(a_hi, 1)

            order = [(hh, n) for hh in range(2) for n in range(STEPS)]
            with act.Fori(0, 2) as i:
                act.wait_ge(a_scores, 18 * i + 1)
                nc.scalar.activation(QRS[:, :], QR[:, ds(i, 1), :].rearrange("p a n -> p (a n)"), ACT.Copy)
                for hh in range(2):
                    nc.scalar.activation(QS[:, hh, :], QN[:, ds(2 * i + hh, 1), :].rearrange("p a n -> p (a n)"), ACT.Copy)\
                      .then_inc(q_staged, 1)
                probs(i, 0, 0)
                for x, (hh, n) in enumerate(order):
                    if x + 1 < len(order):
                        probs(i, *order[x + 1])
                    keys(i, hh, n)
                    scaled(i, hh, n)
            def c_step(name, j, p):
                s = c_act[p]
                level = int(name[1:]) if name[0] in "wt" else 0
                if name == "prep0":
                    act.wait_ge(c_dve[p], C_DVE.at(j, "scan"))
                    nc.scalar.activation(PX[p][:, :, 1:65], CIN[p][:, 12:16, :], ACT.Exp, scale=-DECAY).then_inc(s, 1)
                    nc.scalar.activation(PI_S[p][:, :, :], CIN[p][:, 12:16, :], ACT.Exp, scale=DECAY).then_inc(s, 1)
                elif name == "prep2":
                    act.wait_ge(c_pe[p], C_PE.at(j, "bg"))
                    act.wait_ge(c_dve[p], C_DVE.at(j, "rb"))
                    for h in range(2):
                        last = nc.scalar.activation(BT_B[p][half(h), :, half(h)], per_head(4 * p + 3)[half(h), :, 64:128],
                                                    ACT.Copy, scale=-1.0)
                    last.then_inc(s, 1)
                    act.wait_ge(c_dve[p], C_DVE.at(j, "rk"))
                    for h in range(2):
                        last = nc.scalar.activation(
                            KT_B[p][half(h), :, half(h)].rearrange("p (b m) n -> p b m n", b=2),
                            k_group(p)[half(h), :, :].rearrange("p b (m n) -> p b m n", m=2)[:, :, :, 128:192], ACT.Copy)
                    last.then_inc(s, 1)
                elif name == "prep3":
                    act.wait_ge(c_pe[p], C_PE.at(j, "vt"))
                    nc.scalar.activation(VT_B[p][:, :, :], per_head(4 * p + 2), ACT.Copy).then_inc(s, 1)
                elif name[0] == "w":
                    act.wait_ge(c_pe[p], C_PE.at(j, "lw%d" % level))
                    nc.scalar.activation(W_B[p][:, :, :], per_head(4 * p + 1), ACT.Copy).then_inc(s, 1)
                elif name == "carry1":
                    act.wait_ge(c_pe[p], C_PE.at(j, "x"))
                    nc.scalar.activation(X_B[p][:, :, :], per_head(4 * p + 1), ACT.Copy).then_inc(s, 1)
                elif name == "carry2":
                    act.wait_ge(c_pe[p], C_PE.at(j, "u"))
                    nc.scalar.activation(U_B[p][:, :, :], per_head(4 * p + 2), ACT.Copy).then_inc(s, 1)
                elif name == "carry3":
                    act.wait_ge(c_pe[p], C_PE.at(j, "o"))
                    nc.scalar.activation(CO[:, :, chunk_columns(j, p)], stacked(p, 1, 0), ACT.Copy).then_inc(s, 1)

            act.wait_ge(a_hi, 73)
            act.wait_ge(e_wg, 16)
            nc.scalar.activation(WG[0:64, 0, :], WG[0:64, 0, :], ACT.Tanh).then_inc(wg_ready, 1)
            nc.scalar.activation(WG[:, 1, :], WG[:, 1, :], ACT.Sigmoid).then_inc(wg_ready, 1)
            for m in range(4):
                p = m % 2
                if m >= 2:
                    act.wait_ge(e_out[p], 32)
                act.wait_ge(e_pe, E_PE.at(m, "w") - 1)
                nc.scalar.activation(rows(PREP[p][:, SIGR, :]), banks((5 * m) % 2), ACT.Sigmoid, bias=col("c_w0", m))\
                  .then_inc(e_act, 1)
                act.wait_ge(e_pe, E_PE.at(m, "a") - 1)
                nc.scalar.activation(rows(PREP[p][:, KKAR, :]), banks((5 * m + 1) % 2), ACT.Sigmoid, bias=col("c_a0", m))\
                  .then_inc(e_act, 1)
                act.wait_ge(e_pe, E_PE.at(m, "g") - 1)
                nc.scalar.activation(rows(BG[p][:, GR, :]), banks((5 * m + 2) % 2), ACT.Copy).then_inc(e_act, 1)
                act.wait_ge(e_dve, E_DVE.at(m, "kk0") - 1)
                nc.scalar.activation(NORM[p][:, :], PREP[p][:, KKR, :], ACT.Square).then_inc(e_act, 1)
                act.wait_ge(e_pe, E_PE.at(m, "norm") - 1)
                nc.scalar.activation(rows(NORM[p][:, :]), banks((5 * m + 3) % 2), ACT.Ln, bias=EPS[:, 1:2]).then_inc(e_act, 1)
                act.wait_ge(e_act, E_ACT.at(m, "ln") - 1)
                nc.scalar.activation(NORM[p][:, :], NORM[p][:, :], ACT.Exp, scale=-0.5).then_inc(e_act, 1)
            act.wait_ge(c_ready, 1)
            run_chunks(act, c_step)
            def f_ln(m):
                act.wait_ge(f_var, m + 1)
                nc.scalar.activation(rows(INC[m % 2][:, :]), banks(1), ACT.Ln, bias=EPS[:, 2:3], scale=1 / 64).then_inc(f_act, 1)
                act.wait_ge(f_act, F_ACT.at(m, "ln") - 1)
                nc.scalar.activation(INC[m % 2][:, :], INC[m % 2][:, :], ACT.Exp, scale=-0.5).then_inc(f_act, 1)
                act.wait_ge(f_dve, F_DVE.at(m, "scaled") - 1)
                nc.scalar.activation(CO[:, m, :], CO[:, m, :], ACT.Identity, scale=col("c_lnx_g", m),
                                     bias=col("c_lnx_b", m)).then_inc(f_act, 1)
                act.wait_ge(f_dve, F_DVE.at(m, "gated") - 1)
                nc.scalar.activation(XH[:, m, :], CO[:, m, :], ACT.Copy).then_inc(f_act, 1)

            for m in range(4):
                act.wait_ge(f_dve, F_DVE.at(m, "centred") - 1)
                nc.scalar.activation(SQC[m % 2][:, :], CO[:, m, :], ACT.Square).then_inc(f_act, 1)
                f_ln(m)
            for n, (out, p, j) in enumerate((("s_c_p", 1, (0, 7)), ("s_c_s", 0, C_SAMPLE))):
                act.wait_ge(c_dve[p], C_DVE.at(j, "m"))
                for h in range(2):
                    act.dma_start(io[out][half(h)], MB[n][half(h), :, half(h)]).then_inc(c_state_out, 16)
            act.wait_ge(c_state_out, 64)
            act.wait_ge(f_dve, F_DVE.at(3, "lo") - 1)
            act.dma_start(XR[:, :, :], XROW).then_inc(x_back, 16)
            layer_end(1)
            act.wait_ge(gate_added, 20)
            act.dma_start(io["y"], Y[:, :, :]).then_inc(y_out, 16)
            act.wait_ge(y_out, 16)
            act.wait_ge(kr_out, 16)

        @block.vector
        def _(dve):
            step = Steps(dve, dve_step)
            dve.sem_inc(conv_done, 2)
            for n, e in enumerate((1e-5, 1e-6, 64e-5, 0.0)):
                nc.vector.memset(EPS[:, n:n + 1], e).then_inc(eps_set, 1)
            for k in range(8):
                dve.wait_ge(xh_ready, k + 1)
                nc.vector.tensor_tensor(XL[:, k, :], X32[:, k, :], XH[:, k, :], ALU.subtract).then_inc(xl_ready, 1)
            dve.wait_ge(params_in, 32)
            step(nc.vector.tensor_copy(WBAH[:, :], small("w_beta_alpha", 64)))
            nc.vector.tensor_tensor(WBAL[:, :], small("w_beta_alpha", 64), WBAH[:, :], ALU.subtract).then_inc(ba_split, 1)
            with dve.Fori(0, 8) as i:
                step.enter(i, 10)
                for s in range(2):
                    dve.wait_ge(slot_act, 2 * i + s + 7)
                    step(nc.vector.tensor_copy(U0[:, s, S0 - 3:S0],
                                               SMALL[:, ds(sp_["hist_conv0"] + 6 * i + 3 * s, 3)]))
                    kept = op["conv0"] + 12 * i + 6 * s
                    step(nc.vector.tensor_copy(KEPT[:, ds(kept, 3)], U0[:, s, S0 + 61:S0 + 64]))
                    step(nc.vector.tensor_copy(KEPT[:, ds(kept + 3, 3)], U0[:, s, NT - 3:NT]))
                    y = XCQ[:, ds(2 * i + s, 1), 4:NT].rearrange("p a n -> p (a n)")
                    for j in (1, 2):
                        step(nc.vector.scalar_tensor_tensor(y, U0[:, s, 4 - j:NT - j], col_at("conv0_w%d" % (3 - j), 2 * i + s),
                                                            y, ALU.mult, ALU.add))
                    nc.vector.scalar_tensor_tensor(y, U0[:, s, 1:NT - 3], col_at("conv0_w0", 2 * i + s), y,
                                                   ALU.mult, ALU.add).then_inc(conv_done, 1)
            step.leave(8)
            dve.wait_ge(ba_done, 1)
            dve.wait_ge(ba_act, 1)
            step(nc.vector.tensor_tensor(GTMP[:, 0, :].rearrange("p (c h) -> p c h", h=4), PSBA[:, :, 4:8],
                                         small("dt_bias", 36).rearrange("p (c h) -> p c h", h=4), ALU.add))
            nc.vector.scalar_tensor_tensor(GTMP[:, 1, :], GTMP[:, 0, :], -1.0, GTMP[:, 0, :], ALU.mult, ALU.max).then_inc(ba_vec, 1)
            dve.wait_ge(ba_act, 4)
            step(nc.vector.scalar_tensor_tensor(GTMP[:, 0, :], GTMP[:, 0, :], 0.0, GTMP[:, 1, :], ALU.max, ALU.add))
            step(nc.vector.scalar_tensor_tensor(GB[:, :], GTMP[:, 0, :], -1.0, GTMP[:, 2, :], ALU.mult, ALU.mult))
            nc.vector.memset(GB[64:128, 32:36], 0.0).then_inc(g_ready, 1)
            dve.wait_ge(ba_copied, 2)
            step(nc.vector.scalar_tensor_tensor(NBEG[:, :], EGC[:, :], -1.0, BETA36[:, :], ALU.mult, ALU.mult))
            lam = col4("a_lambda")
            nc.vector.scalar_tensor_tensor(LAM[:, 4:8], lam, -1.0, lam, ALU.mult, ALU.max).then_inc(lam_vec, 1)
            step(nc.vector.tensor_scalar(LAM[:, 0:4], lam, -1.0, 0.0, ALU.mult, ALU.max))
            dve.wait_ge(lam_act, 2)
            step(nc.vector.tensor_tensor(LAM[:, 0:4], LAM[:, 0:4], LAM[:, 4:8], ALU.add))
            step(nc.vector.tensor_scalar(LAM[:, 12:16], LAM[:, 0:4], 8.0, None, ALU.mult))
            nc.vector.tensor_scalar(LAM[:, 8:12], LAM[:, 0:4], -8.0, None, ALU.mult).then_inc(lam_vec, 1)
            for m in range(4):
                dve.wait_ge(rg_read, 2 * m + 2)
                step(nc.vector.tensor_tensor(MIX[1][:, 4:NT], MIX[1][:, 4:NT], XCQ[:, m, 4:NT], ALU.mult))
                dve.wait_ge(rg_act, 3 * m + 2)
                step(nc.vector.tensor_scalar(MIX[0][:, :], MIX[3][:, :], 1.0, None, ALU.add))
                nc.vector.reciprocal(MIX[0][:, :], MIX[0][:, :]).then_inc(rg_vec, 1)
                dve.wait_ge(rg_vec, 4 * m + 1)
                step(nc.vector.tensor_tensor(MIX[3][:, :], MIX[3][:, :], MIX[0][:, :], ALU.mult))
                nc.vector.tensor_scalar(MIX[3][:, :], MIX[3][:, :], 1e-34, None, ALU.max).then_inc(rg_vec, 1)
                dve.wait_ge(rg_act, 3 * m + 3)
                step(nc.vector.tensor_tensor(MIX[1][:, 4:NT], MIX[1][:, 4:NT], MIX[3][:, 4:NT], ALU.mult))
                step(nc.vector.tensor_tensor_scan(MIX[0][:, S0:S0 + 64], MIX[2][:, S0:S0 + 64], MIX[1][:, S0:S0 + 64],
                                                  small("h0", 1, m), ALU.mult, ALU.add))
                step(nc.vector.tensor_tensor_scan(MIX[0][:, P0:NT], MIX[2][:, P0:NT], MIX[1][:, P0:NT], 0.0,
                                                  ALU.mult, ALU.add))
                for n, c in enumerate((S0 + 63, NT - 1)):
                    step(nc.vector.tensor_copy(KEPT[:, op["h"] + 2 * m + n:op["h"] + 2 * m + n + 1], MIX[0][:, c:c + 1]))
                step(nc.vector.memset(MIX[0][:, S0 + 64:P0], 0.0))
                dve.wait_ge(gate_in, 16 * m + 16)
                nc.vector.tensor_tensor(MIX[0][:, 4:NT], MIX[0][:, 4:NT], MIX[4][:, 4:NT], ALU.mult).then_inc(rg_vec, 1)
                dve.wait_ge(xh_ready, 8 + m + 1)
                nc.vector.tensor_tensor(XL[:, m, 4:NT], MIX[0][:, 4:NT], XH[:, m, 4:NT], ALU.subtract).then_inc(rg_vec, 1)
            for j in range(8):
                dve.wait_ge(norm_root, j + 1)
                x = XCQ[:, 4 + j, 4:NT]
                nc.vector.scalar_tensor_tensor(x, x, 128.0 ** -0.5 if j < 4 else 1.0, RN[2 + j % 2][:, 4:NT],
                                               ALU.mult, ALU.mult).then_inc(norm_done, 1)
            step(nc.vector.memset(SP[:, :, :], 0.0))

            def g_step(name, j, p):
                s, b, sample = gdn_dve[p], 4 * p, is_sample(j, G_SAMPLE)
                state = SS if sample else SP
                here = tile_place(j, p)
                if name == "decays":
                    if not starts_set(j):
                        dve.wait_ge(gdn_pe[p], G_PE.before(j))
                    nc.vector.tensor_tensor(LM[p][:, :, :], heads_of(UPPER), heads_of(GB[:, here]), ALU.mult).then_inc(s, 1)
                    if sample:
                        for x in (KT, QT, VT):
                            last = nc.vector.memset(x[0][:, :, 64:128], 0.0)
                        last.then_inc(pad_zeroed, 1)
                elif name == "diffs":
                    dve.wait_ge(gdn_pe[p], G_PE.at(j, "rows"))
                    step(nc.vector.tensor_tensor(DA[p][:, :, :], per_head(b), heads_of(GC[:, here]), ALU.subtract))
                    nc.vector.tensor_tensor(KOC[p][:, :], per_head(b)[:, :, 127], GC[:, here], ALU.subtract)
                    step(nc.vector.tensor_scalar(DB[p][:, :, :], DA[p][:, :, :], 0.0, None, ALU.max))
                    nc.vector.tensor_scalar(DA[p][:, :, :], DA[p][:, :, :], 0.0, None, ALU.min).then_inc(s, 1)
                elif name == "grams":
                    dve.wait_ge(gdn_act[p], G_ACT.at(j, "exps"))
                    step(nc.vector.tensor_tensor(DB[p][:, :, :], DB[p][:, :, :], heads_of(BETA36[:, here]), ALU.mult))
                    dve.wait_ge(gdn_pe[p], G_PE.at(j, "gram"))
                    nc.vector.tensor_tensor(DB[p][:, :, :], per_head(b + 1), DB[p][:, :, :], ALU.mult).then_inc(s, 1)
                    dve.wait_ge(s, G_DVE.at(j, "lower"))
                    nc.vector.tensor_tensor(LM[p][:, :, :], DB[p][:, :, :], heads_of(level_mask(0)), ALU.mult).then_inc(s, 1)
                elif name == "blocks":
                    dve.wait_ge(s, G_DVE.at(j, "m0"))
                    nc.vector.tensor_tensor(TA[p][:, :, :], heads_of(IDENT), LM[p][:, :, :], ALU.subtract).then_inc(s, 1)
                    dve.wait_ge(gdn_pe[p], G_PE.at(j, "m_turned"))
                    nc.vector.tensor_tensor(TT[p][:, :, :], heads_of(IDENT), per_head(b + 1), ALU.subtract).then_inc(s, 1)
                    dve.wait_ge(gdn_pool[p], G_POOL.at(j, "upper"))
                    nc.vector.tensor_tensor(DA[p][:, :, :], per_head(b + 2), DA[p][:, :, :], ALU.mult).then_inc(s, 1)
                elif name[0] == "t":
                    dve.wait_ge(gdn_pe[p], G_PE.at(j, "tt" + name[1]))
                    nc.vector.tensor_tensor(TT[p][:, :, :], TT[p][:, :, :], per_head(b + 2), ALU.subtract).then_inc(s, 1)
                    if name != "t6":
                        dve.wait_ge(gdn_pe[p], G_PE.at(j, "ta" + name[1]))
                        nc.vector.tensor_tensor(TA[p][:, :, :], TA[p][:, :, :], per_head(b + 3), ALU.subtract).then_inc(s, 1)
                    else:
                        dve.wait_ge(gdn_pe[p], G_PE.at(j, "ks"))
                        step(nc.vector.tensor_tensor(RR[p][:, :, :], per_head(b), heads_of(NBEG[:, here]), ALU.mult))
                        dve.wait_ge(gdn_act[p], G_ACT.at(j, "vb"))
                        nc.vector.tensor_tensor(RR[p][:, :, :], RR[p][:, :, :], VB[p][:, :, :], ALU.add).then_inc(s, 1)
                elif name == "carry2":
                    dve.wait_ge(gdn_pe[p], G_PE.at(j, "o"))
                    step(nc.vector.tensor_tensor(state[:, :, :], state[:, :, :],
                                                 EG[p][:, :, 127:128].to_broadcast([128, 4, 128]), ALU.mult))
                    dve.wait_ge(gdn_pe[p], G_PE.at(j, "s"))
                    nc.vector.tensor_tensor(state[:, :, :], state[:, :, :], per_head(b + 3), ALU.add).then_inc(s, 1)

            run_chunks(dve, g_step, G_FIRST, G_SECOND, G_SAMPLE,
                       lambda i: step.enter(i, 2 * 5, 1), lambda: step.leave(4))
            dve.wait_ge(gdn_act[1], G_ACT.at((0, 3), "out"))
            dve.wait_ge(gdn_act[0], G_ACT.at(G_SAMPLE, "out"))
            nc.vector.memset(OT[:, :, 0:S0], 0.0)
            nc.vector.memset(OT[:, :, S0 + 64:P0], 0.0).then_inc(o_zeroed, 1)

            def o_lo(h):
                dve.wait_ge(xh_ready, 12 + h + 1)
                nc.vector.tensor_tensor(XL[:, 4 + h, :], OT[:, h, :], XH[:, 4 + h, :], ALU.subtract).then_inc(mix_ready[0], 1)

            dve.wait_ge(z_in, 16)
            for h in range(4):
                dve.wait_ge(o_root, h + 1)
                step(nc.vector.scalar_tensor_tensor(OT[:, h, :], OT[:, h, :], col("b_norm_g"), RN[2 + h % 2][:, :],
                                                    ALU.mult, ALU.mult))
                nc.vector.tensor_tensor(OT[:, h, :], OT[:, h, :], ZT[:, h, :], ALU.mult).then_inc(o_gated, 1)
                if h >= 1:
                    o_lo(h - 1)
            o_lo(3)

            def norm(n):
                dve.wait_ge(ln_mean, 1 + n)
                for k in range(8):
                    nc.vector.scalar_tensor_tensor(rows(Y[:, k, :]), banks(0), -1 / 1024, rows(Y[:, k, :]),
                                                   ALU.mult, ALU.add).then_inc(ln_sub, 1)
                dve.wait_ge(ln_root, 1 + n)
                dve.wait_ge(ln_sub, 8 + 8 * n)
                dve.wait_ge(ln_sq, 8 + 8 * n)

                for k in range(8):
                    nc.vector.tensor_tensor(Y[:, k, :], Y[:, k, :], RS[:, :], ALU.mult).then_inc(ln_scaled, 1)
                gaps(ln_lo, 8 * n + 8, gaps_zeroed)

            def gaps(s, value, done):
                dve.wait_ge(s, value)
                for x in (XH, XL):
                    nc.vector.memset(x[:, :, 0:S0].bitcast(F32), 0.0)
                    last = nc.vector.memset(x[:, :, S0 + 64:P0].bitcast(F32), 0.0)
                last.then_inc(done, 1)

            def convolve(l, g, t):
                dve.wait_ge(up_read, 4 * g + t + 2 + 45 * l)
                f = 2 * g + (t if t < 2 else 20 + t)
                u, y = UF[:, t % 2, :], CB[:, t, 4:NT]
                hist, kept = sp_["hist_ffn"] + 88 * l + 2 * f, op["ffn"] + 176 * l + 4 * f
                step(nc.vector.tensor_copy(u[:, S0 - 2:S0], SMALL[:, ds(hist, 2)]))
                nc.vector.tensor_copy(KEPT[:, ds(kept, 2)], u[:, S0 + 62:S0 + 64])
                nc.vector.tensor_copy(KEPT[:, ds(kept + 2, 2)], u[:, NT - 2:NT])
                step(nc.vector.scalar_tensor_tensor(y, u[:, 3:NT - 1], col_at("ffn_w1%d" % l, f), y, ALU.mult, ALU.add))
                nc.vector.scalar_tensor_tensor(y, u[:, 2:NT - 2], col_at("ffn_w0%d" % l, f), y, ALU.mult, ALU.add)\
                  .then_inc(ffn_conv, 1)

            def multiply(l, g, tiles=range(2)):
                for j in tiles:
                    dve.wait_ge(ffn_silu, 2 * g + j + 1 + 22 * l)
                    dve.wait_ge(ffn_conv, 4 * g + 2 + j + 3 + 46 * l)
                    nc.vector.tensor_tensor(CB[:, 2 + j, :], CB[:, 2 + j, :], CB[:, j, :], ALU.mult).then_inc(ffn_mul, 1)

            def low(l, g):
                for j in range(2):
                    dve.wait_ge(h_hi, 2 * g + j + 1 + 22 * l)
                    last = nc.vector.tensor_tensor(HL[:, j, :], CB[:, 2 + j, :], HH[:, j, :], ALU.subtract)
                last.then_inc(h_done, 1)

            def add_down(l, g, unit, tiles=range(8), first=False):
                for m in tiles:
                    if m % 4 < 3:
                        dve.wait_ge(part_done, 6 * g + OUT_PART[l] + 3 * (m // 4) + m % 4 + 1)
                    else:
                        dve.wait_ge(unit_done, unit + m // 4 + 3)
                    if first:
                        nc.vector.scalar_tensor_tensor(rows(Y[:, m, :]), rows(Y[:, m, :]), ALPHA, banks(m % 2),
                                                       ALU.mult, ALU.add).then_inc(down_read, 1)
                    else:
                        nc.vector.tensor_tensor(rows(Y[:, m, :]), rows(Y[:, m, :]), banks(m % 2), ALU.add)\
                          .then_inc(down_read, 1)

            def layer_end(l):
                first = OUT_UNIT[l]
                dve.sem_inc(out_read, 2)
                dve.sem_inc(down_read, 2)
                dve.sem_inc(ffn_conv, 2)
                dve.sem_inc(h_done, 1)
                dve.sem_inc(gate_added, 2)
                dve.wait_ge(x_back, 16 + 16 * l)
                with dve.Fori(0, 4) as i:
                    for s in range(2):
                        dve.wait_ge(unit_done, 2 * i + s + first + 3)
                        nc.vector.scalar_tensor_tensor(
                            rows(Y[:, ds(2 * i + s, 1), :].rearrange("p a n -> p (a n)")),
                            rows(XR[:, ds(2 * i + s, 1), :].rearrange("p a n -> p (a n)")), ALPHA, banks(s),
                            ALU.mult, ALU.add).then_inc(out_read, 1)
                dve.wait_ge(out_read, 10 + 10 * l)
                norm(2 * l)
                for t in range(4):
                    convolve(l, 0, t)
                multiply(l, 0)
                low(l, 0)

                def chunk(g, first=False):
                    unit = 6 * g + first_unit + 10
                    for t in range(4):
                        convolve(l, g, t)
                    dve.wait_ge(down_read, 8 * g - 6 + 90 * l)
                    add_down(l, g - 1, unit, range(0, 3), first)
                    multiply(l, g, [0])
                    add_down(l, g - 1, unit, range(3, 5), first)
                    multiply(l, g, [1])
                    add_down(l, g - 1, unit, range(5, 8), first)
                    low(l, g)

                first_unit = first
                chunk(1, True)
                with dve.Fori(2, 11) as g:
                    step.enter(g - 2, 8)
                    chunk(g)
                step.leave(9)
                dve.wait_ge(down_read, 82 + 90 * l)
                add_down(l, 10, first + 72)
                dve.wait_ge(down_read, 90 + 90 * l)
                dve.wait_ge(p_hi, 1 + l)
                for j in range(2):
                    nc.vector.tensor_tensor(PL[:, j, :], P32[:, j, :], PH[:, j, :], ALU.subtract).then_inc(p_split, 1)
                norm(2 * l + 1)
                with dve.Fori(0, 4) as i:
                    step.enter(i, 2)
                    for s in range(2):
                        m = ds(2 * i + s, 1)
                        dve.wait_ge(gate_read, 2 * i + s + 3 + 10 * l)
                        dve.wait_ge(wp_read, 8 + 8 * l)
                        step(nc.vector.tensor_tensor(SG[s][:, :], SG[s][:, :],
                                                     PP[:, m, :].rearrange("p a n -> p (a n)"), ALU.mult))
                        y = Y[:, m, :].rearrange("p a n -> p (a n)")
                        nc.vector.tensor_tensor(y, y, SG[s][:, :], ALU.add).then_inc(gate_added, 1)
                step.leave(4)

            layer_end(0)
            for k in range(8):
                dve.wait_ge(x_hi, k + 1)
                nc.vector.tensor_tensor(XL[:, k, :], Y[:, k, :], XH[:, k, :], ALU.subtract).then_inc(x_lo, 1)
            gaps(x_lo, 8, in_ready)
            dve.wait_ge(x_out, 16)
            with dve.Fori(0, 7) as i:
                step.enter(i, 10)
                for s in range(2):
                    dve.wait_ge(in1_read, 2 * i + s + 3)
                    step(nc.vector.tensor_copy(U1[:, s, S0 - 1:S0], SMALL[:, ds(sp_["hist_shift"] + 2 * i + s, 1)]))
                    kept = op["shift"] + 4 * i + 2 * s
                    step(nc.vector.tensor_copy(KEPT[:, ds(kept, 1)], U1[:, s, S0 + 63:S0 + 64]))
                    step(nc.vector.tensor_copy(KEPT[:, ds(kept + 1, 1)], U1[:, s, NT - 1:NT]))
                    step(nc.vector.memset(DX[:, s, 0:4], 0.0))
                    step(nc.vector.tensor_tensor(DX[:, s, 4:NT], U1[:, s, 3:NT - 1], U1[:, s, 4:NT], ALU.subtract))
                    nc.vector.scalar_tensor_tensor(DX[:, s, 4:NT], DX[:, s, 4:NT], col_at("c_mu", 2 * i + s), U1[:, s, 4:NT],
                                                   ALU.mult, ALU.add).then_inc(shifted, 1)
            step.leave(7)
            for j in range(5):
                x, g = (QA[:, j, :], col("d_qa_g", j)) if j < 3 else (CR[:, j - 3, :], col("d_kva_g", j - 3))
                dve.wait_ge(m_root, 1 + j // 3)
                nc.vector.scalar_tensor_tensor(x, x, g, RSD[j // 3][:, :], ALU.mult, ALU.mult).then_inc(m_scaled, 1)
            dve.wait_ge(m_hi, 1)
            nc.vector.tensor_tensor(CL[:, :, NT:NK], CCK[:, :, :], CH[:, :, NT:NK], ALU.subtract).then_inc(m_lo, 1)
            for j in range(5):
                dve.wait_ge(m_hi, j + 2)
                l, x, h = (QAL[:, j, :], QA[:, j, :], QAH[:, j, :]) if j < 3 else (
                    CL[:, j - 3, 0:NT], CR[:, j - 3, :], CH[:, j - 3, 0:NT])
                nc.vector.tensor_tensor(l, x, h, ALU.subtract).then_inc(m_lo, 1)

            def rotate(out, x, slot, tmp, done):
                step(nc.vector.tensor_tensor(rows(tmp), banks(slot), rows(ROPE[:, 1, :]), ALU.mult))
                step(nc.vector.tensor_tensor(out, x, ROPE[:, 0, :], ALU.mult))
                nc.vector.tensor_tensor(out, out, tmp, ALU.add).then_inc(done, 1)

            dve.wait_ge(mla_in, 16)
            dve.wait_ge(swapped, 1)
            rotate(KRR[:, 0:NT], KRW[:, :], 0, TK[:, :], kr_done)
            dve.wait_ge(kr_out, 16)
            for r in range(2):
                dve.wait_ge(swapped, 2 + r)
                dve.wait_ge(qkv_read, 10)
                rotate(QR[:, r, :], QR[:, r, :], r, TQ[r][:, :], q_rotated)

            def top(i, hh, n):
                t0, nq = queries(n)
                s, g = 18 * i + 9 * hh + n, (9 * hh + n) % 2
                nk = 256 if n == 8 else 128 * (n + 1)
                dve.wait_ge(a_scores, s + 2)
                dve.wait_ge(a_scaled, s)
                sc = PS[0:nq, 2 * g:2 * g + 2, :].rearrange("p b n -> p (b n)")
                if n < 8:
                    step(nc.vector.memset(sc[0:64, nk - 64:nk], -1e30))
                else:
                    step(nc.vector.memset(sc[:, nk - 64:nk], -1e30))
                step(nc.vector.tensor_reduce(AST[g][0:nq, 3:4], sc[:, 0:nk], AX.X, ALU.max))
                nc.vector.tensor_scalar(AST[g][0:nq, 0:1], AST[g][0:nq, 3:4], -D_SCALE, None, ALU.mult).then_inc(a_max, 1)

            def keys2(i, hh, n):
                t0, nq = queries(n)
                s, g = 18 * i + 9 * hh + n, (9 * hh + n) % 2
                dve.wait_ge(a_probs, s + 3)
                nc.vector.reciprocal(AST[g][0:nq, 2:3], AST[g][0:nq, 1:2]).then_inc(a_inv, 1)
                if 4 <= n < 8:
                    dve.wait_ge(a_turned, s + 2)
                    dve.wait_ge(a_out, s + 1)
                    nk = 128 * (n - 3)
                    nc.vector.tensor_copy(PTB[:, 512:512 + nk], PS[:, 5, 0:nk]).then_inc(a_keys2, 1)

            def low_out(i, hh, n):
                t0, nq = queries(n)
                s = 18 * i + 9 * hh + n
                dve.wait_ge(a_hi, 2 * s + 2)
                m, own = ds(2 * i + hh + 4, 1), 64 if n == 8 else 128
                nc.vector.tensor_tensor(XL[:, m, t0:t0 + own].rearrange("p a n -> p (a n)"), PS[:, 7, 0:own],
                                        XH[:, m, t0:t0 + own].rearrange("p a n -> p (a n)"), ALU.subtract).then_inc(a_hi, 1)

            order = [(hh, n) for hh in range(2) for n in range(STEPS)]
            with dve.Fori(0, 2) as i:
                step.enter(i, 2 * 9 * 2)
                top(i, 0, 0)
                for x, (hh, n) in enumerate(order):
                    if x + 1 < len(order):
                        top(i, *order[x + 1])
                    keys2(i, hh, n)
                    low_out(i, hh, n)
            step.leave(2)
            def level_blocks(l, p):
                return nc.vector.tensor_tensor(LM_B[p][:, :, :], per_head(4 * p), heads_of(level_mask(l)), ALU.mult)

            def c_step(name, j, p):
                s = c_dve[p]
                level = int(name[1:]) if name[0] in "wt" else 0
                r, k, kk, kka = [CIN[p][:, n:n + 4, :] for n in (0, 8, 16, 20)]
                if name == "prep0":
                    dve.wait_ge(c_in[p], 48 * j[0] + 48 + 48 * j[1])
                    decay = CIN[p][:, 12:16, :].rearrange("p m n -> p (m n)")
                    nc.vector.tensor_tensor_scan(decay, RUN[:, :], decay, 0.0, ALU.mult, ALU.add).then_inc(s, 1)
                elif name == "prep1":
                    dve.wait_ge(c_act[p], C_ACT.at(j, "pi"))
                    nc.vector.tensor_tensor(ARI[p][:, :, 0:64], kk, PX[p][:, :, 0:64], ALU.mult).then_inc(s, 1)
                    nc.vector.tensor_tensor(B_S[p][:, :, :], kka, PI_S[p][:, :, :], ALU.mult).then_inc(s, 1)
                    for h in range(2):
                        last = nc.vector.tensor_tensor(K_B[p][half(h), :, half(h)], k[half(h), :, :],
                                                       PI_S[p][half(h), :, :], ALU.mult)
                    last.then_inc(s, 1)
                    nc.vector.tensor_tensor(ARI[p][:, :, 64:128], r, PX[p][:, :, 1:65], ALU.mult).then_inc(s, 1)
                elif name == "prep2":
                    dve.wait_ge(c_pe[p], C_PE.at(j, "l"))
                    level_blocks(0, p).then_inc(s, 1)
                    dve.wait_ge(s, C_DVE.at(j, "lm0"))
                    nc.vector.tensor_tensor(TA_B[p][:, :, :], heads_of(IDENT), LM_B[p][:, :, :], ALU.subtract).then_inc(s, 1)
                    dve.wait_ge(c_pe[p], C_PE.at(j, "bg"))
                    upper = small("pair_upper", 64)
                    nc.vector.scalar_tensor_tensor(RB_S[p][:, :, :], per_head(4 * p + 3)[:, :, 0:64], -1.0, pairs_of(upper),
                                                   ALU.mult, ALU.mult).then_inc(s, 1)
                    for h in range(2):
                        strict = small("pair_strict", 64)[half(h), :].unsqueeze(1).unsqueeze(1).to_broadcast([64, 2, 2, 64])
                        last = nc.vector.tensor_tensor(
                            AK_B[p][half(h), :, half(h)].rearrange("p (b m) n -> p b m n", b=2),
                            k_group(p)[half(h), :, :].rearrange("p b (m n) -> p b m n", m=2)[:, :, :, 0:64], strict, ALU.mult)
                    last.then_inc(s, 1)
                    nc.vector.tensor_tensor(
                        RK_S[p][:, :, :].rearrange("p (b m) n -> p b m n", b=2),
                        k_group(p).rearrange("p b (m n) -> p b m n", m=2)[:, :, :, 64:128],
                        upper.unsqueeze(1).unsqueeze(1).to_broadcast([128, 2, 2, 64]), ALU.mult).then_inc(s, 1)
                elif name == "prep3":
                    dve.wait_ge(c_pe[p], C_PE.at(j, "mt"))
                    nc.vector.tensor_tensor(TT_B[p][:, :, :], heads_of(IDENT), per_head(4 * p + 1), ALU.subtract).then_inc(s, 1)
                    dve.wait_ge(s, C_DVE.at(j, "ta0"))
                    level_blocks(1, p).then_inc(s, 1)
                elif name[0] == "w":
                    if level < 5:
                        dve.wait_ge(c_pe[p], C_PE.at(j, "lw%d" % level))
                        level_blocks(level + 1, p).then_inc(s, 1)
                elif name[0] == "t":
                    dve.wait_ge(c_pe[p], C_PE.at(j, "tt%d" % level))
                    nc.vector.tensor_tensor(TT_B[p][:, :, :], TT_B[p][:, :, :], per_head(4 * p + 2), ALU.subtract).then_inc(s, 1)
                    if level < 5:
                        dve.wait_ge(c_pe[p], C_PE.at(j, "ta%d" % level))
                        nc.vector.tensor_tensor(TA_B[p][:, :, :], TA_B[p][:, :, :], per_head(4 * p + 3), ALU.subtract)\
                            .then_inc(s, 1)
                elif name == "carry3":
                    state = MB[is_sample(j)]
                    dve.wait_ge(c_pe[p], C_PE.at(j, "m"))
                    nc.vector.tensor_tensor(state[:, :, :], state[:, :, :], per_head(4 * p + 3), ALU.add).then_inc(s, 1)
                    dve.wait_ge(s, C_DVE.at(j, "m0"))
                    nc.vector.tensor_tensor(state[:, :, :], state[:, :, :], PX[p][:, :, 64:65].to_broadcast([128, 4, 128]),
                                            ALU.mult).then_inc(s, 1)

            dve.wait_ge(a_hi, 73)
            for m in range(4):
                p = m % 2
                r, k, v = [RKV[p][:, n, :] for n in range(3)]
                kk, k2, kka, x = PREP[p][:, KKR, :], PREP[p][:, K2R, :], PREP[p][:, KKAR, :], NORM[p][:, :]
                dve.wait_ge(e_in[p], 16 * (m // 2) + 16)
                if m >= 2:
                    dve.wait_ge(e_out[p], 32)
                nc.vector.tensor_scalar(kk, k, col("c_k_k", m), None, ALU.mult).then_inc(e_dve, 1)
                dve.wait_ge(e_act, E_ACT.at(m, "a") - 1)
                nc.vector.scalar_tensor_tensor(k2, kka, -1.0, k, ALU.add, ALU.mult).then_inc(e_dve, 1)
                dve.wait_ge(e_dve, E_DVE.at(m, "k2a") - 1)
                nc.vector.scalar_tensor_tensor(k2, k2, col("c_k_a", m), k, ALU.mult, ALU.add).then_inc(e_dve, 1)
                dve.wait_ge(e_act, E_ACT.at(m, "inv") - 1)
                nc.vector.tensor_tensor(kk, kk, x, ALU.mult).then_inc(e_dve, 1)
                dve.wait_ge(e_dve, E_DVE.at(m, "kk") - 1)
                nc.vector.tensor_tensor(kka, kk, kka, ALU.mult).then_inc(e_dve, 1)
                nc.vector.scalar_tensor_tensor(x, r, col("c_r_k", m), k2, ALU.mult, ALU.mult).then_inc(e_dve, 1)
                dve.wait_ge(e_pe, E_PE.at(m, "bonus") - 1)
                nc.vector.tensor_tensor(rows(BG[p][:, BONUSR, :]), banks((5 * m + 4) % 2), rows(v), ALU.mult).then_inc(e_dve, 1)
            for p in range(2):
                dve.wait_ge(e_out[p], 64)
            for x in ZEROED:
                nc.vector.memset(x[:, :, :], 0.0)
            step(nc.vector.memset(RUN[:, :], 1.0))
            nc.vector.memset(RUN[:, :].rearrange("p (c t) -> p c t", t=64)[:, :, 0:1], 0.0)
            for p in range(2):
                nc.vector.memset(PX[p][:, :, 0:1], 1.0)
                nc.vector.tensor_copy(ARI[p][:, :, 128:192], pairs_of(PAIR_ID))
            nc.vector.memset(CO[:, :, 0:S0], 0.0)
            nc.vector.memset(CO[:, :, S0 + 64:P0], 0.0)
            nc.vector.engine_nop().then_inc(c_ready, 1)
            dve.wait_ge(c_ready, 1)
            run_chunks(dve, c_step)
            for m in range(4):
                o = CO[:, m, :]
                dve.wait_ge(f_mean, m + 1)
                nc.vector.scalar_tensor_tensor(rows(o), banks(0), -1 / 64, rows(o), ALU.mult, ALU.add).then_inc(f_dve, 1)
                dve.wait_ge(f_act, F_ACT.at(m, "inv") - 1)
                nc.vector.tensor_tensor(o, o, INC[m % 2][:, :], ALU.mult).then_inc(f_dve, 1)
                dve.wait_ge(f_in[m % 2], 16 * (m // 2) + 16)
                dve.wait_ge(f_act, F_ACT.at(m, "affine") - 1)
                nc.vector.tensor_tensor(o, o, BGL[m % 2][:, BONUSR, :], ALU.add).then_inc(f_dve, 1)
                dve.wait_ge(f_dve, F_DVE.at(m, "plus") - 1)
                nc.vector.tensor_tensor(o, o, BGL[m % 2][:, GR, :], ALU.mult).then_inc(f_dve, 1)
                dve.wait_ge(f_act, F_ACT.at(m, "hi") - 1)
                nc.vector.tensor_tensor(XL[:, m, :], o, XH[:, m, :], ALU.subtract).then_inc(f_dve, 1)
            dve.wait_ge(f_dve, F_DVE.at(3, "lo") - 1)
            dve.sem_inc(mix_ready[1], 4)
            layer_end(1)
            nc.vector.engine_nop().then_inc(kept_ready, 1)


def kernel(**inputs):
    import numpy as np
    import concourse.bacc as bacc
    from concourse import mybir
    from concourse.bass_utils import run_bass_kernel_spmd

    nc = bacc.Bacc("TRN2", target_bir_lowering=False, num_devices=1)
    arrays, io = {}, {}
    for name, v in lay_out(inputs).items():
        arrays["in_" + name] = v
        io[name] = nc.dram_tensor("in_" + name, v.shape, mybir.dt.float32, kind="ExternalInput").ap()
    for name, shape in outputs().items():
        io[name] = nc.dram_tensor("out_" + name, shape, mybir.dt.float32, kind="ExternalOutput").ap()
    build(nc, io, arrays["in_units"].shape[0])
    r = run_bass_kernel_spmd(nc, [arrays], core_ids=[0])
    return gather({name: r.results[0]["out_" + name] for name in outputs()})
```

```python
def _np():
    import numpy as np
    return np


def column_plan():
    names = [("a_conv_w0", 4), ("a_conv_w1", 4), ("a_conv_w2", 4), ("a_conv_w3", 4)]
    plan, at = {}, 0
    for name, n in [("conv0_w0", 16), ("conv0_w1", 16), ("conv0_w2", 16), ("conv0_w3", 16), ("conv0_b", 16),
                    ("a_b_r", 4), ("a_b_i", 4), ("a_lambda", 4), ("b_norm_g", 1), ("c_mu", 14), ("c_w0", 4), ("c_a0", 4),
                    ("c_k_k", 4), ("c_k_a", 4), ("c_r_k", 4), ("c_lnx_g", 4), ("c_lnx_b", 4), ("d_qa_g", 3), ("d_kva_g", 2)]:
        plan[name] = at
        at += n
    for layer in range(2):
        for name, n in [("ffn_w0", 44), ("ffn_w1", 44), ("ffn_w2", 44), ("ffn_b", 44), ("ln_mix_g", 8), ("ln_mix_b", 8),
                        ("ln_ffn_g", 8), ("ln_ffn_b", 8), ("ple_b", 8)]:
            plan[name + str(layer)] = at
            at += n
    return plan, at


def small_plan():
    plan, at = {}, 0
    for name, n in [("identity", 128), ("ones", 128), ("pair_ones", 128), ("upper", 128), ("level", 7 * 128), ("half_swap", 128),
                    ("pair_upper", 64), ("pair_strict", 64), ("pair_identity", 64),
                    ("w_beta_alpha", 64), ("dt_bias", 36), ("a_log", 36),
                    ("hist_conv0", 48), ("h0", 4), ("hist_shift", 14), ("hist_ffn", 2 * 88)]:
        plan[name] = at
        at += n
    return plan, at


def out_plan():
    plan, at = {}, 0
    for name, n in [("conv0", 16 * 6), ("h", 8), ("shift", 28), ("ffn", 2 * 44 * 4)]:
        plan[name] = at
        at += n
    return plan, at


S0, P0, NT = 4, 72, 1096


def lay_out(inp):
    np = _np()
    f32 = np.float32
    a = {k: np.asarray(v) for k, v in inp.items()}

    def tokens(sample, prompt):
        n = sample.shape[1]
        t = np.zeros((n, NT), f32)
        t[:, S0:S0 + 64] = sample.T
        t[:, P0:] = prompt.T
        return np.ascontiguousarray(t.reshape(n // 128, 128, NT).transpose(1, 0, 2))

    def unit(w):
        k, m = w.shape
        u = w.reshape(k // 128, 128, m // 128, 128).transpose(1, 2, 0, 3).reshape(128, -1)
        out = np.zeros((128, 1024), f32)
        out[:, :u.shape[1]] = u
        return out

    units = []

    def full(w):
        for m in range(w.shape[1] // 128):
            units.append(unit(w[:, m * 128:(m + 1) * 128]))

    def ffn(layer):
        up, down = a["ffn_w_up"][layer], a["ffn_w_down"][layer]

        def ups(g):
            for f in (2 * g, 2 * g + 1, 22 + 2 * g, 23 + 2 * g):
                units.append(unit(up[:, f * 128:(f + 1) * 128]))

        def downs(g):
            for d in range(2):
                units.append(unit(down[g * 256:(g + 1) * 256, d * 512:(d + 1) * 512]))
        ups(0)
        for g in range(1, 11):
            ups(g)
            downs(g - 1)
        downs(10)

    def ple(layer):
        for d in range(2):
            units.append(unit(a["ple_w_proj"][layer][:, d * 512:(d + 1) * 512]))
        full(a["ple_w_gate"][layer])

    full(a["w_in0"][:, :2048])
    for m in range(4):
        for first in (2048, 2560):
            full(a["w_in0"][:, first + 128 * m:first + 128 * m + 128])
    full(a["w_out0"])
    ffn(0)
    ple(0)
    w1 = a["w_in1"]
    full(w1[:, :1792])
    full(w1[:, 1792:2432])
    full(np.concatenate([w1[:, 2432:2496], w1[:, 2432:2496]], 1))
    qb = a["d_w_qb"]
    cols = [qb[:, h * 192:h * 192 + 128] for h in range(4)]
    cols += [np.concatenate([qb[:, h * 192 + 128:(h + 1) * 192] for h in (2 * r, 2 * r + 1)], 1) for r in range(2)]
    for m in range(0, 6, 2):
        units.append(unit(np.concatenate(cols[m:m + 2], 1)))
    kvb = a["d_w_kvb"]
    for m in range(0, 4, 2):
        units.append(unit(np.concatenate([kvb[:, h * 256:h * 256 + 128] for h in (m, m + 1)], 1)))
    v = np.concatenate([kvb[:, h * 256 + 128:(h + 1) * 256] for h in range(4)], 1)
    units.append(np.ascontiguousarray(v.reshape(2, 128, 512).transpose(1, 0, 2).reshape(128, 1024)))
    full(a["w_out1"])
    ffn(1)
    ple(1)

    def col(v):
        return np.asarray(v).reshape(-1, 128).T

    cp, ncol = column_plan()
    columns = np.zeros((128, ncol), f32)

    def put(name, v):
        c = col(v)
        columns[:, cp[name]:cp[name] + c.shape[1]] = c
    for j in range(4):
        put("conv0_w%d" % j, np.concatenate([a["a_conv_w"][j], a["b_conv_w"][j]]))
    put("conv0_b", a["a_conv_b"])
    for n in ("a_b_r", "a_b_i", "a_lambda", "b_norm_g", "c_mu", "c_w0", "c_a0", "c_k_k", "c_k_a", "c_r_k", "c_lnx_g",
              "c_lnx_b", "d_qa_g", "d_kva_g"):
        put(n, a[n])
    for i in range(2):
        for j in range(3):
            put("ffn_w%d%d" % (j, i), a["ffn_conv_w"][i][j])
        put("ffn_b%d" % i, a["ffn_conv_b"][i])
        put("ln_mix_g%d" % i, a["ln_mix_g"][i])
        put("ln_mix_b%d" % i, a["ln_mix_b"][i])
        put("ln_ffn_g%d" % i, a["ln_ffn_g"][i])
        put("ln_ffn_b%d" % i, a["ln_ffn_b"][i])
        put("ple_b%d" % i, a["ple_b_gate"][i])

    sp, nsmall = small_plan()
    small = np.zeros((128, nsmall), f32)

    def sput(name, v):
        v = np.asarray(v).reshape(128, -1)
        small[:, sp[name]:sp[name] + v.shape[1]] = v
    t = np.arange(128)
    same_half = (t[:, None] // 64) == (t[None, :] // 64)
    sput("identity", np.eye(128, dtype=f32))
    sput("ones", np.ones((128, 128), f32))
    sput("pair_ones", same_half.astype(f32))
    sput("upper", (t[:, None] <= t[None, :]).astype(f32))
    sput("level", np.stack([((t[:, None] // m) % 2 == 1) & (t[None, :] // m == t[:, None] // m - 1)
                            for m in (1, 2, 4, 8, 16, 32, 64)], 1).astype(f32))
    swap = np.zeros((128, 128), f32)
    swap[(t // 64) * 64 + (t % 64 + 32) % 64, t] = 1
    sput("half_swap", swap)
    sput("pair_upper", (t[:, None] % 64 <= np.arange(64)[None, :]).astype(f32))
    sput("pair_strict", (t[:, None] % 64 < np.arange(64)[None, :]).astype(f32))
    sput("pair_identity", (t[:, None] % 64 == np.arange(64)[None, :]).astype(f32))
    sput("w_beta_alpha", a["w_in0"][:, 3072:3080].reshape(8, 128, 8).transpose(1, 0, 2))
    w_gates = np.zeros((128, 4, 2, 128), f32)
    for g, key in enumerate(("a_w_r", "a_w_i")):
        for b in range(8):
            h = (b % 2) * 64
            w_gates[h:h + 64, b // 2, g, h:h + 64] = a[key][b]
    sput("dt_bias", np.broadcast_to(a["b_dt_bias"], (128, 9, 4)))
    sput("a_log", np.broadcast_to(a["b_a_log"], (128, 9, 4)))
    hist = np.concatenate([a["state_a_conv"][0], a["state_b_conv"][0]], 1)
    sput("hist_conv0", hist.reshape(3, 16, 128).transpose(2, 1, 0))
    sput("h0", a["state_a_h"].reshape(4, 128).T)
    sput("hist_shift", a["state_c_shift"].reshape(14, 128).T)
    sput("hist_ffn", a["state_ffn_conv"][:, 0].reshape(2, 2, 44, 128).transpose(3, 0, 2, 1))

    inv = (f32(10000.0) ** (-np.arange(32, dtype=f32) / f32(32))).astype(f32)
    pos = np.zeros(NT, f32)
    pos[S0:S0 + 64] = 128 + np.arange(64)
    pos[P0:] = np.arange(1024)
    ang = (pos[:, None] * inv[None, :]).astype(f32)
    cos, sin = np.cos(ang).T.astype(f32), np.sin(ang).T.astype(f32)
    rope = np.stack([np.concatenate([cos] * 4, 0), np.concatenate([-sin, sin] * 2, 0)], 1)
    ckv = a["cache_d_ckv"][0].T.reshape(2, 128, 128).transpose(1, 0, 2)
    kr = np.concatenate([a["cache_d_krope"][0].T] * 2, 0)
    return {
        "x": tokens(a["x_sample"][0], a["x_prompt"][0]),
        "p": np.stack([tokens(a["p_sample"][i, 0], a["p_prompt"][i, 0]) for i in range(2)]),
        "units": np.stack(units), "columns": columns, "small": small,
        "w_gates": w_gates, "w_lora": np.stack([np.concatenate([a["c_w2"], a["c_a2"]], 0), a["c_g2"]], 1),
        "s_b": np.ascontiguousarray(a["state_b_s"][0].transpose(1, 0, 2)),
        "s_c": np.ascontiguousarray(a["state_c_s"][0].reshape(4, 2, 64, 64).transpose(1, 3, 0, 2).reshape(128, 4, 64)),
        "rope": np.ascontiguousarray(rope), "cache_ckv": np.ascontiguousarray(ckv), "cache_krope": kr,
    }


def outputs():
    _, n = out_plan()
    return {"y": (128, 8, NT), "kept": (128, n), "s_b_p": (128, 4, 128), "s_b_s": (128, 4, 128),
            "s_c_p": (128, 4, 64), "s_c_s": (128, 4, 64), "ckv": (128, 2, NT), "krope": (64, NT)}


def gather(r):
    np = _np()
    op, _ = out_plan()

    def rows(v, at, n):
        return np.ascontiguousarray(v[:, :, at:at + n].transpose(2, 1, 0).reshape(1, n, -1))

    def kept(name, tiles, each):
        return r["kept"][:, op[name]:op[name] + tiles * each].reshape(128, tiles, each)
    y, ckv = r["y"], r["ckv"]
    conv, h, shift = kept("conv0", 16, 6), kept("h", 4, 2), kept("shift", 14, 2)
    f = kept("ffn", 88, 4)
    out = [rows(y, P0, 1024), rows(y, S0, 64)]
    for at in (3, 0):
        out.append(rows(conv[:, 0:4], at, 3))
    for at in (1, 0):
        out.append(rows(h, at, 1)[0])
    for at in (3, 0):
        out.append(rows(conv[:, 4:16], at, 3))
    for n in ("s_b_p", "s_b_s"):
        out.append(np.ascontiguousarray(r[n].transpose(1, 0, 2))[None])
    for at in (1, 0):
        out.append(rows(shift, at, 1))
    for n in ("s_c_p", "s_c_s"):
        out.append(np.ascontiguousarray(r[n].reshape(2, 64, 4, 64).transpose(2, 0, 3, 1).reshape(1, 8, 64, 64)))
    out += [rows(ckv, P0, 1024), rows(ckv, S0, 64)]
    kr = r["krope"][:, None, :]
    out += [rows(kr, P0, 1024), rows(kr, S0, 64)]
    for at in (2, 0):
        out.append(np.stack([rows(f[:, i * 44:(i + 1) * 44], at, 2) for i in range(2)]))
    return tuple(out)


def build(nc, io, NU):
    import concourse.bass as bass
    from concourse import mybir
    from contextlib import ExitStack

    F32, F32R = mybir.dt.float32, mybir.dt.float32r
    ACT, ALU, AX = mybir.ActivationFunctionType, mybir.AluOpType, mybir.AxisListType
    ds = bass.ds
    NB, BW = 4, NT // 4
    TILE = NT * 4
    cp, NCOL = column_plan()
    sp_, NSMALL = small_plan()
    op, NKEPT = out_plan()
    PROMPT_TILES = 8
    SAMPLE = PROMPT_TILES
    ALPHA = 4.0 ** 0.25

    ctx = ExitStack()
    with ctx:
        def sb(name, shape, dt=F32):
            return ctx.enter_context(nc.sbuf_tensor(name, shape, dt))

        def sem(name):
            return ctx.enter_context(nc.semaphore(name))

        RAW = sb("RAW", [128, 2, 1024])
        WHI = sb("WHI", [128, 2, 1024], F32R)
        WLO = sb("WLO", [128, 2, 1024], F32R)
        COL = sb("COL", [128, NCOL])
        SMALL = sb("SMALL", [128, NSMALL])
        KEPT = sb("KEPT", [128, NKEPT])
        EPS = sb("EPS", [128, 5])
        WBAH, WBAL = sb("WBAH", [128, 64], F32R), sb("WBAL", [128, 64], F32R)
        BETA36, GTMP, GB = sb("BETA36", [128, 36]), sb("GTMP", [128, 3, 36]), sb("GB", [128, 36])
        GC, EGC, NBEG = sb("GC", [128, 36]), sb("EGC", [128, 36]), sb("NBEG", [128, 36])
        LAM = sb("LAM", [128, 16])
        KOC = [sb("KOC%d" % p, [128, 4]) for p in range(2)]
        base = -(-nc.sbuf_base // 32) * 32
        SLAB = (nc.sbuf_usable_end - base) // 32 * 32
        PS = ctx.enter_context(nc.psum_tensor("PS", [128, 8, 512], F32))

        def at(name, shape, offset, dt=F32):
            assert offset % 32 == 0
            n = 4
            for x in shape[1:]:
                n *= x
            assert offset + n <= SLAB, (name, offset + n, SLAB)
            return nc.alloc_sbuf_tensor_at(name, shape, dt, offset=base + offset)

        XH = at("XH", [128, 8, NT], 0, F32R)
        XL = at("XL", [128, 8, NT], 8 * TILE, F32R)
        AR = 16 * TILE
        X32 = at("X32", [128, 8, NT], AR)
        XCQ = at("XCQ", [128, 16, NT], AR)
        U0 = at("U0", [128, 2, NT], AR + 16 * TILE)
        MIX = [at("MIX%d" % n, [128, NT], AR + (18 + n) * TILE) for n in range(5)]
        BAR = at("BAR", [128, NT], AR + 18 * TILE)
        RGW = at("RGW", [128, 2, 128], AR + 23 * TILE)
        OT = at("OT", [128, 4, NT], AR)

        SET = 4 * 128 * 4
        SETS = [[AR + 16 * TILE + n * SET for n in range(14)],
                [4 * TILE + n * SET for n in range(8)] + [12 * TILE + n * SET for n in range(6)]]

        def pair(name, n):
            return [at("%s%d" % (name, p), [128, 4, 128], SETS[p][n]) for p in range(2)]

        KT, QT, VT, DA, DB, EG, LM = [pair(x, n) for n, x in enumerate(("KT", "QT", "VT", "DA", "DB", "EG", "LM"))]
        TA, TT, WW, VB, KO, RR, VN = [pair(x, 7 + n) for n, x in enumerate(("TA", "TT", "WW", "VB", "KO", "RR", "VN"))]
        SP, SS = at("SP", [128, 4, 128], AR + 16 * TILE + 14 * SET), at("SS", [128, 4, 128], AR + 16 * TILE + 15 * SET)
        RN = [at("RN%d" % n, [128, NT], AR + (18 + n) * TILE) for n in range(4)]

        ZT = at("ZT", [128, 4, NT], AR + 4 * TILE)
        Y = at("Y", [128, 8, NT], AR)
        XR = at("XR", [128, 8, NT], AR + 8 * TILE)
        CB = at("CB", [128, 4, NT], AR + 8 * TILE)
        UF = at("UF", [128, 2, NT], AR + 12 * TILE)
        HH, HL = at("HH", [128, 2, NT], AR + 14 * TILE, F32R), at("HL", [128, 2, NT], AR + 16 * TILE, F32R)
        PP = at("PP", [128, 8, NT], AR + 8 * TILE)
        P32 = at("P32", [128, 2, NT], AR + 8 * TILE)
        PH, PL = at("PH", [128, 2, NT], AR + 18 * TILE, F32R), at("PL", [128, 2, NT], AR + 20 * TILE, F32R)
        SQ = [at("SQ%d" % n, [128, NT], AR + (16 + n) * TILE) for n in range(2)]
        SG = [at("SG%d" % n, [128, NT], AR + (16 + n) * TILE) for n in range(2)]
        RS = at("RS", [128, NT], AR + 22 * TILE)
        YSUM = [at("YSUM%d" % n, [128, NT], AR + (18, 12)[n] * TILE) for n in range(2)]

        NK = NT + 128
        KW = NK // 4
        QA, CR = at("QA", [128, 3, NT], AR), at("CR", [128, 2, NT], AR + 3 * TILE)
        KRW = at("KRW", [128, NT], AR + 5 * TILE)
        U1 = at("U1", [128, 2, NT], AR + 6 * TILE)
        DX = at("DX", [128, 2, NT], AR + 8 * TILE)
        SQD = [at("SQD%d" % n, [128, NT], AR + (6 + n) * TILE) for n in range(2)]
        RSD = [at("RSD%d" % n, [128, NT], AR + (8 + n) * TILE) for n in range(2)]
        ROPE = at("ROPE", [128, 2, NT], AR + 10 * TILE)
        QAH, QAL = at("QAH", [128, 3, NT], AR + 12 * TILE, F32R), at("QAL", [128, 3, NT], AR + 15 * TILE, F32R)
        CH, CL = at("CH", [128, 2, NK], AR + 18 * TILE, F32R), at("CL", [128, 2, NK], AR + 18 * TILE + 8 * NK, F32R)
        CCK = at("CCK", [128, 2, 128], AR + 18 * TILE + 16 * NK)
        KRR = at("KRR", [128, NK], 0)
        QR = at("QR", [128, 2, NT], 4 * NK)
        QN = at("QN", [128, 4, NT], 8 * TILE)
        TK = at("TK", [128, NT], 8 * TILE)
        TQ = [at("TQ%d" % n, [128, NT], AR + (12 + n) * TILE) for n in range(2)]
        KN = at("KN", [128, 4, NK], AR)
        VTOK = at("VTOK", [128, 10, 512], AR + 16 * NK)
        QS, QRS = at("QS", [128, 2, NT], AR + 12 * TILE), at("QRS", [128, NT], AR + 14 * TILE)
        PB = at("PB", [128, 2, 1024], AR + 15 * TILE)
        PTB = at("PTB", [128, 1024], AR + 15 * TILE + 8192)
        OB = at("OB", [128, 2, 128], AR + 15 * TILE + 12288)
        AST = [at("AST%d" % n, [128, 4], AR + 15 * TILE + 13312 + 32 * n) for n in range(2)]

        place = [AR]

        def room(name, shape, dt=F32):
            t, n = at(name, shape, place[0], dt), 4
            for x in shape[1:]:
                n *= x
            place[0] += -(-n // 32) * 32
            return t

        def both(name, *shape):
            return [room("%s%d" % (name, p), [128, *shape]) for p in range(2)]

        LORA = room("LORA", [128, 2, 512])
        WG = room("WG", [128, 2, NT])
        RKV, PREP, BG, NORM = both("RKV", 3, NT), both("PREP", 4, NT), both("BG", 2, NT), both("NORM", NT)
        K2R, SIGR, KKR, KKAR, BONUSR, GR = 0, 1, 2, 3, 0, 1
        place[0] = AR
        RUN = room("RUN", [128, 256])
        MB = [room("MB%d" % n, [128, 4, 128]) for n in range(2)]
        behind_states = place[0]
        CIN = both("CIN", 24, 64)
        A_B, B_B, K_B, V_B, LM_B, W_B, TA_B, TT_B, AK_B, BT_B, KT_B, VT_B = [both(x, 4, 128) for x in (
            "A_B", "B_B", "K_B", "V_B", "LM_B", "W_B", "TA_B", "TT_B", "AK_B", "BT_B", "KT_B", "VT_B")]
        ARI = both("ARI", 4, 192)
        B_S, PI_S, RB_S, RK_S = [both(x, 4, 64) for x in ("B_S", "PI_S", "RB_S", "RK_S")]
        PX = both("PX", 4, 65)
        U_B, X_B = K_B, W_B
        ZEROED = [x[p] for x in (A_B, B_B, K_B, V_B, AK_B, BT_B, KT_B) for p in range(2)] + MB
        TAIL = SLAB // 32 * 32
        CO = at("CO", [128, 4, NT], TAIL - 4 * TILE)
        assert place[0] <= TAIL - 4 * TILE, (place[0], TAIL - 4 * TILE)
        place[0] = behind_states
        BGL, SQC, INC = both("BGL", 2, NT), both("SQC", NT), both("INC", NT)

        def small(name, n, first=0):
            return SMALL[:, sp_[name] + first:sp_[name] + first + n]

        IDENT, ONES, UPPER = small("identity", 128), small("ones", 128), small("upper", 128)

        def col(name, j=0):
            return COL[:, cp[name] + j:cp[name] + j + 1]

        def col_at(name, j):
            return COL[:, ds(cp[name] + j, 1)]

        BETA = BETA36[:, :].rearrange("p (c h) -> p c h", h=4)
        PSBA = PS[:, 7, 0:72].rearrange("p (c j) -> p c j", j=8)

        def col4(name):
            return COL[:, cp[name]:cp[name] + 4]

        GATE = nc.dram_tensor("gate_rows", [4, 128, NT], F32).ap()
        XROW = nc.dram_tensor("x_rows", [128, 8, NT], F32).ap()
        CROW = nc.dram_tensor("c_rows", [14, 128, NT], F32).ap()
        PROW = nc.dram_tensor("prepared_rows", [16, 128, NT], F32).ap()
        BROW = nc.dram_tensor("bonus_gate_rows", [8, 128, NT], F32).ap()
        ZROW = nc.dram_tensor("z_rows", [4, 128, NT], F32).ap()

        params_in, x_in = sem("params_in"), [sem("x_in%d" % n) for n in range(4)]
        raw_in = [sem("raw_in0"), sem("raw_in1")]
        hi_split, unit_split = sem("hi_split"), sem("unit_split")
        unit_done, part_done = sem("unit_done"), sem("part_done")
        slot_act = sem("slot_act")
        xh_ready, xl_ready = sem("xh_ready"), sem("xl_ready")
        row_out = [sem("row_out0"), sem("row_out1")]
        conv_done = sem("conv_done")
        dve_step, act_step = sem("dve_step"), sem("act_step")
        ba_done, ba_copied = sem("ba_done"), sem("ba_copied")
        eps_set = sem("eps_set")
        ba_split, g_ready, ba_act, ba_vec = sem("ba_split"), sem("g_ready"), sem("ba_act"), sem("ba_vec")
        rg_done, rg_read, rg_vec, rg_act = sem("rg_done"), sem("rg_read"), sem("rg_vec"), sem("rg_act")
        silu_done, lam_vec, lam_act, gate_in = sem("silu_done"), sem("lam_vec"), sem("lam_act"), sem("gate_in")
        gates_in, kept_ready = sem("gates_in"), sem("kept_ready")
        outs_done = sem("outs_done")

        sq_ready, norm_sum, norm_root, norm_done = sem("sq_ready"), sem("norm_sum"), sem("norm_root"), sem("norm_done")
        ba_row = sem("ba_row")
        norm_read, rg_split = sem("norm_read"), sem("rg_split")
        pad_zeroed, state_in = sem("pad_zeroed"), sem("state_in")
        gdn_pe = [sem("gdn_pe%d" % p) for p in range(2)]
        gdn_dve = [sem("gdn_dve%d" % p) for p in range(2)]
        gdn_act = [sem("gdn_act%d" % p) for p in range(2)]
        gdn_pool = [sem("gdn_pool%d" % p) for p in range(2)]
        state_out = sem("state_out")
        o_zeroed, z_in, o_square, o_sum, o_root, o_gated = [sem(x) for x in ("o_zeroed", "z_in", "o_square", "o_sum", "o_root", "o_gated")]
        mix_ready = [sem("mix_ready%d" % l) for l in range(2)]

        x_back, out_read, up_read, down_read = sem("x_back"), sem("out_read"), sem("up_read"), sem("down_read")
        ffn_conv, ffn_silu, ffn_mul, h_hi, h_done = [sem(x) for x in ("ffn_conv", "ffn_silu", "ffn_mul", "h_hi", "h_done")]
        p_in, p_hi, p_split, wp_read = sem("p_in"), sem("p_hi"), sem("p_split"), sem("wp_read")
        gate_read, gate_added, gaps_zeroed = sem("gate_read"), sem("gate_added"), sem("gaps_zeroed")
        ln_total, ln_normed = sem("ln_total"), sem("ln_normed")
        ln_mean, ln_sub, ln_sq, ln_var = sem("ln_mean"), sem("ln_sub"), sem("ln_sq"), sem("ln_var")
        ln_root, ln_scaled, ln_hi, ln_lo = sem("ln_root"), sem("ln_scaled"), sem("ln_hi"), sem("ln_lo")
        in_ready = sem("in_ready")
        in1_read, shifted, row1_out = sem("in1_read"), sem("shifted"), [sem("row1_out0"), sem("row1_out1")]
        mla_in, cache_in, kr_cache_in = sem("mla_in"), sem("cache_in"), sem("kr_cache_in")
        m_square, m_sum, m_root = sem("m_square"), sem("m_sum"), sem("m_root")
        m_scaled, m_hi, m_lo, c_out = sem("m_scaled"), sem("m_hi"), sem("m_lo"), sem("c_out")
        swapped, kr_done, kr_out, qkv_read = sem("swapped"), sem("kr_done"), sem("kr_out"), sem("qkv_read")
        q_rotated, v_done, v_read = sem("q_rotated"), sem("v_done"), sem("v_read")
        a_scores, a_max, a_probs, a_turned, a_keys, a_keys2 = [sem("a_" + x) for x in (
            "scores", "max", "probs", "turned", "keys", "keys2")]
        a_out, a_inv, a_scaled, a_back, a_hi, q_staged = [sem("a_" + x) for x in (
            "out", "inv", "scaled", "back", "hi", "staged")]
        e_wg, wg_ready, e_in, e_out = sem("e_wg"), sem("wg_ready"), [sem("e_in0"), sem("e_in1")], [sem("e_out0"), sem("e_out1")]
        e_pe, e_act, e_dve, f_mean, f_var, f_act, f_dve = [sem(x) for x in (
            "e_pe", "e_act", "e_dve", "f_mean", "f_var", "f_act", "f_dve")]
        f_in = [sem("f_in0"), sem("f_in1")]
        c_ready, lora_in, c_state_in, c_state_set, c_state_out = [sem(x) for x in (
            "c_ready", "lora_in", "c_state_in", "c_state_set", "c_state_out")]
        c_in, c_pe, c_act, c_dve, c_pool = [[sem("%s%d" % (x, p)) for p in range(2)] for x in (
            "c_in", "c_pe", "c_act", "c_dve", "c_pool")]
        x_hi, x_lo, x_out, y_out = sem("x_hi"), sem("x_lo"), sem("x_out"), sem("y_out")

        def in_unit(u):
            return u + 3

        OUT_UNIT, OUT_PART = (24, 108 + 26), (0, 72 + 5)

        def up_unit(l, g):
            return OUT_UNIT[l] + 8 + 6 * g - 2

        def down_unit(l, g):
            return OUT_UNIT[l] + 8 + 6 * g + 8

        class Stages:

            def __init__(self, *names):
                self.index = {n: k + 1 for k, n in enumerate(names)}
                self.count = len(names)

            def at(self, i, name):
                return i * self.count + self.index[name] + 1

            def before(self, i):
                return i * self.count + 1

        def level_mask(l):
            return small("level", 128, 128 * l)

        def heads_of(x):
            if x.shape[1] == 4:
                return x.unsqueeze(2).to_broadcast([128, 4, 128])
            return x.unsqueeze(1).to_broadcast([128, 4, 128])

        def per_head(bank):
            return PS[:, bank, :].rearrange("p (h n) -> p h n", h=4)

        class Steps:

            def __init__(self, eng, s):
                self.eng, self.sem, self.n, self.i, self.per = eng, s, 0, None, 0

            def value(self):
                return self.n if self.i is None else self.i * self.per + self.n

            def __call__(self, instruction):
                instruction.then_inc(self.sem, 1)
                self.n += 1
                self.eng.wait_ge(self.sem, self.value())

            def enter(self, i, per, first=0):
                self.n -= first * per
                self.i, self.per, self.start = i, per, self.n

            def leave(self, count):
                assert self.n - self.start == self.per, (self.n - self.start, self.per)
                self.n, self.i = self.start + self.per * count, None

        def banks(slot, width=BW):
            return PS[:, 4 * slot:4 * slot + 4, 0:width]

        DVE_LOWS = 3
        def bank_half(slot, h):
            return PS[:, 4 * slot + 2 * h:4 * slot + 2 * h + 2, 0:BW]

        def row_half(x, h):
            return x[:, 2 * BW * h:2 * BW * (h + 1)]

        def rows(x, width=BW):
            return x.rearrange("p (b n) -> p b n", n=width)

        G_FIRST = ["decays", "diffs", "grams", "blocks", "w1", "t1", "w2", "t2", "w3"]
        G_SECOND = ["t3", "w4", "t4", "w5", "t5", "w6", "t6", "carry1", "carry2"]
        C_LEVELS = range(1, 6)
        FIRST = ["prep0", "prep1", "prep2", "prep3", "w1", "t1", "w2", "t2"]
        SECOND = ["w3", "t3", "w4", "t4", "w5", "t5", "carry1", "carry2", "carry3"]

        class ChunkStages:

            def __init__(self, *names):
                self.index = {n: k + 1 for k, n in enumerate(names)}
                self.count = len(names)

            def at(self, j, name):
                return j[0] * self.count + (self.index[name] + self.count * j[1])

            def before(self, j):
                return j[0] * self.count + self.count * j[1]

        G_PE = ChunkStages("rows", "gram", "qk", "k_turned", "v_turned", "m_turned",
                           *[x + str(l) for l in range(1, 7) for x in ("w", "tt", "ta")][:-1], "ks", "v_new", "o", "s")
        G_DVE = ChunkStages("decayed", "diff", "lower", "m0", "ta0", "t0", "qk",
                            *[x + str(l) for l in range(1, 7) for x in ("tt", "ta")][:-1], "r", "s")
        G_ACT = ChunkStages("staged", "exps", "ko", "vb", *["w%d" % l for l in range(1, 7)], "v_new", "out")
        G_POOL = ChunkStages("upper", "m1", "q_in", *["m%d" % l for l in range(2, 7)])
        C_PE = ChunkStages("l", "kg", "bg", "mt", "vt",
                           *[x + str(l) for l in C_LEVELS for x in (("lw", "tt", "ta") if l < 5 else ("lw", "tt"))],
                           "x", "u", "o", "m")
        C_ACT = ChunkStages("px", "pi", "bt", "kt", "vt", *["w%d" % l for l in C_LEVELS], "x", "u", "o")
        C_DVE = ChunkStages("scan", "as", "bs", "kb", "rs", "lm0", "ta0", "rb", "ak", "rk", "tt0", "lm1",
                            *[x for l in C_LEVELS for x in (["lm%d" % (l + 1), "tt%d" % l, "ta%d" % l] if l < 5 else ["tt5"])],
                            "m0", "m")
        E_PE = Stages("w", "a", "g", "norm", "bonus")
        E_ACT = Stages("w", "a", "g", "square", "ln", "inv")
        E_DVE = Stages("kk0", "k2a", "k2", "rkk", "bonus", "kk", "b")

        class Order:

            def __init__(self, *stages):
                self.stages = list(stages)

            def at(self, m, name):
                return self.stages.index((m, name)) + 1

        F_ACT = Order(*[(m, x) for m in range(2) for x in ("square", "ln", "inv")],
                      *[s for m in range(4) for s in [(m, "hi")] + [(m + 2, x) for x in ("square", "ln", "inv") if m < 2]])
        F_DVE = Order((0, "centred"), (1, "centred"),
                      *[s for m in range(4) for s in [(m, "scaled"), (m, "plus"), (m, "gated")]
                        + [(m + 2, "centred")] * (m < 2) + [(m, "lo")]])
        C_POOL = ChunkStages("a", "b", "v")
        G_SAMPLE, C_SAMPLE = (0, 4), (0, 8)

        def is_sample(j, sample=C_SAMPLE):
            return isinstance(j[0], int) and j == sample

        def starts_set(j):
            return isinstance(j[0], int) and j == (0, 0)

        def is_first(j, p):
            return isinstance(j[0], int) and j == (0, 0) and p == 0

        def other(j, p):
            return (j[0], j[1] - 1) if p == 0 else j

        def chunk_columns(j, p):
            if is_sample(j):
                return slice(S0, S0 + 64)
            first = P0 + 64 * p + 128 * j[1]
            return slice(first, first + 64) if isinstance(j[0], int) else ds(128 * j[0] + first, 64)

        def tile_columns(j, p):
            return S0 if is_sample(j, G_SAMPLE) else 256 * j[0] + (256 * j[1] + 128 * p + P0)

        def tile_place(j, p):
            return ds(8 * j[0] + (8 * j[1] + 4 * p), 4)

        def run_chunks(eng, do, first_half=FIRST, second_half=SECOND, sample=C_SAMPLE, loop_start=None, loop_end=None):
            def together(j0, p0, j1, p1):
                for n in range(max(len(first_half), len(second_half))):
                    if n < len(second_half):
                        do(second_half[n], j1, p1)
                    if n < len(first_half):
                        do(first_half[n], j0, p0)
            count = sample[1]
            for x in first_half:
                do(x, (0, 0), 0)
            together((0, 0), 1, (0, 0), 0)
            with eng.Fori(1, count) as i:
                if loop_start:
                    loop_start(i)
                together((i, 0), 0, (i, -1), 1)
                together((i, 0), 1, (i, 0), 0)
            if loop_end:
                loop_end()
            together(sample, 0, (0, count - 1), 1)
            for x in second_half:
                do(x, sample, 0)

        DECAY = 0.6065306597126334

        def stacked(p, n, half):
            return PS[:, 4 * p + n, 256 * half:256 * half + 256].rearrange("p (m n) -> p m n", m=4)

        def pairs_of(x, n=64):
            return x.unsqueeze(1).to_broadcast([x.shape[0], 4, n])

        def half(h):
            return slice(64 * h, 64 * h + 64)

        PAIR_ID, PAIR_ONES = small("pair_identity", 64), small("pair_ones", 128)

        def flat(x):
            return x[:, :, :].rearrange("p m n -> p (m n)")

        def k_group(p):
            return PS[:, 4 * p + 1:4 * p + 3, 0:384]

        IN1 = 108
        D_SCALE = 192.0 ** -0.5
        STEPS = 9

        def queries(n):
            return (P0 + 128 * n if n < 8 else S0), 128

        def key_runs(n):
            if n == 8:
                return [(NT, 128, 0), (S0, 128, 128)]
            keys = 128 * (n + 1)
            return [(P0 + k, min(512, keys - k), k) for k in range(0, keys, 512)]

        def key_blocks(n):
            return [(8, 128), (9, 128)] if n == 8 else [(j, 128) for j in range(n + 1)]

        block = ctx.enter_context(nc.Block())
        def matmul_unit(slot, ring, first, nk, hi, lo, width=BW, second_half=None):
            for b in range(NB):
                if b == 2 and second_half:
                    second_half()
                n, last = 0, None
                for k in range(nk):
                    w = slice(first + k * 128, first + (k + 1) * 128)
                    for wt, r in ((WHI, hi), (WHI, lo), (WLO, hi)):
                        last = nc.tensor.matmul(PS[:, 4 * slot + b, 0:width], wt[:, ring, w],
                                                r[:, k, b * width:(b + 1) * width],
                                                start=n == 0, stop=n == 3 * nk - 1)
                        n += 1
            return last

        @block.sync
        def _(sp):
            sp.dma_start(COL[:, :], io["columns"]).then_inc(params_in, 16)
            sp.dma_start(SMALL[:, :], io["small"]).then_inc(params_in, 16)
            for k in range(8):
                sp.dma_start(X32[:, k, :], io["x"][:, k, :]).then_inc(x_in[k // 2], 16)
            for s in range(2):
                sp.dma_start(RAW[:, s, :], io["units"][s]).then_inc(raw_in[s], 16)
            def load_units(first, last):
                with sp.Fori(first, last) as i:
                    for s in range(2):
                        sp.wait_ge(unit_split, 2 * i + s - 1)
                        sp.dma_start(RAW[:, s, :], io["units"][ds(2 * i + s, 1), :, :].rearrange("a p n -> p (a n)"))\
                          .then_inc(raw_in[s], 16)

            load_units(1, OUT_UNIT[1] // 2 + 2)
            sp.wait_ge(a_hi, 73)
            sp.dma_start(WG[:, :, :], CROW[12:14, :, :].rearrange("k p n -> p k n")).then_inc(e_wg, 16)
            sp.dma_start(LORA[:, :, :], io["w_lora"]).then_inc(lora_in, 16)

            def load_rows(m):
                sp.dma_start(RKV[m % 2][:, :, :], CROW[0:12, :, :].rearrange("(k m) p n -> m p k n", m=4)[m])\
                  .then_inc(e_in[m % 2], 16)

            load_rows(0)
            load_rows(1)
            for m in range(4):
                prepared = PROW.rearrange("(k m) p n -> m p k n", m=4)[m]
                sp.wait_ge(e_dve, E_DVE.at(m, "k2") - 1)
                sp.dma_start(prepared[:, 0:2, :], PREP[m % 2][:, 0:2, :]).then_inc(e_out[m % 2], 16)
                sp.wait_ge(e_dve, E_DVE.at(m, "bonus") - 1)
                sp.wait_ge(e_act, E_ACT.at(m, "g") - 1)
                sp.dma_start(BROW.rearrange("(k m) p n -> m p k n", m=4)[m], BG[m % 2][:, :, :]).then_inc(e_out[m % 2], 16)
                sp.wait_ge(e_dve, E_DVE.at(m, "b") - 1)
                sp.dma_start(prepared[:, 2:4, :], PREP[m % 2][:, 2:4, :]).then_inc(e_out[m % 2], 16)
                if m < 2:
                    load_rows(m + 2)
            for p in range(2):
                sp.wait_ge(e_out[p], 96)

            def load_tokens(p, columns):
                for first, rows_of in ((0, CROW[0:4]), (4, CROW[8:12]), (8, PROW)):
                    n = rows_of.shape[0]
                    sp.dma_start(CIN[p][:, first:first + n, :], rows_of[:, :, columns].rearrange("a p n -> p a n"))\
                      .then_inc(c_in[p], 16)

            for p in range(2):
                load_tokens(p, chunk_columns((0, 0), p))
            sp.wait_ge(c_ready, 2)
            for h in range(2):
                sp.dma_start(MB[1][half(h), :, half(h)], io["s_c"][half(h)]).then_inc(c_state_in, 16)
            with sp.Fori(0, 7) as i:
                for p in range(2):
                    sp.wait_ge(c_pool[p], C_POOL.at((i, 0), "v"))
                    sp.wait_ge(c_dve[p], C_DVE.at((i, 0), "rs"))
                    load_tokens(p, chunk_columns((i, 1), p))
            sp.wait_ge(c_pool[0], C_POOL.at((0, 7), "v"))
            sp.wait_ge(c_dve[0], C_DVE.at((0, 7), "rs"))
            load_tokens(0, chunk_columns(C_SAMPLE, 0))
            sp.wait_ge(c_act[0], C_ACT.at(C_SAMPLE, "o"))
            for m in range(4):
                if m >= 2:
                    sp.wait_ge(f_dve, F_DVE.at(m - 2, "gated"))
                sp.dma_start(BGL[m % 2][:, :, :], BROW.rearrange("(k m) p n -> m p k n", m=4)[m]).then_inc(f_in[m % 2], 16)
            load_units(OUT_UNIT[1] // 2 + 2, NU // 2)
            sp.wait_ge(kept_ready, 1)
            sp.dma_start(io["kept"], KEPT[:, :]).then_inc(outs_done, 16)
            sp.wait_ge(outs_done, 16)

        @block.gpsimd
        def _(pool):
            ZERO = EPS[:, 3:4]

            def zeros(h):
                return EPS[half(h), 3:4].unsqueeze(2).to_broadcast([64, 4, 64])

            pool.wait_ge(eps_set, 5)
            def split_units(first, last):
                with pool.Fori(first, last) as i:
                    for s in range(2):
                        pool.wait_ge(raw_in[s], 16 * i + 16)
                        pool.wait_ge(unit_done, 2 * i + s + 1)
                        nc.gpsimd.tensor_tensor(WHI[:, s, :], RAW[:, s, :], ZERO.to_broadcast([128, 1024]), ALU.add)\
                            .then_inc(hi_split, 1)
                        pool.wait_ge(hi_split, 2 * i + s + 1)
                        nc.gpsimd.tensor_tensor(WLO[:, s, :], RAW[:, s, :], WHI[:, s, :], ALU.subtract)\
                          .then_inc(unit_split, 1)

            def norm_low(n):
                for h in range(2):
                    for k in range(8 - h * DVE_LOWS):
                        pool.wait_ge(ln_hi, 8 * h + k + 1 + 16 * n)
                        nc.gpsimd.tensor_tensor(row_half(XL[:, k, :], h), row_half(Y[:, k, :], h), row_half(XH[:, k, :], h),
                                                ALU.subtract).then_inc(ln_lo, 1)

            def layer_end(l, last):
                first = OUT_UNIT[l]
                norm_low(2 * l)
                split_units((first + 10) // 2, (first + 76) // 2)
                norm_low(2 * l + 1)
                split_units((first + 76) // 2, last)

            split_units(0, OUT_UNIT[0] // 2 + 1)

            SPLIT_STEPS = ["blocks", "w1", "w2", "w3"]

            def g_step(name, j, p):
                s = gdn_pool[p]

                def masked(l):
                    nc.gpsimd.tensor_tensor(LM[p][:, :, :], DB[p][:, :, :], heads_of(level_mask(l)), ALU.mult).then_inc(s, 1)

                if name == "diffs":
                    pool.wait_ge(gdn_act[p], G_ACT.at(j, "exps"))
                    nc.gpsimd.tensor_tensor(DA[p][:, :, :], DA[p][:, :, :], heads_of(UPPER), ALU.mult).then_inc(s, 1)
                elif name == "blocks":
                    pool.wait_ge(gdn_pe[p], G_PE.at(j, "m_turned"))
                    pool.wait_ge(gdn_dve[p], G_DVE.at(j, "ta0"))
                    masked(1)
                    nc.gpsimd.tensor_tensor(QT[p][:, :, :], QT[p][:, :, :], EG[p][:, :, :], ALU.mult).then_inc(s, 1)
                elif name[0] == "w" and name != "w6":
                    pool.wait_ge(gdn_pe[p], G_PE.at(j, name))
                    masked(int(name[1]) + 1)
                if is_first(j, p) and name in SPLIT_STEPS:
                    m = SPLIT_STEPS.index(name)
                    pool.wait_ge(rg_vec, 5)
                    nc.gpsimd.tensor_tensor(XH[:, m, 4:NT], XCQ[:, m, 4:NT], ZERO.to_broadcast([128, NT - 4]), ALU.add)\
                      .then_inc(rg_split, 1)
                    pool.wait_ge(rg_split, 2 * m + 1)
                    nc.gpsimd.tensor_tensor(XL[:, m, 4:NT], XCQ[:, m, 4:NT], XH[:, m, 4:NT], ALU.subtract)\
                      .then_inc(rg_split, 1)

            run_chunks(pool, g_step, G_FIRST, G_SECOND, G_SAMPLE)
            for h in range(2):
                pool.wait_ge(xh_ready, 8 + h + 1)
                nc.gpsimd.tensor_tensor(XL[:, 4 + h, :], OT[:, h, :], XH[:, 4 + h, :], ALU.subtract).then_inc(mix_ready[0], 1)
            split_units(OUT_UNIT[0] // 2 + 1, (OUT_UNIT[0] + 10) // 2)
            layer_end(0, OUT_UNIT[1] // 2 + 1)

            def c_step(name, j, p):
                if name != "prep1":
                    return
                pool.wait_ge(c_dve[p], C_DVE.at(j, "as"))
                for h in range(2):
                    last = nc.gpsimd.tensor_tensor(A_B[p][half(h), :, half(h)], ARI[p][half(h), :, 0:64], zeros(h), ALU.add)
                last.then_inc(c_pool[p], 1)
                pool.wait_ge(c_dve[p], C_DVE.at(j, "bs"))
                for h in range(2):
                    last = nc.gpsimd.tensor_tensor(B_B[p][half(h), :, half(h)], B_S[p][half(h), :, :], zeros(h), ALU.add)
                last.then_inc(c_pool[p], 1)
                for h in range(2):
                    last = nc.gpsimd.tensor_tensor(V_B[p][half(h), :, half(h)], CIN[p][half(h), 4:8, :], zeros(h), ALU.add)
                last.then_inc(c_pool[p], 1)

            for p in range(2):
                pool.wait_ge(e_out[p], 96)
            for x in ZEROED[:9]:
                last = nc.gpsimd.memset(x[:, :, :], 0.0)
            last.then_inc(c_ready, 1)
            pool.wait_ge(c_ready, 2)
            run_chunks(pool, c_step)
            split_units(OUT_UNIT[1] // 2 + 1, (OUT_UNIT[1] + 10) // 2)
            layer_end(1, NU // 2)

        @block.tensor
        def _(pe):
            pe.sem_inc(unit_done, 2)
            pe.sem_inc(rg_done, 2)
            pe.sem_inc(norm_sum, 2)
            pe.wait_ge(ba_split, 1)
            for k in range(8):
                pe.wait_ge(xl_ready, k + 1)
                for n, (x, w) in enumerate(((XH, WBAH), (XL, WBAH), (XH, WBAL))):
                    for b in range(NB):
                        last = nc.tensor.matmul(PS[0:8, b, 0:BW], w[:, 8 * k:8 * k + 8], x[:, k, b * BW:(b + 1) * BW],
                                                start=k == 0 and n == 0, stop=k == 7 and n == 2)
            last.then_inc(ba_done, 1)
            pe.wait_ge(ba_row, 1)
            for c in range(9):
                t0 = P0 + 128 * c if c < 8 else S0
                last = nc.tensor.matmul(PS[:, 7, 8 * c:8 * c + 8], BAR[0:8, t0:t0 + 128], IDENT[0:8, 0:8],
                                        start=True, stop=True)
            last.then_inc(ba_done, 1)

            def in_units(i):
                for s in range(2):
                    pe.wait_ge(unit_split, 2 * i + s + 1)
                    pe.wait_ge(slot_act, 2 * i + s + 1)
                    if isinstance(i, int):
                        pe.wait_ge(ba_act, 1)
                        pe.wait_ge(ba_vec, 1)
                    matmul_unit(s, s, 0, 8, XH, XL).then_inc(unit_done, 1)

            in_units(0)
            with pe.Fori(1, 2) as i:
                in_units(i)
            pe.wait_ge(g_ready, 1)
            pe.wait_ge(slot_act, in_unit(3))
            nc.tensor.matmul(PS[:, 7, 128:164], UPPER, GB[:, :], start=True, stop=True).then_inc(ba_done, 1)
            pe.wait_ge(ba_copied, 1)
            with pe.Fori(2, 4) as i:
                in_units(i)
            with pe.Fori(4, 8) as i:
                for s in range(2):
                    pe.wait_ge(rg_read, 2 * i - 7 + s)
                    pe.wait_ge(unit_split, 2 * i + s + 1)
                    pe.wait_ge(slot_act, 2 * i + s + 1)
                    matmul_unit(s, s, 0, 8, XH, XL).then_inc(unit_done, 1)
                pe.wait_ge(gates_in, 16 * i - 48)
                pe.wait_ge(conv_done, 6)
                for g in range(2):
                    pe.wait_ge(slot_act, in_unit(2 * i + g))
                    for b in range(NB):
                        last = nc.tensor.matmul(PS[:, 4 * g + b, 0:BW], RGW[:, g, :],
                                                XCQ[:, ds(i - 4, 1), b * BW:(b + 1) * BW].rearrange("p a n -> p (a n)"),
                                                start=True, stop=True)
                    last.then_inc(rg_done, 1)
            pe.wait_ge(rg_read, 10)
            with pe.Fori(8, 12) as i:
                for s in range(2):
                    pe.wait_ge(norm_read, 2 * i - 15 + s)
                    pe.wait_ge(unit_split, 2 * i + s + 1)
                    pe.wait_ge(slot_act, 2 * i + s + 1)
                    matmul_unit(s, s, 0, 8, XH, XL).then_inc(unit_done, 1)
                for s in range(2):
                    pe.wait_ge(sq_ready, 2 * i - 15 + s)
                    pe.wait_ge(slot_act, in_unit(2 * i + s))
                    for b in range(NB):
                        last = nc.tensor.matmul(PS[:, 4 * s + b, 0:BW], ONES, RN[s][:, b * BW:(b + 1) * BW],
                                                start=True, stop=True)
                    last.then_inc(norm_sum, 1)
            pe.wait_ge(norm_root, 8)

            def by_head(bank, lhs, rhs, start=True, stop=True):
                for h in range(4):
                    last = nc.tensor.matmul(PS[:, bank, 128 * h:128 * h + 128], lhs[:, h, :], rhs[:, h, :],
                                            start=start, stop=stop)
                return last

            def turned(bank, x):
                for h in range(4):
                    last = nc.tensor.transpose(PS[:, bank, 128 * h:128 * h + 128], x[:, h, :], IDENT)
                return last

            def g_step(name, j, p):
                s, b = gdn_pe[p], 4 * p
                state = SS if is_sample(j, G_SAMPLE) else SP
                if name == "decays":
                    pe.wait_ge(gdn_dve[p], G_DVE.at(j, "decayed"))
                    nc.tensor.matmul(PS[:, b, :], ONES, LM[p][:, :, :].rearrange("p h n -> p (h n)"), start=True, stop=True)\
                      .then_inc(s, 1)
                elif name == "diffs":
                    if is_sample(j, G_SAMPLE):
                        pe.wait_ge(pad_zeroed, 1)
                    pe.wait_ge(gdn_act[p], G_ACT.at(j, "staged"))
                    by_head(b + 1, KT[p], KT[p]).then_inc(s, 1)
                    by_head(b + 2, KT[p], QT[p]).then_inc(s, 1)
                    turned(b + 3, KT[p]).then_inc(s, 1)
                elif name == "grams":
                    pe.wait_ge(gdn_act[p], G_ACT.at(j, "exps"))
                    turned(b, VT[p]).then_inc(s, 1)
                elif name == "blocks":
                    pe.wait_ge(gdn_dve[p], G_DVE.at(j, "m0"))
                    turned(b + 1, LM[p]).then_inc(s, 1)
                elif name[0] == "w":
                    l = int(name[1])
                    pe.wait_ge(gdn_dve[p], G_DVE.at(j, "tt%d" % (l - 1) if l > 1 else "t0"))
                    pe.wait_ge(gdn_pool[p], G_POOL.at(j, "m%d" % l))
                    by_head(b + 1, LM[p], TT[p]).then_inc(s, 1)
                elif name[0] == "t":
                    l = int(name[1])
                    pe.wait_ge(gdn_dve[p], G_DVE.at(j, "ta%d" % (l - 1) if l > 1 else "qk"))
                    pe.wait_ge(gdn_act[p], G_ACT.at(j, "w%d" % l))
                    by_head(b + 2, TA[p], WW[p]).then_inc(s, 1)
                    if l < 6:
                        by_head(b + 3, WW[p], TA[p]).then_inc(s, 1)
                    else:
                        if is_sample(j, G_SAMPLE):
                            pe.wait_ge(state_in, 16)
                        elif not is_first(j, p):
                            pe.wait_ge(gdn_dve[1 - p], G_DVE.at(other(j, p), "s"))
                        by_head(b, KT[p], state).then_inc(s, 1)
                elif name == "carry1":
                    pe.wait_ge(gdn_dve[p], G_DVE.at(j, "r"))
                    by_head(b + 1, TT[p], RR[p]).then_inc(s, 1)
                else:
                    pe.wait_ge(gdn_act[p], G_ACT.at(j, "v_new"))
                    for h in range(4):
                        o = PS[:, b + 2, 128 * h:128 * h + 128]
                        nc.tensor.matmul(o, state[:, h, :], QT[p][:, h, :], start=True, stop=False)
                        last = nc.tensor.matmul(o, VN[p][:, h, :], DA[p][:, h, :], start=False, stop=True)
                    last.then_inc(s, 1)
                    by_head(b + 3, KO[p], VN[p]).then_inc(s, 1)

            run_chunks(pe, g_step, G_FIRST, G_SECOND, G_SAMPLE)
            for h in range(4):
                pe.wait_ge(o_square, h + 1)
                if h >= 2:
                    pe.wait_ge(norm_read, 10 + h - 1)
                for b in range(NB):
                    last = nc.tensor.matmul(PS[:, 4 * (h % 2) + b, 0:BW], ONES, RN[h % 2][:, b * BW:(b + 1) * BW],
                                            start=True, stop=True)
                last.then_inc(o_sum, 1)

            def norm_sums(n):
                pe.wait_ge(ln_total, 9 + 9 * n)
                for h in range(2):
                    for b in (2 * h, 2 * h + 1):
                        last = nc.tensor.matmul(PS[:, b, 0:BW], ONES, YSUM[n % 2][:, b * BW:(b + 1) * BW], start=True, stop=True)
                    last.then_inc(ln_mean, 1)
                for h in range(2):
                    for k in range(8):
                        pe.wait_ge(ln_sq, 8 * h + k + 1 + 16 * n)
                        for b in (2 * h, 2 * h + 1):
                            last = nc.tensor.matmul(PS[:, 4 + b, 0:BW], ONES, SQ[k % 2][:, b * BW:(b + 1) * BW],
                                                    start=k == 0, stop=k == 7)
                        last.then_inc(ln_var, 1)

            def normed(n):
                return lambda: pe.wait_ge(ln_lo, 16 + 16 * n)

            def up(l, g, unit):
                for t in range(4):
                    pe.wait_ge(unit_split, unit + t + 1)
                    matmul_unit(t % 2, t % 2, 0, 8, XH, XL).then_inc(unit_done, 1)

            def down(l, g, unit, slots=True):
                pe.wait_ge(h_done, g + 2 + 12 * l)
                for m in range(8):
                    if m % 4 == 0:
                        pe.wait_ge(unit_split, unit + m // 4 + 1)
                    if m < 2:
                        pe.wait_ge(up_read, slots + m + 45 * l)
                    else:
                        pe.wait_ge(down_read, 8 * g + m + 1 + 90 * l)
                    last = matmul_unit(m % 2, m // 4, 256 * (m % 4), 2, HH, HL)
                    last.then_inc(part_done if m % 4 < 3 else unit_done, 1)

            def layer_end(l):
                first = OUT_UNIT[l]
                pe.wait_ge(mix_ready[l], 4)
                if l == 0:
                    pe.wait_ge(rg_split, 8)
                with pe.Fori(0, 4) as i:
                    for s in range(2):
                        pe.wait_ge(unit_split, first + 2 * i + s + 1)
                        pe.wait_ge(out_read, 2 * i + s + 1 + 10 * l)
                        matmul_unit(s, s, 0, 8, XH, XL).then_inc(unit_done, 1)
                pe.wait_ge(out_read, 10 + 10 * l)
                norm_sums(2 * l)
                pe.wait_ge(gaps_zeroed, 1 + 2 * l)
                for t in range(4):
                    pe.wait_ge(unit_split, first + 8 + t + 1)
                    if t >= 2:
                        pe.wait_ge(up_read, t + 45 * l)
                    matmul_unit(t % 2, t % 2, 0, 8, XH, XL, second_half=normed(2 * l)).then_inc(unit_done, 1)
                with pe.Fori(1, 11) as g:
                    for t in range(4):
                        pe.wait_ge(unit_split, 6 * g + first + 6 + t + 1)
                        pe.wait_ge(up_read, 4 * g + t + 45 * l)
                        pe.wait_ge(down_read, 8 * g - 7 + min(t, 1) + 90 * l)
                        matmul_unit(t % 2, t % 2, 0, 8, XH, XL).then_inc(unit_done, 1)
                    down(l, g - 1, 6 * g + first + 10, 4 * g + 4)
                down(l, 10, first + 72, 44)
                pe.wait_ge(down_read, 90 + 90 * l)
                norm_sums(2 * l + 1)
                pe.wait_ge(p_split, 2 + 2 * l)
                pe.wait_ge(ln_root, 2 + 2 * (2 * l + 1))
                for m in range(8):
                    if m % 4 == 0:
                        pe.wait_ge(unit_split, first + 74 + m // 4 + 1)
                    if m >= 2:
                        pe.wait_ge(wp_read, m - 1 + 8 * l)
                    last = matmul_unit(m % 2, m // 4, 256 * (m % 4), 2, PH, PL)
                    last.then_inc(part_done if m % 4 < 3 else unit_done, 1)
                pe.wait_ge(wp_read, 8 + 8 * l)
                pe.wait_ge(gaps_zeroed, 1 + (2 * l + 1))
                with pe.Fori(0, 4) as i:
                    for s in range(2):
                        pe.wait_ge(unit_split, 2 * i + s + first + 77)
                        pe.wait_ge(gate_read, 2 * i + s + 1 + 10 * l)
                        matmul_unit(s, s, 0, 8, XH, XL, second_half=normed(2 * l + 1)).then_inc(unit_done, 1)

            layer_end(0)
            pe.wait_ge(in_ready, 1)
            pe.wait_ge(gate_read, 10)
            with pe.Fori(0, 10) as i:
                for s in range(2):
                    pe.wait_ge(unit_split, 2 * i + s + IN1 + 1)
                    pe.wait_ge(in1_read, 2 * i + s + 1)
                    matmul_unit(s, s, 0, 8, XH, XL, second_half=lambda: pe.wait_ge(x_lo, 16)).then_inc(unit_done, 1)
            pe.wait_ge(in1_read, 22)
            def swap_halves(slot, x):
                for b in range(NB):
                    last = nc.tensor.matmul(PS[:, 4 * slot + b, 0:BW], small("half_swap", 128), x[:, b * BW:(b + 1) * BW],
                                            start=True, stop=True)
                last.then_inc(swapped, 1)

            swap_halves(0, KRW)
            for j in range(5):
                slot, k, nk = (1, j, 3) if j < 3 else (0, j - 3, 2)
                if j == 3:
                    pe.wait_ge(kr_done, 1)
                pe.wait_ge(m_square, j + 1)
                for b in range(NB):
                    last = nc.tensor.matmul(PS[:, 4 * slot + b, 0:BW], ONES, SQD[j % 2][:, b * BW:(b + 1) * BW],
                                            start=k == 0, stop=k == nk - 1)
                last.then_inc(m_sum, 1)
            pe.wait_ge(m_root, 2)
            pe.wait_ge(m_lo, 4)
            for m in range(6):
                if m % 2 == 0:
                    pe.wait_ge(unit_split, IN1 + 20 + m // 2 + 1)
                if m >= 2:
                    pe.wait_ge(qkv_read, m - 1)
                last = matmul_unit(m % 2, (m // 2) % 2, 384 * (m % 2), 3, QAH, QAL)
                last.then_inc(unit_done if m % 2 else part_done, 1)
            pe.wait_ge(m_lo, 6)
            for m in range(4):
                if m % 2 == 0:
                    pe.wait_ge(unit_split, IN1 + 23 + m // 2 + 1)
                pe.wait_ge(qkv_read, 6 + m - 1)
                last = matmul_unit(m % 2, (m // 2 + 1) % 2, 256 * (m % 2), 2, CH, CL, KW)
                last.then_inc(unit_done if m % 2 else part_done, 1)
            for r in range(2):
                pe.wait_ge(qkv_read, 9 + r)
                swap_halves(r, QR[:, r, :])
            pe.wait_ge(unit_split, IN1 + 26)
            pe.wait_ge(q_rotated, 2)
            for j in range(10):
                t0 = P0 + 128 * j if j < 8 else (NT if j == 8 else S0)
                if j >= 8:
                    pe.wait_ge(v_read, j - 7)
                n = 0
                for k in range(2):
                    for c, w in ((CH, WHI), (CL, WHI), (CH, WLO)):
                        last = nc.tensor.matmul(PS[:, j % 8, :], c[:, k, t0:t0 + 128], w[:, 1, 512 * k:512 * k + 512],
                                                start=n == 0, stop=n == 5)
                        n += 1
                last.then_inc(v_done if j < 9 else unit_done, 1)

            def scores(i, hh, n):
                t0, nq = queries(n)
                s = 18 * i + 9 * hh + n
                if n == 0 or n == 1:
                    pe.wait_ge(q_staged, 2 * i + hh + 1)
                pe.wait_ge(a_probs, s + 1)
                g = (9 * hh + n) % 2
                for c, nk, at_ in key_runs(n):
                    out = PS[0:nq, 2 * g + at_ // 512, at_ % 512:at_ % 512 + nk]
                    nc.tensor.matmul(out, QS[:, hh, t0:t0 + nq], KN[:, ds(2 * i + hh, 1), c:c + nk].rearrange("p a n -> p (a n)"),
                                     start=True, stop=False)
                    r = slice(64 * hh, 64 * hh + 64)
                    last = nc.tensor.matmul(out, QRS[r, t0:t0 + nq], KRR[r, c:c + nk], start=False, stop=True)
                last.then_inc(a_scores, 1)

            def turn(i, hh, n):
                t0, nq = queries(n)
                s, g = 18 * i + 9 * hh + n, (9 * hh + n) % 2
                pe.wait_ge(a_probs, s + 3)
                for j, (_, nk) in enumerate(key_blocks(n)):
                    last = nc.tensor.transpose(PS[0:nk, 4 + j // 4, 128 * (j % 4):128 * (j % 4) + nq],
                                               PB[0:nq, g, 128 * j:128 * j + nk], IDENT[0:nq, 0:nq])
                last.then_inc(a_turned, 1)

            def weigh(i, hh, n):
                t0, nq = queries(n)
                s = 18 * i + 9 * hh + n
                pe.wait_ge(a_keys, s + 1)
                if 4 <= n < 8:
                    pe.wait_ge(a_keys2, 8 * i + 4 * hh + n - 3)
                pe.wait_ge(a_scaled, s + 1)
                blocks = key_blocks(n)
                for j, (v, nk) in enumerate(blocks):
                    last = nc.tensor.matmul(PS[0:nq, 6, 0:128], PTB[0:nk, 128 * j:128 * j + nq],
                                            VTOK[0:nk, v, ds(256 * i + 128 * hh, 128)], start=j == 0, stop=j == len(blocks) - 1)
                last.then_inc(a_out, 1)

            def back(i, hh, n):
                t0, nq = queries(n)
                s, g = 18 * i + 9 * hh + n, (9 * hh + n) % 2
                pe.wait_ge(a_scaled, s + 2)
                pe.wait_ge(a_hi, 2 * s + 1)
                nc.tensor.transpose(PS[:, 7, 0:nq], OB[0:nq, g, :], IDENT[0:nq, 0:nq]).then_inc(a_back, 1)

            pe.wait_ge(v_read, 10)
            order = [(hh, n) for hh in range(2) for n in range(STEPS)]
            pe.sem_inc(a_scores, 1)
            pe.sem_inc(a_turned, 1)
            pe.sem_inc(a_out, 1)
            with pe.Fori(0, 2) as i:
                scores(i, 0, 0)
                for x, (hh, n) in enumerate(order):
                    if x + 1 < len(order):
                        scores(i, *order[x + 1])
                    turn(i, hh, n)
                    if x:
                        back(i, *order[x - 1])
                    weigh(i, hh, n)
                back(i, *order[-1])
            def c_blocks(out, lhs, rhs, more=()):
                terms = [(lhs, rhs)] + list(more)
                for m in range(4):
                    for n, (l, r) in enumerate(terms):
                        last = nc.tensor.matmul(out[:, m, :], l[:, m, :], r if len(r.shape) == 2 else r[:, m, :],
                                                start=n == 0, stop=n == len(terms) - 1)
                return last

            def c_step(name, j, p):
                b, s = 4 * p, c_pe[p]
                level = int(name[1:]) if name[0] in "wt" else 0
                if name == "prep2":
                    pe.wait_ge(c_pool[p], C_POOL.at(j, "b"))
                    c_blocks(per_head(b), A_B[p], B_B[p]).then_inc(s, 1)
                    pe.wait_ge(c_dve[p], C_DVE.at(j, "rs"))
                    for m in range(4):
                        last = nc.tensor.matmul(k_group(p)[:, m // 2, 192 * (m % 2):192 * (m % 2) + 192], K_B[p][:, m, :],
                                                ARI[p][:, m, :], start=True, stop=True)
                    last.then_inc(s, 1)
                    for m in range(4):
                        last = nc.tensor.matmul(per_head(b + 3)[:, m, :], B_B[p][:, m, :], ARI[p][:, m, 64:192],
                                                start=True, stop=True)
                    last.then_inc(s, 1)
                elif name == "prep3":
                    pe.wait_ge(c_act[p], C_ACT.at(j, "kt"))
                    pe.wait_ge(c_dve[p], C_DVE.at(j, "rk"))
                    c_blocks(per_head(b + 1), LM_B[p], IDENT).then_inc(s, 1)
                    pe.wait_ge(c_pool[p], C_POOL.at(j, "v"))
                    c_blocks(per_head(b + 2), V_B[p], IDENT).then_inc(s, 1)
                elif name[0] == "w":
                    pe.wait_ge(c_dve[p], C_DVE.at(j, "tt%d" % (level - 1) if level > 1 else "lm1"))
                    c_blocks(per_head(b + 1), LM_B[p], TT_B[p]).then_inc(s, 1)
                elif name[0] == "t":
                    if level == 1:
                        pe.wait_ge(c_act[p], C_ACT.at(j, "vt"))
                    pe.wait_ge(c_dve[p], C_DVE.at(j, "ta%d" % (level - 1)))
                    pe.wait_ge(c_act[p], C_ACT.at(j, "w%d" % level))
                    c_blocks(per_head(b + 2), TA_B[p], W_B[p]).then_inc(s, 1)
                    if level < 5:
                        c_blocks(per_head(b + 3), W_B[p], TA_B[p]).then_inc(s, 1)
                elif name == "carry1":
                    if is_sample(j):
                        pe.wait_ge(c_state_in, 32)
                    elif not is_first(j, p):
                        pe.wait_ge(c_dve[1 - p], C_DVE.at(other(j, p), "m"))
                    c_blocks(per_head(b + 1), A_B[p], MB[is_sample(j)], [(AK_B[p], VT_B[p])]).then_inc(s, 1)
                elif name == "carry2":
                    pe.wait_ge(c_act[p], C_ACT.at(j, "x"))
                    pe.wait_ge(c_dve[p], C_DVE.at(j, "tt5"))
                    c_blocks(per_head(b + 2), TT_B[p], X_B[p]).then_inc(s, 1)
                elif name == "carry3":
                    pe.wait_ge(c_act[p], C_ACT.at(j, "u"))
                    c_blocks(stacked(p, 1, 0), MB[is_sample(j)], ARI[p][:, :, 64:128], [(U_B[p], RB_S[p]), (VT_B[p], RK_S[p])])\
                        .then_inc(s, 1)
                    c_blocks(per_head(b + 3), BT_B[p], U_B[p], [(KT_B[p], VT_B[p])]).then_inc(s, 1)

            def e_product(m, use, lhs, rhs, partitions):
                for n in range(NB):
                    last = nc.tensor.matmul(PS[:, 4 * ((5 * m + use) % 2) + n, 0:BW], lhs, rhs[partitions, n * BW:(n + 1) * BW],
                                            start=True, stop=True)
                return last

            whole = slice(0, 128)
            pe.wait_ge(a_hi, 73)
            pe.wait_ge(lora_in, 16)
            pe.wait_ge(wg_ready, 2)
            for m in range(4):
                if m:
                    pe.wait_ge(e_act, E_ACT.at(m - 1, "ln") - 1)
                e_product(m, 0, LORA[0:64, 0, 128 * m:128 * m + 128], WG[:, 0, :], half(0)).then_inc(e_pe, 1)
                if m:
                    pe.wait_ge(e_dve, E_DVE.at(m - 1, "bonus") - 1)
                e_product(m, 1, LORA[64:128, 0, 128 * m:128 * m + 128], WG[:, 0, :], half(1)).then_inc(e_pe, 1)
                pe.wait_ge(e_act, E_ACT.at(m, "w") - 1)
                e_product(m, 2, LORA[:, 1, 128 * m:128 * m + 128], WG[:, 1, :], whole).then_inc(e_pe, 1)
                pe.wait_ge(e_act, E_ACT.at(m, "square") - 1)
                e_product(m, 3, PAIR_ONES, NORM[m % 2], whole).then_inc(e_pe, 1)
                pe.wait_ge(e_dve, E_DVE.at(m, "rkk") - 1)
                pe.wait_ge(e_act, E_ACT.at(m, "g") - 1)
                e_product(m, 4, PAIR_ONES, NORM[1 - m % 2], whole).then_inc(e_pe, 1)
            pe.wait_ge(e_dve, E_DVE.at(3, "b") - 1)
            run_chunks(pe, c_step)
            pe.wait_ge(c_act[0], C_ACT.at(C_SAMPLE, "o"))
            pe.wait_ge(c_dve[0], C_DVE.at(C_SAMPLE, "m"))
            for m in range(5):
                if m < 4:
                    if m:
                        pe.wait_ge(f_dve, F_DVE.at(m - 1, "centred"))
                    for n in range(NB):
                        last = nc.tensor.matmul(PS[:, n, 0:BW], PAIR_ONES, CO[:, m, n * BW:(n + 1) * BW], start=True, stop=True)
                    last.then_inc(f_mean, 1)
                if m:
                    pe.wait_ge(f_act, F_ACT.at(m - 1, "square"))
                    if m > 1:
                        pe.wait_ge(f_act, F_ACT.at(m - 2, "ln"))
                    for n in range(NB):
                        last = nc.tensor.matmul(PS[:, 4 + n, 0:BW], PAIR_ONES, SQC[(m - 1) % 2][:, n * BW:(n + 1) * BW],
                                                start=True, stop=True)
                    last.then_inc(f_var, 1)
            layer_end(1)

        @block.scalar
        def _(act):
            step = Steps(act, act_step)

            act.wait_ge(eps_set, 5)
            for free in (slot_act, rg_read, norm_read):
                act.sem_inc(free, 2)
            for s in range(2):
                act.sem_inc(row_out[s], 16)
            for k in range(8):
                act.wait_ge(x_in[k // 2], 32)
                nc.scalar.activation(XH[:, k, :], X32[:, k, :], ACT.Copy).then_inc(xh_ready, 1)
            act.wait_ge(ba_done, 1)
            nc.scalar.activation(rows(BAR[0:8, :]), banks(0)[0:8], ACT.Copy).then_inc(ba_row, 1)
            act.wait_ge(ba_done, 2)
            nc.scalar.activation(BETA, PSBA[:, :, 0:4], ACT.Sigmoid).then_inc(ba_act, 1)
            act.wait_ge(ba_vec, 1)
            nc.scalar.activation(GTMP[:, 1, :], GTMP[:, 1, :], ACT.Exp, scale=-1.0).then_inc(ba_act, 1)
            nc.scalar.activation(GTMP[:, 2, :], small("a_log", 36), ACT.Exp).then_inc(ba_act, 1)
            act.wait_ge(lam_vec, 1)
            nc.scalar.activation(LAM[:, 4:8], LAM[:, 4:8], ACT.Exp, scale=-1.0).then_inc(lam_act, 1)
            act.wait_ge(ba_act, 2)
            nc.scalar.activation(GTMP[:, 1, :], GTMP[:, 1, :], ACT.Ln, bias=1.0).then_inc(ba_act, 1)
            act.wait_ge(lam_act, 1)
            nc.scalar.activation(LAM[:, 4:8], LAM[:, 4:8], ACT.Ln, bias=1.0).then_inc(lam_act, 1)
            with act.Fori(0, 2) as i:
                for s in range(2):
                    act.wait_ge(unit_done, in_unit(2 * i + s))
                    act.wait_ge(row_out[s], 16 * i + 16)
                    nc.scalar.activation(rows(U0[:, s, :]), banks(s), ACT.Gelu_apprx_tanh).then_inc(slot_act, 1)
                    act.wait_ge(slot_act, in_unit(2 * i + s))
                    act.dma_start(GATE[ds(2 * i + s, 1), :, :].rearrange("a p n -> p (a n)"), U0[:, s, :])\
                       .then_inc(row_out[s], 16)
            act.wait_ge(ba_done, 3)
            nc.scalar.activation(GC[:, :], PS[:, 7, 128:164], ACT.Copy).then_inc(ba_copied, 1)
            act.wait_ge(ba_copied, 1)
            nc.scalar.activation(EGC[:, :], GC[:, :], ACT.Exp).then_inc(ba_copied, 1)

            def tap(s, j):
                nc.scalar.activation(rows(U0[:, s, :]), banks(s), ACT.Copy)
                nc.scalar.activation(rows(XCQ[:, ds(j, 1), :].rearrange("p a n -> p (a n)")), banks(s), ACT.Identity,
                                     scale=col_at("conv0_w3", j), bias=col_at("conv0_b", j)).then_inc(slot_act, 1)

            for s in range(2):
                act.wait_ge(row_out[s], 48)
            with act.Fori(0, 2) as i:
                for s in range(2):
                    act.wait_ge(unit_done, in_unit(4 + s) + 2 * i)
                    act.wait_ge(conv_done, 2 * i + s + 1)
                    tap(s, 2 * i + s)
            with act.Fori(0, 4) as m:
                act.wait_ge(rg_done, 2 * m + 2)
                act.dma_start(RGW[:, :, :], io["w_gates"][:, ds(m, 1), :, :].rearrange("p a g n -> p (a g) n"))\
                   .then_inc(gates_in, 16)
                for s in range(2):
                    act.wait_ge(unit_done, in_unit(8 + s) + 2 * m)
                    act.wait_ge(conv_done, 2 * m + s + 5)
                    tap(s, 2 * m + s + 4)
                act.wait_ge(rg_vec, m + 1)
                act.dma_start(MIX[4][:, :], GATE[ds(m, 1), :, :].rearrange("a p n -> p (a n)")).then_inc(gate_in, 16)
                for g, bias in enumerate(("a_b_r", "a_b_i")):
                    act.wait_ge(rg_done, 2 * m + g + 3)
                    nc.scalar.activation(rows(MIX[g][:, :]), banks(g), ACT.Sigmoid, bias=col_at(bias, m)).then_inc(rg_read, 1)
                act.wait_ge(rg_read, 2 * m + 3)
                nc.scalar.activation(MIX[3][:, :], MIX[0][:, :], ACT.Tanh, scale=LAM[:, ds(12 + m, 1)]).then_inc(rg_act, 1)
                act.wait_ge(rg_act, 6 * m + 1)
                nc.scalar.activation(MIX[2][:, :], MIX[3][:, :], ACT.Ln, bias=1.0).then_inc(rg_act, 1)
                act.wait_ge(rg_act, 6 * m + 2)
                nc.scalar.activation(MIX[3][:, :], MIX[3][:, :], ACT.Ln, bias=EPS[:, 4:5], scale=2.0).then_inc(rg_act, 1)
                nc.scalar.activation(MIX[2][:, :], MIX[2][:, :], ACT.Exp, scale=-0.5).then_inc(rg_act, 1)
                act.wait_ge(rg_act, 6 * m + 3)
                nc.scalar.activation(MIX[3][:, :], MIX[3][:, :], ACT.Exp, scale=0.5).then_inc(rg_act, 1)
                nc.scalar.activation(MIX[0][:, :], MIX[0][:, :], ACT.Exp, scale=LAM[:, ds(8 + m, 1)]).then_inc(rg_act, 1)
            act.wait_ge(conv_done, 14)
            with act.Fori(0, 4) as n:
                for s in range(2):
                    x = XCQ[:, ds(4 + 2 * n + s, 1), 4:NT]
                    nc.scalar.activation(x, x, ACT.Silu).then_inc(silu_done, 1)
                act.wait_ge(rg_vec, 5)
                for s in range(2):
                    act.wait_ge(silu_done, 3 * n + s + 1)
                    act.wait_ge(norm_sum, 2 * n + s + 1)
                    nc.scalar.activation(RN[s][:, :], XCQ[:, ds(4 + 2 * n + s, 1), :].rearrange("p a n -> p (a n)"),
                                         ACT.Square).then_inc(sq_ready, 1)
                act.wait_ge(unit_done, in_unit(16) + 2 * n)
                act.wait_ge(conv_done, n + 14)
                tap(0, 12 + n)
                act.wait_ge(unit_done, in_unit(17) + 2 * n)
                act.wait_ge(row_out[1], 16 * n + 48)
                nc.scalar.activation(rows(U0[:, 1, :]), banks(1), ACT.Silu).then_inc(slot_act, 1)
                act.wait_ge(slot_act, in_unit(17) + 2 * n)
                act.dma_start(ZROW[ds(n, 1), :, :].rearrange("a p n -> p (a n)"), U0[:, 1, :]).then_inc(row_out[1], 16)
                act.wait_ge(conv_done, n + 15)
                x = XCQ[:, ds(12 + n, 1), 4:NT]
                nc.scalar.activation(x, x, ACT.Silu).then_inc(silu_done, 1)
                for s in range(2):
                    act.wait_ge(norm_sum, 2 * n + s + 3)
                    act.wait_ge(norm_done, 2 * n + s + 1)
                    nc.scalar.activation(rows(RN[2 + s][:, :]), banks(s), ACT.Ln, bias=EPS[:, 1:2]).then_inc(norm_read, 1)
                for s in range(2):
                    act.wait_ge(norm_read, 2 * n + s + 3)
                    nc.scalar.activation(RN[2 + s][:, :], RN[2 + s][:, :], ACT.Exp, scale=-0.5).then_inc(norm_root, 1)
            act.wait_ge(row_out[1], 112)
            act.dma_start(SS[:, :, :], io["s_b"]).then_inc(state_in, 16)
            act.wait_ge(norm_done, 10)
            act.wait_ge(silu_done, 12)

            def g_step(name, j, p):
                s, b = gdn_act[p], 4 * p
                n = 64 if is_sample(j, G_SAMPLE) else 128
                t0 = tile_columns(j, p)
                if name == "decays":
                    if not starts_set(j):
                        act.wait_ge(gdn_pe[p], G_PE.before(j))
                    for first, x, scale in ((8, KT, 1.0), (4, QT, 128.0 ** -0.5), (12, VT, 1.0)):
                        last = nc.scalar.activation(x[p][:, :, 0:n], XCQ[:, first:first + 4, ds(t0, n)], ACT.Copy, scale=scale)
                    last.then_inc(s, 1)
                elif name == "diffs":
                    act.wait_ge(gdn_dve[p], G_DVE.at(j, "diff"))
                    nc.scalar.activation(DA[p][:, :, :], DA[p][:, :, :], ACT.Exp)
                    nc.scalar.activation(DB[p][:, :, :], DB[p][:, :, :], ACT.Exp, scale=-1.0)
                    nc.scalar.activation(KOC[p][:, :], KOC[p][:, :], ACT.Exp)
                    nc.scalar.activation(EG[p][:, :, :], per_head(b), ACT.Exp).then_inc(s, 1)
                elif name == "grams":
                    act.wait_ge(s, G_ACT.at(j, "exps"))
                    act.wait_ge(gdn_pe[p], G_PE.at(j, "k_turned"))
                    for h in range(4):
                        last = nc.scalar.activation(KO[p][:, h, :], PS[:, b + 3, 128 * h:128 * h + 128], ACT.Copy,
                                                    scale=KOC[p][:, h:h + 1])
                    last.then_inc(s, 1)
                elif name == "blocks":
                    act.wait_ge(gdn_pe[p], G_PE.at(j, "v_turned"))
                    for h in range(4):
                        beta = BETA36[:, ds(8 * j[0] + (8 * j[1] + 4 * p + h), 1)]
                        last = nc.scalar.activation(VB[p][:, h, :], PS[:, b, 128 * h:128 * h + 128], ACT.Copy, scale=beta)
                    last.then_inc(s, 1)
                elif name[0] == "w":
                    act.wait_ge(gdn_pe[p], G_PE.at(j, name))
                    nc.scalar.activation(WW[p][:, :, :], per_head(b + 1), ACT.Copy).then_inc(s, 1)
                elif name == "carry1":
                    act.wait_ge(gdn_pe[p], G_PE.at(j, "v_new"))
                    nc.scalar.activation(VN[p][:, :, :], per_head(b + 1), ACT.Copy).then_inc(s, 1)
                elif name == "carry2":
                    act.wait_ge(gdn_pe[p], G_PE.at(j, "o"))
                    nc.scalar.activation(OT[:, :, ds(t0, n)], per_head(b + 2)[:, :, 0:n], ACT.Copy).then_inc(s, 1)

            run_chunks(act, g_step, G_FIRST, G_SECOND, G_SAMPLE)
            act.wait_ge(gdn_dve[1], G_DVE.at((0, 3), "s"))
            act.dma_start(io["s_b_p"], SP[:, :, :]).then_inc(state_out, 16)
            act.wait_ge(gdn_dve[0], G_DVE.at(G_SAMPLE, "s"))
            act.dma_start(io["s_b_s"], SS[:, :, :]).then_inc(state_out, 16)
            act.wait_ge(o_zeroed, 1)
            act.dma_start(ZT[:, :, :], ZROW.rearrange("t p n -> p t n")).then_inc(z_in, 16)
            act.dma_start(XR[:, :, :], io["x"]).then_inc(x_back, 16)

            def o_squares(h):
                if h >= 2:
                    act.wait_ge(o_sum, h - 1)
                nc.scalar.activation(RN[h % 2][:, :], OT[:, h, :], ACT.Square).then_inc(o_square, 1)

            def o_logs(h):
                act.wait_ge(o_sum, h + 1)
                if h >= 2:
                    act.wait_ge(o_gated, h - 1)
                nc.scalar.activation(rows(RN[2 + h % 2][:, :]), banks(h % 2), ACT.Ln, bias=EPS[:, 1:2], scale=1 / 128)\
                  .then_inc(norm_read, 1)

            def o_roots(h):
                act.wait_ge(norm_read, 10 + h + 1)
                nc.scalar.activation(RN[2 + h % 2][:, :], RN[2 + h % 2][:, :], ACT.Exp, scale=-0.5).then_inc(o_root, 1)

            for stage, h in ((o_squares, 0), (o_squares, 1), (o_logs, 0), (o_logs, 1), (o_squares, 2), (o_squares, 3),
                             (o_roots, 0), (o_roots, 1), (o_logs, 2), (o_logs, 3), (o_roots, 2), (o_roots, 3)):
                stage(h)
            for h in range(4):
                act.wait_ge(o_gated, h + 1)
                nc.scalar.activation(XH[:, 4 + h, :], OT[:, h, :], ACT.Copy).then_inc(xh_ready, 1)
            act.wait_ge(state_out, 32)

            def norm(n, between=None):
                def square(h, k):
                    act.wait_ge(ln_sub, 8 * h + k + 1 + 16 * n)
                    if k >= 2:
                        act.wait_ge(ln_var, 8 * h + k - 1 + 16 * n)
                    nc.scalar.activation(row_half(SQ[k % 2], h), row_half(Y[:, k, :], h), ACT.Square).then_inc(ln_sq, 1)

                def root(h):
                    act.wait_ge(ln_var, 8 + 8 * h + 16 * n)
                    x = row_half(RS, h)
                    step(nc.scalar.activation(rows(x), bank_half(1, h), ACT.Ln, bias=EPS[:, 0:1], scale=1 / 1024))
                    nc.scalar.activation(x, x, ACT.Exp, scale=-0.5).then_inc(ln_root, 1)

                def high(h, k):
                    act.wait_ge(ln_normed, 8 * h + k + 1 + 16 * n)
                    nc.scalar.activation(row_half(XH[:, k, :], h), row_half(Y[:, k, :], h), ACT.Copy).then_inc(ln_hi, 1)

                for k in range(8):
                    square(0, k)
                square(1, 0)
                square(1, 1)
                root(0)
                for k in range(2, 8):
                    square(1, k)
                    high(0, k - 2)
                root(1)
                high(0, 6)
                high(0, 7)
                for k in range(8):
                    high(1, k)
                    if between:
                        between(k)

            def chunk(l, g, unit, first=False):
                for t in range(4):
                    act.wait_ge(unit_done, unit + t + 3)
                    act.wait_ge(ffn_conv, 4 * g + t + 1 + 46 * l)
                    nc.scalar.activation(rows(UF[:, t % 2, :]), banks(t % 2), ACT.Copy)
                    if t == 0:
                        act.wait_ge(h_done, g + 1 + 12 * l)
                    f = 2 * g + (t if t < 2 else 20 + t)
                    nc.scalar.activation(rows(CB[:, t, :]), banks(t % 2), ACT.Identity, scale=col_at("ffn_w2%d" % l, f),
                                         bias=col_at("ffn_b%d" % l, f)).then_inc(up_read, 1)
                    if t >= 2:
                        act.wait_ge(ffn_conv, 4 * g + t + 1 + 46 * l)
                        nc.scalar.activation(CB[:, t - 2, :], CB[:, t - 2, :], ACT.Silu).then_inc(ffn_silu, 1)
                if not first:
                    act.wait_ge(unit_done, unit + 8)
                for j in range(2):
                    act.wait_ge(ffn_mul, 2 * g + j + 1 + 22 * l)
                    nc.scalar.activation(HH[:, j, :], CB[:, 2 + j, :], ACT.Copy).then_inc(h_hi, 1)

            def layer_end(l):
                first, part = OUT_UNIT[l], OUT_PART[l]
                act.sem_inc(up_read, 1)
                act.sem_inc(gate_read, 2)
                norm(2 * l)
                chunk(l, 0, first + 8, True)
                with act.Fori(1, 11) as g:
                    chunk(l, g, 6 * g + first + 6)
                act.dma_start(P32[:, :, :], io["p"][l]).then_inc(p_in, 16)
                act.wait_ge(p_in, 16 + 16 * l)
                nc.scalar.activation(PH[:, :, :], P32[:, :, :], ACT.Copy).then_inc(p_hi, 1)
                act.wait_ge(p_split, 2 + 2 * l)

                def ple_projected(m):
                    if m % 4 < 3:
                        act.wait_ge(part_done, part + 66 + 3 * (m // 4) + m % 4 + 1)
                    else:
                        act.wait_ge(unit_done, first + 74 + m // 4 + 3)
                    nc.scalar.activation(rows(PP[:, m, :]), banks(m % 2), ACT.Copy).then_inc(wp_read, 1)

                norm(2 * l + 1, ple_projected)
                act.wait_ge(wp_read, 8 + 8 * l)
                with act.Fori(0, 4) as i:
                    for s in range(2):
                        act.wait_ge(unit_done, 2 * i + s + first + 79)
                        act.wait_ge(gate_added, 2 * i + s + 1 + 10 * l)
                        nc.scalar.activation(rows(SG[s][:, :]), banks(s), ACT.Sigmoid, bias=col_at("ple_b%d" % l, 2 * i + s))\
                          .then_inc(gate_read, 1)

            layer_end(0)
            act.wait_ge(unit_done, 110)
            act.wait_ge(gate_added, 10)
            act.dma_start(XROW, Y[:, :, :]).then_inc(x_out, 16)
            for h in range(2):
                for k in range(8):
                    nc.scalar.activation(row_half(XH[:, k, :], h), row_half(Y[:, k, :], h), ACT.Copy).then_inc(x_hi, 1)
            act.sem_inc(in1_read, 2)
            act.sem_inc(a_probs, 2)
            act.sem_inc(a_scaled, 1)
            act.sem_inc(a_hi, 1)
            for s in range(2):
                act.sem_inc(row1_out[s], 16)
            act.wait_ge(x_out, 16)
            act.wait_ge(in_ready, 1)
            act.wait_ge(x_lo, 16)
            with act.Fori(0, 7) as i:
                for s in range(2):
                    act.wait_ge(unit_done, 2 * i + s + IN1 + 3)
                    act.wait_ge(row1_out[s], 16 * i + 16)
                    nc.scalar.activation(rows(U1[:, s, :]), banks(s), ACT.Copy).then_inc(in1_read, 1)
                for s in range(2):
                    act.wait_ge(shifted, 2 * i + s + 1)
                    act.dma_start(CROW[ds(2 * i + s, 1), :, :].rearrange("a p n -> p (a n)"), DX[:, s, :])\
                       .then_inc(row1_out[s], 16)
            for m, x in enumerate((QA[:, 0, :], QA[:, 1, :], QA[:, 2, :], CR[:, 0, :], CR[:, 1, :], KRW[:, :])):
                act.wait_ge(unit_done, IN1 + 14 + m + 3)
                nc.scalar.activation(rows(x), banks(m % 2), ACT.Copy).then_inc(in1_read, 1)
            for s in range(2):
                act.wait_ge(row1_out[s], 16 * 8)
            act.dma_start(ROPE[:, :, :], io["rope"]).then_inc(mla_in, 16)
            act.dma_start(CCK[:, :, :], io["cache_ckv"]).then_inc(cache_in, 16)
            act.dma_start(KRR[:, NT:NK], io["cache_krope"]).then_inc(kr_cache_in, 16)
            act.wait_ge(in1_read, 22)
            for j in range(5):
                if j >= 2:
                    act.wait_ge(m_sum, j - 1)
                x = QA[:, j, :] if j < 3 else CR[:, j - 3, :]
                nc.scalar.activation(SQD[j % 2][:, :], x, ACT.Square).then_inc(m_square, 1)
            for slot in range(2):
                act.wait_ge(m_sum, 3 + 2 * slot)
                step(nc.scalar.activation(rows(RSD[slot][:, :]), banks(1 - slot), ACT.Ln, bias=EPS[:, 1:2],
                                          scale=1 / 384 if slot == 0 else 1 / 256))
                nc.scalar.activation(RSD[slot][:, :], RSD[slot][:, :], ACT.Exp, scale=-0.5).then_inc(m_root, 1)
            act.wait_ge(cache_in, 16)
            nc.scalar.activation(CH[:, :, NT:NK], CCK[:, :, :], ACT.Copy).then_inc(m_hi, 1)
            for j in range(5):
                act.wait_ge(m_scaled, j + 1)
                h, x = (QAH[:, j, :], QA[:, j, :]) if j < 3 else (CH[:, j - 3, 0:NT], CR[:, j - 3, :])
                nc.scalar.activation(h, x, ACT.Copy).then_inc(m_hi, 1)
            act.dma_start(io["ckv"], CR[:, :, :]).then_inc(c_out, 16)
            act.wait_ge(kr_done, 1)
            act.dma_start(io["krope"], KRR[0:64, 0:NT]).then_inc(kr_out, 16)
            for m in range(6):
                if m % 2:
                    act.wait_ge(unit_done, IN1 + 20 + m // 2 + 3)
                else:
                    act.wait_ge(part_done, 72 + m // 2 + 1)
                nc.scalar.activation(rows(QN[:, m, :] if m < 4 else QR[:, m - 4, :]), banks(m % 2), ACT.Copy)\
                  .then_inc(qkv_read, 1)
            act.wait_ge(c_out, 16)
            act.wait_ge(m_lo, 6)
            for m in range(4):
                if m % 2:
                    act.wait_ge(unit_done, IN1 + 23 + m // 2 + 3)
                else:
                    act.wait_ge(part_done, 75 + m // 2 + 1)
                nc.scalar.activation(rows(KN[:, m, :], KW), banks(m % 2, KW), ACT.Copy).then_inc(qkv_read, 1)
            act.wait_ge(q_rotated, 2)
            for j in range(10):
                if j < 9:
                    act.wait_ge(v_done, j + 1)
                else:
                    act.wait_ge(unit_done, IN1 + 26 + 2)
                nc.scalar.activation(VTOK[:, j, :], PS[:, j % 8, :], ACT.Copy).then_inc(v_read, 1)

            def probs(i, hh, n):
                t0, nq = queries(n)
                s, g = 18 * i + 9 * hh + n, (9 * hh + n) % 2
                nk = 256 if n == 8 else 128 * (n + 1)
                act.wait_ge(a_max, s + 1)
                act.wait_ge(a_turned, s)
                nc.scalar.activation(PB[0:nq, g, 0:nk], PS[0:nq, 2 * g:2 * g + 2, :].rearrange("p b n -> p (b n)")[:, 0:nk],
                                     ACT.Exp, scale=D_SCALE, bias=AST[g][0:nq, 0:1], accum_out=AST[g][0:nq, 1:2])\
                  .then_inc(a_probs, 1)

            def keys(i, hh, n):
                s = 18 * i + 9 * hh + n
                act.wait_ge(a_turned, s + 2)
                act.wait_ge(a_out, s + 1)
                nk = 256 if n == 8 else 128 * min(4, n + 1)
                nc.scalar.activation(PTB[:, 0:nk], PS[:, 4, 0:nk], ACT.Copy).then_inc(a_keys, 1)

            def scaled(i, hh, n):
                t0, nq = queries(n)
                s, g = 18 * i + 9 * hh + n, (9 * hh + n) % 2
                act.wait_ge(a_out, s + 2)
                act.wait_ge(a_inv, s + 1)
                nc.scalar.activation(OB[0:nq, g, :], PS[0:nq, 6, 0:128], ACT.Copy, scale=AST[g][0:nq, 2:3]).then_inc(a_scaled, 1)

            def high_out(i, hh, n):
                t0, nq = queries(n)
                s, own = 18 * i + 9 * hh + n, 64 if n == 8 else 128
                act.wait_ge(a_back, s + 1)
                nc.scalar.activation(XH[:, ds(2 * i + hh + 4, 1), t0:t0 + own].rearrange("p a n -> p (a n)"), PS[:, 7, 0:own],
                                     ACT.Copy).then_inc(a_hi, 1)

            order = [(hh, n) for hh in range(2) for n in range(STEPS)]
            with act.Fori(0, 2) as i:
                act.wait_ge(a_scores, 18 * i + 1)
                nc.scalar.activation(QRS[:, :], QR[:, ds(i, 1), :].rearrange("p a n -> p (a n)"), ACT.Copy)
                for hh in range(2):
                    nc.scalar.activation(QS[:, hh, :], QN[:, ds(2 * i + hh, 1), :].rearrange("p a n -> p (a n)"), ACT.Copy)\
                      .then_inc(q_staged, 1)
                probs(i, 0, 0)
                for x, (hh, n) in enumerate(order):
                    keys(i, hh, n)
                    if x:
                        high_out(i, *order[x - 1])
                    if x + 1 < len(order):
                        probs(i, *order[x + 1])
                    scaled(i, hh, n)
                high_out(i, *order[-1])
            def c_step(name, j, p):
                s = c_act[p]
                level = int(name[1:]) if name[0] in "wt" else 0
                if name == "prep0":
                    act.wait_ge(c_dve[p], C_DVE.at(j, "scan"))
                    nc.scalar.activation(PX[p][:, :, 1:65], CIN[p][:, 12:16, :], ACT.Exp, scale=-DECAY).then_inc(s, 1)
                    nc.scalar.activation(PI_S[p][:, :, :], CIN[p][:, 12:16, :], ACT.Exp, scale=DECAY).then_inc(s, 1)
                elif name == "prep2":
                    act.wait_ge(c_pe[p], C_PE.at(j, "bg"))
                    act.wait_ge(c_dve[p], C_DVE.at(j, "rb"))
                    for h in range(2):
                        last = nc.scalar.activation(BT_B[p][half(h), :, half(h)], per_head(4 * p + 3)[half(h), :, 64:128],
                                                    ACT.Copy, scale=-1.0)
                    last.then_inc(s, 1)
                    act.wait_ge(c_dve[p], C_DVE.at(j, "rk"))
                    for h in range(2):
                        last = nc.scalar.activation(
                            KT_B[p][half(h), :, half(h)].rearrange("p (b m) n -> p b m n", b=2),
                            k_group(p)[half(h), :, :].rearrange("p b (m n) -> p b m n", m=2)[:, :, :, 128:192], ACT.Copy)
                    last.then_inc(s, 1)
                elif name == "prep3":
                    act.wait_ge(c_pe[p], C_PE.at(j, "vt"))
                    nc.scalar.activation(VT_B[p][:, :, :], per_head(4 * p + 2), ACT.Copy).then_inc(s, 1)
                elif name[0] == "w":
                    act.wait_ge(c_pe[p], C_PE.at(j, "lw%d" % level))
                    nc.scalar.activation(W_B[p][:, :, :], per_head(4 * p + 1), ACT.Copy).then_inc(s, 1)
                elif name == "carry1":
                    act.wait_ge(c_pe[p], C_PE.at(j, "x"))
                    nc.scalar.activation(X_B[p][:, :, :], per_head(4 * p + 1), ACT.Copy).then_inc(s, 1)
                elif name == "carry2":
                    act.wait_ge(c_pe[p], C_PE.at(j, "u"))
                    nc.scalar.activation(U_B[p][:, :, :], per_head(4 * p + 2), ACT.Copy).then_inc(s, 1)
                elif name == "carry3":
                    act.wait_ge(c_pe[p], C_PE.at(j, "o"))
                    nc.scalar.activation(CO[:, :, chunk_columns(j, p)], stacked(p, 1, 0), ACT.Copy).then_inc(s, 1)

            act.wait_ge(a_hi, 73)
            act.wait_ge(e_wg, 16)
            nc.scalar.activation(WG[0:64, 0, :], WG[0:64, 0, :], ACT.Tanh).then_inc(wg_ready, 1)
            nc.scalar.activation(WG[:, 1, :], WG[:, 1, :], ACT.Sigmoid).then_inc(wg_ready, 1)
            for m in range(4):
                p = m % 2
                if m >= 2:
                    act.wait_ge(e_out[p], 48)
                act.wait_ge(e_pe, E_PE.at(m, "w") - 1)
                nc.scalar.activation(rows(PREP[p][:, SIGR, :]), banks((5 * m) % 2), ACT.Sigmoid, bias=col("c_w0", m))\
                  .then_inc(e_act, 1)
                act.wait_ge(e_pe, E_PE.at(m, "a") - 1)
                nc.scalar.activation(rows(PREP[p][:, KKAR, :]), banks((5 * m + 1) % 2), ACT.Sigmoid, bias=col("c_a0", m))\
                  .then_inc(e_act, 1)
                act.wait_ge(e_pe, E_PE.at(m, "g") - 1)
                nc.scalar.activation(rows(BG[p][:, GR, :]), banks((5 * m + 2) % 2), ACT.Copy).then_inc(e_act, 1)
                act.wait_ge(e_dve, E_DVE.at(m, "kk0") - 1)
                nc.scalar.activation(NORM[p][:, :], PREP[p][:, KKR, :], ACT.Square).then_inc(e_act, 1)
                act.wait_ge(e_pe, E_PE.at(m, "norm") - 1)
                nc.scalar.activation(rows(NORM[p][:, :]), banks((5 * m + 3) % 2), ACT.Ln, bias=EPS[:, 1:2]).then_inc(e_act, 1)
                act.wait_ge(e_act, E_ACT.at(m, "ln") - 1)
                nc.scalar.activation(NORM[p][:, :], NORM[p][:, :], ACT.Exp, scale=-0.5).then_inc(e_act, 1)
            act.wait_ge(c_ready, 2)
            run_chunks(act, c_step)
            def f_root(m):
                act.wait_ge(f_dve, F_DVE.at(m, "centred"))
                nc.scalar.activation(SQC[m % 2][:, :], CO[:, m, :], ACT.Square).then_inc(f_act, 1)
                act.wait_ge(f_var, m + 1)
                nc.scalar.activation(rows(INC[m % 2][:, :]), banks(1), ACT.Ln, bias=EPS[:, 2:3], scale=1 / 64).then_inc(f_act, 1)
                act.wait_ge(f_act, F_ACT.at(m, "ln"))
                nc.scalar.activation(INC[m % 2][:, :], INC[m % 2][:, :], ACT.Exp, scale=-0.5).then_inc(f_act, 1)

            f_root(0)
            f_root(1)
            for m in range(4):
                act.wait_ge(f_dve, F_DVE.at(m, "gated"))
                nc.scalar.activation(XH[:, m, :], CO[:, m, :], ACT.Copy).then_inc(f_act, 1)
                if m < 2:
                    f_root(m + 2)
            for n, (out, p, j) in enumerate((("s_c_p", 1, (0, 7)), ("s_c_s", 0, C_SAMPLE))):
                act.wait_ge(c_dve[p], C_DVE.at(j, "m"))
                for h in range(2):
                    act.dma_start(io[out][half(h)], MB[n][half(h), :, half(h)]).then_inc(c_state_out, 16)
            act.wait_ge(c_state_out, 64)
            act.wait_ge(f_dve, F_DVE.at(3, "lo"))
            act.dma_start(XR[:, :, :], XROW).then_inc(x_back, 16)
            layer_end(1)
            act.wait_ge(gate_added, 20)
            act.dma_start(io["y"], Y[:, :, :]).then_inc(y_out, 16)
            act.wait_ge(y_out, 16)
            act.wait_ge(kr_out, 16)

        @block.vector
        def _(dve):
            step = Steps(dve, dve_step)
            dve.sem_inc(conv_done, 2)
            dve.sem_inc(rg_vec, 1)
            dve.sem_inc(norm_done, 2)
            for n, e in enumerate((1e-5, 1e-6, 64e-5, 0.0, 1e-34)):
                nc.vector.memset(EPS[:, n:n + 1], e).then_inc(eps_set, 1)
            dve.wait_ge(params_in, 32)
            step(nc.vector.tensor_copy(WBAH[:, :], small("w_beta_alpha", 64)))
            nc.vector.tensor_tensor(WBAL[:, :], small("w_beta_alpha", 64), WBAH[:, :], ALU.subtract).then_inc(ba_split, 1)
            lam = col4("a_lambda")
            nc.vector.scalar_tensor_tensor(LAM[:, 4:8], lam, -1.0, lam, ALU.mult, ALU.max).then_inc(lam_vec, 1)
            step(nc.vector.tensor_scalar(LAM[:, 0:4], lam, -1.0, 0.0, ALU.mult, ALU.max))
            for k in range(8):
                dve.wait_ge(xh_ready, k + 1)
                nc.vector.tensor_tensor(XL[:, k, :], X32[:, k, :], XH[:, k, :], ALU.subtract).then_inc(xl_ready, 1)
            dve.wait_ge(ba_done, 2)
            dve.wait_ge(ba_act, 1)
            step(nc.vector.tensor_tensor(GTMP[:, 0, :].rearrange("p (c h) -> p c h", h=4), PSBA[:, :, 4:8],
                                         small("dt_bias", 36).rearrange("p (c h) -> p c h", h=4), ALU.add))
            nc.vector.scalar_tensor_tensor(GTMP[:, 1, :], GTMP[:, 0, :], -1.0, GTMP[:, 0, :], ALU.mult, ALU.max).then_inc(ba_vec, 1)
            dve.wait_ge(ba_act, 4)
            step(nc.vector.scalar_tensor_tensor(GTMP[:, 0, :], GTMP[:, 0, :], 0.0, GTMP[:, 1, :], ALU.max, ALU.add))
            step(nc.vector.scalar_tensor_tensor(GB[:, :], GTMP[:, 0, :], -1.0, GTMP[:, 2, :], ALU.mult, ALU.mult))
            nc.vector.memset(GB[64:128, 32:36], 0.0).then_inc(g_ready, 1)
            dve.wait_ge(lam_act, 2)
            step(nc.vector.tensor_tensor(LAM[:, 0:4], LAM[:, 0:4], LAM[:, 4:8], ALU.add))
            step(nc.vector.tensor_scalar(LAM[:, 12:16], LAM[:, 0:4], 8.0, None, ALU.mult))
            step(nc.vector.tensor_scalar(LAM[:, 8:12], LAM[:, 0:4], -8.0, None, ALU.mult))

            def convolve0(s, j, read):
                dve.wait_ge(slot_act, read)
                step(nc.vector.tensor_copy(U0[:, s, S0 - 3:S0], SMALL[:, ds(sp_["hist_conv0"] + 3 * j, 3)]))
                step(nc.vector.tensor_copy(KEPT[:, ds(op["conv0"] + 6 * j, 3)], U0[:, s, S0 + 61:S0 + 64]))
                step(nc.vector.tensor_copy(KEPT[:, ds(op["conv0"] + 3 + 6 * j, 3)], U0[:, s, NT - 3:NT]))
                y = XCQ[:, ds(j, 1), 4:NT].rearrange("p a n -> p (a n)")
                for k in (1, 2):
                    step(nc.vector.scalar_tensor_tensor(y, U0[:, s, 4 - k:NT - k], col_at("conv0_w%d" % (3 - k), j),
                                                        y, ALU.mult, ALU.add))
                nc.vector.scalar_tensor_tensor(y, U0[:, s, 1:NT - 3], col_at("conv0_w0", j), y,
                                               ALU.mult, ALU.add).then_inc(conv_done, 1)

            with dve.Fori(0, 2) as i:
                step.enter(i, 2 * 5)
                for s in range(2):
                    convolve0(s, 2 * i + s, in_unit(4 + s) + 2 * i)
            step.leave(2)
            dve.wait_ge(ba_copied, 2)
            step(nc.vector.scalar_tensor_tensor(NBEG[:, :], EGC[:, :], -1.0, BETA36[:, :], ALU.mult, ALU.mult))
            with dve.Fori(0, 4) as m:
                step.enter(m, 2 * 5 + 9)
                for s in range(2):
                    convolve0(s, 2 * m + s + 4, in_unit(8 + s) + 2 * m)
                dve.wait_ge(rg_read, 2 * m + 4)
                step(nc.vector.tensor_tensor(MIX[1][:, 4:NT], MIX[1][:, 4:NT],
                                             XCQ[:, ds(m, 1), 4:NT].rearrange("p a n -> p (a n)"), ALU.mult))
                step(nc.vector.tensor_copy(LAM[:, 0:1], SMALL[:, ds(sp_["h0"] + m, 1)]))
                dve.wait_ge(rg_act, 6 * m + 4)
                step(nc.vector.tensor_tensor(MIX[1][:, 4:NT], MIX[1][:, 4:NT], MIX[2][:, 4:NT], ALU.mult))
                dve.wait_ge(rg_act, 6 * m + 5)
                step(nc.vector.tensor_tensor(MIX[1][:, 4:NT], MIX[1][:, 4:NT], MIX[3][:, 4:NT], ALU.mult))
                dve.wait_ge(rg_act, 6 * m + 6)
                step(nc.vector.tensor_tensor_scan(MIX[2][:, S0:S0 + 64], MIX[0][:, S0:S0 + 64], MIX[1][:, S0:S0 + 64],
                                                  LAM[:, 0:1], ALU.mult, ALU.add))
                step(nc.vector.tensor_tensor_scan(MIX[2][:, P0:NT], MIX[0][:, P0:NT], MIX[1][:, P0:NT], 0.0,
                                                  ALU.mult, ALU.add))
                for n, c in enumerate((S0 + 63, NT - 1)):
                    step(nc.vector.tensor_copy(KEPT[:, ds(op["h"] + n + 2 * m, 1)], MIX[2][:, c:c + 1]))
                step(nc.vector.memset(MIX[2][:, S0 + 64:P0], 0.0))
                dve.wait_ge(gate_in, 16 * m + 16)
                nc.vector.tensor_tensor(XCQ[:, ds(m, 1), 4:NT].rearrange("p a n -> p (a n)"), MIX[2][:, 4:NT],
                                        MIX[4][:, 4:NT], ALU.mult).then_inc(rg_vec, 1)
            step.leave(4)
            with dve.Fori(0, 4) as n:
                step.enter(n, 5)
                convolve0(0, 12 + n, in_unit(16) + 2 * n)
                for s in range(2):
                    dve.wait_ge(norm_root, 2 * n + s + 1)
                    x = XCQ[:, ds(4 + 2 * n + s, 1), 4:NT].rearrange("p a n -> p (a n)")
                    nc.vector.tensor_tensor(x, x, RN[2 + s][:, 4:NT], ALU.mult).then_inc(norm_done, 1)
            step.leave(4)
            dve.wait_ge(row_out[1], 112)
            step(nc.vector.memset(SP[:, :, :], 0.0))

            def g_step(name, j, p):
                s, b, sample = gdn_dve[p], 4 * p, is_sample(j, G_SAMPLE)
                state = SS if sample else SP
                here = tile_place(j, p)
                if name == "decays":
                    if not starts_set(j):
                        dve.wait_ge(gdn_pe[p], G_PE.before(j))
                    nc.vector.tensor_tensor(LM[p][:, :, :], heads_of(UPPER), heads_of(GB[:, here]), ALU.mult).then_inc(s, 1)
                    if sample:
                        for x in (KT, QT, VT):
                            last = nc.vector.memset(x[0][:, :, 64:128], 0.0)
                        last.then_inc(pad_zeroed, 1)
                elif name == "diffs":
                    dve.wait_ge(gdn_pe[p], G_PE.at(j, "rows"))
                    step(nc.vector.tensor_tensor(DA[p][:, :, :], per_head(b), heads_of(GC[:, here]), ALU.subtract))
                    nc.vector.tensor_tensor(KOC[p][:, :], per_head(b)[:, :, 127], GC[:, here], ALU.subtract)
                    step(nc.vector.tensor_scalar(DB[p][:, :, :], DA[p][:, :, :], 0.0, None, ALU.max))
                    nc.vector.tensor_scalar(DA[p][:, :, :], DA[p][:, :, :], 0.0, None, ALU.min).then_inc(s, 1)
                elif name == "grams":
                    dve.wait_ge(gdn_act[p], G_ACT.at(j, "exps"))
                    step(nc.vector.tensor_tensor(DB[p][:, :, :], DB[p][:, :, :], heads_of(BETA36[:, here]), ALU.mult))
                    dve.wait_ge(gdn_pe[p], G_PE.at(j, "gram"))
                    nc.vector.tensor_tensor(DB[p][:, :, :], per_head(b + 1), DB[p][:, :, :], ALU.mult).then_inc(s, 1)
                    dve.wait_ge(s, G_DVE.at(j, "lower"))
                    nc.vector.tensor_tensor(LM[p][:, :, :], DB[p][:, :, :], heads_of(level_mask(0)), ALU.mult).then_inc(s, 1)
                elif name == "blocks":
                    dve.wait_ge(s, G_DVE.at(j, "m0"))
                    nc.vector.tensor_tensor(TA[p][:, :, :], heads_of(IDENT), LM[p][:, :, :], ALU.subtract).then_inc(s, 1)
                    dve.wait_ge(gdn_pe[p], G_PE.at(j, "m_turned"))
                    nc.vector.tensor_tensor(TT[p][:, :, :], heads_of(IDENT), per_head(b + 1), ALU.subtract).then_inc(s, 1)
                    dve.wait_ge(gdn_pool[p], G_POOL.at(j, "upper"))
                    nc.vector.tensor_tensor(DA[p][:, :, :], per_head(b + 2), DA[p][:, :, :], ALU.mult).then_inc(s, 1)
                elif name[0] == "t":
                    dve.wait_ge(gdn_pe[p], G_PE.at(j, "tt" + name[1]))
                    nc.vector.tensor_tensor(TT[p][:, :, :], TT[p][:, :, :], per_head(b + 2), ALU.subtract).then_inc(s, 1)
                    if name != "t6":
                        dve.wait_ge(gdn_pe[p], G_PE.at(j, "ta" + name[1]))
                        nc.vector.tensor_tensor(TA[p][:, :, :], TA[p][:, :, :], per_head(b + 3), ALU.subtract).then_inc(s, 1)
                    else:
                        dve.wait_ge(gdn_pe[p], G_PE.at(j, "ks"))
                        step(nc.vector.tensor_tensor(RR[p][:, :, :], per_head(b), heads_of(NBEG[:, here]), ALU.mult))
                        dve.wait_ge(gdn_act[p], G_ACT.at(j, "vb"))
                        nc.vector.tensor_tensor(RR[p][:, :, :], RR[p][:, :, :], VB[p][:, :, :], ALU.add).then_inc(s, 1)
                elif name == "carry2":
                    dve.wait_ge(gdn_pe[p], G_PE.at(j, "o"))
                    step(nc.vector.tensor_tensor(state[:, :, :], state[:, :, :],
                                                 EG[p][:, :, 127:128].to_broadcast([128, 4, 128]), ALU.mult))
                    dve.wait_ge(gdn_pe[p], G_PE.at(j, "s"))
                    nc.vector.tensor_tensor(state[:, :, :], state[:, :, :], per_head(b + 3), ALU.add).then_inc(s, 1)

            run_chunks(dve, g_step, G_FIRST, G_SECOND, G_SAMPLE,
                       lambda i: step.enter(i, 2 * 5, 1), lambda: step.leave(4))
            dve.wait_ge(gdn_act[1], G_ACT.at((0, 3), "out"))
            dve.wait_ge(gdn_act[0], G_ACT.at(G_SAMPLE, "out"))
            nc.vector.memset(OT[:, :, 0:S0], 0.0)
            nc.vector.memset(OT[:, :, S0 + 64:P0], 0.0).then_inc(o_zeroed, 1)

            def o_lo(h):
                dve.wait_ge(xh_ready, 8 + h + 1)
                nc.vector.tensor_tensor(XL[:, 4 + h, :], OT[:, h, :], XH[:, 4 + h, :], ALU.subtract).then_inc(mix_ready[0], 1)

            dve.wait_ge(z_in, 16)
            for h in range(4):
                dve.wait_ge(o_root, h + 1)
                step(nc.vector.scalar_tensor_tensor(OT[:, h, :], OT[:, h, :], col("b_norm_g"), RN[2 + h % 2][:, :],
                                                    ALU.mult, ALU.mult))
                nc.vector.tensor_tensor(OT[:, h, :], OT[:, h, :], ZT[:, h, :], ALU.mult).then_inc(o_gated, 1)
            for h in (2, 3):
                o_lo(h)

            def norm(n, name):
                for h in range(2):
                    dve.wait_ge(ln_mean, h + 1 + 2 * n)
                    for k in range(8):
                        y = rows(row_half(Y[:, k, :], h))
                        nc.vector.scalar_tensor_tensor(y, bank_half(0, h), -1 / 1024, y, ALU.mult, ALU.add).then_inc(ln_sub, 1)

                def affine(h, k):
                    y = row_half(Y[:, k, :], h)
                    dve.wait_ge(ln_scaled, 8 * h + k + 1 + 16 * n)
                    nc.vector.tensor_scalar(y, y, col("ln_%s_g%d" % (name, n // 2), k), col("ln_%s_b%d" % (name, n // 2), k),
                                            ALU.mult, ALU.add).then_inc(ln_normed, 1)

                for h in range(2):
                    dve.wait_ge(ln_root, h + 1 + 2 * n)
                    dve.wait_ge(ln_sub, 8 + 8 * h + 16 * n)
                    for k in range(8):
                        y = row_half(Y[:, k, :], h)
                        dve.wait_ge(ln_sq, 8 * h + k + 1 + 16 * n)
                        nc.vector.tensor_tensor(y, y, row_half(RS, h), ALU.mult).then_inc(ln_scaled, 1)
                        if k:
                            affine(h, k - 1)
                    affine(h, 7)
                    if h == 0:
                        gaps(ln_lo, 8 + 16 * n, gaps_zeroed)
                for k in range(8 - DVE_LOWS, 8):
                    dve.wait_ge(ln_hi, 8 + k + 1 + 16 * n)
                    nc.vector.tensor_tensor(row_half(XL[:, k, :], 1), row_half(Y[:, k, :], 1), row_half(XH[:, k, :], 1),
                                            ALU.subtract).then_inc(ln_lo, 1)

            def clear_sum(n):
                nc.vector.memset(YSUM[n % 2][:, :], 0.0).then_inc(ln_total, 1)

            def sum_up(n, m, y):
                dve.wait_ge(ln_total, 9 * n + 1 + m)
                nc.vector.tensor_tensor(YSUM[n % 2][:, :], YSUM[n % 2][:, :], y, ALU.add).then_inc(ln_total, 1)

            def gaps(s, value, done):
                dve.wait_ge(s, value)
                for x in (XH, XL):
                    nc.vector.memset(x[:, :, 0:S0].bitcast(F32), 0.0)
                    last = nc.vector.memset(x[:, :, S0 + 64:P0].bitcast(F32), 0.0)
                last.then_inc(done, 1)

            def convolve(l, g, t):
                dve.wait_ge(up_read, 4 * g + t + 2 + 45 * l)
                f = 2 * g + (t if t < 2 else 20 + t)
                u, y = UF[:, t % 2, :], CB[:, t, 4:NT]
                hist, kept = sp_["hist_ffn"] + 88 * l + 2 * f, op["ffn"] + 176 * l + 4 * f
                step(nc.vector.tensor_copy(u[:, S0 - 2:S0], SMALL[:, ds(hist, 2)]))
                nc.vector.tensor_copy(KEPT[:, ds(kept, 2)], u[:, S0 + 62:S0 + 64])
                nc.vector.tensor_copy(KEPT[:, ds(kept + 2, 2)], u[:, NT - 2:NT])
                step(nc.vector.scalar_tensor_tensor(y, u[:, 3:NT - 1], col_at("ffn_w1%d" % l, f), y, ALU.mult, ALU.add))
                nc.vector.scalar_tensor_tensor(y, u[:, 2:NT - 2], col_at("ffn_w0%d" % l, f), y, ALU.mult, ALU.add)\
                  .then_inc(ffn_conv, 1)

            def multiply(l, g, tiles=range(2)):
                for j in tiles:
                    dve.wait_ge(ffn_silu, 2 * g + j + 1 + 22 * l)
                    dve.wait_ge(ffn_conv, 4 * g + 2 + j + 3 + 46 * l)
                    nc.vector.tensor_tensor(CB[:, 2 + j, :], CB[:, 2 + j, :], CB[:, j, :], ALU.mult).then_inc(ffn_mul, 1)

            def low(l, g):
                for j in range(2):
                    dve.wait_ge(h_hi, 2 * g + j + 1 + 22 * l)
                    last = nc.vector.tensor_tensor(HL[:, j, :], CB[:, 2 + j, :], HH[:, j, :], ALU.subtract)
                last.then_inc(h_done, 1)

            def add_down(l, g, unit, tiles=range(8), first=False, last=False):
                for m in tiles:
                    if m % 4 < 3:
                        dve.wait_ge(part_done, 6 * g + OUT_PART[l] + 3 * (m // 4) + m % 4 + 1)
                    else:
                        dve.wait_ge(unit_done, unit + m // 4 + 3)
                    if first:
                        nc.vector.scalar_tensor_tensor(rows(Y[:, m, :]), rows(Y[:, m, :]), ALPHA, banks(m % 2),
                                                       ALU.mult, ALU.add).then_inc(down_read, 1)
                    else:
                        nc.vector.tensor_tensor(rows(Y[:, m, :]), rows(Y[:, m, :]), banks(m % 2), ALU.add)\
                          .then_inc(down_read, 1)
                    if last:
                        dve.wait_ge(down_read, 8 * g + m + 3 + 90 * l)
                        sum_up(2 * l + 1, m, Y[:, m, :])

            def layer_end(l):
                first = OUT_UNIT[l]
                dve.sem_inc(out_read, 2)
                dve.sem_inc(down_read, 2)
                dve.sem_inc(ffn_conv, 2)
                dve.sem_inc(h_done, 1)
                dve.sem_inc(gate_added, 2)
                dve.wait_ge(x_back, 16 + 16 * l)
                clear_sum(2 * l)
                with dve.Fori(0, 4) as i:
                    for s in range(2):
                        dve.wait_ge(unit_done, 2 * i + s + first + 3)
                        nc.vector.scalar_tensor_tensor(
                            rows(Y[:, ds(2 * i + s, 1), :].rearrange("p a n -> p (a n)")),
                            rows(XR[:, ds(2 * i + s, 1), :].rearrange("p a n -> p (a n)")), ALPHA, banks(s),
                            ALU.mult, ALU.add).then_inc(out_read, 1)
                        dve.wait_ge(out_read, 2 * i + s + 3 + 10 * l)
                        sum_up(2 * l, 2 * i + s, Y[:, ds(2 * i + s, 1), :].rearrange("p a n -> p (a n)"))
                norm(2 * l, "mix")
                for t in range(4):
                    convolve(l, 0, t)
                multiply(l, 0)
                low(l, 0)

                def chunk(g, first=False):
                    unit = 6 * g + first_unit + 10
                    for t in range(3):
                        convolve(l, g, t)
                    dve.wait_ge(down_read, 8 * g - 6 + 90 * l)
                    add_down(l, g - 1, unit, range(0, 1), first)
                    convolve(l, g, 3)
                    add_down(l, g - 1, unit, range(1, 3), first)
                    multiply(l, g, [0])
                    add_down(l, g - 1, unit, range(3, 5), first)
                    multiply(l, g, [1])
                    add_down(l, g - 1, unit, range(5, 8), first)
                    low(l, g)

                first_unit = first
                chunk(1, True)
                with dve.Fori(2, 11) as g:
                    step.enter(g - 2, 8)
                    chunk(g)
                step.leave(9)
                dve.wait_ge(down_read, 82 + 90 * l)
                clear_sum(2 * l + 1)
                add_down(l, 10, first + 72, range(0, 5), last=True)
                dve.wait_ge(p_hi, 1 + l)
                for j in range(2):
                    nc.vector.tensor_tensor(PL[:, j, :], P32[:, j, :], PH[:, j, :], ALU.subtract).then_inc(p_split, 1)
                add_down(l, 10, first + 72, range(5, 8), last=True)
                norm(2 * l + 1, "ffn")
                with dve.Fori(0, 4) as i:
                    step.enter(i, 2)
                    for s in range(2):
                        m = ds(2 * i + s, 1)
                        dve.wait_ge(gate_read, 2 * i + s + 3 + 10 * l)
                        dve.wait_ge(wp_read, 8 + 8 * l)
                        step(nc.vector.tensor_tensor(SG[s][:, :], SG[s][:, :],
                                                     PP[:, m, :].rearrange("p a n -> p (a n)"), ALU.mult))
                        y = Y[:, m, :].rearrange("p a n -> p (a n)")
                        nc.vector.tensor_tensor(y, y, SG[s][:, :], ALU.add).then_inc(gate_added, 1)
                step.leave(4)

            layer_end(0)
            for h in range(2):
                for k in range(8):
                    dve.wait_ge(x_hi, 8 * h + k + 1)
                    nc.vector.tensor_tensor(row_half(XL[:, k, :], h), row_half(Y[:, k, :], h), row_half(XH[:, k, :], h),
                                            ALU.subtract).then_inc(x_lo, 1)
                if h == 0:
                    gaps(x_lo, 8, in_ready)
            dve.wait_ge(x_out, 16)
            with dve.Fori(0, 7) as i:
                step.enter(i, 10)
                for s in range(2):
                    dve.wait_ge(in1_read, 2 * i + s + 3)
                    step(nc.vector.tensor_copy(U1[:, s, S0 - 1:S0], SMALL[:, ds(sp_["hist_shift"] + 2 * i + s, 1)]))
                    kept = op["shift"] + 4 * i + 2 * s
                    step(nc.vector.tensor_copy(KEPT[:, ds(kept, 1)], U1[:, s, S0 + 63:S0 + 64]))
                    step(nc.vector.tensor_copy(KEPT[:, ds(kept + 1, 1)], U1[:, s, NT - 1:NT]))
                    step(nc.vector.memset(DX[:, s, 0:4], 0.0))
                    step(nc.vector.tensor_tensor(DX[:, s, 4:NT], U1[:, s, 3:NT - 1], U1[:, s, 4:NT], ALU.subtract))
                    nc.vector.scalar_tensor_tensor(DX[:, s, 4:NT], DX[:, s, 4:NT], col_at("c_mu", 2 * i + s), U1[:, s, 4:NT],
                                                   ALU.mult, ALU.add).then_inc(shifted, 1)
            step.leave(7)
            def rotate(out, x, slot, tmp, done):
                step(nc.vector.tensor_tensor(rows(tmp), banks(slot), rows(ROPE[:, 1, :]), ALU.mult))
                step(nc.vector.tensor_tensor(out, x, ROPE[:, 0, :], ALU.mult))
                nc.vector.tensor_tensor(out, out, tmp, ALU.add).then_inc(done, 1)

            dve.wait_ge(mla_in, 16)
            dve.wait_ge(swapped, 1)
            rotate(KRR[:, 0:NT], KRW[:, :], 0, TK[:, :], kr_done)
            for j in range(5):
                x, g = (QA[:, j, :], col("d_qa_g", j)) if j < 3 else (CR[:, j - 3, :], col("d_kva_g", j - 3))
                dve.wait_ge(m_root, 1 + j // 3)
                nc.vector.scalar_tensor_tensor(x, x, g, RSD[j // 3][:, :], ALU.mult, ALU.mult).then_inc(m_scaled, 1)
            dve.wait_ge(m_hi, 1)
            nc.vector.tensor_tensor(CL[:, :, NT:NK], CCK[:, :, :], CH[:, :, NT:NK], ALU.subtract).then_inc(m_lo, 1)
            for j in range(5):
                dve.wait_ge(m_hi, j + 2)
                l, x, h = (QAL[:, j, :], QA[:, j, :], QAH[:, j, :]) if j < 3 else (
                    CL[:, j - 3, 0:NT], CR[:, j - 3, :], CH[:, j - 3, 0:NT])
                nc.vector.tensor_tensor(l, x, h, ALU.subtract).then_inc(m_lo, 1)

            dve.wait_ge(kr_out, 16)
            for r in range(2):
                dve.wait_ge(swapped, 2 + r)
                dve.wait_ge(qkv_read, 10)
                rotate(QR[:, r, :], QR[:, r, :], r, TQ[r][:, :], q_rotated)

            def top(i, hh, n):
                t0, nq = queries(n)
                s, g = 18 * i + 9 * hh + n, (9 * hh + n) % 2
                nk = 256 if n == 8 else 128 * (n + 1)
                dve.wait_ge(a_scores, s + 2)
                dve.wait_ge(a_scaled, s)
                sc = PS[0:nq, 2 * g:2 * g + 2, :].rearrange("p b n -> p (b n)")
                if n < 8:
                    step(nc.vector.memset(sc[0:64, nk - 64:nk], -1e30))
                else:
                    step(nc.vector.memset(sc[:, nk - 64:nk], -1e30))
                step(nc.vector.tensor_reduce(AST[g][0:nq, 3:4], sc[:, 0:nk], AX.X, ALU.max))
                nc.vector.tensor_scalar(AST[g][0:nq, 0:1], AST[g][0:nq, 3:4], -D_SCALE, None, ALU.mult).then_inc(a_max, 1)

            def keys2(i, hh, n):
                t0, nq = queries(n)
                s, g = 18 * i + 9 * hh + n, (9 * hh + n) % 2
                dve.wait_ge(a_probs, s + 3)
                nc.vector.reciprocal(AST[g][0:nq, 2:3], AST[g][0:nq, 1:2]).then_inc(a_inv, 1)
                if 4 <= n < 8:
                    dve.wait_ge(a_turned, s + 2)
                    dve.wait_ge(a_out, s + 1)
                    nk = 128 * (n - 3)
                    nc.vector.tensor_copy(PTB[:, 512:512 + nk], PS[:, 5, 0:nk]).then_inc(a_keys2, 1)

            def low_out(i, hh, n):
                t0, nq = queries(n)
                s = 18 * i + 9 * hh + n
                dve.wait_ge(a_hi, 2 * s + 2)
                m, own = ds(2 * i + hh + 4, 1), 64 if n == 8 else 128
                nc.vector.tensor_tensor(XL[:, m, t0:t0 + own].rearrange("p a n -> p (a n)"), PS[:, 7, 0:own],
                                        XH[:, m, t0:t0 + own].rearrange("p a n -> p (a n)"), ALU.subtract).then_inc(a_hi, 1)

            order = [(hh, n) for hh in range(2) for n in range(STEPS)]
            with dve.Fori(0, 2) as i:
                step.enter(i, 2 * 9 * 2)
                top(i, 0, 0)
                for x, (hh, n) in enumerate(order):
                    if x + 1 < len(order):
                        top(i, *order[x + 1])
                    keys2(i, hh, n)
                    if x:
                        low_out(i, *order[x - 1])
                low_out(i, *order[-1])
            step.leave(2)
            def level_blocks(l, p):
                return nc.vector.tensor_tensor(LM_B[p][:, :, :], per_head(4 * p), heads_of(level_mask(l)), ALU.mult)

            def c_step(name, j, p):
                s = c_dve[p]
                level = int(name[1:]) if name[0] in "wt" else 0
                r, k, kk, kka = [CIN[p][:, n:n + 4, :] for n in (0, 8, 16, 20)]
                if name == "prep0":
                    dve.wait_ge(c_in[p], 48 * j[0] + 48 + 48 * j[1])
                    decay = CIN[p][:, 12:16, :].rearrange("p m n -> p (m n)")
                    nc.vector.tensor_tensor_scan(decay, RUN[:, :], decay, 0.0, ALU.mult, ALU.add).then_inc(s, 1)
                elif name == "prep1":
                    dve.wait_ge(c_act[p], C_ACT.at(j, "pi"))
                    nc.vector.tensor_tensor(ARI[p][:, :, 0:64], kk, PX[p][:, :, 0:64], ALU.mult).then_inc(s, 1)
                    nc.vector.tensor_tensor(B_S[p][:, :, :], kka, PI_S[p][:, :, :], ALU.mult).then_inc(s, 1)
                    for h in range(2):
                        last = nc.vector.tensor_tensor(K_B[p][half(h), :, half(h)], k[half(h), :, :],
                                                       PI_S[p][half(h), :, :], ALU.mult)
                    last.then_inc(s, 1)
                    nc.vector.tensor_tensor(ARI[p][:, :, 64:128], r, PX[p][:, :, 1:65], ALU.mult).then_inc(s, 1)
                elif name == "prep2":
                    dve.wait_ge(c_pe[p], C_PE.at(j, "l"))
                    level_blocks(0, p).then_inc(s, 1)
                    dve.wait_ge(s, C_DVE.at(j, "lm0"))
                    nc.vector.tensor_tensor(TA_B[p][:, :, :], heads_of(IDENT), LM_B[p][:, :, :], ALU.subtract).then_inc(s, 1)
                    dve.wait_ge(c_pe[p], C_PE.at(j, "bg"))
                    upper = small("pair_upper", 64)
                    nc.vector.scalar_tensor_tensor(RB_S[p][:, :, :], per_head(4 * p + 3)[:, :, 0:64], -1.0, pairs_of(upper),
                                                   ALU.mult, ALU.mult).then_inc(s, 1)
                    for h in range(2):
                        strict = small("pair_strict", 64)[half(h), :].unsqueeze(1).unsqueeze(1).to_broadcast([64, 2, 2, 64])
                        last = nc.vector.tensor_tensor(
                            AK_B[p][half(h), :, half(h)].rearrange("p (b m) n -> p b m n", b=2),
                            k_group(p)[half(h), :, :].rearrange("p b (m n) -> p b m n", m=2)[:, :, :, 0:64], strict, ALU.mult)
                    last.then_inc(s, 1)
                    nc.vector.tensor_tensor(
                        RK_S[p][:, :, :].rearrange("p (b m) n -> p b m n", b=2),
                        k_group(p).rearrange("p b (m n) -> p b m n", m=2)[:, :, :, 64:128],
                        upper.unsqueeze(1).unsqueeze(1).to_broadcast([128, 2, 2, 64]), ALU.mult).then_inc(s, 1)
                elif name == "prep3":
                    dve.wait_ge(c_pe[p], C_PE.at(j, "mt"))
                    nc.vector.tensor_tensor(TT_B[p][:, :, :], heads_of(IDENT), per_head(4 * p + 1), ALU.subtract).then_inc(s, 1)
                    dve.wait_ge(s, C_DVE.at(j, "ta0"))
                    level_blocks(1, p).then_inc(s, 1)
                elif name[0] == "w":
                    if level < 5:
                        dve.wait_ge(c_pe[p], C_PE.at(j, "lw%d" % level))
                        level_blocks(level + 1, p).then_inc(s, 1)
                elif name[0] == "t":
                    dve.wait_ge(c_pe[p], C_PE.at(j, "tt%d" % level))
                    nc.vector.tensor_tensor(TT_B[p][:, :, :], TT_B[p][:, :, :], per_head(4 * p + 2), ALU.subtract).then_inc(s, 1)
                    if level < 5:
                        dve.wait_ge(c_pe[p], C_PE.at(j, "ta%d" % level))
                        nc.vector.tensor_tensor(TA_B[p][:, :, :], TA_B[p][:, :, :], per_head(4 * p + 3), ALU.subtract)\
                            .then_inc(s, 1)
                elif name == "carry3":
                    state = MB[is_sample(j)]
                    dve.wait_ge(c_pe[p], C_PE.at(j, "m"))
                    nc.vector.tensor_tensor(state[:, :, :], state[:, :, :], per_head(4 * p + 3), ALU.add).then_inc(s, 1)
                    dve.wait_ge(s, C_DVE.at(j, "m0"))
                    nc.vector.tensor_tensor(state[:, :, :], state[:, :, :], PX[p][:, :, 64:65].to_broadcast([128, 4, 128]),
                                            ALU.mult).then_inc(s, 1)

            dve.wait_ge(a_hi, 73)
            for m in range(4):
                p = m % 2
                r, k, v = [RKV[p][:, n, :] for n in range(3)]
                kk, k2, kka, x = PREP[p][:, KKR, :], PREP[p][:, K2R, :], PREP[p][:, KKAR, :], NORM[p][:, :]
                dve.wait_ge(e_in[p], 16 * (m // 2) + 16)
                if m >= 2:
                    dve.wait_ge(e_out[p], 48)
                nc.vector.tensor_scalar(kk, k, col("c_k_k", m), None, ALU.mult).then_inc(e_dve, 1)
                dve.wait_ge(e_act, E_ACT.at(m, "a") - 1)
                nc.vector.scalar_tensor_tensor(k2, kka, -1.0, k, ALU.add, ALU.mult).then_inc(e_dve, 1)
                dve.wait_ge(e_dve, E_DVE.at(m, "k2a") - 1)
                nc.vector.scalar_tensor_tensor(k2, k2, col("c_k_a", m), k, ALU.mult, ALU.add).then_inc(e_dve, 1)
                dve.wait_ge(e_dve, E_DVE.at(m, "k2") - 1)
                nc.vector.scalar_tensor_tensor(NORM[1 - p][:, :], r, col("c_r_k", m), k2, ALU.mult, ALU.mult).then_inc(e_dve, 1)
                dve.wait_ge(e_pe, E_PE.at(m, "bonus") - 1)
                nc.vector.tensor_tensor(rows(BG[p][:, BONUSR, :]), banks((5 * m + 4) % 2), rows(v), ALU.mult).then_inc(e_dve, 1)
                dve.wait_ge(e_act, E_ACT.at(m, "inv") - 1)
                nc.vector.tensor_tensor(kk, kk, x, ALU.mult).then_inc(e_dve, 1)
                dve.wait_ge(e_dve, E_DVE.at(m, "kk") - 1)
                nc.vector.tensor_tensor(kka, kk, kka, ALU.mult).then_inc(e_dve, 1)
            for p in range(2):
                dve.wait_ge(e_out[p], 96)
            for x in ZEROED[9:]:
                nc.vector.memset(x[:, :, :], 0.0)
            step(nc.vector.memset(RUN[:, :], 1.0))
            nc.vector.memset(RUN[:, :].rearrange("p (c t) -> p c t", t=64)[:, :, 0:1], 0.0)
            for p in range(2):
                nc.vector.memset(PX[p][:, :, 0:1], 1.0)
                nc.vector.tensor_copy(ARI[p][:, :, 128:192], pairs_of(PAIR_ID))
            nc.vector.memset(CO[:, :, 0:S0], 0.0)
            nc.vector.memset(CO[:, :, S0 + 64:P0], 0.0)
            nc.vector.engine_nop().then_inc(c_ready, 1)
            dve.wait_ge(c_ready, 2)
            run_chunks(dve, c_step)
            def centre(m):
                dve.wait_ge(f_mean, m + 1)
                o = rows(CO[:, m, :])
                nc.vector.scalar_tensor_tensor(o, banks(0), -1 / 64, o, ALU.mult, ALU.add).then_inc(f_dve, 1)

            centre(0)
            centre(1)
            for m in range(4):
                o = CO[:, m, :]
                dve.wait_ge(f_act, F_ACT.at(m, "inv"))
                nc.vector.scalar_tensor_tensor(o, o, col("c_lnx_g", m), INC[m % 2][:, :], ALU.mult, ALU.mult).then_inc(f_dve, 1)
                dve.wait_ge(f_in[m % 2], 16 * (m // 2) + 16)
                dve.wait_ge(f_dve, F_DVE.at(m, "scaled"))
                nc.vector.scalar_tensor_tensor(o, o, col("c_lnx_b", m), BGL[m % 2][:, BONUSR, :], ALU.add, ALU.add)\
                  .then_inc(f_dve, 1)
                dve.wait_ge(f_dve, F_DVE.at(m, "plus"))
                nc.vector.tensor_tensor(o, o, BGL[m % 2][:, GR, :], ALU.mult).then_inc(f_dve, 1)
                if m < 2:
                    centre(m + 2)
                dve.wait_ge(f_act, F_ACT.at(m, "hi"))
                nc.vector.tensor_tensor(XL[:, m, :], o, XH[:, m, :], ALU.subtract).then_inc(f_dve, 1)
            dve.wait_ge(f_dve, F_DVE.at(3, "lo"))
            dve.sem_inc(mix_ready[1], 4)
            layer_end(1)
            nc.vector.engine_nop().then_inc(kept_ready, 1)


def kernel(**inputs):
    import numpy as np
    import concourse.bacc as bacc
    from concourse import mybir
    from concourse.bass_utils import run_bass_kernel_spmd

    nc = bacc.Bacc("TRN2", target_bir_lowering=False, num_devices=1)
    arrays, io = {}, {}
    for name, v in lay_out(inputs).items():
        arrays["in_" + name] = v
        io[name] = nc.dram_tensor("in_" + name, v.shape, mybir.dt.float32, kind="ExternalInput").ap()
    for name, shape in outputs().items():
        io[name] = nc.dram_tensor("out_" + name, shape, mybir.dt.float32, kind="ExternalOutput").ap()
    build(nc, io, arrays["in_units"].shape[0])
    r = run_bass_kernel_spmd(nc, [arrays], core_ids=[0])
    return gather({name: r.results[0]["out_" + name] for name in outputs()})
```
